# Optimizing a Trainium2 kernel written in Bass

```python
import jax, jax.numpy as jnp
from jax import lax
import numpy as np
import math

D_MODEL = 1024
BATCH = 1
SEQ = 512
DEPTH = 1

CHUNK = 64
EPS = 1e-6
RWKV_HEAD = 64
RWKV_HEADS = 8
RWKV_WIDTH = RWKV_HEADS * RWKV_HEAD
DECAY_LORA = 64
ICLR_LORA = 64
GATE_LORA = 128
GN_EPS = 64e-5
MLSTM_HEADS = 4
MLSTM_DK = 64
MLSTM_DV = 128
MLSTM_QK = MLSTM_HEADS * MLSTM_DK
MLSTM_WIDTH = MLSTM_HEADS * MLSTM_DV
CONV_WIDTH = 4
GATE_SOFTCAP = 15.0
MIX_WIDTH = RWKV_WIDTH + MLSTM_WIDTH
RWKV_COLS = 3 * RWKV_WIDTH + DECAY_LORA + ICLR_LORA + GATE_LORA
MLSTM_COLS = 2 * MLSTM_QK + 2 * MLSTM_WIDTH + 2 * MLSTM_HEADS
IN_COLS = RWKV_COLS + MLSTM_COLS
N_GROUPS = 4
EXPERTS_PER_GROUP = 8
N_EXPERTS = N_GROUPS * EXPERTS_PER_GROUP
TOP_K = 2
D_EXPERT = 256


def rms_norm(x, w):
    xf = x.astype(jnp.float32)
    y = xf * lax.rsqrt(jnp.mean(xf * xf, axis=-1, keepdims=True) + EPS)
    return (y * w.astype(jnp.float32)).astype(x.dtype)

def modulate(xn, shift, scale):
    return xn * (1.0 + scale[:, None, :]) + shift[:, None, :]

def token_shift(u, mu):
    prev = jnp.pad(u, ((0, 0), (1, 0), (0, 0)))[:, :-1]
    return u + (prev - u) * mu

def causal_dwconv(u, w, b):
    ch = u.shape[-1]
    out = lax.conv_general_dilated(
        u, w[:, None, :].astype(u.dtype), window_strides=(1,),
        padding=[(w.shape[0] - 1, 0)], dimension_numbers=('NWC', 'WIO', 'NWC'),
        feature_group_count=ch)
    return out + b

def softcap(z):
    return GATE_SOFTCAP * jnp.tanh(z / GATE_SOFTCAP)

def rwkv7_group(u, mu, w0, w_up, a0, a_up, g_up, k_k, k_a, r_k, gn_w, gn_b):
    bsz, seq, _ = u.shape
    f32 = jnp.float32
    u = token_shift(u, mu)
    o1 = RWKV_WIDTH
    o2 = 2 * RWKV_WIDTH
    o3 = 3 * RWKV_WIDTH
    o4 = o3 + DECAY_LORA
    o5 = o4 + ICLR_LORA
    r, k, v, wd, ad, gd = jnp.split(u, [o1, o2, o3, o4, o5], axis=-1)
    w_log = -jax.nn.softplus(-(w0 + jnp.tanh(wd) @ w_up)) - 0.5
    decay = jnp.exp(-jnp.exp(w_log.astype(f32)))
    a = jax.nn.sigmoid(a0 + ad @ a_up)
    g = jax.nn.sigmoid(gd) @ g_up
    heads = lambda t: t.reshape(bsz, seq, RWKV_HEADS, RWKV_HEAD).astype(f32)
    kk = heads(k * k_k)
    kk = kk / jnp.maximum(jnp.sqrt(jnp.sum(kk * kk, axis=-1, keepdims=True)), 1e-12)
    k = k * (1.0 + (a - 1.0) * k_a)
    r_h, k_h, v_h, w_h, a_h = heads(r), heads(k), heads(v), heads(decay), heads(a)
    b_h = kk * a_h

    def step(state, inp):
        r_t, w_t, k_t, v_t, kk_t, b_t = inp
        sa = jnp.einsum('bhij,bhj->bhi', state, -kk_t)
        state = (state * w_t[:, :, None, :] + sa[..., None] * b_t[:, :, None, :]
                 + v_t[..., None] * k_t[:, :, None, :])
        return state, jnp.einsum('bhij,bhj->bhi', state, r_t)

    xs = tuple(jnp.swapaxes(t, 0, 1) for t in (r_h, w_h, k_h, v_h, kk, b_h))
    state0 = jnp.zeros((bsz, RWKV_HEADS, RWKV_HEAD, RWKV_HEAD), f32)
    _, y = lax.scan(step, state0, xs)
    y = jnp.swapaxes(y, 0, 1)
    mean = jnp.mean(y, axis=-1, keepdims=True)
    var = jnp.mean(jnp.square(y - mean), axis=-1, keepdims=True)
    y = (y - mean) * lax.rsqrt(var + GN_EPS)
    y = y.reshape(bsz, seq, RWKV_WIDTH) * gn_w + gn_b
    bonus = jnp.sum(r_h * k_h * r_k.astype(f32), axis=-1, keepdims=True) * v_h
    y = (y + bonus.reshape(bsz, seq, RWKV_WIDTH)) * g
    return y.astype(u.dtype)

def to_chunks(t):
    bsz, seq, nh = t.shape[:3]
    t = t.reshape((bsz, seq // CHUNK, CHUNK, nh) + t.shape[3:])
    return t.transpose((1, 0, 3, 2) + tuple(range(4, t.ndim)))

def mlstm_chunkwise(q, k, v, log_i, log_f):
    bsz, seq = q.shape[:2]
    f32 = jnp.float32
    causal = jnp.tril(jnp.ones((CHUNK, CHUNK), dtype=bool))

    def step(carry, inp):
        c_mat, n_vec, m = carry
        qc, kc, vc, li, lf = inp
        b = jnp.cumsum(lf, axis=-1)
        d_mat = jnp.where(causal, b[..., :, None] - b[..., None, :] + li[..., None, :], -jnp.inf)
        inter = b + m[..., None]
        m_t = jnp.maximum(inter, jnp.max(d_mat, axis=-1))
        scores = jnp.einsum('bhtd,bhsd->bhts', qc, kc) * jnp.exp(d_mat - m_t[..., None])
        w_inter = jnp.exp(inter - m_t)
        num = (jnp.einsum('bhts,bhsv->bhtv', scores, vc)
               + w_inter[..., None] * jnp.einsum('bhtd,bhdv->bhtv', qc, c_mat))
        den = jnp.sum(scores, axis=-1) + w_inter * jnp.einsum('bhtd,bhd->bht', qc, n_vec)
        h = num / jnp.maximum(jnp.abs(den), jnp.exp(-m_t))[..., None]
        end_log = b[..., -1:] - b + li
        m_new = jnp.maximum(b[..., -1] + m, jnp.max(end_log, axis=-1))
        carry_w = jnp.exp(b[..., -1] + m - m_new)
        kw = kc * jnp.exp(end_log - m_new[..., None])[..., None]
        c_mat = carry_w[..., None, None] * c_mat + jnp.einsum('bhsd,bhsv->bhdv', kw, vc)
        n_vec = carry_w[..., None] * n_vec + jnp.sum(kw, axis=-2)
        return (c_mat, n_vec, m_new), h

    carry0 = (jnp.zeros((bsz, MLSTM_HEADS, MLSTM_DK, MLSTM_DV), f32),
              jnp.zeros((bsz, MLSTM_HEADS, MLSTM_DK), f32),
              jnp.zeros((bsz, MLSTM_HEADS), f32))
    xs = (to_chunks(q * (MLSTM_DK ** -0.5)), to_chunks(k), to_chunks(v),
          to_chunks(log_i), to_chunks(log_f))
    _, h = lax.scan(step, carry0, xs)
    return h.transpose(1, 0, 3, 2, 4).reshape(bsz, seq, MLSTM_HEADS, MLSTM_DV)

def mlstm_group(u, conv_w, conv_b, i_b, f_b, hn_w):
    bsz, seq, _ = u.shape
    f32 = jnp.float32
    o1 = 2 * MLSTM_QK
    o2 = o1 + MLSTM_WIDTH
    o3 = o2 + MLSTM_WIDTH
    o4 = o3 + MLSTM_HEADS
    qk, v, o, ig, fg = jnp.split(u, [o1, o2, o3, o4], axis=-1)
    qk = jax.nn.silu(causal_dwconv(qk, conv_w, conv_b))
    q, k = jnp.split(qk, 2, axis=-1)
    log_i = softcap((ig + i_b).astype(f32))
    log_f = jax.nn.log_sigmoid(softcap((fg + f_b).astype(f32)))
    heads_k = lambda t: t.reshape(bsz, seq, MLSTM_HEADS, MLSTM_DK).astype(f32)
    h = mlstm_chunkwise(heads_k(q), heads_k(k),
                        v.reshape(bsz, seq, MLSTM_HEADS, MLSTM_DV).astype(f32), log_i, log_f)
    h = h * lax.rsqrt(jnp.mean(h * h, axis=-1, keepdims=True) + EPS)
    h = h.reshape(bsz, seq, MLSTM_WIDTH) * hn_w
    return (h * jax.nn.sigmoid(o.astype(f32))).astype(u.dtype)

def hier_moe(xn, w_group, b_group, w_router, b_router, w_gate, w_up, w_down):
    bsz, seq, _ = xn.shape
    f32 = jnp.float32
    g_logits = (xn @ w_group + b_group).astype(f32)
    g_prob = jax.nn.softmax(g_logits, axis=-1)
    g_idx = jnp.argmax(g_logits, axis=-1)
    g_onehot = jax.nn.one_hot(g_idx, N_GROUPS, dtype=f32)
    g_w = jnp.max(g_prob, axis=-1)
    e_logits = (xn @ w_router + b_router).astype(f32).reshape(bsz, seq, N_GROUPS, EXPERTS_PER_GROUP)
    sel = jnp.sum(e_logits * g_onehot[..., None], axis=2)
    top_v, top_i = lax.top_k(sel, TOP_K)
    top_w = jax.nn.softmax(top_v, axis=-1)
    within = jnp.sum(jax.nn.one_hot(top_i, EXPERTS_PER_GROUP, dtype=f32) * top_w[..., None], axis=-2)
    combine = (g_onehot[..., None] * within[..., None, :] * g_w[..., None, None])
    combine = combine.reshape(bsz, seq, N_EXPERTS).astype(xn.dtype)

    def per_sequence(args):
        xs, cw = args
        hg = jnp.einsum('sd,edf->sef', xs, w_gate)
        hu = jnp.einsum('sd,edf->sef', xs, w_up)
        act = jax.nn.silu(hg) * hu * cw[..., None]
        return jnp.einsum('sef,efd->sd', act, w_down)

    return lax.map(per_sequence, (xn, combine))

def first_inputs(seed: int = 0) -> dict:
    key = jax.random.key(seed)
    ks = jax.random.split(key, 32)
    L, D = DEPTH, D_MODEL

    def nrm(i, shape, scale):
        return scale * jax.random.normal(ks[i], shape, jnp.float32)

    def uni(i, shape, lo, hi):
        return jax.random.uniform(ks[i], shape, jnp.float32, lo, hi)

    return {
        'x': nrm(0, (BATCH, SEQ, D), 1.0),
        'c': nrm(1, (BATCH, D), 1.0),
        'ada_w': nrm(2, (L, D, 6 * D), 0.5 * D ** -0.5),
        'ada_b': nrm(3, (L, 6 * D), 0.01),
        'mix_norm_w': 1.0 + nrm(4, (L, D), 0.02),
        'w_in': nrm(5, (L, D, IN_COLS), D ** -0.5),
        'rwkv_mu': uni(6, (L, RWKV_COLS), 0.0, 1.0),
        'rwkv_w0': uni(7, (L, RWKV_WIDTH), -4.0, 0.0),
        'rwkv_w_up': nrm(8, (L, DECAY_LORA, RWKV_WIDTH), DECAY_LORA ** -0.5),
        'rwkv_a0': nrm(9, (L, RWKV_WIDTH), 0.5),
        'rwkv_a_up': nrm(10, (L, ICLR_LORA, RWKV_WIDTH), ICLR_LORA ** -0.5),
        'rwkv_g_up': nrm(11, (L, GATE_LORA, RWKV_WIDTH), GATE_LORA ** -0.5),
        'rwkv_k_k': 0.85 + nrm(12, (L, RWKV_WIDTH), 0.05),
        'rwkv_k_a': 1.0 + nrm(13, (L, RWKV_WIDTH), 0.05),
        'rwkv_r_k': nrm(14, (L, RWKV_HEADS, RWKV_HEAD), 0.1),
        'rwkv_gn_w': 1.0 + nrm(15, (L, RWKV_WIDTH), 0.02),
        'rwkv_gn_b': nrm(16, (L, RWKV_WIDTH), 0.01),
        'mlstm_conv_w': nrm(17, (L, CONV_WIDTH, 2 * MLSTM_QK), CONV_WIDTH ** -0.5),
        'mlstm_conv_b': nrm(18, (L, 2 * MLSTM_QK), 0.01),
        'mlstm_i_b': -3.0 + nrm(19, (L, MLSTM_HEADS), 0.1),
        'mlstm_f_b': jnp.linspace(3.0, 6.0, MLSTM_HEADS, dtype=jnp.float32)[None, :] + nrm(20, (L, MLSTM_HEADS), 0.1),
        'mlstm_hn_w': 1.0 + nrm(21, (L, MLSTM_WIDTH), 0.02),
        'w_out': nrm(22, (L, MIX_WIDTH, D), MIX_WIDTH ** -0.5),
        'ffn_norm_w': 1.0 + nrm(23, (L, D), 0.02),
        'moe_w_group': nrm(24, (L, D, N_GROUPS), D ** -0.5),
        'moe_b_group': nrm(25, (L, N_GROUPS), 0.01),
        'moe_w_router': nrm(26, (L, D, N_EXPERTS), D ** -0.5),
        'moe_b_router': nrm(27, (L, N_EXPERTS), 0.01),
        'moe_w_gate': nrm(28, (L, N_EXPERTS, D, D_EXPERT), D ** -0.5),
        'moe_w_up': nrm(29, (L, N_EXPERTS, D, D_EXPERT), D ** -0.5),
        'moe_w_down': nrm(30, (L, N_EXPERTS, D_EXPERT, D), D_EXPERT ** -0.5),
        'final_norm_w': 1.0 + nrm(31, (D,), 0.02),
    }

def first_block(x, c, ada_w, ada_b, mix_norm_w, w_in, rwkv_mu, rwkv_w0, rwkv_w_up, rwkv_a0,
              rwkv_a_up, rwkv_g_up, rwkv_k_k, rwkv_k_a, rwkv_r_k, rwkv_gn_w, rwkv_gn_b,
              mlstm_conv_w, mlstm_conv_b, mlstm_i_b, mlstm_f_b, mlstm_hn_w, w_out, ffn_norm_w,
              moe_w_group, moe_b_group, moe_w_router, moe_b_router, moe_w_gate, moe_w_up,
              moe_w_down, final_norm_w):
    for l in range(DEPTH):
        mod = jax.nn.silu(c) @ ada_w[l] + ada_b[l]
        sh_m, sc_m, g_m, sh_f, sc_f, g_f = jnp.split(mod, 6, axis=-1)
        h = modulate(rms_norm(x, mix_norm_w[l]), sh_m, sc_m)
        proj = h @ w_in[l]
        y_r = rwkv7_group(proj[..., :RWKV_COLS], rwkv_mu[l], rwkv_w0[l], rwkv_w_up[l], rwkv_a0[l],
                          rwkv_a_up[l], rwkv_g_up[l], rwkv_k_k[l], rwkv_k_a[l], rwkv_r_k[l],
                          rwkv_gn_w[l], rwkv_gn_b[l])
        y_m = mlstm_group(proj[..., RWKV_COLS:], mlstm_conv_w[l], mlstm_conv_b[l], mlstm_i_b[l],
                          mlstm_f_b[l], mlstm_hn_w[l])
        y = jnp.concatenate([y_r, y_m], axis=-1) @ w_out[l]
        x = x + g_m[:, None, :] * y
        h = modulate(rms_norm(x, ffn_norm_w[l]), sh_f, sc_f)
        y = hier_moe(h, moe_w_group[l], moe_b_group[l], moe_w_router[l], moe_b_router[l],
                     moe_w_gate[l], moe_w_up[l], moe_w_down[l])
        x = x + g_f[:, None, :] * y
    return rms_norm(x, final_norm_w)


D_CONV = D_MODEL
CONV_WIDTH_2 = 31
SSM_EXPAND = 2
D_INNER = SSM_EXPAND * D_MODEL
HEAD_DIM = 64
N_SSM_HEADS = D_INNER // HEAD_DIM
D_STATE = 128
SSM_CONV_WIDTH = 4
D_XBC = D_INNER + 2 * N_GROUPS * D_STATE
D_FF = ((8 * D_MODEL // 3 + 255) // 256) * 256
IN_COLS_2 = 2 * D_CONV + D_INNER + D_XBC + N_SSM_HEADS + 2 * D_MODEL
NORM_EPS = 1e-6
LN_EPS = 1e-5


def rms_norm_2(x, w, eps=NORM_EPS):
    xf = x.astype(jnp.float32)
    y = xf * lax.rsqrt(jnp.mean(xf * xf, axis=-1, keepdims=True) + eps)
    return (y * w.astype(jnp.float32)).astype(x.dtype)

def layer_norm(x, w, b, eps=LN_EPS):
    xf = x.astype(jnp.float32)
    mu = jnp.mean(xf, axis=-1, keepdims=True)
    var = jnp.mean(jnp.square(xf - mu), axis=-1, keepdims=True)
    y = (xf - mu) * lax.rsqrt(var + eps)
    return (y * w.astype(jnp.float32) + b.astype(jnp.float32)).astype(x.dtype)

def causal_depthwise_conv(u, w, b):
    k, ch = w.shape
    out = lax.conv_general_dilated(
        u, w[:, None, :].astype(u.dtype), window_strides=(1,), padding=[(k - 1, 0)],
        dimension_numbers=("NWC", "WIO", "NWC"), feature_group_count=ch)
    return out + b.astype(u.dtype)

def adaln(c, w, b):
    mod = jax.nn.silu(c) @ w + b
    shift, scale, gate = jnp.split(mod, 3, axis=-1)
    return shift[:, None, :], scale[:, None, :], gate[:, None, :]

def ssd_chunked_scan(xs, dt, a, bm, cm):
    b, L, H, P = xs.shape
    G, N = bm.shape[2], bm.shape[3]
    J = H // G
    nc = L // CHUNK

    def to_chunks(t):
        return jnp.moveaxis(t.reshape(b, nc, CHUNK, *t.shape[2:]), 1, 0)

    xdt = (xs * dt[..., None]).reshape(b, L, G, J, P)
    da = (dt * a).reshape(b, L, G, J)
    xc, ac, bc, cc = to_chunks(xdt), to_chunks(da), to_chunks(bm), to_chunks(cm)
    causal = jnp.tril(jnp.ones((CHUNK, CHUNK), dtype=bool))[None, :, :, None, None]

    def step(state, inp):
        xk, ak, bk, ck = inp
        acs = jnp.cumsum(ak, axis=1)
        seg = acs[:, :, None] - acs[:, None, :]
        decay = jnp.exp(jnp.where(causal, seg, -jnp.inf))
        cb = jnp.einsum("blgn,bsgn->blsg", ck, bk)
        y_diag = jnp.einsum("blsg,blsgj,bsgjp->blgjp", cb, decay, xk)
        y_off = jnp.einsum("blgn,bgjpn,blgj->blgjp", ck, state, jnp.exp(acs))
        last = acs[:, -1]
        w_in = jnp.exp(last[:, None] - acs)
        new_state = state * jnp.exp(last)[..., None, None] + jnp.einsum(
            "bsgn,bsgj,bsgjp->bgjpn", bk, w_in, xk)
        return new_state, y_diag + y_off

    init = jnp.zeros((b, G, J, P, N), jnp.float32)
    _, ys = lax.scan(step, init, (xc, ac, bc, cc))
    return jnp.moveaxis(ys, 0, 1).reshape(b, L, H, P)

def mixer_sublayer(h, w_in, conv_dw_w, conv_dw_b, conv_ln_w, conv_ln_b, w_conv_out,
                   ssm_conv_w, ssm_conv_b, dt_bias, a_log, d_skip, ssm_norm_w, w_ssm_out, w_out):
    b, L, _ = h.shape
    proj = h @ w_in
    splits = np.cumsum([2 * D_CONV, D_INNER, D_XBC, N_SSM_HEADS, D_MODEL]).tolist()
    conv_in, z, xbc, dt_raw, g_conv, g_ssm = jnp.split(proj, splits, axis=-1)

    a_half, b_half = jnp.split(conv_in, 2, axis=-1)
    u = a_half * jax.nn.sigmoid(b_half)
    u = causal_depthwise_conv(u, conv_dw_w, conv_dw_b)
    u = jax.nn.silu(layer_norm(u, conv_ln_w, conv_ln_b))
    y_conv = u @ w_conv_out

    xbc = jax.nn.silu(causal_depthwise_conv(xbc, ssm_conv_w, ssm_conv_b))
    xs, bm, cm = jnp.split(xbc, [D_INNER, D_INNER + N_GROUPS * D_STATE], axis=-1)
    xs_f = xs.astype(jnp.float32).reshape(b, L, N_SSM_HEADS, HEAD_DIM)
    bm_f = bm.astype(jnp.float32).reshape(b, L, N_GROUPS, D_STATE)
    cm_f = cm.astype(jnp.float32).reshape(b, L, N_GROUPS, D_STATE)
    dt = jax.nn.softplus(dt_raw.astype(jnp.float32) + dt_bias.astype(jnp.float32))
    a = -jnp.exp(a_log.astype(jnp.float32))
    y = ssd_chunked_scan(xs_f, dt, a, bm_f, cm_f) + d_skip.astype(jnp.float32)[:, None] * xs_f
    y = y.reshape(b, L, D_INNER) * jax.nn.silu(z.astype(jnp.float32))
    yg = y.reshape(b, L, N_GROUPS, D_INNER // N_GROUPS)
    yg = yg * lax.rsqrt(jnp.mean(yg * yg, axis=-1, keepdims=True) + NORM_EPS)
    y = (yg.reshape(b, L, D_INNER) * ssm_norm_w.astype(jnp.float32)).astype(h.dtype)
    y_ssm = y @ w_ssm_out

    merged = jax.nn.sigmoid(g_conv) * y_conv + jax.nn.sigmoid(g_ssm) * y_ssm
    return merged @ w_out

def ffn_sublayer(h, w_ffn_in, w_ffn_down):
    gate, up = jnp.split(h @ w_ffn_in, 2, axis=-1)
    return (jax.nn.silu(gate) * up) @ w_ffn_down

def second_inputs(seed: int = 0) -> dict:
    key = jax.random.key(seed)
    ks = jax.random.split(key, 32)
    f32 = jnp.float32
    nrm = lambda k, shape, s: jax.random.normal(k, shape, f32) * s
    gain = lambda k, shape: 1.0 + 0.05 * jax.random.normal(k, shape, f32)
    Ld = DEPTH
    u_dt = jax.random.uniform(ks[13], (Ld, N_SSM_HEADS), f32)
    dt0 = jnp.exp(u_dt * (math.log(0.1) - math.log(0.001)) + math.log(0.001))
    dt_bias = dt0 + jnp.log(-jnp.expm1(-dt0))
    a_log = jnp.log(jax.random.uniform(ks[14], (Ld, N_SSM_HEADS), f32, 1.0, 16.0))
    return {
        "x": jax.random.normal(ks[0], (BATCH, SEQ, D_MODEL), f32),
        "c": jax.random.normal(ks[1], (BATCH, D_MODEL), f32),
        "w_ada_mix": nrm(ks[2], (Ld, D_MODEL, 3 * D_MODEL), D_MODEL ** -0.5),
        "b_ada_mix": nrm(ks[3], (Ld, 3 * D_MODEL), 0.01),
        "norm_mix_w": gain(ks[4], (Ld, D_MODEL)),
        "w_in": nrm(ks[5], (Ld, D_MODEL, IN_COLS_2), D_MODEL ** -0.5),
        "conv_dw_w": nrm(ks[6], (Ld, CONV_WIDTH_2, D_CONV), CONV_WIDTH_2 ** -0.5),
        "conv_dw_b": nrm(ks[7], (Ld, D_CONV), 0.01),
        "conv_ln_w": gain(ks[8], (Ld, D_CONV)),
        "conv_ln_b": nrm(ks[9], (Ld, D_CONV), 0.01),
        "w_conv_out": nrm(ks[10], (Ld, D_CONV, D_MODEL), D_CONV ** -0.5),
        "ssm_conv_w": nrm(ks[11], (Ld, SSM_CONV_WIDTH, D_XBC), SSM_CONV_WIDTH ** -0.5),
        "ssm_conv_b": nrm(ks[12], (Ld, D_XBC), 0.01),
        "dt_bias": dt_bias,
        "a_log": a_log,
        "d_skip": gain(ks[15], (Ld, N_SSM_HEADS)),
        "ssm_norm_w": gain(ks[16], (Ld, D_INNER)),
        "w_ssm_out": nrm(ks[17], (Ld, D_INNER, D_MODEL), D_INNER ** -0.5),
        "w_out": nrm(ks[18], (Ld, D_MODEL, D_MODEL), D_MODEL ** -0.5),
        "w_ada_ffn": nrm(ks[19], (Ld, D_MODEL, 3 * D_MODEL), D_MODEL ** -0.5),
        "b_ada_ffn": nrm(ks[20], (Ld, 3 * D_MODEL), 0.01),
        "norm_ffn_w": gain(ks[21], (Ld, D_MODEL)),
        "w_ffn_in": nrm(ks[22], (Ld, D_MODEL, 2 * D_FF), D_MODEL ** -0.5),
        "w_ffn_down": nrm(ks[23], (Ld, D_FF, D_MODEL), D_FF ** -0.5),
        "final_norm_w": gain(ks[24], (D_MODEL,)),
    }

def second_block(x, c, w_ada_mix, b_ada_mix, norm_mix_w, w_in, conv_dw_w, conv_dw_b, conv_ln_w,
              conv_ln_b, w_conv_out, ssm_conv_w, ssm_conv_b, dt_bias, a_log, d_skip, ssm_norm_w,
              w_ssm_out, w_out, w_ada_ffn, b_ada_ffn, norm_ffn_w, w_ffn_in, w_ffn_down,
              final_norm_w):
    for i in range(DEPTH):
        shift, scale, gate = adaln(c, w_ada_mix[i], b_ada_mix[i])
        h = rms_norm_2(x, norm_mix_w[i]) * (1.0 + scale) + shift
        x = x + gate * mixer_sublayer(
            h, w_in[i], conv_dw_w[i], conv_dw_b[i], conv_ln_w[i], conv_ln_b[i], w_conv_out[i],
            ssm_conv_w[i], ssm_conv_b[i], dt_bias[i], a_log[i], d_skip[i], ssm_norm_w[i],
            w_ssm_out[i], w_out[i])
        shift, scale, gate = adaln(c, w_ada_ffn[i], b_ada_ffn[i])
        h = rms_norm_2(x, norm_ffn_w[i]) * (1.0 + scale) + shift
        x = x + gate * ffn_sublayer(h, w_ffn_in[i], w_ffn_down[i])
    return rms_norm_2(x, final_norm_w)


def setup_inputs(seed=0):
    out = dict(first_inputs(seed))
    for name, value in second_inputs(seed + 1).items():
        if name != "x":
            out[name + "_2"] = value
    return out


def reference(
    x, c, ada_w, ada_b, mix_norm_w, w_in, rwkv_mu, rwkv_w0, rwkv_w_up, rwkv_a0, rwkv_a_up,
    rwkv_g_up, rwkv_k_k, rwkv_k_a, rwkv_r_k, rwkv_gn_w, rwkv_gn_b, mlstm_conv_w, mlstm_conv_b,
    mlstm_i_b, mlstm_f_b, mlstm_hn_w, w_out, ffn_norm_w, moe_w_group, moe_b_group, moe_w_router,
    moe_b_router, moe_w_gate, moe_w_up, moe_w_down, final_norm_w, c_2, w_ada_mix_2, b_ada_mix_2,
    norm_mix_w_2, w_in_2, conv_dw_w_2, conv_dw_b_2, conv_ln_w_2, conv_ln_b_2, w_conv_out_2,
    ssm_conv_w_2, ssm_conv_b_2, dt_bias_2, a_log_2, d_skip_2, ssm_norm_w_2, w_ssm_out_2,
    w_out_2, w_ada_ffn_2, b_ada_ffn_2, norm_ffn_w_2, w_ffn_in_2, w_ffn_down_2, final_norm_w_2,
):
    x = first_block(
        x, c, ada_w, ada_b, mix_norm_w, w_in, rwkv_mu, rwkv_w0, rwkv_w_up, rwkv_a0, rwkv_a_up,
        rwkv_g_up, rwkv_k_k, rwkv_k_a, rwkv_r_k, rwkv_gn_w, rwkv_gn_b, mlstm_conv_w,
        mlstm_conv_b, mlstm_i_b, mlstm_f_b, mlstm_hn_w, w_out, ffn_norm_w, moe_w_group,
        moe_b_group, moe_w_router, moe_b_router, moe_w_gate, moe_w_up, moe_w_down, final_norm_w,
    )
    return second_block(
        x, c_2, w_ada_mix_2, b_ada_mix_2, norm_mix_w_2, w_in_2, conv_dw_w_2, conv_dw_b_2,
        conv_ln_w_2, conv_ln_b_2, w_conv_out_2, ssm_conv_w_2, ssm_conv_b_2, dt_bias_2, a_log_2,
        d_skip_2, ssm_norm_w_2, w_ssm_out_2, w_out_2, w_ada_ffn_2, b_ada_ffn_2, norm_ffn_w_2,
        w_ffn_in_2, w_ffn_down_2, final_norm_w_2,
    )


_drawn_inputs = setup_inputs


def setup_inputs(seed=0):
    import zlib

    import numpy as np

    out = dict(_drawn_inputs(seed))
    spreads = {}
    factors = {'ada_b': 4.462,
     'mix_norm_w': 7.935,
     'rwkv_w_up': 22.04,
     'rwkv_k_k': 200.0,
     'rwkv_k_a': 4.494,
     'rwkv_gn_w': 64.0,
     'rwkv_gn_b': 200.0,
     'mlstm_conv_b': 200.0,
     'mlstm_i_b': 64.0,
     'mlstm_hn_w': 64.0,
     'ffn_norm_w': 31.816,
     'moe_b_group': 64.0,
     'moe_b_router': 64.0,
     'b_ada_mix_2': 5.571,
     'conv_dw_b_2': 8.0,
     'conv_ln_w_2': 3.976,
     'conv_ln_b_2': 35.732,
     'ssm_conv_b_2': 8.0,
     'd_skip_2': 8.0,
     'ssm_norm_w_2': 3.068,
     'b_ada_ffn_2': 4.781,
     'rwkv_w0': 8.0,
     'mlstm_conv_w': 8.0,
     'mlstm_f_b': 8.0}
    for name, (base, spread) in spreads.items():
        noise = np.random.default_rng([zlib.crc32(name.encode()), seed]).standard_normal(out[name].shape)
        drawn = base * np.exp(spread * noise) if base else spread * noise
        out[name] = __import__('jax').numpy.asarray(drawn.astype(out[name].dtype))
    for name, factor in factors.items():
        out[name] = (out[name] * factor).astype(out[name].dtype)
    return out
```

```python
from contextlib import ExitStack

import numpy as np
import concourse.bass as bass
from concourse import mybir

ALU = mybir.AluOpType
ACT = mybir.ActivationFunctionType
F32 = mybir.dt.float32
AX = mybir.AxisListType

P = 128
T = 512
D = 1024
KD = D // P
TT = T // P
RING = 6
UNIT = 8 * P
PAD = 4
TP = T + PAD

RW = 4
R_TILES = 14
M_TILES = 12
C64 = 64
DECAY = float(np.exp(-0.5))
MH = 4
CAP = 15.0
NE = 32
NG = 4
EG = 8
F_TILES = 22
TAPS = 31
UP = 30

COLUMNS = [
    ("c", 8), ("c_2", 8), ("ada_b", 48), ("b_ada_mix_2", 24), ("b_ada_ffn_2", 24),
    ("mix_norm_w", 8), ("ffn_norm_w", 8), ("final_norm_w", 8), ("norm_mix_w_2", 8),
    ("norm_ffn_w_2", 8), ("final_norm_w_2", 8), ("rwkv_mu", 14), ("rwkv_w0", 4), ("rwkv_a0", 4),
    ("rwkv_k_k", 4), ("rwkv_k_a", 4), ("rwkv_r_k", 4), ("rwkv_gn_w", 4), ("rwkv_gn_b", 4),
    ("mlstm_conv_w", 16), ("mlstm_conv_b", 4), ("mlstm_hn_w", 4), ("mlstm_i_b", 1),
    ("mlstm_f_b", 1), ("conv_dw_w_2", TAPS * 8), ("conv_dw_b_2", 8), ("conv_ln_w_2", 8),
    ("conv_ln_b_2", 8), ("ssm_conv_w_2", 4 * 24), ("ssm_conv_b_2", 24), ("ssm_norm_w_2", 16),
    ("d_skip_2", 16), ("dt_bias_2", 4), ("a_log_2", 4),
    ("eps_norm", 1), ("eps_gn", 1), ("eps_ln", 1), ("one", 1),
]
COL, NCOL = {}, 0
for _name, _n in COLUMNS:
    COL[_name] = NCOL
    NCOL += _n

CONSTS = [
    ("ident", 128), ("ones", 128), ("head_ones", 128), ("strict64", 128), ("causal64", 128),
    ("causal", 128), ("levels", 6 * 128), ("same_head", 128), ("reset64", T), ("reset128", T),
    ("sel4", 4 * 128), ("sel4_half", 4 * 128), ("sel8", 8 * 128), ("sel8_pair", 4 * 128),
    ("rank4", 4), ("rank8", 8), ("half_col", 2),
]
CON, NCON = {}, 0
for _name, _n in CONSTS:
    CON[_name] = NCON
    NCON += _n

SMALLS = [("gates", 8 * 8), ("router", 8 * 36), ("dt", 8 * 32), ("lora_up", 512), ("g_up", 512),
          ("router_b", 36)]
SMA, NSMA = {}, 0
for _name, _n in SMALLS:
    SMA[_name] = NSMA
    NSMA += _n

MOD_EARLY = 16
MOD_LATE = 32 + 24 + 24
SH_M, SC_M, G_M, SH_F, SC_F, G_F = (8 * i for i in range(6))
SH_2, SC_2, G_2, SH_3, SC_3, G_3 = (48 + 8 * i for i in range(6))


GOES_ON = {
    "dt_done": ("v_turned", 4),
    "b_turned": ("gate_cols_done", 1),
    "ssm_cols_done": ("max_done", 4),
    "cb_done": ("inter_done", 4),
    "x_turned": ("k_turned", 2),
    "states_done": ("qk_done", 4),
    "acs_done": ("exp_m_done", 4),
    "pair_acs_done": ("num_done", 4),
    "y_off_done": ("den_done", 4),
    "y_diag_done": ("m_state_done", 3),
    "group_sum_done": ("m_sum_done", 4),
    "ln_mean_done": ("lora_done", 12),
    "ln_var_done": ("kk_sum_done", 4),
    "xbc_raw": ("gate_raw", 2),
    "z": ("forget", 1),
    "conv_gate": ("q_k", 4),
    "a_pos": ("v_tok", 4),
    "xbc": ("m_weights", 3),
    "dt_raw": ("exp_m", 1),
    "dt_log": ("decay", 4),
    "end_exp": ("den_abs", 4),
    "b_tok": ("m_square", 4),
    "seg_exp": ("m_std", 4),
    "exp_acs": ("r_lora", 2),
    "group_square": ("rate", 4),
    "group_std": ("r_a", 4),
    "ln_square": ("gate_r", 4),
    "ln_std": ("kk_square", 4),
    "conv_act": ("kk_std", 4),
    "sig": ("cum", 12),
    "ffn_silu": ("r_tok", 16),
    "pads2": ("m_conv", 16),
    "conv_u": ("m_logs", 4),
    "xbc_conv": ("q_head", 4),
    "end_arg": ("gate_cols", 5),
    "conv_y": ("decay_arg", 16),
    "rows": ("q_inter", 4),
    "cb": ("k_tok", 4),
    "x_tok": ("decay_masked", 4),
    "states": ("probs", 4),
    "seg_arg": ("m_state", 3),
    "seg": ("den", 4),
    "y_off": ("m_out", 4),
    "y_skip": ("shift_diff", 14),
    "y_sum": ("shifted", 14),
    "y_gated": ("kk_raw", 4),
    "y_ssm": ("bonus_in", 4),
    "ln_centred": ("kk_unit", 4),
    "ln_scaled": ("rate_sums", 4),
    "merge_conv": ("rate_before", 4),
    "merge_ssm": ("bonus", 4),
    "merged": ("r_ready", 16),
    "x_mix2": ("r_state", 8),
    "ffn_act": ("pairs", 32),
    "x_ffn2": ("inv", 88),
    "norm_ffn_square": ("norm_mix_square", 8),
    "norm_ffn_sum": ("norm_mix_sum", 1),
    "norm_ffn_std": ("norm_mix_std", 1),
    "norm_ffn_scaled": ("norm_mix_scaled", 8),
    "norm_ffn_h": ("norm_mix_h", 8),
    "norm_mix2_square": ("norm_ffn_square", 8),
    "norm_mix2_sum": ("norm_ffn_sum", 1),
    "norm_mix2_std": ("norm_ffn_std", 1),
    "norm_mix2_scaled": ("norm_ffn_scaled", 8),
    "norm_mix2_h": ("norm_ffn_h", 8),
    "norm_ffn2_square": ("norm_mix2_square", 8),
    "norm_ffn2_sum": ("norm_mix2_sum", 1),
    "norm_ffn2_std": ("norm_mix2_std", 1),
    "norm_ffn2_scaled": ("norm_mix2_scaled", 8),
    "norm_ffn2_h": ("norm_mix2_h", 8),
    "norm_out2_square": ("norm_out_square", 8),
    "norm_out2_sum": ("norm_out_sum", 1),
    "norm_out2_std": ("norm_out_std", 1),
    "norm_out2_h": ("norm_out_h", 8),
}


class Steps:

    def __init__(self, engine, semaphore):
        self.engine, self.semaphore, self.count = engine, semaphore, 0

    def mark(self, instruction):
        instruction.then_inc(self.semaphore, 1)
        self.count += 1

    def wait(self):
        self.engine.wait_ge(self.semaphore, self.count)


def two_block_program(nc, x_d, w_d, col_d, con_d, sma_d, combine_d, out_d):
    with ExitStack() as ctx:
        signals = {}

        def S(name):
            while name in GOES_ON:
                name = GOES_ON[name][0]
            if name not in signals:
                signals[name] = ctx.enter_context(nc.semaphore(name))
            return signals[name]

        def at_count(name, n):
            semaphore = S(name)
            while name in GOES_ON:
                name, before = GOES_ON[name]
                n = n + before
            return semaphore, n

        def sb(name, shape):
            return ctx.enter_context(nc.sbuf_tensor(name, shape, F32))

        ring = sb("ring", [P, RING, UNIT])
        xT = sb("xT", [P, KD, T])
        hT = sb("hT", [P, KD, T])
        col = sb("col", [P, NCOL])
        con = sb("con", [P, NCON])
        sma = sb("sma", [P, NSMA])
        mod = sb("mod", [P, 96])
        mod_in = sb("mod_in", [P, 16])
        rstd = sb("rstd", [P, 2, T])
        gain = sb("gain", [P, 8])
        AW = 29900
        arena = sb("arena", [P, AW])
        bank = [ctx.enter_context(nc.psum_tensor(f"bank{b}", [P, T], F32)) for b in range(8)]

        def area(offset, *shape):
            n = int(np.prod(shape))
            assert offset + n <= AW, (offset, n)
            v = arena[:, offset:offset + n]
            if len(shape) == 2:
                v = v.rearrange("p (a b) -> p a b", a=shape[0])
            if len(shape) == 3:
                v = v.rearrange("p (a b c) -> p a b c", a=shape[0], b=shape[1])
            return v

        def column(name, i=0, rows=P):
            return col[0:rows, COL[name] + i:COL[name] + i + 1]

        def constant(name, i=0, n=P, rows=P):
            return con[0:rows, CON[name] + i * n:CON[name] + i * n + n]

        ident, ones, head_ones = constant("ident"), constant("ones"), constant("head_ones")
        gates_w = sma[:, SMA["gates"]:SMA["gates"] + 64].rearrange("p (k n) -> p k n", k=8)
        router_w = sma[:, SMA["router"]:SMA["router"] + 288].rearrange("p (k n) -> p k n", k=8)
        dt_w = sma[:, SMA["dt"]:SMA["dt"] + 256].rearrange("p (k n) -> p k n", k=8)
        lora_up = sma[:, SMA["lora_up"]:SMA["lora_up"] + 512]
        g_up = sma[:, SMA["g_up"]:SMA["g_up"] + 512]
        router_b = sma[:, SMA["router_b"]:SMA["router_b"] + 36]

        m_proj = area(0, M_TILES, TP)
        r_proj = area(6192, R_TILES, TP)
        q_k = area(13416, 4, T)
        v_aug = area(15464, TT, MH, 256)
        k_tok = area(19560, TT, 256)
        q_head = area(20584, MH, T)
        q_inter = area(22632, MH, T)
        gate_row = [area(24680 + T * i, T) for i in range(6)]
        probs = area(27752, 2, MH * P)
        m_state = area(28776, 2, 256)
        m_cols = area(29288, 2 * TT * MH)
        m_carry = area(29320, MH * TT)
        m_small = area(29336, 64)
        y_mlstm = area(2064, 4, T)

        def x_in(t, lo=0, n=T):
            return r_proj[:, t, PAD + lo:PAD + lo + n]

        at = {}


        def column_half(i):
            return con[:, CON["half_col"] + i:CON["half_col"] + i + 1]

        y_rwkv = y_mlstm

        decay = area(0, TT, MH * P)
        g_row, f_row, b_row, max_row, w_row, k_row = gate_row

        def m_rows(row, lo=0, n=T):
            return row[0:MH, lo:lo + n]

        def pe_mlstm(pe, mm, take):
            for tt in range(TT):
                out = take(("v_tok", tt), ("v_tok", tt + 1))
                if tt == 0:
                    pe.wait_ge(*at_count("m_proj", 8))
                for h in range(MH):
                    last = mm(out[:, h * P:h * P + P], m_proj[:, 4 + h, PAD + tt * P:PAD + tt * P + P], ident)
                last.then_inc(S("v_turned"), 1)
            out = take(("gate_cols",), ("gate_cols", 5))
            pe.wait_ge(*at_count("m_weights", 3))
            for i, row in enumerate((g_row, k_row)):
                for tt in range(TT):
                    c = (i * TT + tt) * MH
                    mm(out[:, c:c + MH], m_rows(row, tt * P, P), ident[0:MH, 0:MH])
            for h in range(MH):
                last = mm(out[:, 32 + TT * h:32 + TT * h + TT], constant("sel4", h, rows=MH), m_small[0:MH, 16:16 + TT])
            last.then_inc(S("gate_cols_done"), 1)
            for h in range(MH):
                out = take(("max", h), ("decay_arg", TT * (h + 1)))
                mm(out[:, :], constant("sel4", h, rows=MH), m_rows(max_row)).then_inc(S("max_done"), 1)
            for h in range(MH):
                out = take(("inter", h), ("q_inter", h + 1))
                mm(out[:, :], constant("sel4", h, rows=MH), m_rows(w_row)).then_inc(S("inter_done"), 1)
            pe.wait_ge(*at_count("q_k", 4))
            for i in range(2):
                out = take(("k_tok", i), ("k_tok", 2 * i + 2))
                for tt in range(2):
                    for j in range(2):
                        last = mm(out[:, tt * 256 + j * P:tt * 256 + j * P + P],
                                  q_k[:, 2 + j, (2 * i + tt) * P:(2 * i + tt + 1) * P], ident)
                last.then_inc(S("k_turned"), 1)
            pe.wait_ge(*at_count("q_head", MH))
            pe.wait_ge(*at_count("pads", 3))
            pe.wait_ge(*at_count("exp_m", 1))
            for tt in range(TT):
                tok = slice(tt * P, tt * P + P)
                out = take(("qk", tt), ("probs", tt + 1))
                for h in range(MH):
                    last = mm(out[:, h * P:h * P + P], q_k[:, 2 + h // 2, tok], q_head[:, h, tok])
                last.then_inc(S("qk_done"), 1)
                out = take(("exp_m", tt), ("den", tt + 1))
                for h in range(MH):
                    last = mm(out[:, h * P:h * P + P], constant("sel4", h, rows=MH), m_rows(f_row, tt * P, P))
                last.then_inc(S("exp_m_done"), 1)
                pe.wait_ge(*at_count("probs", tt + 1))
                if tt:
                    pe.wait_ge(*at_count("m_state", tt))
                    pe.wait_ge(*at_count("q_inter", MH))
                else:
                    pe.wait_ge(*at_count("v_tok", TT))
                num = take(("num", tt), ("m_out", tt + 1))
                for h in range(MH):
                    last = mm(num[:, h * P:h * P + P], v_aug[:, tt, h, 0:P], probs[:, tt % 2, h * P:h * P + P], True, tt == 0)
                    if tt:
                        last = mm(num[:, h * P:h * P + P], m_state[:, h // 2, 0:P], q_inter[:, h, tok], False, True)
                last.then_inc(S("num_done"), 1)
                den = take(("den", tt), ("den_abs", tt + 1))
                last = mm(den[:, :], ones, probs[:, tt % 2, :], True, tt == 0)
                if tt:
                    for h in range(MH):
                        last = mm(den[:, h * P:h * P + P], m_state[:, h // 2, P:2 * P], q_inter[:, h, tok], False, True)
                last.then_inc(S("den_done"), 1)
                if tt < TT - 1:
                    out = take(("m_state", tt), ("m_state", tt + 1))
                    pe.wait_ge(*at_count("k_tok", tt + 1))
                    for h in range(MH):
                        r = 64 * (h % 2)
                        last = mm(out[r:r + 64, h // 2 * 256:h // 2 * 256 + 256], k_tok[:, tt, h * 64:h * 64 + 64], v_aug[:, tt, h, :])
                    last.then_inc(S("m_state_done"), 1)
            for h in range(MH):
                out = take(("m_sum", h), ("m_std", h + 1))
                pe.wait_ge(*at_count("m_square", h + 1))
                mm(out[:, :], ones, q_head[:, h, :]).then_inc(S("m_sum_done"), 1)

        def act_mlstm_gates(act, steps):
            act.wait_ge(*at_count("gate_bias", 2))
            for i, row in enumerate((g_row, f_row)):
                act.wait_ge(*at_count("gates_done", i + 1))
                act.activation(m_rows(row), bank[at[("gate", i)]][0:MH, :], ACT.Tanh, bias=m_small[0:MH, i:i + 1],
                               scale=1 / CAP).then_inc(S("gate_raw"), 1)
            act.wait_ge(*at_count("gate_raw", 2))
            steps.mark(act.activation(m_rows(f_row), m_rows(f_row), ACT.Exp, scale=-CAP))
            steps.wait()
            act.activation(m_rows(f_row), m_rows(f_row), ACT.Ln, bias=column("one", rows=MH)).then_inc(S("forget"), 1)

        def act_mlstm(act, steps):
            for t in range(4):
                act.wait_ge(*at_count("m_conv", 16 + t - 3))
                act.activation(q_k[:, t, :], q_k[:, t, :], ACT.Silu, bias=column("mlstm_conv_b", t)).then_inc(S("q_k"), 1)
            for tt in range(TT):
                act.wait_ge(*at_count("v_turned", tt + 1))
                act.activation(v_aug[:, tt, :, 0:P], bank[at[("v_tok", tt)]][:, :].rearrange("p (h v) -> p h v", h=MH),
                               ACT.Copy).then_inc(S("v_tok"), 1)
            act.wait_ge(*at_count("m_logs", 4))
            act.activation(m_rows(w_row), m_rows(w_row), ACT.Exp, scale=-1.0).then_inc(S("m_weights"), 1)
            act.activation(m_rows(k_row), m_rows(k_row), ACT.Exp).then_inc(S("m_weights"), 1)
            act.activation(m_small[0:MH, 16:16 + TT], m_small[0:MH, 8:8 + TT], ACT.Exp, scale=-1.0).then_inc(S("m_weights"), 1)
            act.activation(m_rows(f_row), m_rows(f_row), ACT.Exp).then_inc(S("exp_m"), 1)
            for tt in range(TT):
                act.wait_ge(*at_count("decay_arg", MH * TT))
                act.activation(decay[:, tt, :], decay[:, tt, :], ACT.Exp, scale=-1.0).then_inc(S("decay"), 1)
            for tt in range(TT):
                act.wait_ge(*at_count("den_done", tt + 1))
                if tt:
                    act.wait_ge(*at_count("den", tt))
                act.activation(den_abs[:, :], bank[at[("den", tt)]][:, :], ACT.Abs).then_inc(S("den_abs"), 1)
            for h in range(MH):
                act.wait_ge(*at_count("m_out", TT))
                act.activation(q_head[:, h, :], y_mlstm[:, h, :], ACT.Square).then_inc(S("m_square"), 1)
            for h in range(MH):
                act.wait_ge(*at_count("m_sum_done", h + 1))
                act.activation(q_inter[:, h, :], bank[at[("m_sum", h)]][:, :], ACT.Sqrt, bias=column("eps_norm"),
                               scale=1 / P).then_inc(S("m_std"), 1)

        den_abs = rstd[:, 0, :]
        den_max = rstd[:, 1, :]

        def dve_mlstm(dve, steps):
            dve.wait_ge(*at_count("pads", 2))
            for tap in range(4):
                for t in range(4):
                    src = m_proj[:, t, PAD - 3 + tap:PAD - 3 + tap + T]
                    w = column("mlstm_conv_w", 4 * tap + t)
                    if tap == 0:
                        dve.wait_ge(*at_count("m_proj", t + 1))
                        dve.tensor_scalar(q_k[:, t, :], src, w, None, ALU.mult).then_inc(S("m_conv"), 1)
                    else:
                        dve.wait_ge(*at_count("m_conv", 4 * (tap - 1) + t + 1))
                        dve.scalar_tensor_tensor(q_k[:, t, :], src, w, q_k[:, t, :], ALU.mult, ALU.add).then_inc(S("m_conv"), 1)
            dve.wait_ge(*at_count("forget", 1))
            steps.mark(dve.tensor_tensor_scan(m_rows(b_row), constant("reset128", 0, T, MH), m_rows(f_row), 0.0, ALU.mult, ALU.add))
            steps.mark(dve.memset(m_rows(w_row), 0.0))
            steps.wait()
            steps.mark(dve.scalar_tensor_tensor(m_rows(g_row), m_rows(g_row), CAP, m_rows(b_row), ALU.mult, ALU.add))
            steps.mark(dve.tensor_scalar(w_row[0:MH, P:T:P], b_row[0:MH, P - 1:T - P:P], -1.0, None, ALU.mult))
            steps.wait()
            steps.mark(dve.tensor_tensor_scan(m_rows(max_row), m_rows(w_row), m_rows(g_row), 0.0, ALU.add, ALU.max))
            steps.mark(dve.memset(m_small[0:MH, 4:4 + TT], 0.0))
            steps.wait()
            steps.mark(dve.tensor_tensor(m_small[0:MH, 5:4 + TT], max_row[0:MH, P - 1:T - P:P], b_row[0:MH, P - 1:T - P:P], ALU.subtract))
            steps.wait()

            def by_tile(x):
                return x.rearrange("h (c t) -> h c t", c=TT)

            carried = m_small[0:MH, 4:4 + TT].rearrange("h (c t) -> h c t", t=1).broadcast_to([MH, TT, P])
            m_last = max_row[0:MH, P - 1:T:P]
            last_b = m_last.rearrange("h (c t) -> h c t", t=1).broadcast_to([MH, TT, P])
            dve.tensor_tensor(by_tile(m_rows(w_row)), by_tile(m_rows(max_row)), carried, ALU.subtract).then_inc(S("m_logs"), 1)
            dve.tensor_tensor(by_tile(m_rows(k_row)), by_tile(m_rows(g_row)), last_b, ALU.subtract).then_inc(S("m_logs"), 1)
            dve.tensor_tensor(m_small[0:MH, 8:8 + TT], m_last, m_small[0:MH, 4:4 + TT], ALU.subtract).then_inc(S("m_logs"), 1)
            dve.tensor_tensor(m_rows(f_row), m_rows(b_row), m_rows(max_row), ALU.subtract).then_inc(S("m_logs"), 1)
            for h in range(MH):
                dve.wait_ge(*at_count("q_k", h // 2 + 1))
                dve.tensor_scalar(q_head[:, h, :], q_k[:, h // 2, :], column_half(h % 2), 0.125, ALU.mult, ALU.mult).then_inc(S("q_head"), 1)
            dve.wait_ge(*at_count("unit_done", at[("unit", "mod", 1)]))
            dve.tensor_tensor(mod[:, MOD_EARLY:96], bank[6][:, 0:MOD_LATE],
                              col[:, COL["ada_b"] + MOD_EARLY:COL["ada_b"] + 96], ALU.add).then_inc(S("mod"), 1)
            dve.wait_ge(*at_count("gate_cols_done", 1))
            cols = bank[at[("gate_cols",)]]
            dve.tensor_copy(m_cols[:, :], cols[:, 0:32]).then_inc(S("gate_cols"), 1)
            for h in range(MH):
                r = slice(64 * (h % 2), 64 * (h % 2) + 64)
                dve.tensor_copy(m_carry[r, h // 2 * TT:h // 2 * TT + TT], cols[r, 32 + TT * h:32 + TT * h + TT]).then_inc(S("gate_cols"), 1)
            dve.wait_ge(*at_count("gate_cols", 5))
            dve.wait_ge(*at_count("m_conv", 16))
            for h in range(MH):
                dve.wait_ge(*at_count("max_done", h + 1))
                for tt in range(TT):
                    dve.tensor_scalar(decay[:, tt, h * P:h * P + P], bank[at[("max", h)]][:, tt * P:tt * P + P],
                                      m_cols[:, tt * MH + h:tt * MH + h + 1], 0.0, ALU.subtract, ALU.max).then_inc(S("decay_arg"), 1)
            dve.wait_ge(*at_count("q_head", MH))
            for h in range(MH):
                dve.wait_ge(*at_count("inter_done", h + 1))
                dve.tensor_tensor(q_inter[:, h, :], q_head[:, h, :], bank[at[("inter", h)]][:, :], ALU.mult).then_inc(S("q_inter"), 1)
            for tt in range(TT):
                dve.wait_ge(*at_count("k_turned", tt // 2 + 1))
                dve.tensor_tensor(k_tok[:, tt, :].rearrange("p (h d) -> p h d", h=MH),
                                  bank[at[("k_tok", tt // 2)]][:, tt % 2 * 256:tt % 2 * 256 + 256].rearrange("p (h d) -> p h d", h=MH),
                                  m_cols[:, (TT + tt) * MH:(TT + tt + 1) * MH].rearrange("p (h d) -> p h d", d=1).broadcast_to([P, MH, 64]),
                                  ALU.mult).then_inc(S("k_tok"), 1)
            for tt in range(TT):
                dve.wait_ge(*at_count("decay", tt + 1))
                dve.tensor_tensor(decay[:, tt, :].rearrange("p (h t) -> p h t", h=MH), decay[:, tt, :].rearrange("p (h t) -> p h t", h=MH),
                                  constant("causal").rearrange("p (a t) -> p a t", a=1).broadcast_to([P, MH, P]), ALU.mult).then_inc(S("decay_masked"), 1)
            for tt in range(TT):
                dve.wait_ge(*at_count("decay_masked", tt + 1))
                dve.wait_ge(*at_count("qk_done", tt + 1))
                if tt >= 2:
                    dve.wait_ge(*at_count("den_done", tt - 1))
                dve.tensor_tensor(probs[:, tt % 2, :], bank[at[("qk", tt)]][:, :], decay[:, tt, :], ALU.mult).then_inc(S("probs"), 1)
                if tt < TT - 1:
                    dve.wait_ge(*at_count("m_state_done", tt + 1))
                    new = bank[at[("m_state", tt)]][:, :]
                    if tt == 0:
                        dve.tensor_copy(m_state[:, :, :].rearrange("p a b -> p (a b)"), new).then_inc(S("m_state"), 1)
                    else:
                        dve.wait_ge(*at_count("den_done", tt + 1))
                        for j in range(2):
                            ins = dve.scalar_tensor_tensor(m_state[:, j, :], m_state[:, j, :], m_carry[:, j * TT + tt:j * TT + tt + 1],
                                                           new[:, j * 256:j * 256 + 256], ALU.mult, ALU.add)
                        ins.then_inc(S("m_state"), 1)
                dve.wait_ge(*at_count("den_abs", tt + 1))
                dve.wait_ge(*at_count("exp_m_done", tt + 1))
                dve.tensor_tensor(den_max, den_abs, bank[at[("exp_m", tt)]][:, :], ALU.max).then_inc(S("den"), 1)
                dve.wait_ge(*at_count("den", tt + 1))
                steps.mark(dve.reciprocal(den_max, den_max))
                steps.wait()
                dve.wait_ge(*at_count("num_done", tt + 1))
                dve.tensor_tensor(y_mlstm[:, :, tt * P:tt * P + P], bank[at[("num", tt)]][:, :].rearrange("p (h t) -> p h t", h=MH),
                                  den_max.rearrange("p (h t) -> p h t", h=MH), ALU.mult).then_inc(S("m_out"), 1)
            for h in range(MH):
                dve.wait_ge(*at_count("m_std", h + 1))
                steps.mark(dve.reciprocal(q_inter[:, h, :], q_inter[:, h, :]))
                steps.wait()
                steps.mark(dve.scalar_tensor_tensor(y_mlstm[:, h, :], y_mlstm[:, h, :], column("mlstm_hn_w", h), q_inter[:, h, :], ALU.mult, ALU.mult))
                steps.wait()
                dve.tensor_tensor(y_mlstm[:, h, :], y_mlstm[:, h, :], m_proj[:, 8 + h, PAD:TP], ALU.mult).then_inc(S("y_mlstm"), 1)
        WA_TILE, G_TILE = 12, 13
        rate = area(13416, RW, T)
        b_in = area(15464, RW, T)
        kk = area(17512, RW, T)
        gate_r = area(19560, RW, T)
        bonus = area(21608, RW, T)
        sums = area(23656, RW, T)
        cum_p = area(25704, RW, T)
        cum_inv = area(27752, RW, T)
        v_tok_r, b_tok = area(13416, TT, 512), area(23656, TT, 512)
        k_tok_r, kk_tok = hT[:, 0:4, :], hT[:, 4:8, :]
        r_b = area(25704, 2, 8 * P)
        r_k = area(27752, 2, 8 * P)
        shift_tmp = area(4128, 4, T)
        inv_x, inv_xt = area(0, 4 * P), area(512, 4 * P)
        level_t, prod_t = area(1024, 4 * P), area(4128, 4 * P)
        a_t, bk_t = area(4640, 4 * P), area(5152, 4 * P)
        bv = area(5664, 4, 64)
        V0 = 6192 + 8 * TP
        w_t, u_tok = area(V0, 4, P), area(V0 + 512, 512)
        S0 = 6192 + 12 * TP
        sa = area(S0, 512)
        r_state = area(1536, 4, P)
        chunk_p = rstd[:, 0, :].rearrange("p (r c x) -> p r c x", r=4, c=8)[:, :, :, 0:1]
        y_rwkv = area(6192 + 4 * TP, RW, TP)[:, :, PAD:TP]
        masked_p = gain

        def heads(parity):
            return [parity, parity + 2, parity + 4, parity + 6]

        def pe_rwkv(pe, mm, take):
            pe.wait_ge(*at_count("r_lora", 2))
            for n in range(RW):
                out = take(("decay_up", n), ("rate", n + 1))
                mm(out[:, :], lora_up[0:64, n * P:n * P + P], r_proj[0:64, WA_TILE, PAD:TP]).then_inc(S("lora_done"), 1)
            for n in range(RW):
                out = take(("a_up", n), ("r_a", n + 1))
                mm(out[:, :], lora_up[64:128, n * P:n * P + P], r_proj[64:128, WA_TILE, PAD:TP]).then_inc(S("lora_done"), 1)
            for n in range(RW):
                out = take(("g_up", n), ("gate_r", n + 1))
                mm(out[:, :], g_up[:, n * P:n * P + P], r_proj[:, G_TILE, PAD:TP]).then_inc(S("lora_done"), 1)
            for n in range(RW):
                out = take(("kk_sum", n), ("kk_std", n + 1))
                pe.wait_ge(*at_count("kk_square", n + 1))
                mm(out[:, :], head_ones, sums[:, n, :]).then_inc(S("kk_sum_done"), 1)
            for n in range(RW):
                out = take(("bonus_sum", n), ("bonus", n + 1))
                pe.wait_ge(*at_count("bonus_in", n + 1))
                mm(out[:, :], head_ones, bonus[:, n, :]).then_inc(S("bonus_done"), 1)
            pe.wait_ge(*at_count("r_ready", 4 * RW))
            for i, src in enumerate((r_proj[:, 8:12, PAD:TP], b_in, r_proj[:, 4:8, PAD:TP], kk)):
                for tt in range(TT):
                    out = take(("r_tok", i, tt), ("r_tok", 4 * i + tt + 1))
                    for n in range(RW):
                        last = mm(out[:, n * P:n * P + P], src[:, n, tt * P:tt * P + P], ident)
                    last.then_inc(S("r_turned"), 1)
            for tt in range(TT):
                tok = slice(tt * P, tt * P + P)
                for par in range(2):
                    g = 2 * tt + par
                    rows = slice(64 * par, 64 * par + 64)
                    hs = heads(par)

                    def pairs(key, lhs, rhs, freed):
                        out = take(key, freed)
                        for i, h in enumerate(hs):
                            n = h // 2
                            last = mm(out[:, i * P:i * P + P], lhs[rows, n, tok], rhs[rows, n, tok])
                        last.then_inc(S("pairs_done"), 1)

                    r_f, k_f = r_proj[:, 0:4, PAD:TP], r_proj[:, 4:8, PAD:TP]
                    pairs(("a_t", g), b_in, kk, ("pairs", 4 * g + 1))
                    pairs(("bk_t", g), k_f, kk, ("pairs", 4 * g + 2))
                    pairs(("r_b", g), b_in, r_f, ("pairs", 4 * g + 3))
                    pairs(("r_k", g), k_f, r_f, ("pairs", 4 * g + 4))
                    for l in range(6):
                        pe.wait_ge(*at_count("level", 6 * g + l + 1))
                        if l:
                            pe.wait_ge(*at_count("inv", 11 * g + 2 * l))
                        out = take(("ox", g, l), ("prod", 5 * g + l) if l else ("inv", 11 * g + 2))
                        for i in range(4):
                            c = slice(i * P, i * P + P)
                            last = mm(out[:, c], level_t[:, c], ident if l == 0 else inv_x[:, c])
                        last.then_inc(S("ox_done"), 1)
                        if l == 0:
                            continue
                        pe.wait_ge(*at_count("prod", 5 * g + l))
                        out_t = take(("xox_t", g, l), ("inv", 11 * g + 2 * l + 1))
                        for i in range(4):
                            c = slice(i * P, i * P + P)
                            last = mm(out_t[:, c], prod_t[:, c], inv_xt[:, c])
                        last.then_inc(S("xox_done"), 1)
                        if l == 5:
                            continue
                        out = take(("xox", g, l), ("inv", 11 * g + 2 * l + 2))
                        for i in range(4):
                            c = slice(i * P, i * P + P)
                            last = mm(out[:, c], inv_xt[:, c], prod_t[:, c])
                        last.then_inc(S("xox_done"), 1)
                    pe.wait_ge(*at_count("inv", 11 * g + 11))
                    out = take(("w_t", g), ("w_t", g + 1))
                    for i, h in enumerate(hs):
                        last = mm(out[rows, i * P:i * P + P], kk_tok[:, tt, h * 64:h * 64 + 64], inv_xt[:, i * P:i * P + P])
                    last.then_inc(S("w_done"), 1)
                    out = take(("bv", g), ("bv", g + 1))
                    for i, h in enumerate(hs):
                        last = mm(out[:, i * 64:i * 64 + 64], bk_t[:, i * P:i * P + P], v_tok_r[:, tt, h * 64:h * 64 + 64])
                    last.then_inc(S("bv_done"), 1)
                    pe.wait_ge(*at_count("bv", g + 1))
                    out = take(("u", g), ("u", g + 1))
                    for i, h in enumerate(hs):
                        last = mm(out[:, i * 64:i * 64 + 64], inv_xt[:, i * P:i * P + P], bv[:, i, :])
                    last.then_inc(S("u_done"), 1)
                y_state = None
                for half in range(2):
                    c = 2 * tt + half
                    rows = slice(64 * half, 64 * half + 64)
                    pe.wait_ge(*at_count("r_state", c + 1))
                    if half == 0:
                        pe.wait_ge(*at_count("w_t", 2 * tt + 2))
                    out = take(("ws", c), ("sa", c + 1))
                    for n in range(RW):
                        last = mm(out[:, n * P:n * P + P], w_t[:, n, :], r_state[:, n, :])
                    last.then_inc(S("ws_done"), 1)
                    if half == 0:
                        y_state = take(("y_state", tt), ("y_state", tt + 1))
                    for n in range(RW):
                        last = mm(y_state[:, n * P + 64 * half:n * P + 64 * half + 64], r_state[:, n, :],
                                  r_proj[:, n, PAD + c * C64:PAD + c * C64 + C64])
                    last.then_inc(S("y_state_done"), 1)
                    pe.wait_ge(*at_count("sa", c + 1))
                    if c < 7:
                        out = take(("new_state", c), ("r_state_sum", c + 1))
                        for n in range(RW):
                            cc = slice(n * P, n * P + P)
                            mm(out[:, cc], b_tok[rows, tt, cc], sa[rows, cc], True, False)
                            last = mm(out[:, cc], k_tok_r[rows, tt, cc], v_tok_r[rows, tt, cc], False, True)
                        last.then_inc(S("new_state_done"), 1)
                out = take(("y_in", tt), ("y_raw", tt + 1))
                for h in range(8):
                    cc, o = slice(h // 2 * P, h // 2 * P + P), slice(64 * (h % 2), 64 * (h % 2) + 64)
                    m = (h % 2 * 4 + h // 2) * P
                    mm(out[o, cc], sa[:, h * 64:h * 64 + 64], r_b[:, tt % 2, m:m + P], True, False)
                    last = mm(out[o, cc], v_tok_r[:, tt, h * 64:h * 64 + 64], r_k[:, tt % 2, m:m + P], False, True)
                last.then_inc(S("y_in_done"), 1)
            for n in range(RW):
                out = take(("gn_mean", n), ("gn_centred", n + 1))
                if n == 0:
                    pe.wait_ge(*at_count("y_raw", TT))
                mm(out[:, :], head_ones, y_rwkv[:, n, :]).then_inc(S("gn_mean_done"), 1)
            for n in range(RW):
                out = take(("gn_var", n), ("gn_std", n + 1))
                pe.wait_ge(*at_count("gn_square", n + 1))
                mm(out[:, :], head_ones, rate[:, n, :]).then_inc(S("gn_var_done"), 1)

        def act_rwkv(act, steps):
            act.wait_ge(*at_count("shifted", 2))
            act.activation(r_proj[0:64, WA_TILE, PAD:TP], r_proj[0:64, WA_TILE, PAD:TP], ACT.Tanh).then_inc(S("r_lora"), 1)
            act.activation(x_in(G_TILE), x_in(G_TILE), ACT.Sigmoid).then_inc(S("r_lora"), 1)
            act.wait_ge(*at_count("y_mlstm", MH))
            for n in range(RW):
                act.wait_ge(*at_count("lora_done", n + 1))
                act.activation(rate[:, n, :], bank[at[("decay_up", n)]][:, :], ACT.Sigmoid, bias=column("rwkv_w0", n)).then_inc(S("rate"), 1)
            for n in range(RW):
                act.wait_ge(*at_count("lora_done", RW + n + 1))
                act.activation(b_in[:, n, :], bank[at[("a_up", n)]][:, :], ACT.Sigmoid, bias=column("rwkv_a0", n)).then_inc(S("r_a"), 1)
            for n in range(RW):
                act.wait_ge(*at_count("lora_done", 2 * RW + n + 1))
                act.activation(gate_r[:, n, :], bank[at[("g_up", n)]][:, :], ACT.Copy).then_inc(S("gate_r"), 1)
            for n in range(RW):
                act.wait_ge(*at_count("kk_raw", n + 1))
                act.activation(sums[:, n, :], kk[:, n, :], ACT.Square).then_inc(S("kk_square"), 1)
            for n in range(RW):
                act.wait_ge(*at_count("kk_sum_done", n + 1))
                act.activation(cum_p[:, n, :], bank[at[("kk_sum", n)]][:, :], ACT.Sqrt).then_inc(S("kk_std"), 1)
            for n in range(RW):
                act.wait_ge(*at_count("kk_unit", n + 1))
                act.wait_ge(*at_count("rate_before", n + 1))
                act.activation(cum_p[:, n, :], sums[:, n, :], ACT.Exp, scale=-DECAY).then_inc(S("cum"), 1)
                act.activation(cum_inv[:, n, :], sums[:, n, :], ACT.Exp, scale=DECAY).then_inc(S("cum"), 1)
                act.activation(rate[:, n, :], rate[:, n, :], ACT.Exp, scale=-DECAY).then_inc(S("cum"), 1)
            act.wait_ge(*at_count("bonus", RW))
            act.wait_ge(*at_count("r_ready", 4 * RW))
            for i, dst in enumerate((v_tok_r, b_tok, k_tok_r, kk_tok)):
                for tt in range(TT):
                    act.wait_ge(*at_count("r_turned", 4 * i + tt + 1))
                    act.activation(dst[:, tt, :], bank[at[("r_tok", i, tt)]][:, :], ACT.Copy).then_inc(S("r_tok"), 1)
            for tt in range(TT):
                for par in range(2):
                    g = 2 * tt + par
                    for l in range(1, 6):
                        act.wait_ge(*at_count("ox_done", 6 * g + l + 1))
                        if g or l > 1:
                            act.wait_ge(*at_count("xox_done", 9 * g + 2 * (l - 1)))
                        act.activation(prod_t[:, :], bank[at[("ox", g, l)]][:, :], ACT.Copy).then_inc(S("prod"), 1)
            for n in range(RW):
                act.wait_ge(*at_count("gn_centred", n + 1))
                act.activation(rate[:, n, :], y_rwkv[:, n, :], ACT.Square).then_inc(S("gn_square"), 1)
            for n in range(RW):
                act.wait_ge(*at_count("gn_var_done", n + 1))
                act.activation(cum_p[:, n, :], bank[at[("gn_var", n)]][:, :], ACT.Sqrt, bias=column("eps_gn"), scale=1 / 64).then_inc(S("gn_std"), 1)

        def dve_rwkv(dve, steps):
            order = [12, 13, 4, 5, 6, 7, 0, 1, 2, 3, 8, 9, 10, 11]
            for i, t in enumerate(order):
                dve.wait_ge(*at_count("r_proj", t + 1))
                if i >= 4:
                    dve.wait_ge(*at_count("shifted", i - 3))
                dve.tensor_tensor(shift_tmp[:, i % 4, :], x_in(t, -1), x_in(t), ALU.subtract).then_inc(S("shift_diff"), 1)
                dve.wait_ge(*at_count("shift_diff", i + 1))
                dve.scalar_tensor_tensor(x_in(t), shift_tmp[:, i % 4, :], column("rwkv_mu", t), x_in(t), ALU.mult, ALU.add).then_inc(S("shifted"), 1)
            dve.wait_ge(*at_count("shifted", R_TILES))
            for n in range(RW):
                dve.tensor_scalar(kk[:, n, :], x_in(4 + n), column("rwkv_k_k", n), None, ALU.mult).then_inc(S("kk_raw"), 1)
            steps.mark(dve.tensor_scalar(gain[:, 0:4], col[:, COL["rwkv_k_a"]:COL["rwkv_k_a"] + 4], -1.0, 1.0, ALU.mult, ALU.add))
            steps.wait()
            for n in range(RW):
                dve.wait_ge(*at_count("r_a", n + 1))
                steps.mark(dve.tensor_scalar(shift_tmp[:, n, :], b_in[:, n, :], column("rwkv_k_a", n), gain[:, n:n + 1], ALU.mult, ALU.add))
            steps.wait()
            dve.wait_ge(*at_count("kk_raw", RW))
            for n in range(RW):
                steps.mark(dve.tensor_tensor(x_in(4 + n), x_in(4 + n), shift_tmp[:, n, :], ALU.mult))
            steps.wait()
            for n in range(RW):
                dve.scalar_tensor_tensor(bonus[:, n, :], x_in(n), column("rwkv_r_k", n), x_in(4 + n), ALU.mult, ALU.mult).then_inc(S("bonus_in"), 1)
            for n in range(RW):
                dve.wait_ge(*at_count("kk_std", n + 1))
                steps.mark(dve.tensor_scalar(cum_p[:, n, :], cum_p[:, n, :], 1e-12, None, ALU.max))
            steps.wait()
            for n in range(RW):
                steps.mark(dve.reciprocal(cum_p[:, n, :], cum_p[:, n, :]))
            steps.wait()
            for n in range(RW):
                dve.wait_ge(*at_count("kk_square", n + 1))
                dve.tensor_tensor(kk[:, n, :], kk[:, n, :], cum_p[:, n, :], ALU.mult).then_inc(S("kk_unit"), 1)
            for n in range(RW):
                dve.wait_ge(*at_count("rate", n + 1))
                dve.wait_ge(*at_count("kk_sum_done", n + 1))
                dve.tensor_tensor_scan(sums[:, n, :], constant("reset64", 0, T), rate[:, n, :], 0.0, ALU.mult, ALU.add).then_inc(S("rate_sums"), 1)
            dve.wait_ge(*at_count("rate_sums", RW))
            for n in range(RW):
                dve.tensor_tensor(rate[:, n, :], sums[:, n, :], rate[:, n, :], ALU.subtract).then_inc(S("rate_before"), 1)
            dve.wait_ge(*at_count("kk_unit", RW))
            for n in range(RW):
                steps.mark(dve.tensor_tensor(b_in[:, n, :], b_in[:, n, :], kk[:, n, :], ALU.mult))
            steps.wait()
            for n in range(RW):
                dve.wait_ge(*at_count("bonus_done", n + 1))
                dve.tensor_tensor(bonus[:, n, :], bank[at[("bonus_sum", n)]][:, :], x_in(8 + n), ALU.mult).then_inc(S("bonus"), 1)
            for n in range(RW):
                dve.wait_ge(*at_count("cum", 3 * n + 3))
                for x, f in ((kk, rate), (b_in, cum_inv), (r_proj[:, 4:8, PAD:TP], cum_inv), (r_proj[:, 0:4, PAD:TP], cum_p)):
                    dve.tensor_tensor(x[:, n, :], x[:, n, :], f[:, n, :], ALU.mult).then_inc(S("r_ready"), 1)
            steps.mark(dve.tensor_copy(chunk_p, cum_p[:, :, C64 - 1:T:C64]))
            dve.memset(r_state[:, :, :], 0.0).then_inc(S("r_state"), 1)
            steps.wait()
            dve.wait_ge(*at_count("r_turned", 4 * TT))
            dve.wait_ge(*at_count("r_ready", 4 * RW))

            def masked(dst, key, g, i, mask, heads_view=None):
                dve.wait_ge(*at_count("pairs_done", 4 * g + i + 1))
                dve.tensor_tensor(dst.rearrange("p (h t) -> p h t", h=4), bank[at[(key, g)]][:, :].rearrange("p (h t) -> p h t", h=4),
                                  constant(mask).rearrange("p (a t) -> p a t", a=1).broadcast_to([P, 4, P]), ALU.mult).then_inc(S("pairs"), 1)

            def wide(x):
                return x.rearrange("p (h t) -> p h t", h=4)

            eye = ident.rearrange("p (a t) -> p a t", a=1).broadcast_to([P, 4, P])
            for tt in range(TT):
                for par in range(2):
                    g = 2 * tt + par
                    rows = slice(64 * par, 64 * par + 64)
                    if g:
                        dve.wait_ge(*at_count("level", 6 * g))
                        dve.wait_ge(*at_count("bv_done", g))
                    if tt >= 2 and par == 0:
                        dve.wait_ge(*at_count("y_in_done", tt - 1))
                    masked(a_t[:, :], "a_t", g, 0, "strict64")
                    masked(bk_t[:, :], "bk_t", g, 1, "strict64")
                    masked(r_b[:, tt % 2, par * 512:par * 512 + 512], "r_b", g, 2, "causal64")
                    masked(r_k[:, tt % 2, par * 512:par * 512 + 512], "r_k", g, 3, "causal64")
                    for l in range(6):
                        if l == 0:
                            dve.wait_ge(*at_count("level", 6 * g + 1))
                            if g:
                                dve.wait_ge(*at_count("u_done", g))
                            dve.tensor_tensor(wide(inv_xt[:, :]), eye, wide(level_t[:, :]), ALU.subtract).then_inc(S("inv"), 1)
                            dve.wait_ge(*at_count("ox_done", 6 * g + 1))
                            dve.tensor_tensor(wide(inv_x[:, :]), eye, wide(bank[at[("ox", g, 0)]][:, :]), ALU.subtract).then_inc(S("inv"), 1)
                            continue
                        dve.wait_ge(*at_count("inv", 11 * g + 2 * l))
                        dve.wait_ge(*at_count("xox_done", 9 * g + 2 * l - (l == 5)))
                        dve.tensor_tensor(inv_xt[:, :], inv_xt[:, :], bank[at[("xox_t", g, l)]][:, :], ALU.subtract).then_inc(S("inv"), 1)
                        if l < 5:
                            dve.tensor_tensor(inv_x[:, :], inv_x[:, :], bank[at[("xox", g, l)]][:, :], ALU.subtract).then_inc(S("inv"), 1)
                    dve.wait_ge(*at_count("w_done", g + 1))
                    dve.tensor_copy(w_t[rows, :, :], wide(bank[at[("w_t", g)]][rows, :])).then_inc(S("w_t"), 1)
                    dve.wait_ge(*at_count("bv_done", g + 1))
                    dve.tensor_copy(bv[:, :, :].rearrange("p a b -> p (a b)"), bank[at[("bv", g)]][:, 0:256]).then_inc(S("bv"), 1)
                    dve.wait_ge(*at_count("u_done", g + 1))
                    dve.tensor_copy(u_tok.rearrange("p (n two d) -> p n two d", n=4, two=2)[:, :, par, :],
                                    bank[at[("u", g)]][:, 0:256].rearrange("p (n d) -> p n d", n=4)).then_inc(S("u"), 1)
                dve.wait_ge(*at_count("u", 2 * tt + 2))
                for half in range(2):
                    c = 2 * tt + half
                    rows = slice(64 * half, 64 * half + 64)
                    dve.wait_ge(*at_count("ws_done", c + 1))
                    if tt:
                        dve.wait_ge(*at_count("y_in_done", tt))
                    dve.scalar_tensor_tensor(sa[rows, :], bank[at[("ws", c)]][rows, :], -1.0, u_tok[rows, :], ALU.mult, ALU.subtract).then_inc(S("sa"), 1)
                    if c == 7:
                        continue
                    dve.wait_ge(*at_count("new_state_done", c + 1))
                    dve.wait_ge(*at_count("r_state", c + 1))
                    dve.tensor_tensor(r_state[:, :, :].rearrange("p n i -> p (n i)"), r_state[:, :, :].rearrange("p n i -> p (n i)"),
                                      bank[at[("new_state", c)]][:, :], ALU.add).then_inc(S("r_state_sum"), 1)
                    dve.wait_ge(*at_count("r_state_sum", c + 1))
                    for n in range(RW):
                        ins = dve.scalar_tensor_tensor(r_state[:, n, :], r_state[:, n, :], chunk_p[:, n, c, :], constant("same_head"), ALU.mult, ALU.mult)
                    ins.then_inc(S("r_state"), 1)
                dve.wait_ge(*at_count("y_state_done", 2 * tt + 2))
                dve.tensor_copy(y_rwkv[:, :, tt * P:tt * P + P], wide(bank[at[("y_state", tt)]][:, :])).then_inc(S("y_state"), 1)
                dve.wait_ge(*at_count("y_state", tt + 1))
                dve.wait_ge(*at_count("y_in_done", tt + 1))
                dve.tensor_tensor(y_rwkv[:, :, tt * P:tt * P + P], y_rwkv[:, :, tt * P:tt * P + P], wide(bank[at[("y_in", tt)]][:, :]), ALU.add).then_inc(S("y_raw"), 1)
            dve.wait_ge(*at_count("y_raw", TT))
            for n in range(RW):
                dve.wait_ge(*at_count("gn_mean_done", n + 1))
                dve.scalar_tensor_tensor(y_rwkv[:, n, :], bank[at[("gn_mean", n)]][:, :], -1 / 64, y_rwkv[:, n, :], ALU.mult, ALU.add).then_inc(S("gn_centred"), 1)
            for n in range(RW):
                dve.wait_ge(*at_count("gn_std", n + 1))
                steps.mark(dve.reciprocal(cum_p[:, n, :], cum_p[:, n, :]))
            steps.wait()
            for n in range(RW):
                steps.mark(dve.scalar_tensor_tensor(y_rwkv[:, n, :], y_rwkv[:, n, :], column("rwkv_gn_w", n), cum_p[:, n, :], ALU.mult, ALU.mult))
            steps.wait()
            for n in range(RW):
                steps.mark(dve.scalar_tensor_tensor(y_rwkv[:, n, :], y_rwkv[:, n, :], column("rwkv_gn_b", n), bonus[:, n, :], ALU.add, ALU.add))
            steps.wait()
            for n in range(RW):
                dve.wait_ge(*at_count("gate_r", n + 1))
                dve.tensor_tensor(y_rwkv[:, n, :], y_rwkv[:, n, :], gate_r[:, n, :], ALU.mult).then_inc(S("y_rwkv"), 1)

        def pool_rwkv(pool):
            for g in range(2 * TT):
                pool.wait_ge(*at_count("pairs", 4 * g + 1))
                for l in range(6):
                    if g or l:
                        pool.wait_ge(*at_count("ox_done", 6 * g + l))
                    if l == 1:
                        pool.wait_ge(*at_count("inv", 11 * g + 1))
                    pool.tensor_tensor(level_t[:, :].rearrange("p (h t) -> p h t", h=4), a_t[:, :].rearrange("p (h t) -> p h t", h=4),
                                       constant("levels", l).rearrange("p (a t) -> p a t", a=1).broadcast_to([P, 4, P]), ALU.mult).then_inc(S("level"), 1)
        moe_sum = area(0, KD, T)
        expert_act = area(4096, 2, 2, T)
        expert_silu = area(6144, 2, T)
        expert_w = area(7168, 2, T)
        logits = area(8192, TT, 36)
        one_group, masked_e = area(8400, TT, NG), area(8464, TT * NG * EG)
        chosen = area(8600, TT, EG)
        ranked = area(8640, TT, EG)
        first, second = area(8680, TT, EG), area(8720, TT, EG)
        tiny = area(8760, 12 * TT)
        combine = area(8820, TT, NE)
        combine_t = area(8960, T)
        exp_g = area(9480, TT, NG)

        def expert_unit(e, x):
            return at["moe_units"] + 6 * e - 2 + x

        def pe_moe(pe, mm, take, unit, unit_landed, freed, turn):
            out = take(("router",), ("logits", 1))
            pe.wait_ge(*at_count("norm_ffn_h", KD))
            for tt in range(TT):
                for k in range(KD):
                    last = mm(out[:, tt * 36:tt * 36 + 36], hT[:, k, tt * P:tt * P + P], router_w[:, k, :], k == 0, k == KD - 1)
            last.then_inc(S("router_done"), 1)
            out = take(("combine_t",), ("combine_t", 1))
            pe.wait_ge(*at_count("combine", 1))
            for tt in range(TT):
                last = mm(out[0:NE, tt * P:tt * P + P], combine[:, tt, :], ident)
            last.then_inc(S("combine_turned"), 1)
            u0 = at["moe_units"] = unit[0]

            def weights(e, x):
                x = x + 2 if isinstance(e, int) and e == 0 else x
                q, slot = divmod(u0 - 2 + x, RING)
                pe.wait_ge(*at_count(f"landed{slot}", (e + (q + 1)) * 16))
                return ring[:, slot, :].rearrange("p (k n) -> p k n", k=8)

            def gate_up(e, wait):
                for x in range(4):
                    w = weights(e, x)
                    if wait:
                        pe.wait_ge(*at_count("moe_silu" if x < 2 else "moe_up", (e - 1) * 2 + x % 2 + 1))
                    for k in range(KD):
                        last = mm(bank[x][:, :], w[:, k, :], hT[:, k, :], k == 0, k == KD - 1)
                    last.then_inc(S("unit_done"), 1)

            def down(e, first):
                w = [weights(e, 4), weights(e, 5)]
                pe.wait_ge(*at_count("moe_act", e * 2))
                for n in range(KD):
                    if n >= 4:
                        pe.wait_ge(*at_count("moe_add", (e - 1) * 8 + (n - 3)))
                    elif not first:
                        pe.wait_ge(*at_count("moe_add", (e - 2) * 8 + (n + 5)))
                    par = down.parity
                    for f in range(2):
                        last = mm(bank[4 + n % 4][:, :], w[f][:, n, :], expert_act[:, par, f, :], f == 0, f == 1)
                        if n == KD - 1:
                            last.then_inc(S("unit_done"), 1)
                    if n < KD - 1:
                        last.then_inc(S("down_done"), 1)

            for b in range(8):
                if freed[b] is not None:
                    pe.wait_ge(*at_count(*freed[b]))
            for x in range(4):
                w = weights(0, x)
                for k in range(KD):
                    last = mm(bank[x][:, :], w[:, k, :], hT[:, k, :], k == 0, k == KD - 1)
                last.then_inc(S("unit_done"), 1)
            gate_up(1, True)
            down.parity = 0
            down(1, True)
            with pe.Fori(0, (NE - 2) // 2) as i:
                for j in range(2):
                    e = i * 2 + (2 + j)
                    gate_up(e, True)
                    down.parity = (j + 1) % 2
                    down(e, False)
            q, slot = divmod(u0 + 4 + 6 * (NE - 1), RING)
            down.parity = 1
            pe_last_down(pe, mm, u0)
            unit[0] = u0 + 6 * NE
            freed[:] = [("moe_silu", 2 * NE - 1), ("moe_silu", 2 * NE), ("moe_up", 2 * NE - 1), ("moe_up", 2 * NE)] + [
                ("moe_add", KD * (NE - 1) + n + 1) for n in range(4, 8)]

        def pe_last_down(pe, mm, u0):
            u = u0 + 4 + 6 * (NE - 1)
            w = []
            for f in range(2):
                pe.wait_ge(*at_count(f"landed{(u + f) % RING}", 16 * ((u + f) // RING + 1)))
                w.append(ring[:, (u + f) % RING, :].rearrange("p (k n) -> p k n", k=8))
            pe.wait_ge(*at_count("moe_act", 2 * NE))
            for n in range(KD):
                pe.wait_ge(*at_count("moe_add", KD * (NE - 1) + n - 3))
                for f in range(2):
                    last = mm(bank[4 + n % 4][:, :], w[f][:, n, :], expert_act[:, (NE - 1) % 2, f, :], f == 0, f == 1)
                    if n == KD - 1:
                        last.then_inc(S("unit_done"), 1)
                if n < KD - 1:
                    last.then_inc(S("down_done"), 1)

        def act_moe(act, steps):
            act.wait_ge(*at_count("group_arg", 1))
            act.activation(exp_g[:, :, :], exp_g[:, :, :], ACT.Exp).then_inc(S("group_exp"), 1)
            act.wait_ge(*at_count("second_arg", 1))
            act.activation(tiny[:, 4 * TT:5 * TT], tiny[:, 4 * TT:5 * TT], ACT.Exp).then_inc(S("second_exp"), 1)
            act.wait_ge(*at_count("combine_turned", 1))
            act.activation(combine_t[0:NE, :], bank[at[("combine_t",)]][0:NE, :], ACT.Copy).then_inc(S("combine_t"), 1)
            act.wait_ge(*at_count("combine_t", 1))
            act.dma_start(combine_d, combine_t[0:NE, :]).then_inc(S("combine_stored"), 16)

            def silu(e, wait):
                for f in range(2):
                    act.wait_ge(*at_count("unit_done", e * 6 + (at["moe_units"] - 2 + f + 1 + (0 if wait else 2))))
                    if wait:
                        act.wait_ge(*at_count("moe_act", (e - 1) * 2 + f + 1))
                    act.activation(expert_silu[:, f, :], bank[f][:, :], ACT.Silu).then_inc(S("moe_silu"), 1)

            silu(0, False)
            silu(1, True)
            with act.Fori(0, (NE - 2) // 2) as i:
                for j in range(2):
                    silu(i * 2 + (2 + j), True)

        def dve_moe(dve, steps):
            def wide(x, n):
                return x.rearrange("p (t a) -> p t a", a=1).broadcast_to([P, TT, n])

            gm, gw, g_rank, m1, m2, w1, w2, rk = (tiny[:, i * TT:i * TT + TT] for i in (0, 1, 2, 3, 4, 5, 6, 7))
            dve.wait_ge(*at_count("router_done", 1))
            dve.tensor_tensor(logits[:, :, :], bank[at[("router",)]][:, 0:4 * 36].rearrange("p (t n) -> p t n", t=TT),
                              router_b.rearrange("p (a n) -> p a n", a=1).broadcast_to([P, TT, 36]), ALU.add).then_inc(S("logits"), 1)
            dve.wait_ge(*at_count("logits", 1))
            gl = logits[:, :, 0:NG]

            def step(ins):
                steps.mark(ins)
                steps.wait()

            def first_max(dst, src, top, ranks, n):
                step(dve.tensor_tensor(dst, src, wide(top, n), ALU.is_equal))
                step(dve.tensor_tensor(dst, dst, ranks.rearrange("p (a n) -> p a n", a=1).broadcast_to([P, TT, n]), ALU.mult))
                step(dve.tensor_reduce(rk, dst, AX.X, ALU.max))
                step(dve.tensor_tensor(dst, dst, wide(rk, n), ALU.is_equal))

            step(dve.tensor_reduce(gm, gl, AX.X, ALU.max))
            dve.tensor_tensor(exp_g[:, :, :], gl, wide(gm, NG), ALU.subtract).then_inc(S("group_arg"), 1)
            first_max(one_group[:, :, :], gl, gm, constant("rank4", 0, 4), NG)
            step(dve.tensor_tensor(masked_e.rearrange("p (t g e) -> p t g e", t=TT, g=NG), logits[:, :, NG:].rearrange("p t (g e) -> p t g e", g=NG),
                                   one_group.rearrange("p t (g a) -> p t g a", a=1).broadcast_to([P, TT, NG, EG]), ALU.mult))
            step(dve.tensor_reduce(chosen[:, :, :], masked_e.rearrange("p (t g e) -> p t e g", t=TT, g=NG), AX.X, ALU.add))
            step(dve.tensor_reduce(m1, chosen[:, :, :], AX.X, ALU.max))
            first_max(first[:, :, :], chosen[:, :, :], m1, constant("rank8", 0, 8), EG)
            step(dve.scalar_tensor_tensor(ranked[:, :, :], first[:, :, :], -3.0e38, chosen[:, :, :], ALU.mult, ALU.add))
            step(dve.tensor_reduce(m2, ranked[:, :, :], AX.X, ALU.max))
            first_max(second[:, :, :], ranked[:, :, :], m2, constant("rank8", 0, 8), EG)
            dve.tensor_tensor(m2, m2, m1, ALU.subtract).then_inc(S("second_arg"), 1)
            dve.wait_ge(*at_count("group_exp", 1))
            step(dve.tensor_reduce(gw, exp_g[:, :, :], AX.X, ALU.add))
            dve.wait_ge(*at_count("second_exp", 1))
            step(dve.tensor_scalar(w1, m2, 1.0, None, ALU.add))
            step(dve.tensor_tensor(w1, w1, gw, ALU.mult))
            step(dve.reciprocal(w1, w1))
            step(dve.tensor_tensor(w2, w1, m2, ALU.mult))
            step(dve.tensor_tensor(first[:, :, :], first[:, :, :], wide(w1, EG), ALU.mult))
            step(dve.tensor_tensor(second[:, :, :], second[:, :, :], wide(w2, EG), ALU.mult))
            step(dve.tensor_tensor(first[:, :, :], first[:, :, :], second[:, :, :], ALU.add))
            dve.tensor_tensor(combine.rearrange("p t (g e) -> p t g e", g=NG), one_group.rearrange("p t (g a) -> p t g a", a=1).broadcast_to([P, TT, NG, EG]),
                              first.rearrange("p t (a e) -> p t a e", a=1).broadcast_to([P, TT, NG, EG]), ALU.mult).then_inc(S("combine"), 1)

            def weigh(e, par, wait):
                base = at["moe_units"] - 2 + (0 if wait else 2)
                for f in range(2):
                    dve.wait_ge(*at_count("unit_done", e * 6 + (base + 2 + f + 1)))
                    dve.wait_ge(*at_count("moe_silu", e * 2 + (f + 1)))
                    dve.tensor_tensor(expert_silu[:, f, :], expert_silu[:, f, :], bank[2 + f][:, :], ALU.mult).then_inc(S("moe_up"), 1)
                for f in range(2):
                    if f == 0:
                        dve.wait_ge(*at_count(f"expert_w{par}", weigh.landed))
                    dve.wait_ge(*at_count("moe_up", e * 2 + (f + 1)))
                    dve.tensor_tensor(expert_act[:, par, f, :], expert_silu[:, f, :], expert_w[:, par, :], ALU.mult).then_inc(S("moe_act"), 1)

            def add(e, first_one, last_one=False):
                for n in range(KD):
                    if n < KD - 1:
                        dve.wait_ge(*at_count("down_done", (e - 1) * 7 + (n + 1)))
                    else:
                        dve.wait_ge(*at_count("unit_done", e * 6 + (at["moe_units"] - 2 + 6) if not last_one else at["moe_units"] + 6 * NE))
                    b = bank[4 + n % 4][:, :]
                    if first_one:
                        dve.tensor_copy(moe_sum[:, n, :], b).then_inc(S("moe_add"), 1)
                    else:
                        if n == 0:
                            dve.wait_ge(*at_count("moe_add", (e - 1) * 8))
                        dve.tensor_tensor(moe_sum[:, n, :], moe_sum[:, n, :], b, ALU.add).then_inc(S("moe_add"), 1)

            weigh.landed = 16
            weigh(0, 0, False)
            weigh(1, 1, True)
            add(1, True)
            with dve.Fori(0, (NE - 2) // 2) as i:
                for j in range(2):
                    weigh.landed = i * 16 + 32
                    weigh(i * 2 + (2 + j), j, True)
                    add(i * 2 + (2 + j), False)
            add(NE, False, last_one=True)
            dve.wait_ge(*at_count("moe_add", KD * NE))

        def pool_moe(pool):
            pool.wait_ge(*at_count("combine_stored", 16))
            for e in range(2):
                pool.dma_start(expert_w[:, e, :], combine_d[e:e + 1, :].broadcast_to([P, T])).then_inc(S(f"expert_w{e}"), 16)
            with pool.Fori(0, (NE - 2) // 2) as i:
                for j in range(2):
                    pool.wait_ge(*at_count("moe_act", i * 4 + 2 * (j + 1)))
                    pool.dma_start(expert_w[:, j, :], combine_d[bass.ds(i * 2 + (2 + j), 1), :].broadcast_to([P, T])).then_inc(S(f"expert_w{j}"), 16)
        SH = 8
        y_ssm = area(0, 16, T)
        conv_u = area(8192, 2, UP + T)
        conv_y = area(9276, KD, T)
        xbc_raw = area(13372, 6, TP)
        xbc = area(16468, 6, T)
        x_dt = area(19540, TT, 512)
        x_w = area(21588, 2, 512)
        b_tok2 = area(22612, TT, P)
        states = area(23124, TT - 1, 512)
        cb = area(24660, TT, P)
        seg = area(25172, 2, T)
        exp_acs = area(26196, T)
        row_acs, row_dtw = area(26708, T), area(27220, T)
        row_tmp, row_dt = rstd[:, 0, :], rstd[:, 1, :]
        ssm_cols = area(27732, 3 * TT * SH)
        last_exp = area(27828, SH * TT)
        a_pos = area(27860, NG)
        ln_square = area(13372, KD, T)
        merged = area(19540, KD, T)
        sig = area(25172, 2, T)
        G_UNITS = 14
        DT, DTW, ACS = range(3)

        def ssm_col(which, tt):
            c = (which * TT + tt) * SH
            return ssm_cols[:, c:c + SH]

        def channel(g, i):
            return 4 * g + i if i < 4 else (16 if i == 4 else 20) + g

        def pe_mix2(pe, mm, take, project, h_tiles):
            counts = [list(range(1, KD + 1))]

            def group_in(g):
                first = counts.pop() if counts else None
                for i in range(6):
                    project(("xbc", g, i), ("xbc_raw", 6 * g + i + 1), h_tiles, "norm_mix2_h", first if i == 0 else None)
                for i in range(4):
                    project(("z", g, i), ("z", 4 * g + i + 1), h_tiles, None, None)
                for i in range(2):
                    project(("conv_a", g, i), ("conv_u", 2 * g + i + 1), h_tiles, None, None)
                    project(("conv_b", g, i), ("conv_gate", 2 * g + i + 1), h_tiles, None, None)

            group_in(0)
            for g in range(NG):
                out = take(("dt", g), ("dt_raw", g + 1))
                for k in range(KD):
                    last = mm(out[0:SH, :], dt_w[:, k, SH * g:SH * g + SH], h_tiles[k], k == 0, k == KD - 1)
                last.then_inc(S("dt_done"), 1)
                if g < NG - 1:
                    group_in(g + 1)
                pe.wait_ge(*at_count("xbc", 6 * g + 6))
                out = take(("b_tok", g), ("b_tok", g + 1))
                for tt in range(TT):
                    last = mm(out[:, tt * P:tt * P + P], xbc[:, 4, tt * P:tt * P + P], ident)
                last.then_inc(S("b_turned"), 1)
                out = take(("ssm_cols", g), ("ssm_cols", 2 * g + 2))
                pe.wait_ge(*at_count("rows", g + 1))
                for which, row in ((DT, row_dt), (DTW, row_dtw), (ACS, row_acs)):
                    for tt in range(TT):
                        c = (which * TT + tt) * SH
                        mm(out[:, c:c + SH], row[0:SH, tt * P:tt * P + P], ident[0:SH, 0:SH])
                for h in range(SH):
                    last = mm(out[:, 96 + TT * h:96 + TT * h + TT], constant("sel8", h, rows=SH), row_acs[0:SH, P - 1:T:P])
                last.then_inc(S("ssm_cols_done"), 1)
                out = take(("cb", g), ("cb", g + 1))
                for tt in range(TT):
                    last = mm(out[:, tt * P:tt * P + P], xbc[:, 4, tt * P:tt * P + P], xbc[:, 5, tt * P:tt * P + P])
                last.then_inc(S("cb_done"), 1)
                for tt in range(TT):
                    out = take(("x_tok", g, tt), ("x_tok", 2 * (TT * g + tt) + 2))
                    for i in range(4):
                        last = mm(out[:, i * P:i * P + P], xbc[:, i, tt * P:tt * P + P], ident)
                    last.then_inc(S("x_turned"), 1)
                    if tt == 0:
                        pe.wait_ge(*at_count("b_tok", g + 1))
                    if tt < TT - 1:
                        pe.wait_ge(*at_count("x_tok", 2 * (TT * g + tt) + 2))
                        out = take(("states", g, tt), ("states", 3 * g + tt + 1))
                        mm(out[:, :], b_tok2[:, tt, :], x_w[:, tt % 2, :]).then_inc(S("states_done"), 1)
                for j in range(SH // 2):
                    n = 4 * g + j
                    diag = None
                    for o in range(2):
                        h, m = 2 * j + o, SH * g + 2 * j + o
                        out = take(("acs", m), ("seg_arg", TT * (m + 1)))
                        mm(out[:, :], constant("sel8", h, rows=SH), row_acs[0:SH, :]).then_inc(S("acs_done"), 1)
                    if j == 0:
                        pe.wait_ge(*at_count("states", 3 * g + 3))
                    out = take(("exp_acs", n), ("exp_acs", n + 1))
                    mm(out[:, :], constant("sel8_pair", j, rows=SH), row_acs[0:SH, :]).then_inc(S("pair_acs_done"), 1)
                    off = take(("y_off", n), ("y_off", n + 1))
                    for tt in range(1, TT):
                        last = mm(off[:, tt * P:tt * P + P], states[:, tt - 1, j * P:j * P + P], xbc[:, 5, tt * P:tt * P + P])
                    last.then_inc(S("y_off_done"), 1)
                    diag = take(("y_diag", n), ("y_skip", n + 1))
                    for o in range(2):
                        h, m = 2 * j + o, SH * g + 2 * j + o
                        pe.wait_ge(*at_count("seg", m + 1))
                        for tt in range(TT):
                            last = mm(diag[64 * o:64 * o + 64, tt * P:tt * P + P], x_dt[:, tt, h * 64:h * 64 + 64], seg[:, m % 2, tt * P:tt * P + P])
                        last.then_inc(S("y_diag_done"), 1)
                out = take(("group_sum", g), ("group_std", g + 1))
                for j in range(4):
                    pe.wait_ge(*at_count("group_square", 4 * g + j + 1))
                    last = mm(out[:, :], ones, xbc[:, j, :], j == 0, j == 3)
                last.then_inc(S("group_sum_done"), 1)
            out = take(("ln_mean",), ("ln_centred", KD))
            pe.wait_ge(*at_count("conv_y", KD * TAPS))
            for k in range(KD):
                last = mm(out[:, :], ones, conv_y[:, k, :], k == 0, k == KD - 1)
            last.then_inc(S("ln_mean_done"), 1)
            out = take(("ln_var",), ("ln_std", 1))
            for k in range(KD):
                pe.wait_ge(*at_count("ln_square", k + 1))
                last = mm(out[:, :], ones, ln_square[:, k, :], k == 0, k == KD - 1)
            last.then_inc(S("ln_var_done"), 1)
            conv_tiles = [conv_y[:, k, :] for k in range(KD)]
            ssm_tiles = [y_ssm[:, k, :] for k in range(16)]
            for n in range(KD):
                project(("g_conv", n), ("sig", 2 * n + 1), h_tiles, None, None)
                project(("conv_out", n), ("merge_conv", n + 1), conv_tiles, "conv_act", list(range(1, KD + 1)) if n == 0 else None)
                project(("g_ssm", n), ("sig", 2 * n + 2), h_tiles, None, None)
                if n == 0:
                    pe.wait_ge(*at_count("y_ssm", 16))
                project(("ssm_out", n), ("merge_ssm", n + 1), ssm_tiles, None, None)
            merged_tiles = [merged[:, k, :] for k in range(KD)]
            for n in range(KD):
                project(("w_out2", n), ("x_mix2", n + 1), merged_tiles, "merged", list(range(1, KD + 1)) if n == 0 else None)

        def act_mix2(act, steps):
            def group_out(g):
                for i in range(6):
                    act.wait_ge(*at_count("unit_done", at[("unit", "xbc", g, i)]))
                    if g:
                        act.wait_ge(*at_count("xbc_conv", 24 * g))
                    elif i == 0:
                        act.wait_ge(*at_count("pads2", 2))
                    act.activation(xbc_raw[:, i, PAD:TP], bank[at[("xbc", g, i)]][:, :], ACT.Copy).then_inc(S("xbc_raw"), 1)
                for i in range(4):
                    act.wait_ge(*at_count("unit_done", at[("unit", "z", g, i)]))
                    act.activation(y_ssm[:, 4 * g + i, :], bank[at[("z", g, i)]][:, :], ACT.Silu).then_inc(S("z"), 1)
                for i in range(2):
                    act.wait_ge(*at_count("unit_done", at[("unit", "conv_b", g, i)]))
                    if g:
                        act.wait_ge(*at_count("conv_y", 2 * g * TAPS))
                    act.activation(conv_u[:, i, UP:UP + T], bank[at[("conv_b", g, i)]][:, :], ACT.Sigmoid).then_inc(S("conv_gate"), 1)

            act.wait_ge(*at_count("x_moe", KD))
            act.activation(a_pos[0:SH, :], col[0:SH, COL["a_log_2"]:COL["a_log_2"] + NG], ACT.Exp).then_inc(S("a_pos"), 1)
            group_out(0)
            for g in range(NG):
                for i in range(6):
                    act.wait_ge(*at_count("xbc_conv", 24 * g + 18 + i + 1))
                    act.activation(xbc[:, i, :], xbc[:, i, :], ACT.Silu, bias=column("ssm_conv_b_2", channel(g, i))).then_inc(S("xbc"), 1)
                act.wait_ge(*at_count("dt_done", g + 1))
                if g == 0:
                    act.wait_ge(*at_count("norm_mix2_h", KD))
                act.activation(row_dt[0:SH, :], bank[at[("dt", g)]][0:SH, :], ACT.Identity, bias=column("dt_bias_2", g, SH)).then_inc(S("dt_raw"), 1)
                act.wait_ge(*at_count("dt_raw", g + 1))
                steps.mark(act.activation(row_tmp[0:SH, :], row_dt[0:SH, :], ACT.Abs))
                steps.wait()
                steps.mark(act.activation(row_tmp[0:SH, :], row_tmp[0:SH, :], ACT.Exp, scale=-1.0))
                steps.wait()
                act.activation(row_tmp[0:SH, :], row_tmp[0:SH, :], ACT.Ln, bias=column("one", rows=SH)).then_inc(S("dt_log"), 1)
                act.wait_ge(*at_count("end_arg", g + 1))
                act.activation(row_tmp[0:SH, :], row_tmp[0:SH, :], ACT.Exp).then_inc(S("end_exp"), 1)
                if g < NG - 1:
                    group_out(g + 1)
                act.wait_ge(*at_count("b_turned", g + 1))
                act.activation(b_tok2[:, :, :].rearrange("p a b -> p (a b)"), bank[at[("b_tok", g)]][:, :], ACT.Copy).then_inc(S("b_tok"), 1)
                act.wait_ge(*at_count("ssm_cols_done", g + 1))
                act.wait_ge(*at_count("ssm_cols", 2 * g + 1))
                act.activation(last_exp[:, :], bank[at[("ssm_cols", g)]][:, 96:96 + SH * TT], ACT.Exp, scale=-1.0).then_inc(S("ssm_cols"), 1)
                for j in range(4):
                    n = 4 * g + j
                    for o in range(2):
                        m = 2 * n + o
                        act.wait_ge(*at_count("seg_arg", TT * (m + 1)))
                        act.activation(seg[:, m % 2, :], seg[:, m % 2, :], ACT.Exp, scale=-1.0).then_inc(S("seg_exp"), 1)
                    act.wait_ge(*at_count("pair_acs_done", n + 1))
                    if n:
                        act.wait_ge(*at_count("y_sum", n))
                    act.activation(exp_acs, bank[at[("exp_acs", n)]][:, :], ACT.Exp, scale=-1.0).then_inc(S("exp_acs"), 1)
                for j in range(4):
                    act.wait_ge(*at_count("y_gated", 4 * g + j + 1))
                    act.activation(xbc[:, j, :], y_ssm[:, 4 * g + j, :], ACT.Square).then_inc(S("group_square"), 1)
                act.wait_ge(*at_count("group_sum_done", g + 1))
                act.activation(exp_acs, bank[at[("group_sum", g)]][:, :], ACT.Sqrt, bias=column("eps_norm"), scale=1 / 512).then_inc(S("group_std"), 1)
            for k in range(KD):
                act.wait_ge(*at_count("ln_centred", k + 1))
                act.activation(ln_square[:, k, :], conv_y[:, k, :], ACT.Square).then_inc(S("ln_square"), 1)
            act.wait_ge(*at_count("ln_var_done", 1))
            act.activation(rstd[:, 0, :], bank[at[("ln_var",)]][:, :], ACT.Sqrt, bias=column("eps_ln"), scale=1 / D).then_inc(S("ln_std"), 1)
            for k in range(KD):
                act.wait_ge(*at_count("ln_scaled", k + 1))
                act.activation(conv_y[:, k, :], conv_y[:, k, :], ACT.Silu, bias=column("conv_ln_b_2", k)).then_inc(S("conv_act"), 1)
            for n in range(KD):
                act.wait_ge(*at_count("unit_done", at[("unit", "g_conv", n)]))
                if n:
                    act.wait_ge(*at_count("merge_conv", n))
                act.activation(sig[:, 0, :], bank[at[("g_conv", n)]][:, :], ACT.Sigmoid).then_inc(S("sig"), 1)
                act.wait_ge(*at_count("unit_done", at[("unit", "g_ssm", n)]))
                if n:
                    act.wait_ge(*at_count("merged", n))
                act.activation(sig[:, 1, :], bank[at[("g_ssm", n)]][:, :], ACT.Sigmoid).then_inc(S("sig"), 1)

        def dve_mix2(dve, steps):
            def wide(x, n):
                return x.rearrange("p (h a) -> p h a", a=1).broadcast_to([P, x.shape[1], n])

            def by_head(x):
                return x.rearrange("p (h d) -> p h d", h=SH)

            dve.memset(xbc_raw[:, :, 0:PAD], 0.0).then_inc(S("pads2"), 1)
            dve.memset(conv_u[:, :, 0:UP], 0.0).then_inc(S("pads2"), 1)

            def gate_u(g):
                for i in range(2):
                    dve.wait_ge(*at_count("conv_gate", 2 * g + i + 1))
                    dve.wait_ge(*at_count("unit_done", at[("unit", "conv_a", g, i)]))
                    dve.tensor_tensor(conv_u[:, i, UP:UP + T], conv_u[:, i, UP:UP + T], bank[at[("conv_a", g, i)]][:, :], ALU.mult).then_inc(S("conv_u"), 1)

            dve.wait_ge(*at_count("pads2", 2))
            for g in range(NG):
                if g:
                    dve.wait_ge(*at_count("group_sum_done", g))
                for tap in range(4):
                    for i in range(6):
                        src = xbc_raw[:, i, PAD - 3 + tap:PAD - 3 + tap + T]
                        w = column("ssm_conv_w_2", 24 * tap + channel(g, i))
                        if tap == 0:
                            dve.wait_ge(*at_count("xbc_raw", 6 * g + i + 1))
                            dve.tensor_scalar(xbc[:, i, :], src, w, None, ALU.mult).then_inc(S("xbc_conv"), 1)
                        else:
                            dve.wait_ge(*at_count("xbc_conv", 24 * g + 6 * (tap - 1) + i + 1))
                            dve.scalar_tensor_tensor(xbc[:, i, :], src, w, xbc[:, i, :], ALU.mult, ALU.add).then_inc(S("xbc_conv"), 1)
                if g == 0:
                    dve.wait_ge(*at_count("a_pos", 1))
                    gate_u(0)
                dve.wait_ge(*at_count("dt_log", g + 1))
                steps.mark(dve.scalar_tensor_tensor(row_dt[0:SH, :], row_dt[0:SH, :], 0.0, row_tmp[0:SH, :], ALU.max, ALU.add))
                steps.wait()
                steps.mark(dve.tensor_scalar(row_tmp[0:SH, :], row_dt[0:SH, :], a_pos[0:SH, g:g + 1], None, ALU.mult))
                steps.wait()
                steps.mark(dve.tensor_tensor_scan(row_acs[0:SH, :], constant("reset128", 0, T, SH), row_tmp[0:SH, :], 0.0, ALU.mult, ALU.add))
                steps.wait()
                tiles = lambda x: x[0:SH, :].rearrange("h (c t) -> h c t", c=TT)
                dve.tensor_tensor(tiles(row_tmp), tiles(row_acs), row_acs[0:SH, P - 1:T:P].rearrange("h (c t) -> h c t", t=1).broadcast_to([SH, TT, P]),
                                  ALU.subtract).then_inc(S("end_arg"), 1)
                dve.wait_ge(*at_count("conv_u", 2 * g + 2))
                for tap in range(TAPS):
                    for i in range(2):
                        k = 2 * g + i
                        src = conv_u[:, i, tap:tap + T]
                        w = column("conv_dw_w_2", 8 * tap + k)
                        if tap == 0:
                            dve.tensor_scalar(conv_y[:, k, :], src, w, column("conv_dw_b_2", k), ALU.mult, ALU.add).then_inc(S("conv_y"), 1)
                        else:
                            dve.wait_ge(*at_count("conv_y", 2 * (g * TAPS + tap - 1) + i + 1))
                            dve.scalar_tensor_tensor(conv_y[:, k, :], src, w, conv_y[:, k, :], ALU.mult, ALU.add).then_inc(S("conv_y"), 1)
                dve.wait_ge(*at_count("end_exp", g + 1))
                dve.tensor_tensor(row_dtw[0:SH, :], row_tmp[0:SH, :], row_dt[0:SH, :], ALU.mult).then_inc(S("rows"), 1)
                if g < NG - 1:
                    dve.wait_ge(*at_count("conv_y", 2 * (g + 1) * TAPS))
                    gate_u(g + 1)
                dve.wait_ge(*at_count("ssm_cols_done", g + 1))
                dve.tensor_copy(ssm_cols[:, :], bank[at[("ssm_cols", g)]][:, 0:96]).then_inc(S("ssm_cols"), 1)
                dve.wait_ge(*at_count("cb_done", g + 1))
                dve.tensor_tensor(cb[:, :, :], bank[at[("cb", g)]][:, :].rearrange("p (c t) -> p c t", c=TT),
                                  constant("causal").rearrange("p (a t) -> p a t", a=1).broadcast_to([P, TT, P]), ALU.mult).then_inc(S("cb"), 1)
                dve.wait_ge(*at_count("ssm_cols", 2 * g + 2))
                for tt in range(TT):
                    dve.wait_ge(*at_count("x_turned", TT * g + tt + 1))
                    src = by_head(bank[at[("x_tok", g, tt)]][:, :])
                    dve.tensor_tensor(by_head(x_dt[:, tt, :]), src, wide(ssm_col(DT, tt), 64), ALU.mult).then_inc(S("x_tok"), 1)
                    if tt >= 2:
                        dve.wait_ge(*at_count("states_done", 3 * g + tt - 1))
                    dve.tensor_tensor(by_head(x_w[:, tt % 2, :]), src, wide(ssm_col(DTW, tt), 64), ALU.mult).then_inc(S("x_tok"), 1)
                    if tt == TT - 1:
                        continue
                    if tt:
                        dve.wait_ge(*at_count("states", 3 * g + tt))
                        steps.mark(dve.tensor_tensor(by_head(states[:, tt, :]), by_head(states[:, tt - 1, :]),
                                                     wide(last_exp[:, tt:SH * TT:TT], 64), ALU.mult))
                        steps.wait()
                    dve.wait_ge(*at_count("states_done", 3 * g + tt + 1))
                    new = bank[at[("states", g, tt)]][:, :]
                    if tt:
                        dve.tensor_tensor(states[:, tt, :], states[:, tt, :], new, ALU.add).then_inc(S("states"), 1)
                    else:
                        dve.tensor_copy(states[:, 0, :], new).then_inc(S("states"), 1)

                def decays(m):
                    dve.wait_ge(*at_count("acs_done", m + 1))
                    if m >= 2:
                        dve.wait_ge(*at_count("y_diag_done", m - 1))
                    for tt in range(TT):
                        dve.tensor_scalar(seg[:, m % 2, tt * P:tt * P + P], bank[at[("acs", m)]][:, tt * P:tt * P + P],
                                          ssm_col(ACS, tt)[:, m % SH:m % SH + 1], 0.0, ALU.subtract, ALU.max).then_inc(S("seg_arg"), 1)

                def weighted(m):
                    dve.wait_ge(*at_count("seg_exp", m + 1))
                    dve.wait_ge(*at_count("cb", g + 1))
                    dve.tensor_tensor(seg[:, m % 2, :], seg[:, m % 2, :], cb[:, :, :].rearrange("p a b -> p (a b)"), ALU.mult).then_inc(S("seg"), 1)

                for j in range(4):
                    n = 4 * g + j
                    decays(2 * n)
                    decays(2 * n + 1)
                    weighted(2 * n)
                    weighted(2 * n + 1)
                    dve.wait_ge(*at_count("exp_acs", n + 1))
                    dve.wait_ge(*at_count("y_off_done", n + 1))
                    dve.tensor_tensor(exp_acs[:, P:T], exp_acs[:, P:T], bank[at[("y_off", n)]][:, P:T], ALU.mult).then_inc(S("y_off"), 1)
                    dve.wait_ge(*at_count("y_diag_done", 2 * n + 2))
                    dve.scalar_tensor_tensor(xbc[:, j, :], xbc[:, j, :], column("d_skip_2", n), bank[at[("y_diag", n)]][:, :],
                                             ALU.mult, ALU.add).then_inc(S("y_skip"), 1)
                    dve.wait_ge(*at_count("y_skip", n + 1))
                    dve.wait_ge(*at_count("y_off", n + 1))
                    dve.tensor_tensor(xbc[:, j, P:T], xbc[:, j, P:T], exp_acs[:, P:T], ALU.add).then_inc(S("y_sum"), 1)
                    dve.wait_ge(*at_count("y_sum", n + 1))
                    dve.tensor_tensor(y_ssm[:, n, :], y_ssm[:, n, :], xbc[:, j, :], ALU.mult).then_inc(S("y_gated"), 1)
                dve.wait_ge(*at_count("group_std", g + 1))
                steps.mark(dve.reciprocal(exp_acs, exp_acs))
                steps.wait()
                for j in range(4):
                    n = 4 * g + j
                    dve.scalar_tensor_tensor(y_ssm[:, n, :], y_ssm[:, n, :], column("ssm_norm_w_2", n), exp_acs, ALU.mult, ALU.mult).then_inc(S("y_ssm"), 1)
            dve.wait_ge(*at_count("ln_mean_done", 1))
            for k in range(KD):
                dve.scalar_tensor_tensor(conv_y[:, k, :], bank[at[("ln_mean",)]][:, :], -1 / D, conv_y[:, k, :], ALU.mult, ALU.add).then_inc(S("ln_centred"), 1)
            dve.wait_ge(*at_count("ln_std", 1))
            steps.mark(dve.reciprocal(rstd[:, 1, :], rstd[:, 0, :]))
            steps.wait()
            for k in range(KD):
                dve.scalar_tensor_tensor(conv_y[:, k, :], conv_y[:, k, :], column("conv_ln_w_2", k), rstd[:, 1, :], ALU.mult, ALU.mult).then_inc(S("ln_scaled"), 1)
            for n in range(KD):
                dve.wait_ge(*at_count("sig", 2 * n + 1))
                dve.wait_ge(*at_count("unit_done", at[("unit", "conv_out", n)]))
                dve.tensor_tensor(merged[:, n, :], sig[:, 0, :], bank[at[("conv_out", n)]][:, :], ALU.mult).then_inc(S("merge_conv"), 1)
                dve.wait_ge(*at_count("sig", 2 * n + 2))
                dve.wait_ge(*at_count("unit_done", at[("unit", "ssm_out", n)]))
                dve.tensor_tensor(sig[:, 1, :], sig[:, 1, :], bank[at[("ssm_out", n)]][:, :], ALU.mult).then_inc(S("merge_ssm"), 1)
                dve.wait_ge(*at_count("merge_ssm", n + 1))
                dve.wait_ge(*at_count("merge_conv", n + 1))
                dve.tensor_tensor(merged[:, n, :], merged[:, n, :], sig[:, 1, :], ALU.add).then_inc(S("merged"), 1)
            for n in range(KD):
                dve.wait_ge(*at_count("unit_done", at[("unit", "w_out2", n)]))
                dve.scalar_tensor_tensor(xT[:, n, :], bank[at[("w_out2", n)]][:, :], mod[:, G_2 + n:G_2 + n + 1], xT[:, n, :],
                                         ALU.mult, ALU.add).then_inc(S("x_mix2"), 1)
        ffn_act = area(0, F_TILES, T)
        ffn_silu = area(11264, 2, T)

        def pe_ffn2(pe, mm, take, project, h_tiles):
            for n in range(F_TILES):
                first = list(range(1, KD + 1)) if n == 0 else None
                project(("ffn_gate", n), ("ffn_silu", n + 1), h_tiles, "norm_ffn2_h", first)
                project(("ffn_up", n), ("ffn_act", n + 1), h_tiles, None, None)
            act_tiles = [ffn_act[:, k, :] for k in range(F_TILES)]
            for n in range(KD):
                project(("ffn_down", n), ("x_ffn2", n + 1), act_tiles, "ffn_act", list(range(1, F_TILES + 1)) if n == 0 else None)

        def act_ffn2(act, steps):
            for n in range(F_TILES):
                act.wait_ge(*at_count("unit_done", at[("unit", "ffn_gate", n)]))
                if n >= 2:
                    act.wait_ge(*at_count("ffn_act", n - 1))
                act.activation(ffn_silu[:, n % 2, :], bank[at[("ffn_gate", n)]][:, :], ACT.Silu).then_inc(S("ffn_silu"), 1)

        def dve_ffn2(dve, steps):
            for n in range(F_TILES):
                dve.wait_ge(*at_count("ffn_silu", n + 1))
                dve.wait_ge(*at_count("unit_done", at[("unit", "ffn_up", n)]))
                dve.tensor_tensor(ffn_act[:, n, :], ffn_silu[:, n % 2, :], bank[at[("ffn_up", n)]][:, :], ALU.mult).then_inc(S("ffn_act"), 1)
            for n in range(KD):
                dve.wait_ge(*at_count("unit_done", at[("unit", "ffn_down", n)]))
                dve.scalar_tensor_tensor(xT[:, n, :], bank[at[("ffn_down", n)]][:, :], mod[:, G_3 + n:G_3 + n + 1], xT[:, n, :],
                                         ALU.mult, ALU.add).then_inc(S("x_ffn2"), 1)
        def act_square(act, name, k):
            act.activation(hT[:, k, :], xT[:, k, :], ACT.Square).then_inc(S(name + "_square"), 1)

        def act_std(act, name):
            act.wait_ge(*at_count(name + "_sum", 1))
            act.activation(rstd[:, 0, :], bank[at[(name, "sum")]][:, :], ACT.Sqrt, bias=column("eps_norm"), scale=1 / D).then_inc(S(name + "_std"), 1)

        def act_shift(act, name, shift):
            for k in range(KD):
                act.wait_ge(*at_count(name + "_scaled", k + 1))
                act.activation(hT[:, k, :], hT[:, k, :], ACT.Identity, bias=mod[:, shift + k:shift + k + 1]).then_inc(S(name + "_h"), 1)

        def dve_norm(dve, steps, name, weight, scale, in_place=False):
            if scale is not None:
                steps.mark(dve.scalar_tensor_tensor(gain[:, :], mod[:, scale:scale + KD], 1.0,
                                                    col[:, COL[weight]:COL[weight] + KD], ALU.add, ALU.mult))
            dve.wait_ge(*at_count(name + "_std", 1))
            steps.mark(dve.reciprocal(rstd[:, 1, :], rstd[:, 0, :]))
            steps.wait()
            for k in range(KD):
                g = gain[:, k:k + 1] if scale is not None else column(weight, k)
                dst = xT if in_place else hT
                dve.scalar_tensor_tensor(dst[:, k, :], xT[:, k, :], g, rstd[:, 1, :], ALU.mult, ALU.mult).then_inc(
                    S(name + ("_scaled" if scale is not None else "_h")), 1)

        block = ctx.enter_context(nc.Block())

        @block.tensor
        def _(pe):
            unit = [0]
            turn = [0]
            freed = [None] * 8

            def mm(out, lhsT, rhs, start=True, stop=True):
                return pe.matmul(out, lhsT, rhs, start=start, stop=stop, skip_group_check=True)

            def take(key, freed_by, b=None):
                if b is None:
                    b = turn[0]
                    turn[0] = (b + 1) % 8
                if freed[b] is not None:
                    pe.wait_ge(*at_count(*freed[b]))
                freed[b] = freed_by
                at[key] = b
                return bank[b]

            def unit_landed():
                u = unit[0]
                unit[0] += 1
                pe.wait_ge(*at_count(f"landed{u % RING}", 16 * (u // RING + 1)))
                return ring[:, u % RING, :].rearrange("p (k n) -> p k n", k=8)

            def project(key, freed_by, rhs, ready, counts):
                out = None
                n = len(rhs)
                for u in range(-(-n // 8)):
                    w = unit_landed()
                    if out is None:
                        out = take(key, freed_by)
                    for k in range(min(8, n - 8 * u)):
                        i = 8 * u + k
                        if counts:
                            pe.wait_ge(*at_count(ready, counts[i]))
                        last = mm(out[:, :], w[:, k, :], rhs[i], i == 0, i == n - 1)
                    last.then_inc(S("unit_done"), 1)
                at[("unit",) + key] = unit[0]

            def norm_sum(name, freed_by):
                out = take((name, "sum"), freed_by)
                for k in range(KD):
                    pe.wait_ge(*at_count(name + "_square", k + 1))
                    last = mm(out[:, :], ones, hT[:, k, :], k == 0, k == KD - 1)
                last.then_inc(S(name + "_sum"), 1)

            def modulation(key, units, out, first):
                for n in range(units):
                    w = unit_landed()
                    c = 0 if first + n < 48 else 8
                    for k in range(8):
                        last = mm(out[:, n:n + 1], w[:, k, :], mod_in[:, c + k:c + k + 1], k == 0, k == 7)
                    last.then_inc(S("unit_done"), 1)
                at[("unit",) + key] = unit[0]

            pe.wait_ge(*at_count("mod_in", 1))
            out = take(("mod", 0), ("mod", 1), b=7)
            modulation(("mod", 0), MOD_EARLY, out, 0)
            pe.wait_ge(*at_count("consts_landed", 16))
            norm_sum("norm_mix", ("norm_mix_std", 1))
            h_tiles = [hT[:, k, :] for k in range(KD)]

            def h_counts(first):
                return list(range(1, KD + 1)) if first else None

            for t in range(M_TILES):
                project(("m", t), ("m_proj", t + 1), h_tiles, "norm_mix_h", h_counts(t == 0))
            pe.wait_ge(*at_count("smalls_landed", 16))
            for i in range(2):
                out = take(("gate", i), ("gate_raw", i + 1))
                for k in range(KD):
                    last = mm(out[0:MH, :], gates_w[:, k, 4 * i:4 * i + 4], h_tiles[k], k == 0, k == 7)
                last.then_inc(S("gates_done"), 1)
            for t in range(R_TILES):
                project(("r", t), ("r_proj", t + 1), h_tiles, None, None)
            out = take(("mod", 1), ("mod", 2), b=6)
            modulation(("mod", 1), MOD_LATE, out, MOD_EARLY)
            pe_mlstm(pe, mm, take)
            pe_rwkv(pe, mm, take)
            y_tiles = [y_rwkv[:, k, :] for k in range(4)] + [y_mlstm[:, k, :] for k in range(4)]
            pe.wait_ge(*at_count("y_mlstm", MH))
            pe.wait_ge(*at_count("y_rwkv", RW))
            for n in range(KD):
                project(("w_out", n), ("x_mix", n + 1), y_tiles, None, None)
            norm_sum("norm_ffn", ("norm_ffn_std", 1))
            pe_moe(pe, mm, take, unit, unit_landed, freed, turn)
            norm_sum("norm_out", ("norm_out_std", 1))
            norm_sum("norm_mix2", ("norm_mix2_std", 1))
            pe_mix2(pe, mm, take, project, h_tiles)
            norm_sum("norm_ffn2", ("norm_ffn2_std", 1))
            pe_ffn2(pe, mm, take, project, h_tiles)
            norm_sum("norm_out2", ("norm_out2_std", 1))

        @block.sync
        def _(sp):
            sp.dma_start(col[:, :], col_d).then_inc(S("columns_landed"), 16)
            units = w_d.shape[0]
            for u in range(RING):
                sp.dma_start(ring[:, u, :], w_d[u]).then_inc(S(f"landed{u}"), 16)
                if u == 0:
                    sp.dma_start(xT[:, :, :].rearrange("p a b -> p (a b)"), x_d).then_inc(S("x_landed"), 16)
                    sp.dma_start(con[:, :], con_d).then_inc(S("consts_landed"), 16)
                    sp.dma_start(sma[:, :], sma_d).then_inc(S("smalls_landed"), 16)
            total = units
            rounds = total // RING
            with sp.Fori(1, rounds) as i:
                for u in range(RING):
                    sp.wait_ge(*at_count("unit_done", (i - 1) * RING + u + 1))
                    sp.dma_start(ring[:, u, :], w_d[i * RING + u]).then_inc(S(f"landed{u}"), 16)
            for u in range(total % RING):
                sp.wait_ge(*at_count("unit_done", (rounds - 1) * RING + u + 1))
                sp.dma_start(ring[:, u, :], w_d[rounds * RING + u]).then_inc(S(f"landed{u}"), 16)
            for k in range(KD):
                sp.wait_ge(*at_count("norm_out2_h", k + 1))
                sp.dma_start(out_d[:, k * T:k * T + T], hT[:, k, :]).then_inc(S("stored"), 16)
            sp.wait_ge(*at_count("stored", 16 * KD))
        @block.scalar
        def _(act):
            steps = Steps(act, S("scalar_step"))
            act.wait_ge(*at_count("columns_landed", 16))
            act.activation(mod_in[:, :], col[:, 0:16], ACT.Silu).then_inc(S("mod_in"), 1)
            act.wait_ge(*at_count("x_landed", 16))
            for k in range(KD):
                act_square(act, "norm_mix", k)
            act_std(act, "norm_mix")
            act_shift(act, "norm_mix", SH_M)
            act.wait_ge(*at_count("pads", 1))
            for t in range(M_TILES):
                act.wait_ge(*at_count("unit_done", at[("unit", "m", t)]))
                act.activation(m_proj[:, t, PAD:TP], bank[at[("m", t)]][:, :], ACT.Sigmoid if t >= 8 else ACT.Copy).then_inc(S("m_proj"), 1)
            act_mlstm_gates(act, steps)
            act.wait_ge(*at_count("pads", 2))
            for t in range(R_TILES):
                act.wait_ge(*at_count("unit_done", at[("unit", "r", t)]))
                act.activation(x_in(t), bank[at[("r", t)]][:, :], ACT.Copy).then_inc(S("r_proj"), 1)
            act_mlstm(act, steps)
            act_rwkv(act, steps)
            for k in range(KD):
                act.wait_ge(*at_count("x_mix", k + 1))
                act_square(act, "norm_ffn", k)
            act_std(act, "norm_ffn")
            act_shift(act, "norm_ffn", SH_F)
            act_moe(act, steps)
            for k in range(KD):
                act.wait_ge(*at_count("x_moe", k + 1))
                act_square(act, "norm_out", k)
            act_std(act, "norm_out")
            for k in range(KD):
                act.wait_ge(*at_count("norm_out_h", k + 1))
                act_square(act, "norm_mix2", k)
            act_std(act, "norm_mix2")
            act_shift(act, "norm_mix2", SH_2)
            act_mix2(act, steps)
            for k in range(KD):
                act.wait_ge(*at_count("x_mix2", k + 1))
                act_square(act, "norm_ffn2", k)
            act_std(act, "norm_ffn2")
            act_shift(act, "norm_ffn2", SH_3)
            act_ffn2(act, steps)
            for k in range(KD):
                act.wait_ge(*at_count("x_ffn2", k + 1))
                act_square(act, "norm_out2", k)
            act_std(act, "norm_out2")

        @block.vector
        def _(dve):
            steps = Steps(dve, S("vector_step"))
            dve.wait_ge(*at_count("columns_landed", 16))
            for i, name in enumerate(("mlstm_i_b", "mlstm_f_b")):
                dve.tensor_scalar(m_small[0:MH, i:i + 1], column(name, rows=MH), 1 / CAP, None, ALU.mult).then_inc(S("gate_bias"), 1)
            dve.wait_ge(*at_count("unit_done", at[("unit", "mod", 0)]))
            dve.tensor_tensor(mod[:, 0:MOD_EARLY], bank[7][:, 0:MOD_EARLY], col[:, COL["ada_b"]:COL["ada_b"] + MOD_EARLY], ALU.add).then_inc(S("mod"), 1)
            dve.wait_ge(*at_count("mod", 1))
            dve_norm(dve, steps, "norm_mix", "mix_norm_w", SC_M)
            dve_mlstm(dve, steps)
            dve_rwkv(dve, steps)
            dve.wait_ge(*at_count("mod", 2))
            for n in range(KD):
                dve.wait_ge(*at_count("unit_done", at[("unit", "w_out", n)]))
                dve.scalar_tensor_tensor(xT[:, n, :], bank[at[("w_out", n)]][:, :], mod[:, G_M + n:G_M + n + 1], xT[:, n, :],
                                         ALU.mult, ALU.add).then_inc(S("x_mix"), 1)
            dve_norm(dve, steps, "norm_ffn", "ffn_norm_w", SC_F)
            dve_moe(dve, steps)
            for k in range(KD):
                dve.scalar_tensor_tensor(xT[:, k, :], moe_sum[:, k, :], mod[:, G_F + k:G_F + k + 1], xT[:, k, :],
                                         ALU.mult, ALU.add).then_inc(S("x_moe"), 1)
            dve.wait_ge(*at_count("x_moe", KD))
            dve_norm(dve, steps, "norm_out", "final_norm_w", None, in_place=True)
            dve.wait_ge(*at_count("norm_out_h", KD))
            dve_norm(dve, steps, "norm_mix2", "norm_mix_w_2", SC_2)
            dve_mix2(dve, steps)
            dve.wait_ge(*at_count("x_mix2", KD))
            dve_norm(dve, steps, "norm_ffn2", "norm_ffn_w_2", SC_3)
            dve_ffn2(dve, steps)
            dve.wait_ge(*at_count("x_ffn2", KD))
            dve_norm(dve, steps, "norm_out2", "final_norm_w_2", None)

        @block.gpsimd
        def _(pool):
            pool.memset(m_proj[:, :, 0:PAD], 0.0).then_inc(S("pads"), 1)
            pool.memset(r_proj[:, :, 0:PAD], 0.0).then_inc(S("pads"), 1)
            pool.memset(v_aug[:, :, :, P:2 * P], 1.0).then_inc(S("pads"), 1)
            pool_rwkv(pool)
            pool_moe(pool)



def _units(w, columns=None):
    w = w if columns is None else w[:, columns]
    k, n = w.shape
    kt = k // P
    units = -(-kt // 8)
    t = w.reshape(kt, P, n // P, P).transpose(2, 1, 0, 3)
    if kt % 8:
        t = np.concatenate([t, np.zeros((n // P, P, units * 8 - kt, P), w.dtype)], axis=2)
    return t.reshape(n // P, P, units, UNIT).transpose(0, 2, 1, 3).reshape(-1, P, UNIT)


def weight_stream(a):
    ada, w_in, w2 = a["ada_w"][0], a["w_in"][0], a["w_in_2"][0]
    parts = [_units(ada[:, :2048])]
    parts += [_units(w_in, slice(1792, 1792 + 1536)), _units(w_in, slice(0, 1792))]
    parts += [_units(ada[:, 2048:]), _units(a["w_ada_mix_2"][0]), _units(a["w_ada_ffn_2"][0])]
    parts += [_units(a["w_out"][0])]
    down = a["moe_w_down"][0].reshape(NE, 2, P, D)
    gate, up = ([_units(a[n][0, e]) for e in range(NE)] for n in ("moe_w_gate", "moe_w_up"))
    parts += [gate[0], up[0]]
    for e in range(1, NE):
        parts += [gate[e], up[e], down[e - 1]]
    parts += [down[NE - 1]]
    x0, z0 = 4096, 2048
    for g in range(NG):
        parts += [_units(w2, slice(x0 + 512 * g, x0 + 512 * g + 512)),
                  _units(w2, slice(x0 + 2048 + 128 * g, x0 + 2048 + 128 * g + 128)),
                  _units(w2, slice(x0 + 2560 + 128 * g, x0 + 2560 + 128 * g + 128)),
                  _units(w2, slice(z0 + 512 * g, z0 + 512 * g + 512))]
        ab = [_units(w2, slice(1024 * h + 128 * (2 * g + i), 1024 * h + 128 * (2 * g + i) + 128))
              for i in range(2) for h in range(2)]
        parts += ab
    g0 = x0 + 3072 + 32
    g_conv, g_ssm = _units(w2, slice(g0, g0 + 1024)), _units(w2, slice(g0 + 1024, g0 + 2048))
    conv_out, ssm_out = _units(a["w_conv_out_2"][0]), _units(a["w_ssm_out_2"][0])
    for n in range(KD):
        parts += [g_conv[n:n + 1], conv_out[n:n + 1], g_ssm[n:n + 1], ssm_out[2 * n:2 * n + 2]]
    parts += [_units(a["w_out_2"][0])]
    f_in = _units(a["w_ffn_in_2"][0])
    for n in range(F_TILES):
        parts += [f_in[n:n + 1], f_in[F_TILES + n:F_TILES + n + 1]]
    parts += [_units(a["w_ffn_down_2"][0])]
    return np.concatenate(parts)


def column_array(a):
    out = np.zeros((P, NCOL), np.float32)

    def put(name, v):
        v = v.reshape(-1, P).T
        out[:, COL[name]:COL[name] + v.shape[1]] = v

    for name, _ in COLUMNS:
        if name == "d_skip_2":
            put(name, np.repeat(a[name][0], 64))
        elif name in ("mlstm_i_b", "mlstm_f_b"):
            out[:4, COL[name]] = a[name][0]
        elif name in ("dt_bias_2", "a_log_2"):
            out[:8, COL[name]:COL[name] + 4] = a[name][0].reshape(4, 8).T
        elif name.startswith("eps") or name == "one":
            out[:, COL[name]] = {"eps_norm": 1e-6, "eps_gn": 64e-5, "eps_ln": 1e-5, "one": 1.0}[name]
        else:
            put(name, a[name])
    return out


def const_array():
    i = np.arange(P)
    s, t = i[:, None], i[None, :]
    out = np.zeros((P, NCON), np.float32)

    def put(name, v):
        out[:v.shape[0], CON[name]:CON[name] + v.shape[1]] = v

    put("ident", s == t)
    put("ones", np.ones((P, P)))
    same = s // 64 == t // 64
    put("head_ones", same)
    put("same_head", same)
    put("strict64", same & (s < t))
    put("causal64", same & (s <= t))
    put("causal", s <= t)
    put("levels", np.concatenate([(s // (2 << l) == t // (2 << l)) & ((s >> l) % 2 == 0) & ((t >> l) % 2 == 1)
                                  for l in range(6)], axis=1))
    tok = np.arange(T)
    put("reset64", np.broadcast_to(tok % 64 != 0, (P, T)))
    put("reset128", np.broadcast_to(tok % 128 != 0, (P, T)))
    put("sel4", np.concatenate([np.arange(4)[:, None] == h + 0 * t for h in range(4)], axis=1))
    put("sel4_half", np.concatenate([(np.arange(4)[:, None] == h) & (t // 64 == h % 2) for h in range(4)], axis=1))
    put("sel8", np.concatenate([np.arange(8)[:, None] == h + 0 * t for h in range(8)], axis=1))
    put("sel8_pair", np.concatenate([np.arange(8)[:, None] == 2 * j + t // 64 for j in range(4)], axis=1))
    put("rank4", np.broadcast_to(4.0 - np.arange(4), (P, 4)))
    put("rank8", np.broadcast_to(8.0 - np.arange(8), (P, 8)))
    put("half_col", np.stack([i < 64, i >= 64], axis=1))
    return out


def small_array(a):
    out = np.zeros((P, NSMA), np.float32)

    def put(name, v):
        out[:, SMA[name]:SMA[name] + v.shape[1]] = v

    rows = lambda w: w.reshape(KD, P, -1).transpose(1, 0, 2).reshape(P, -1)
    put("gates", rows(a["w_in"][0][:, 3328:]))
    put("router", rows(np.concatenate([a["moe_w_group"][0], a["moe_w_router"][0]], axis=1)))
    put("dt", rows(a["w_in_2"][0][:, 7168:7200]))
    put("lora_up", np.concatenate([a["rwkv_w_up"][0], a["rwkv_a_up"][0]], axis=0))
    put("g_up", a["rwkv_g_up"][0])
    put("router_b", np.broadcast_to(np.concatenate([a["moe_b_group"][0], a["moe_b_router"][0]]), (P, 36)))
    return out


def kernel(**inputs):
    import concourse.bacc as _bacc
    from concourse.bass_utils import run_bass_kernel_spmd as _run

    a = {k: np.asarray(v) for k, v in inputs.items()}
    arrays = {
        "x_dram": np.ascontiguousarray(a["x"][0].reshape(T, KD, P).transpose(2, 1, 0).reshape(P, KD * T)),
        "weights_dram": weight_stream(a),
        "columns_dram": column_array(a),
        "consts_dram": const_array(),
        "smalls_dram": small_array(a),
    }
    nc = _bacc.Bacc("TRN2", target_bir_lowering=False, num_devices=1)
    args = [nc.dram_tensor(n, v.shape, F32, kind="ExternalInput").ap() for n, v in arrays.items()]
    out = nc.dram_tensor("out_dram", (P, KD * T), F32, kind="ExternalOutput").ap()
    combine = nc.dram_tensor("combine_dram", (NE, T), F32, kind="Internal").ap()
    two_block_program(nc, *args, combine, out)
    r = _run(nc, [arrays], core_ids=[0])
    y = r.results[0]["out_dram"]
    return np.ascontiguousarray(np.asarray(y).reshape(P, KD, T).transpose(2, 1, 0)).reshape(1, T, D)
```

```python
from contextlib import ExitStack

import numpy as np
import concourse.bass as bass
from concourse import mybir

ALU = mybir.AluOpType
ACT = mybir.ActivationFunctionType
F32 = mybir.dt.float32
F32R = mybir.dt.float32r
AX = mybir.AxisListType

P = 128
T = 512
D = 1024
KD = D // P
TT = T // P
RING = 6
UNIT = 8 * P
PAD = 4
TP = T + PAD

RW = 4
R_TILES = 14
M_TILES = 12
C64 = 64
DECAY = float(np.exp(-0.5))
MH = 4
CAP = 15.0
NE = 32
NG = 4
EG = 8
F_TILES = 22
TAPS = 31
UP = 30

COLUMNS = [
    ("ada_b", 48), ("b_ada_mix_2", 24), ("b_ada_ffn_2", 24),
    ("mix_norm_w", 8), ("ffn_norm_w", 8), ("final_norm_w", 8), ("norm_mix_w_2", 8),
    ("norm_ffn_w_2", 8), ("final_norm_w_2", 8), ("rwkv_mu", 14), ("rwkv_w0", 4), ("rwkv_a0", 4),
    ("rwkv_k_k", 4), ("rwkv_k_a", 4), ("rwkv_r_k", 4), ("rwkv_gn_w", 4), ("rwkv_gn_b", 4),
    ("mlstm_conv_w", 16), ("mlstm_conv_b", 4), ("mlstm_hn_w", 4), ("mlstm_i_b", 1),
    ("mlstm_f_b", 1), ("conv_dw_w_2", TAPS * 8), ("conv_dw_b_2", 8), ("conv_ln_w_2", 8),
    ("conv_ln_b_2", 8), ("ssm_conv_w_2", 4 * 24), ("ssm_conv_b_2", 24), ("ssm_norm_w_2", 16),
    ("d_skip_2", 16), ("dt_bias_2", 4), ("a_log_2", 4),
    ("eps_norm", 1), ("eps_gn", 1), ("eps_ln", 1), ("one", 1), ("zero", 1),
]
COL, NCOL = {}, 0
for _name, _n in COLUMNS:
    COL[_name] = NCOL
    NCOL += _n

CONSTS = [
    ("ident", 128), ("ones", 128), ("head_ones", 128), ("strict64", 128), ("causal64", 128),
    ("causal", 128), ("levels", 6 * 128), ("same_head", 128), ("reset64", T), ("reset128", T),
    ("sel4", 4 * 128), ("sel8", 8 * 128), ("sel8_pair", 4 * 128),
    ("rank4", 4), ("rank8", 8), ("half_col", 2), ("token_id", 4), ("expert_id", 32),
]
CON, NCON = {}, 0
for _name, _n in CONSTS:
    CON[_name] = NCON
    NCON += _n

SMALLS = [("gates", 8 * 8), ("router", 8 * 36), ("dt", 8 * 32), ("lora_up", 512), ("g_up", 512),
          ("router_b", 36)]
SMA, NSMA = {}, 0
for _name, _n in SMALLS:
    SMA[_name] = NSMA
    NSMA += _n

MODS = 96
MOD_EARLY = 16
MOD_RING = 5
SH_M, SC_M, G_M, SH_F, SC_F, G_F = (8 * i for i in range(6))
SH_2, SC_2, G_2, SH_3, SC_3, G_3 = (48 + 8 * i for i in range(6))


GOES_ON = {
    "dt_done": ("v_turned", 4),
    "b_turned": ("gate_cols_done", 1),
    "ssm_cols_done": ("max_done", 4),
    "cb_done": ("inter_done", 4),
    "x_turned": ("k_turned", 2),
    "states_done": ("qk_done", 4),
    "acs_done": ("exp_m_done", 4),
    "pair_acs_done": ("num_done", 4),
    "y_off_done": ("den_done", 4),
    "y_diag_done": ("m_state_done", 3),
    "group_sum_done": ("m_sum_done", 4),
    "ln_mean_done": ("lora_done", 12),
    "ln_var_done": ("kk_sum_done", 4),
    "xbc_raw": ("gate_raw", 2),
    "z": ("forget", 1),
    "conv_gate": ("q_k", 4),
    "a_pos": ("v_tok", 4),
    "xbc": ("m_weights", 3),
    "dt_raw": ("exp_m", 1),
    "dt_log": ("decay", 4),
    "end_exp": ("den_abs", 4),
    "b_tok": ("m_square", 4),
    "seg_exp": ("m_std", 4),
    "exp_acs": ("r_lora", 2),
    "group_square": ("rate", 4),
    "group_std": ("r_a", 4),
    "ln_square": ("gate_r", 4),
    "ln_std": ("kk_square", 4),
    "conv_act": ("kk_std", 4),
    "sig": ("cum", 12),
    "ffn_silu": ("r_tok", 16),
    "pads2": ("m_conv", 16),
    "conv_u": ("m_logs", 4),
    "xbc_conv": ("q_head", 4),
    "end_arg": ("gate_cols", 5),
    "conv_y": ("decay_arg", 16),
    "rows": ("q_inter", 4),
    "cb": ("k_tok", 4),
    "x_tok": ("decay_masked", 4),
    "states": ("probs", 4),
    "seg_arg": ("m_state", 3),
    "seg": ("den", 4),
    "y_off": ("m_out", 4),
    "y_skip": ("shift_diff", 14),
    "y_sum": ("shifted", 14),
    "y_gated": ("kk_raw", 4),
    "y_ssm": ("bonus_in", 4),
    "ln_centred": ("kk_unit", 4),
    "ln_scaled": ("rate_sums", 4),
    "merge_conv": ("rate_before", 4),
    "merge_ssm": ("bonus", 4),
    "merged": ("r_ready", 16),
    "x_mix2": ("r_state", 8),
    "ffn_act": ("pairs", 32),
    "x_ffn2": ("inv", 88),
    "norm_ffn_square": ("norm_mix_square", 8),
    "norm_ffn_sum": ("norm_mix_sum", 1),
    "norm_ffn_std": ("norm_mix_std", 1),
    "norm_ffn_scaled": ("norm_mix_scaled", 8),
    "norm_ffn_h": ("norm_mix_h", 8),
    "norm_mix2_square": ("norm_ffn_square", 8),
    "norm_mix2_sum": ("norm_ffn_sum", 1),
    "norm_mix2_std": ("norm_ffn_std", 1),
    "norm_mix2_scaled": ("norm_ffn_scaled", 8),
    "norm_mix2_h": ("norm_ffn_h", 8),
    "norm_ffn2_square": ("norm_mix2_square", 8),
    "norm_ffn2_sum": ("norm_mix2_sum", 1),
    "norm_ffn2_std": ("norm_mix2_std", 1),
    "norm_ffn2_scaled": ("norm_mix2_scaled", 8),
    "norm_ffn2_h": ("norm_mix2_h", 8),
    "norm_out2_square": ("norm_out_square", 8),
    "norm_out2_sum": ("norm_out_sum", 1),
    "norm_out2_std": ("norm_out_std", 1),
    "norm_out2_h": ("norm_out_h", 8),
    "router_done": ("bonus_done", 4),
    "h_turned": ("r_turned", 16),
    "ranks_done": ("pairs_done", 32),
    "down_done": ("ox_done", 48),
    "combine_turned": ("xox_done", 72),
    "rows_turned": ("w_done", 8),
    "sparse_down": ("bv_done", 8),
    "y_turned": ("u_done", 8),
    "group_exp": ("prod", 40),
    "second_exp": ("gn_square", 4),
    "h_tok": ("gn_std", 4),
    "logits": ("w_t", 8),
    "group_arg": ("bv", 8),
    "second_arg": ("u", 8),
    "assigned": ("sa", 8),
    "totals": ("r_state_sum", 7),
    "combine": ("y_state", 4),
    "moe_up": ("y_raw", 4),
    "sparse_act": ("gn_centred", 4),
}


class Steps:

    def __init__(self, engine, semaphore):
        self.engine, self.semaphore, self.count = engine, semaphore, 0

    def mark(self, instruction):
        instruction.then_inc(self.semaphore, 1)
        self.count += 1

    def wait(self):
        self.engine.wait_ge(self.semaphore, self.count)


def two_block_program(nc, x_d, w_d, mod_w_d, c_d, col_d, con_d, sma_d, combine_d, h_d, y_d, table_d, out_d):
    with ExitStack() as ctx:
        signals = {}

        def S(name):
            while name in GOES_ON:
                name = GOES_ON[name][0]
            if name not in signals:
                signals[name] = ctx.enter_context(nc.semaphore(name))
            return signals[name]

        def at_count(name, n):
            semaphore = S(name)
            while name in GOES_ON:
                name, before = GOES_ON[name]
                n = n + before
            return semaphore, n

        base = {}

        def sb(name, shape):
            base[name] = -(-nc.sbuf_base // 32) * 32
            return ctx.enter_context(nc.sbuf_tensor(name, shape, F32))

        def halves(name, over, offset, *shape):
            return nc.alloc_sbuf_tensor_at(name, [P, *shape], F32R, offset=base[over] + 4 * offset)

        ring = sb("ring", [P, RING, UNIT])
        xT = sb("xT", [P, KD, T])
        hT = sb("hT", [P, KD, T])
        col = sb("col", [P, NCOL])
        con = sb("con", [P, NCON])
        sma = sb("sma", [P, NSMA])
        mod = sb("mod", [P, 96])
        rstd = sb("rstd", [P, 2, T])
        gain = sb("gain", [P, 8])
        U32 = mybir.dt.uint32
        slot_table = ctx.enter_context(nc.sbuf_tensor("slot_table", [P, 2 * NE], U32))
        pairs_u = ctx.enter_context(nc.sbuf_tensor("pairs_u", [P, 4 * TT], U32))
        rows_u = ctx.enter_context(nc.sbuf_tensor("rows_u", [P, 4 * TT], U32))
        flag = ctx.enter_context(nc.sbuf_tensor("flag", [1, 1], U32))
        AW = 29920
        arena = sb("arena", [P, AW])
        bank = [ctx.enter_context(nc.psum_tensor(f"bank{b}", [P, T], F32)) for b in range(8)]

        def area(offset, *shape):
            n = int(np.prod(shape))
            assert offset + n <= AW, (offset, n)
            v = arena[:, offset:offset + n]
            if len(shape) == 2:
                v = v.rearrange("p (a b) -> p a b", a=shape[0])
            if len(shape) == 3:
                v = v.rearrange("p (a b c) -> p a b c", a=shape[0], b=shape[1])
            return v

        def column(name, i=0, rows=P):
            return col[0:rows, COL[name] + i:COL[name] + i + 1]

        def constant(name, i=0, n=P, rows=P):
            return con[0:rows, CON[name] + i * n:CON[name] + i * n + n]

        ident, ones, head_ones = constant("ident"), constant("ones"), constant("head_ones")
        gates_w = sma[:, SMA["gates"]:SMA["gates"] + 64].rearrange("p (k n) -> p k n", k=8)
        router_w = sma[:, SMA["router"]:SMA["router"] + 288].rearrange("p (k n) -> p k n", k=8)
        dt_w = sma[:, SMA["dt"]:SMA["dt"] + 256].rearrange("p (k n) -> p k n", k=8)
        lora_up = sma[:, SMA["lora_up"]:SMA["lora_up"] + 512]
        g_up = sma[:, SMA["g_up"]:SMA["g_up"] + 512]
        router_b = sma[:, SMA["router_b"]:SMA["router_b"] + 36]

        hi_ring_r = halves("hi_ring", "arena", AW - 2 * UNIT, 2, UNIT)
        ring_r = halves("lo_ring", "ring", 0, RING, UNIT)
        hT_r = halves("h_lo", "hT", 0, KD, T)
        m_proj = area(0, M_TILES, TP)
        r_proj = area(6192, R_TILES, TP)
        q_k = area(13416, 4, T)
        v_aug = area(15464, TT, MH, 256)
        k_tok = area(19560, TT, 256)
        q_head = area(20584, MH, T)
        q_inter = area(22632, MH, T)
        gate_row = [area(24680 + T * i, T) for i in range(6)]
        probs = area(27752, 2, MH * P)
        m_state = area(28776, 2, 256)
        m_cols = area(29288, 2 * TT * MH)
        m_carry = area(29320, MH * TT)
        m_small = area(29336, 64)
        mod_ring = area(19560, MOD_RING, D)
        silu_c = area(13416, 2, D)
        y_mlstm = area(2064, 4, T)

        def x_in(t, lo=0, n=T):
            return r_proj[:, t, PAD + lo:PAD + lo + n]

        at = {}


        def column_half(i):
            return con[:, CON["half_col"] + i:CON["half_col"] + i + 1]

        y_rwkv = y_mlstm

        decay = area(0, TT, MH * P)
        g_row, f_row, b_row, max_row, w_row, k_row = gate_row

        def m_rows(row, lo=0, n=T):
            return row[0:MH, lo:lo + n]

        def pe_mlstm(pe, mm, take):
            for tt in range(TT):
                out = take(("v_tok", tt), ("v_tok", tt + 1))
                if tt == 0:
                    pe.wait_ge(*at_count("m_proj", 8))
                for h in range(MH):
                    last = mm(out[:, h * P:h * P + P], m_proj[:, 4 + h, PAD + tt * P:PAD + tt * P + P], ident)
                last.then_inc(S("v_turned"), 1)
            out = take(("gate_cols",), ("gate_cols", 5))
            pe.wait_ge(*at_count("m_weights", 3))
            for i, row in enumerate((g_row, k_row)):
                for tt in range(TT):
                    c = (i * TT + tt) * MH
                    mm(out[:, c:c + MH], m_rows(row, tt * P, P), ident[0:MH, 0:MH])
            for h in range(MH):
                last = mm(out[:, 32 + TT * h:32 + TT * h + TT], constant("sel4", h, rows=MH), m_small[0:MH, 16:16 + TT])
            last.then_inc(S("gate_cols_done"), 1)
            for h in range(MH):
                out = take(("max", h), ("decay_arg", TT * (h + 1)))
                mm(out[:, :], constant("sel4", h, rows=MH), m_rows(max_row)).then_inc(S("max_done"), 1)
            for h in range(MH):
                out = take(("inter", h), ("q_inter", h + 1))
                mm(out[:, :], constant("sel4", h, rows=MH), m_rows(w_row)).then_inc(S("inter_done"), 1)
            pe.wait_ge(*at_count("q_k", 4))
            for i in range(2):
                out = take(("k_tok", i), ("k_tok", 2 * i + 2))
                for tt in range(2):
                    for j in range(2):
                        last = mm(out[:, tt * 256 + j * P:tt * 256 + j * P + P],
                                  q_k[:, 2 + j, (2 * i + tt) * P:(2 * i + tt + 1) * P], ident)
                last.then_inc(S("k_turned"), 1)
            pe.wait_ge(*at_count("q_head", MH))
            pe.wait_ge(*at_count("pads", 3))
            pe.wait_ge(*at_count("exp_m", 1))
            for tt in range(TT):
                tok = slice(tt * P, tt * P + P)
                out = take(("qk", tt), ("probs", tt + 1))
                for h in range(MH):
                    last = mm(out[:, h * P:h * P + P], q_k[:, 2 + h // 2, tok], q_head[:, h, tok])
                last.then_inc(S("qk_done"), 1)
                out = take(("exp_m", tt), ("den", tt + 1))
                for h in range(MH):
                    last = mm(out[:, h * P:h * P + P], constant("sel4", h, rows=MH), m_rows(f_row, tt * P, P))
                last.then_inc(S("exp_m_done"), 1)
                pe.wait_ge(*at_count("probs", tt + 1))
                if tt:
                    pe.wait_ge(*at_count("m_state", tt))
                    pe.wait_ge(*at_count("q_inter", MH))
                else:
                    pe.wait_ge(*at_count("v_tok", TT))
                num = take(("num", tt), ("m_out", tt + 1))
                for h in range(MH):
                    last = mm(num[:, h * P:h * P + P], v_aug[:, tt, h, 0:P], probs[:, tt % 2, h * P:h * P + P], True, tt == 0)
                    if tt:
                        last = mm(num[:, h * P:h * P + P], m_state[:, h // 2, 0:P], q_inter[:, h, tok], False, True)
                last.then_inc(S("num_done"), 1)
                den = take(("den", tt), ("den_abs", tt + 1))
                last = mm(den[:, :], ones, probs[:, tt % 2, :], True, tt == 0)
                if tt:
                    for h in range(MH):
                        last = mm(den[:, h * P:h * P + P], m_state[:, h // 2, P:2 * P], q_inter[:, h, tok], False, True)
                last.then_inc(S("den_done"), 1)
                if tt < TT - 1:
                    out = take(("m_state", tt), ("m_state", tt + 1))
                    pe.wait_ge(*at_count("k_tok", tt + 1))
                    for h in range(MH):
                        r = 64 * (h % 2)
                        last = mm(out[r:r + 64, h // 2 * 256:h // 2 * 256 + 256], k_tok[:, tt, h * 64:h * 64 + 64], v_aug[:, tt, h, :])
                    last.then_inc(S("m_state_done"), 1)
            for h in range(MH):
                out = take(("m_sum", h), ("m_std", h + 1))
                pe.wait_ge(*at_count("m_square", h + 1))
                mm(out[:, :], ones, q_head[:, h, :]).then_inc(S("m_sum_done"), 1)

        def act_mlstm_gates(act, steps):
            act.wait_ge(*at_count("gate_bias", 2))
            for i, row in enumerate((g_row, f_row)):
                act.wait_ge(*at_count("gates_done", i + 1))
                act.activation(m_rows(row), bank[at[("gate", i)]][0:MH, :], ACT.Tanh, bias=m_small[0:MH, i:i + 1],
                               scale=1 / CAP).then_inc(S("gate_raw"), 1)
            act.wait_ge(*at_count("gate_raw", 2))
            steps.mark(act.activation(m_rows(f_row), m_rows(f_row), ACT.Exp, scale=-CAP))
            steps.wait()
            act.activation(m_rows(f_row), m_rows(f_row), ACT.Ln, bias=column("one", rows=MH)).then_inc(S("forget"), 1)

        def act_mlstm(act, steps):
            for t in range(4):
                act.wait_ge(*at_count("m_conv", 16 + t - 3))
                act.activation(q_k[:, t, :], q_k[:, t, :], ACT.Silu, bias=column("mlstm_conv_b", t)).then_inc(S("q_k"), 1)
            for tt in range(TT):
                act.wait_ge(*at_count("v_turned", tt + 1))
                act.activation(v_aug[:, tt, :, 0:P], bank[at[("v_tok", tt)]][:, :].rearrange("p (h v) -> p h v", h=MH),
                               ACT.Copy).then_inc(S("v_tok"), 1)
            act.wait_ge(*at_count("m_logs", 4))
            act.activation(m_rows(w_row), m_rows(w_row), ACT.Exp, scale=-1.0).then_inc(S("m_weights"), 1)
            act.activation(m_rows(k_row), m_rows(k_row), ACT.Exp).then_inc(S("m_weights"), 1)
            act.activation(m_small[0:MH, 16:16 + TT], m_small[0:MH, 8:8 + TT], ACT.Exp, scale=-1.0).then_inc(S("m_weights"), 1)
            act.activation(m_rows(f_row), m_rows(f_row), ACT.Exp).then_inc(S("exp_m"), 1)
            for tt in range(TT):
                act.wait_ge(*at_count("decay_arg", MH * TT))
                act.activation(decay[:, tt, :], decay[:, tt, :], ACT.Exp, scale=-1.0).then_inc(S("decay"), 1)
            for tt in range(TT):
                act.wait_ge(*at_count("den_done", tt + 1))
                if tt:
                    act.wait_ge(*at_count("den", tt))
                act.activation(den_abs[:, :], bank[at[("den", tt)]][:, :], ACT.Abs).then_inc(S("den_abs"), 1)
            for h in range(MH):
                act.wait_ge(*at_count("m_out", TT))
                act.activation(q_head[:, h, :], y_mlstm[:, h, :], ACT.Square).then_inc(S("m_square"), 1)
            for h in range(MH):
                act.wait_ge(*at_count("m_sum_done", h + 1))
                act.activation(q_inter[:, h, :], bank[at[("m_sum", h)]][:, :], ACT.Sqrt, bias=column("eps_norm"),
                               scale=1 / P).then_inc(S("m_std"), 1)

        den_abs = rstd[:, 0, :]
        den_max = rstd[:, 1, :]

        def dve_mlstm(dve, steps):
            dve.wait_ge(*at_count("pads", 2))
            for tap in range(4):
                for t in range(4):
                    src = m_proj[:, t, PAD - 3 + tap:PAD - 3 + tap + T]
                    w = column("mlstm_conv_w", 4 * tap + t)
                    if tap == 0:
                        dve.wait_ge(*at_count("m_proj", t + 1))
                        dve.tensor_scalar(q_k[:, t, :], src, w, None, ALU.mult).then_inc(S("m_conv"), 1)
                    else:
                        dve.wait_ge(*at_count("m_conv", 4 * (tap - 1) + t + 1))
                        dve.scalar_tensor_tensor(q_k[:, t, :], src, w, q_k[:, t, :], ALU.mult, ALU.add).then_inc(S("m_conv"), 1)
            dve.wait_ge(*at_count("forget", 1))
            steps.mark(dve.tensor_tensor_scan(m_rows(b_row), constant("reset128", 0, T, MH), m_rows(f_row), 0.0, ALU.mult, ALU.add))
            steps.mark(dve.memset(m_rows(w_row), 0.0))
            steps.wait()
            steps.mark(dve.scalar_tensor_tensor(m_rows(g_row), m_rows(g_row), CAP, m_rows(b_row), ALU.mult, ALU.add))
            steps.mark(dve.tensor_scalar(w_row[0:MH, P:T:P], b_row[0:MH, P - 1:T - P:P], -1.0, None, ALU.mult))
            steps.wait()
            steps.mark(dve.tensor_tensor_scan(m_rows(max_row), m_rows(w_row), m_rows(g_row), 0.0, ALU.add, ALU.max))
            steps.mark(dve.memset(m_small[0:MH, 4:4 + TT], 0.0))
            steps.wait()
            steps.mark(dve.tensor_tensor(m_small[0:MH, 5:4 + TT], max_row[0:MH, P - 1:T - P:P], b_row[0:MH, P - 1:T - P:P], ALU.subtract))
            steps.wait()

            def by_tile(x):
                return x.rearrange("h (c t) -> h c t", c=TT)

            carried = m_small[0:MH, 4:4 + TT].rearrange("h (c t) -> h c t", t=1).broadcast_to([MH, TT, P])
            m_last = max_row[0:MH, P - 1:T:P]
            last_b = m_last.rearrange("h (c t) -> h c t", t=1).broadcast_to([MH, TT, P])
            dve.tensor_tensor(by_tile(m_rows(w_row)), by_tile(m_rows(max_row)), carried, ALU.subtract).then_inc(S("m_logs"), 1)
            dve.tensor_tensor(by_tile(m_rows(k_row)), by_tile(m_rows(g_row)), last_b, ALU.subtract).then_inc(S("m_logs"), 1)
            dve.tensor_tensor(m_small[0:MH, 8:8 + TT], m_last, m_small[0:MH, 4:4 + TT], ALU.subtract).then_inc(S("m_logs"), 1)
            dve.tensor_tensor(m_rows(f_row), m_rows(b_row), m_rows(max_row), ALU.subtract).then_inc(S("m_logs"), 1)
            for h in range(MH):
                dve.wait_ge(*at_count("q_k", h // 2 + 1))
                dve.tensor_scalar(q_head[:, h, :], q_k[:, h // 2, :], column_half(h % 2), 0.125, ALU.mult, ALU.mult).then_inc(S("q_head"), 1)
            dve.wait_ge(*at_count("gate_cols_done", 1))
            cols = bank[at[("gate_cols",)]]
            dve.tensor_copy(m_cols[:, :], cols[:, 0:32]).then_inc(S("gate_cols"), 1)
            for h in range(MH):
                r = slice(64 * (h % 2), 64 * (h % 2) + 64)
                dve.tensor_copy(m_carry[r, h // 2 * TT:h // 2 * TT + TT], cols[r, 32 + TT * h:32 + TT * h + TT]).then_inc(S("gate_cols"), 1)
            dve.wait_ge(*at_count("gate_cols", 5))
            dve.wait_ge(*at_count("m_conv", 16))
            for h in range(MH):
                dve.wait_ge(*at_count("max_done", h + 1))
                for tt in range(TT):
                    dve.tensor_scalar(decay[:, tt, h * P:h * P + P], bank[at[("max", h)]][:, tt * P:tt * P + P],
                                      m_cols[:, tt * MH + h:tt * MH + h + 1], 0.0, ALU.subtract, ALU.max).then_inc(S("decay_arg"), 1)
            dve.wait_ge(*at_count("q_head", MH))
            for h in range(MH):
                dve.wait_ge(*at_count("inter_done", h + 1))
                dve.tensor_tensor(q_inter[:, h, :], q_head[:, h, :], bank[at[("inter", h)]][:, :], ALU.mult).then_inc(S("q_inter"), 1)
            for tt in range(TT):
                dve.wait_ge(*at_count("k_turned", tt // 2 + 1))
                dve.tensor_tensor(k_tok[:, tt, :].rearrange("p (h d) -> p h d", h=MH),
                                  bank[at[("k_tok", tt // 2)]][:, tt % 2 * 256:tt % 2 * 256 + 256].rearrange("p (h d) -> p h d", h=MH),
                                  m_cols[:, (TT + tt) * MH:(TT + tt + 1) * MH].rearrange("p (h d) -> p h d", d=1).broadcast_to([P, MH, 64]),
                                  ALU.mult).then_inc(S("k_tok"), 1)
            for tt in range(TT):
                dve.wait_ge(*at_count("decay", tt + 1))
                dve.tensor_tensor(decay[:, tt, :].rearrange("p (h t) -> p h t", h=MH), decay[:, tt, :].rearrange("p (h t) -> p h t", h=MH),
                                  constant("causal").rearrange("p (a t) -> p a t", a=1).broadcast_to([P, MH, P]), ALU.mult).then_inc(S("decay_masked"), 1)
            for tt in range(TT):
                dve.wait_ge(*at_count("decay_masked", tt + 1))
                dve.wait_ge(*at_count("qk_done", tt + 1))
                if tt >= 2:
                    dve.wait_ge(*at_count("den_done", tt - 1))
                dve.tensor_tensor(probs[:, tt % 2, :], bank[at[("qk", tt)]][:, :], decay[:, tt, :], ALU.mult).then_inc(S("probs"), 1)
                if tt < TT - 1:
                    dve.wait_ge(*at_count("m_state_done", tt + 1))
                    new = bank[at[("m_state", tt)]][:, :]
                    if tt == 0:
                        dve.tensor_copy(m_state[:, :, :].rearrange("p a b -> p (a b)"), new).then_inc(S("m_state"), 1)
                    else:
                        dve.wait_ge(*at_count("den_done", tt + 1))
                        for j in range(2):
                            ins = dve.scalar_tensor_tensor(m_state[:, j, :], m_state[:, j, :], m_carry[:, j * TT + tt:j * TT + tt + 1],
                                                           new[:, j * 256:j * 256 + 256], ALU.mult, ALU.add)
                        ins.then_inc(S("m_state"), 1)
                dve.wait_ge(*at_count("den_abs", tt + 1))
                dve.wait_ge(*at_count("exp_m_done", tt + 1))
                dve.tensor_tensor(den_max, den_abs, bank[at[("exp_m", tt)]][:, :], ALU.max).then_inc(S("den"), 1)
                dve.wait_ge(*at_count("den", tt + 1))
                steps.mark(dve.reciprocal(den_max, den_max))
                steps.wait()
                dve.wait_ge(*at_count("num_done", tt + 1))
                dve.tensor_tensor(y_mlstm[:, :, tt * P:tt * P + P], bank[at[("num", tt)]][:, :].rearrange("p (h t) -> p h t", h=MH),
                                  den_max.rearrange("p (h t) -> p h t", h=MH), ALU.mult).then_inc(S("m_out"), 1)
            for h in range(MH):
                dve.wait_ge(*at_count("m_std", h + 1))
                steps.mark(dve.reciprocal(q_inter[:, h, :], q_inter[:, h, :]))
                steps.wait()
                steps.mark(dve.scalar_tensor_tensor(y_mlstm[:, h, :], y_mlstm[:, h, :], column("mlstm_hn_w", h), q_inter[:, h, :], ALU.mult, ALU.mult))
                steps.wait()
                dve.tensor_tensor(y_mlstm[:, h, :], y_mlstm[:, h, :], m_proj[:, 8 + h, PAD:TP], ALU.mult).then_inc(S("y_mlstm"), 1)
        WA_TILE, G_TILE = 12, 13
        rate = area(13416, RW, T)
        b_in = area(15464, RW, T)
        kk = area(17512, RW, T)
        gate_r = area(19560, RW, T)
        bonus = area(21608, RW, T)
        sums = area(23656, RW, T)
        cum_p = area(25704, RW, T)
        cum_inv = area(27752, RW, T)
        v_tok_r, b_tok = area(13416, TT, 512), area(23656, TT, 512)
        k_tok_r, kk_tok = hT[:, 0:4, :], hT[:, 4:8, :]
        r_b = area(25704, 2, 8 * P)
        r_k = area(27752, 2, 8 * P)
        shift_tmp = area(4128, 4, T)
        inv_x, inv_xt = area(0, 4 * P), area(512, 4 * P)
        level_t, prod_t = area(1024, 4 * P), area(4128, 4 * P)
        a_t, bk_t = area(4640, 4 * P), area(5152, 4 * P)
        bv = area(5664, 4, 64)
        V0 = 6192 + 8 * TP
        w_t, u_tok = area(V0, 4, P), area(V0 + 512, 512)
        S0 = 6192 + 12 * TP
        sa = area(S0, 512)
        r_state = area(1536, 4, P)
        chunk_p = rstd[:, 0, :].rearrange("p (r c x) -> p r c x", r=4, c=8)[:, :, :, 0:1]
        y_rwkv = area(6192 + 4 * TP, RW, TP)[:, :, PAD:TP]
        masked_p = gain

        def heads(parity):
            return [parity, parity + 2, parity + 4, parity + 6]

        def pe_rwkv(pe, mm, take):
            pe.wait_ge(*at_count("r_lora", 2))
            for n in range(RW):
                out = take(("decay_up", n), ("rate", n + 1))
                mm(out[:, :], lora_up[0:64, n * P:n * P + P], r_proj[0:64, WA_TILE, PAD:TP]).then_inc(S("lora_done"), 1)
            for n in range(RW):
                out = take(("a_up", n), ("r_a", n + 1))
                mm(out[:, :], lora_up[64:128, n * P:n * P + P], r_proj[64:128, WA_TILE, PAD:TP]).then_inc(S("lora_done"), 1)
            for n in range(RW):
                out = take(("g_up", n), ("gate_r", n + 1))
                mm(out[:, :], g_up[:, n * P:n * P + P], r_proj[:, G_TILE, PAD:TP]).then_inc(S("lora_done"), 1)
            for n in range(RW):
                out = take(("kk_sum", n), ("kk_std", n + 1))
                pe.wait_ge(*at_count("kk_square", n + 1))
                mm(out[:, :], head_ones, sums[:, n, :]).then_inc(S("kk_sum_done"), 1)
            for n in range(RW):
                out = take(("bonus_sum", n), ("bonus", n + 1))
                pe.wait_ge(*at_count("bonus_in", n + 1))
                mm(out[:, :], head_ones, bonus[:, n, :]).then_inc(S("bonus_done"), 1)
            pe.wait_ge(*at_count("r_ready", 4 * RW))
            for i, src in enumerate((r_proj[:, 8:12, PAD:TP], b_in, r_proj[:, 4:8, PAD:TP], kk)):
                for tt in range(TT):
                    out = take(("r_tok", i, tt), ("r_tok", 4 * i + tt + 1))
                    for n in range(RW):
                        last = mm(out[:, n * P:n * P + P], src[:, n, tt * P:tt * P + P], ident)
                    last.then_inc(S("r_turned"), 1)
            for tt in range(TT):
                tok = slice(tt * P, tt * P + P)
                for par in range(2):
                    g = 2 * tt + par
                    rows = slice(64 * par, 64 * par + 64)
                    hs = heads(par)

                    def pairs(key, lhs, rhs, freed):
                        out = take(key, freed)
                        for i, h in enumerate(hs):
                            n = h // 2
                            last = mm(out[:, i * P:i * P + P], lhs[rows, n, tok], rhs[rows, n, tok])
                        last.then_inc(S("pairs_done"), 1)

                    r_f, k_f = r_proj[:, 0:4, PAD:TP], r_proj[:, 4:8, PAD:TP]
                    pairs(("a_t", g), b_in, kk, ("pairs", 4 * g + 1))
                    pairs(("bk_t", g), k_f, kk, ("pairs", 4 * g + 2))
                    pairs(("r_b", g), b_in, r_f, ("pairs", 4 * g + 3))
                    pairs(("r_k", g), k_f, r_f, ("pairs", 4 * g + 4))
                    for l in range(6):
                        pe.wait_ge(*at_count("level", 6 * g + l + 1))
                        if l:
                            pe.wait_ge(*at_count("inv", 11 * g + 2 * l))
                        out = take(("ox", g, l), ("prod", 5 * g + l) if l else ("inv", 11 * g + 2))
                        for i in range(4):
                            c = slice(i * P, i * P + P)
                            last = mm(out[:, c], level_t[:, c], ident if l == 0 else inv_x[:, c])
                        last.then_inc(S("ox_done"), 1)
                        if l == 0:
                            continue
                        pe.wait_ge(*at_count("prod", 5 * g + l))
                        out_t = take(("xox_t", g, l), ("inv", 11 * g + 2 * l + 1))
                        for i in range(4):
                            c = slice(i * P, i * P + P)
                            last = mm(out_t[:, c], prod_t[:, c], inv_xt[:, c])
                        last.then_inc(S("xox_done"), 1)
                        if l == 5:
                            continue
                        out = take(("xox", g, l), ("inv", 11 * g + 2 * l + 2))
                        for i in range(4):
                            c = slice(i * P, i * P + P)
                            last = mm(out[:, c], inv_xt[:, c], prod_t[:, c])
                        last.then_inc(S("xox_done"), 1)
                    pe.wait_ge(*at_count("inv", 11 * g + 11))
                    out = take(("w_t", g), ("w_t", g + 1))
                    for i, h in enumerate(hs):
                        last = mm(out[rows, i * P:i * P + P], kk_tok[:, tt, h * 64:h * 64 + 64], inv_xt[:, i * P:i * P + P])
                    last.then_inc(S("w_done"), 1)
                    out = take(("bv", g), ("bv", g + 1))
                    for i, h in enumerate(hs):
                        last = mm(out[:, i * 64:i * 64 + 64], bk_t[:, i * P:i * P + P], v_tok_r[:, tt, h * 64:h * 64 + 64])
                    last.then_inc(S("bv_done"), 1)
                    pe.wait_ge(*at_count("bv", g + 1))
                    out = take(("u", g), ("u", g + 1))
                    for i, h in enumerate(hs):
                        last = mm(out[:, i * 64:i * 64 + 64], inv_xt[:, i * P:i * P + P], bv[:, i, :])
                    last.then_inc(S("u_done"), 1)
                y_state = None
                for half in range(2):
                    c = 2 * tt + half
                    rows = slice(64 * half, 64 * half + 64)
                    pe.wait_ge(*at_count("r_state", c + 1))
                    if half == 0:
                        pe.wait_ge(*at_count("w_t", 2 * tt + 2))
                    out = take(("ws", c), ("sa", c + 1))
                    for n in range(RW):
                        last = mm(out[:, n * P:n * P + P], w_t[:, n, :], r_state[:, n, :])
                    last.then_inc(S("ws_done"), 1)
                    if half == 0:
                        y_state = take(("y_state", tt), ("y_state", tt + 1))
                    for n in range(RW):
                        last = mm(y_state[:, n * P + 64 * half:n * P + 64 * half + 64], r_state[:, n, :],
                                  r_proj[:, n, PAD + c * C64:PAD + c * C64 + C64])
                    last.then_inc(S("y_state_done"), 1)
                    pe.wait_ge(*at_count("sa", c + 1))
                    if c < 7:
                        out = take(("new_state", c), ("r_state_sum", c + 1))
                        for n in range(RW):
                            cc = slice(n * P, n * P + P)
                            mm(out[:, cc], b_tok[rows, tt, cc], sa[rows, cc], True, False)
                            last = mm(out[:, cc], k_tok_r[rows, tt, cc], v_tok_r[rows, tt, cc], False, True)
                        last.then_inc(S("new_state_done"), 1)
                out = take(("y_in", tt), ("y_raw", tt + 1))
                for h in range(8):
                    cc, o = slice(h // 2 * P, h // 2 * P + P), slice(64 * (h % 2), 64 * (h % 2) + 64)
                    m = (h % 2 * 4 + h // 2) * P
                    mm(out[o, cc], sa[:, h * 64:h * 64 + 64], r_b[:, tt % 2, m:m + P], True, False)
                    last = mm(out[o, cc], v_tok_r[:, tt, h * 64:h * 64 + 64], r_k[:, tt % 2, m:m + P], False, True)
                last.then_inc(S("y_in_done"), 1)
            for n in range(RW):
                out = take(("gn_mean", n), ("gn_centred", n + 1))
                if n == 0:
                    pe.wait_ge(*at_count("y_raw", TT))
                mm(out[:, :], head_ones, y_rwkv[:, n, :]).then_inc(S("gn_mean_done"), 1)
            for n in range(RW):
                out = take(("gn_var", n), ("gn_std", n + 1))
                pe.wait_ge(*at_count("gn_square", n + 1))
                mm(out[:, :], head_ones, rate[:, n, :]).then_inc(S("gn_var_done"), 1)

        def act_rwkv(act, steps):
            act.wait_ge(*at_count("shifted", 2))
            act.activation(r_proj[0:64, WA_TILE, PAD:TP], r_proj[0:64, WA_TILE, PAD:TP], ACT.Tanh).then_inc(S("r_lora"), 1)
            act.activation(x_in(G_TILE), x_in(G_TILE), ACT.Sigmoid).then_inc(S("r_lora"), 1)
            act.wait_ge(*at_count("y_mlstm", MH))
            for n in range(RW):
                act.wait_ge(*at_count("lora_done", n + 1))
                act.activation(rate[:, n, :], bank[at[("decay_up", n)]][:, :], ACT.Sigmoid, bias=column("rwkv_w0", n)).then_inc(S("rate"), 1)
            for n in range(RW):
                act.wait_ge(*at_count("lora_done", RW + n + 1))
                act.activation(b_in[:, n, :], bank[at[("a_up", n)]][:, :], ACT.Sigmoid, bias=column("rwkv_a0", n)).then_inc(S("r_a"), 1)
            for n in range(RW):
                act.wait_ge(*at_count("lora_done", 2 * RW + n + 1))
                act.activation(gate_r[:, n, :], bank[at[("g_up", n)]][:, :], ACT.Copy).then_inc(S("gate_r"), 1)
            for n in range(RW):
                act.wait_ge(*at_count("kk_raw", n + 1))
                act.activation(sums[:, n, :], kk[:, n, :], ACT.Square).then_inc(S("kk_square"), 1)
            for n in range(RW):
                act.wait_ge(*at_count("kk_sum_done", n + 1))
                act.activation(cum_p[:, n, :], bank[at[("kk_sum", n)]][:, :], ACT.Sqrt).then_inc(S("kk_std"), 1)
            for n in range(RW):
                act.wait_ge(*at_count("kk_unit", n + 1))
                act.wait_ge(*at_count("rate_before", n + 1))
                act.activation(cum_p[:, n, :], sums[:, n, :], ACT.Exp, scale=-DECAY).then_inc(S("cum"), 1)
                act.activation(cum_inv[:, n, :], sums[:, n, :], ACT.Exp, scale=DECAY).then_inc(S("cum"), 1)
                act.activation(rate[:, n, :], rate[:, n, :], ACT.Exp, scale=-DECAY).then_inc(S("cum"), 1)
            act.wait_ge(*at_count("bonus", RW))
            act.wait_ge(*at_count("r_ready", 4 * RW))
            for i, dst in enumerate((v_tok_r, b_tok, k_tok_r, kk_tok)):
                for tt in range(TT):
                    act.wait_ge(*at_count("r_turned", 4 * i + tt + 1))
                    act.activation(dst[:, tt, :], bank[at[("r_tok", i, tt)]][:, :], ACT.Copy).then_inc(S("r_tok"), 1)
            for tt in range(TT):
                for par in range(2):
                    g = 2 * tt + par
                    for l in range(1, 6):
                        act.wait_ge(*at_count("ox_done", 6 * g + l + 1))
                        if g or l > 1:
                            act.wait_ge(*at_count("xox_done", 9 * g + 2 * (l - 1)))
                        act.activation(prod_t[:, :], bank[at[("ox", g, l)]][:, :], ACT.Copy).then_inc(S("prod"), 1)
            for n in range(RW):
                act.wait_ge(*at_count("gn_centred", n + 1))
                act.activation(rate[:, n, :], y_rwkv[:, n, :], ACT.Square).then_inc(S("gn_square"), 1)
            for n in range(RW):
                act.wait_ge(*at_count("gn_var_done", n + 1))
                act.activation(cum_p[:, n, :], bank[at[("gn_var", n)]][:, :], ACT.Sqrt, bias=column("eps_gn"), scale=1 / 64).then_inc(S("gn_std"), 1)

        def dve_rwkv(dve, steps):
            order = [12, 13, 4, 5, 6, 7, 0, 1, 2, 3, 8, 9, 10, 11]
            for i, t in enumerate(order):
                dve.wait_ge(*at_count("r_proj", t + 1))
                if i >= 4:
                    dve.wait_ge(*at_count("shifted", i - 3))
                dve.tensor_tensor(shift_tmp[:, i % 4, :], x_in(t, -1), x_in(t), ALU.subtract).then_inc(S("shift_diff"), 1)
                dve.wait_ge(*at_count("shift_diff", i + 1))
                dve.scalar_tensor_tensor(x_in(t), shift_tmp[:, i % 4, :], column("rwkv_mu", t), x_in(t), ALU.mult, ALU.add).then_inc(S("shifted"), 1)
            dve.wait_ge(*at_count("shifted", R_TILES))
            for n in range(RW):
                dve.tensor_scalar(kk[:, n, :], x_in(4 + n), column("rwkv_k_k", n), None, ALU.mult).then_inc(S("kk_raw"), 1)
            steps.mark(dve.tensor_scalar(gain[:, 0:4], col[:, COL["rwkv_k_a"]:COL["rwkv_k_a"] + 4], -1.0, 1.0, ALU.mult, ALU.add))
            steps.wait()
            for n in range(RW):
                dve.wait_ge(*at_count("r_a", n + 1))
                steps.mark(dve.tensor_scalar(shift_tmp[:, n, :], b_in[:, n, :], column("rwkv_k_a", n), gain[:, n:n + 1], ALU.mult, ALU.add))
            steps.wait()
            dve.wait_ge(*at_count("kk_raw", RW))
            for n in range(RW):
                steps.mark(dve.tensor_tensor(x_in(4 + n), x_in(4 + n), shift_tmp[:, n, :], ALU.mult))
            steps.wait()
            for n in range(RW):
                dve.scalar_tensor_tensor(bonus[:, n, :], x_in(n), column("rwkv_r_k", n), x_in(4 + n), ALU.mult, ALU.mult).then_inc(S("bonus_in"), 1)
            for n in range(RW):
                dve.wait_ge(*at_count("kk_std", n + 1))
                steps.mark(dve.tensor_scalar(cum_p[:, n, :], cum_p[:, n, :], 1e-12, None, ALU.max))
            steps.wait()
            for n in range(RW):
                steps.mark(dve.reciprocal(cum_p[:, n, :], cum_p[:, n, :]))
            steps.wait()
            for n in range(RW):
                dve.wait_ge(*at_count("kk_square", n + 1))
                dve.tensor_tensor(kk[:, n, :], kk[:, n, :], cum_p[:, n, :], ALU.mult).then_inc(S("kk_unit"), 1)
            for n in range(RW):
                dve.wait_ge(*at_count("rate", n + 1))
                dve.wait_ge(*at_count("kk_sum_done", n + 1))
                dve.tensor_tensor_scan(sums[:, n, :], constant("reset64", 0, T), rate[:, n, :], 0.0, ALU.mult, ALU.add).then_inc(S("rate_sums"), 1)
            dve.wait_ge(*at_count("rate_sums", RW))
            for n in range(RW):
                dve.tensor_tensor(rate[:, n, :], sums[:, n, :], rate[:, n, :], ALU.subtract).then_inc(S("rate_before"), 1)
            dve.wait_ge(*at_count("kk_unit", RW))
            for n in range(RW):
                steps.mark(dve.tensor_tensor(b_in[:, n, :], b_in[:, n, :], kk[:, n, :], ALU.mult))
            steps.wait()
            for n in range(RW):
                dve.wait_ge(*at_count("bonus_done", n + 1))
                dve.tensor_tensor(bonus[:, n, :], bank[at[("bonus_sum", n)]][:, :], x_in(8 + n), ALU.mult).then_inc(S("bonus"), 1)
            for n in range(RW):
                dve.wait_ge(*at_count("cum", 3 * n + 3))
                for x, f in ((kk, rate), (b_in, cum_inv), (r_proj[:, 4:8, PAD:TP], cum_inv), (r_proj[:, 0:4, PAD:TP], cum_p)):
                    dve.tensor_tensor(x[:, n, :], x[:, n, :], f[:, n, :], ALU.mult).then_inc(S("r_ready"), 1)
            steps.mark(dve.tensor_copy(chunk_p, cum_p[:, :, C64 - 1:T:C64]))
            dve.memset(r_state[:, :, :], 0.0).then_inc(S("r_state"), 1)
            steps.wait()
            dve.wait_ge(*at_count("r_turned", 4 * TT))
            dve.wait_ge(*at_count("r_ready", 4 * RW))

            def masked(dst, key, g, i, mask, heads_view=None):
                dve.wait_ge(*at_count("pairs_done", 4 * g + i + 1))
                dve.tensor_tensor(dst.rearrange("p (h t) -> p h t", h=4), bank[at[(key, g)]][:, :].rearrange("p (h t) -> p h t", h=4),
                                  constant(mask).rearrange("p (a t) -> p a t", a=1).broadcast_to([P, 4, P]), ALU.mult).then_inc(S("pairs"), 1)

            def wide(x):
                return x.rearrange("p (h t) -> p h t", h=4)

            eye = ident.rearrange("p (a t) -> p a t", a=1).broadcast_to([P, 4, P])
            for tt in range(TT):
                for par in range(2):
                    g = 2 * tt + par
                    rows = slice(64 * par, 64 * par + 64)
                    if g:
                        dve.wait_ge(*at_count("level", 6 * g))
                        dve.wait_ge(*at_count("bv_done", g))
                    if tt >= 2 and par == 0:
                        dve.wait_ge(*at_count("y_in_done", tt - 1))
                    masked(a_t[:, :], "a_t", g, 0, "strict64")
                    masked(bk_t[:, :], "bk_t", g, 1, "strict64")
                    masked(r_b[:, tt % 2, par * 512:par * 512 + 512], "r_b", g, 2, "causal64")
                    masked(r_k[:, tt % 2, par * 512:par * 512 + 512], "r_k", g, 3, "causal64")
                    for l in range(6):
                        if l == 0:
                            dve.wait_ge(*at_count("level", 6 * g + 1))
                            if g:
                                dve.wait_ge(*at_count("u_done", g))
                            dve.tensor_tensor(wide(inv_xt[:, :]), eye, wide(level_t[:, :]), ALU.subtract).then_inc(S("inv"), 1)
                            dve.wait_ge(*at_count("ox_done", 6 * g + 1))
                            dve.tensor_tensor(wide(inv_x[:, :]), eye, wide(bank[at[("ox", g, 0)]][:, :]), ALU.subtract).then_inc(S("inv"), 1)
                            continue
                        dve.wait_ge(*at_count("inv", 11 * g + 2 * l))
                        dve.wait_ge(*at_count("xox_done", 9 * g + 2 * l - (l == 5)))
                        dve.tensor_tensor(inv_xt[:, :], inv_xt[:, :], bank[at[("xox_t", g, l)]][:, :], ALU.subtract).then_inc(S("inv"), 1)
                        if l < 5:
                            dve.tensor_tensor(inv_x[:, :], inv_x[:, :], bank[at[("xox", g, l)]][:, :], ALU.subtract).then_inc(S("inv"), 1)
                    dve.wait_ge(*at_count("w_done", g + 1))
                    dve.tensor_copy(w_t[rows, :, :], wide(bank[at[("w_t", g)]][rows, :])).then_inc(S("w_t"), 1)
                    dve.wait_ge(*at_count("bv_done", g + 1))
                    dve.tensor_copy(bv[:, :, :].rearrange("p a b -> p (a b)"), bank[at[("bv", g)]][:, 0:256]).then_inc(S("bv"), 1)
                    dve.wait_ge(*at_count("u_done", g + 1))
                    dve.tensor_copy(u_tok.rearrange("p (n two d) -> p n two d", n=4, two=2)[:, :, par, :],
                                    bank[at[("u", g)]][:, 0:256].rearrange("p (n d) -> p n d", n=4)).then_inc(S("u"), 1)
                dve.wait_ge(*at_count("u", 2 * tt + 2))
                for half in range(2):
                    c = 2 * tt + half
                    rows = slice(64 * half, 64 * half + 64)
                    dve.wait_ge(*at_count("ws_done", c + 1))
                    if tt:
                        dve.wait_ge(*at_count("y_in_done", tt))
                    dve.scalar_tensor_tensor(sa[rows, :], bank[at[("ws", c)]][rows, :], -1.0, u_tok[rows, :], ALU.mult, ALU.subtract).then_inc(S("sa"), 1)
                    if c == 7:
                        continue
                    dve.wait_ge(*at_count("new_state_done", c + 1))
                    dve.wait_ge(*at_count("r_state", c + 1))
                    dve.tensor_tensor(r_state[:, :, :].rearrange("p n i -> p (n i)"), r_state[:, :, :].rearrange("p n i -> p (n i)"),
                                      bank[at[("new_state", c)]][:, :], ALU.add).then_inc(S("r_state_sum"), 1)
                    dve.wait_ge(*at_count("r_state_sum", c + 1))
                    for n in range(RW):
                        ins = dve.scalar_tensor_tensor(r_state[:, n, :], r_state[:, n, :], chunk_p[:, n, c, :], constant("same_head"), ALU.mult, ALU.mult)
                    ins.then_inc(S("r_state"), 1)
                dve.wait_ge(*at_count("y_state_done", 2 * tt + 2))
                dve.tensor_copy(y_rwkv[:, :, tt * P:tt * P + P], wide(bank[at[("y_state", tt)]][:, :])).then_inc(S("y_state"), 1)
                dve.wait_ge(*at_count("y_state", tt + 1))
                dve.wait_ge(*at_count("y_in_done", tt + 1))
                dve.tensor_tensor(y_rwkv[:, :, tt * P:tt * P + P], y_rwkv[:, :, tt * P:tt * P + P], wide(bank[at[("y_in", tt)]][:, :]), ALU.add).then_inc(S("y_raw"), 1)
            dve.wait_ge(*at_count("y_raw", TT))
            for n in range(RW):
                dve.wait_ge(*at_count("gn_mean_done", n + 1))
                dve.scalar_tensor_tensor(y_rwkv[:, n, :], bank[at[("gn_mean", n)]][:, :], -1 / 64, y_rwkv[:, n, :], ALU.mult, ALU.add).then_inc(S("gn_centred"), 1)
            for n in range(RW):
                dve.wait_ge(*at_count("gn_std", n + 1))
                steps.mark(dve.reciprocal(cum_p[:, n, :], cum_p[:, n, :]))
            steps.wait()
            for n in range(RW):
                steps.mark(dve.scalar_tensor_tensor(y_rwkv[:, n, :], y_rwkv[:, n, :], column("rwkv_gn_w", n), cum_p[:, n, :], ALU.mult, ALU.mult))
            steps.wait()
            for n in range(RW):
                steps.mark(dve.scalar_tensor_tensor(y_rwkv[:, n, :], y_rwkv[:, n, :], column("rwkv_gn_b", n), bonus[:, n, :], ALU.add, ALU.add))
            steps.wait()
            for n in range(RW):
                dve.wait_ge(*at_count("gate_r", n + 1))
                dve.tensor_tensor(y_rwkv[:, n, :], y_rwkv[:, n, :], gate_r[:, n, :], ALU.mult).then_inc(S("y_rwkv"), 1)

        def pool_rwkv(pool):
            for g in range(2 * TT):
                pool.wait_ge(*at_count("pairs", 4 * g + 1))
                for l in range(6):
                    if g or l:
                        pool.wait_ge(*at_count("ox_done", 6 * g + l))
                    if l == 1:
                        pool.wait_ge(*at_count("inv", 11 * g + 1))
                    pool.tensor_tensor(level_t[:, :].rearrange("p (h t) -> p h t", h=4), a_t[:, :].rearrange("p (h t) -> p h t", h=4),
                                       constant("levels", l).rearrange("p (a t) -> p a t", a=1).broadcast_to([P, 4, P]), ALU.mult).then_inc(S("level"), 1)
        moe_sum = area(0, KD, T)
        expert_act = area(4096, 2, 2, T)
        expert_silu = area(6144, 2, T)
        expert_w = area(7168, 2, T)
        logits = area(8192, TT, 36)
        one_group, masked_e = area(8400, TT, NG), area(8464, TT * NG * EG)
        chosen = area(8600, TT, EG)
        ranked = area(8640, TT, EG)
        first, second = area(8680, TT, EG), area(8720, TT, EG)
        tiny = area(8760, 12 * TT)
        combine = area(8820, TT, NE)
        combine_t = area(8960, T)
        exp_g = area(9480, TT, NG)
        CAP_E = P
        h_tok = area(10000, 2, D)
        rows_in = area(12048, 2, D)
        rows_t = area(14096, 2, KD * P)
        sparse_silu, sparse_act = area(16144, 2 * P), area(16400, 2, 2 * P)
        y_rows = area(16912, 2, D)
        y_pick = area(18960, 4, D)
        pick = [area(23056, TT, NE), area(23184, TT, NE)]
        assigned, rank = area(23312, TT, NE), area(23440, TT, NE)
        table_row, y_row = area(23568, TT, NE), area(23696, TT, NE)
        picked = area(23824, TT, NE)
        totals = area(23952, NE)
        row_f = area(23984, 4 * TT)
        flag_f = area(24000, 1)
        table_w = slot_table[:, :].bitcast(F32)
        pair_w = pairs_u[:, :].bitcast(F32)

        def expert_unit(e, x):
            return at["moe_units"] + 6 * e - 2 + x

        def pe_moe(pe, mm, take, unit, unit_landed, freed, turn):
            out = take(("router",), ("logits", 1))
            pe.wait_ge(*at_count("norm_ffn_h", KD))
            for tt in range(TT):
                for k in range(KD):
                    last = mm(out[:, tt * 36:tt * 36 + 36], hT[:, k, tt * P:tt * P + P], router_w[:, k, :], k == 0, k == KD - 1)
            last.then_inc(S("router_done"), 1)
            for i in range(2 * TT):
                out = take(("h_tok", i), ("h_tok", i + 1))
                for n in range(4):
                    last = mm(out[:, n * P:n * P + P], hT[:, i % 2 * 4 + n, i // 2 * P:i // 2 * P + P], ident)
                last.then_inc(S("h_turned"), 1)
            out = take(("ranks",), ("totals", 1))
            pe.wait_ge(*at_count("assigned", 1))
            for tt in range(TT):
                for before in range(tt):
                    mm(out[:, tt * NE:tt * NE + NE], ones, assigned[:, before, :], before == 0, False)
                mm(out[:, tt * NE:tt * NE + NE], constant("causal"), assigned[:, tt, :], tt == 0, True)
            for tt in range(TT):
                last = mm(out[:, P:P + NE], ones, assigned[:, tt, :], tt == 0, tt == TT - 1)
            last.then_inc(S("ranks_done"), 1)
            u0 = at["moe_units"] = unit[0]

            def weights(e, x):
                if isinstance(e, int):
                    x = x + 2 if e == 0 else x - 4 if e == NE else x
                q, slot = divmod(u0 - 2 + x, RING)
                pe.wait_ge(*at_count(f"landed{slot}", (e + (q + 1)) * 16))
                return ring[:, slot, :].rearrange("p (k n) -> p k n", k=8)

            def gate_up(e, wait):
                for x in range(4):
                    w = weights(e, x)
                    if wait:
                        pe.wait_ge(*at_count("moe_silu" if x < 2 else "moe_up", (e - 1) * 2 + x % 2 + 1))
                    for k in range(KD):
                        last = mm(bank[x][:, :], w[:, k, :], hT[:, k, :], k == 0, k == KD - 1)
                    last.then_inc(S("unit_done"), 1)

            def down(e, first):
                w = [weights(e, 4), weights(e, 5)]
                pe.wait_ge(*at_count("moe_act", e * 2))
                for n in range(KD):
                    if n >= 4:
                        pe.wait_ge(*at_count("moe_add", (e - 1) * 8 + (n - 3)))
                    elif not first:
                        pe.wait_ge(*at_count("moe_add", (e - 2) * 8 + (n + 5)))
                    par = down.parity
                    for f in range(2):
                        last = mm(bank[4 + n % 4][:, :], w[f][:, n, :], expert_act[:, par, f, :], f == 0, f == 1)
                        if n == KD - 1:
                            last.then_inc(S("unit_done"), 1)
                    if n < KD - 1:
                        last.then_inc(S("down_done"), 1)

            for b in range(8):
                pe.wait_ge(*at_count(*freed[b]))
            pe.wait_ge(*at_count("flag", 1))
            overflow = pe.value_load(flag[0:1, 0:1], min_val=0, max_val=1)
            with pe.If(overflow):
                pe_dense(pe, mm, weights, gate_up, down, u0)
            with pe.Else():
                pe_sparse(pe, mm, weights)
            unit[0] = u0 + 6 * NE
            freed[:] = [("x_moe", KD)] * 8

        def pe_dense(pe, mm, weights, gate_up, down, u0):
            pe.wait_ge(*at_count("combine", 1))
            for tt in range(TT):
                last = mm(bank[4][0:NE, tt * P:tt * P + P], combine[:, tt, :], ident)
            last.then_inc(S("combine_turned"), 1)
            for x in range(4):
                w = weights(0, x)
                for k in range(KD):
                    last = mm(bank[x][:, :], w[:, k, :], hT[:, k, :], k == 0, k == KD - 1)
                last.then_inc(S("unit_done"), 1)
            gate_up(1, True)
            down.parity = 0
            pe.wait_ge(*at_count("combine_t", 1))
            down(1, True)
            with pe.Fori(0, (NE - 2) // 2) as i:
                for j in range(2):
                    e = i * 2 + (2 + j)
                    gate_up(e, True)
                    down.parity = (j + 1) % 2
                    down(e, False)
            pe_last_down(pe, mm, u0)

        def pe_last_down(pe, mm, u0):
            u = u0 + 4 + 6 * (NE - 1)
            w = []
            for f in range(2):
                pe.wait_ge(*at_count(f"landed{(u + f) % RING}", 16 * ((u + f) // RING + 1)))
                w.append(ring[:, (u + f) % RING, :].rearrange("p (k n) -> p k n", k=8))
            pe.wait_ge(*at_count("moe_act", 2 * NE))
            for n in range(KD):
                pe.wait_ge(*at_count("moe_add", KD * (NE - 1) + n - 3))
                for f in range(2):
                    last = mm(bank[4 + n % 4][:, :], w[f][:, n, :], expert_act[:, (NE - 1) % 2, f, :], f == 0, f == 1)
                    if n == KD - 1:
                        last.then_inc(S("unit_done"), 1)
                if n < KD - 1:
                    last.then_inc(S("down_done"), 1)

        def act_moe(act, steps):
            act.wait_ge(*at_count("group_arg", 1))
            act.activation(exp_g[:, :, :], exp_g[:, :, :], ACT.Exp).then_inc(S("group_exp"), 1)
            act.wait_ge(*at_count("second_arg", 1))
            act.activation(tiny[:, 4 * TT:5 * TT], tiny[:, 4 * TT:5 * TT], ACT.Exp).then_inc(S("second_exp"), 1)
            for i in range(2 * TT):
                tt, half = divmod(i, 2)
                act.wait_ge(*at_count("h_turned", i + 1))
                if tt >= 2 and half == 0:
                    act.wait_ge(*at_count(f"h_stored{tt % 2}", 16 * (tt // 2)))
                act.activation(h_tok[:, tt % 2, half * 512:half * 512 + 512], bank[at[("h_tok", i)]][:, :], ACT.Copy).then_inc(S("h_tok"), 1)
                if half:
                    act.wait_ge(*at_count("h_tok", i + 1))
                    act.dma_start(h_d[tt * P:tt * P + P, :], h_tok[:, tt % 2, :]).then_inc(S(f"h_stored{tt % 2}"), 16)
            act.wait_ge(*at_count("flag", 1))
            overflow = act.value_load(flag[0:1, 0:1], min_val=0, max_val=1)
            with act.If(overflow):
                act_dense(act)
            with act.Else():
                act_sparse(act)

        def act_dense(act):
            act.wait_ge(*at_count("combine_turned", 1))
            act.activation(combine_t[0:NE, :], bank[4][0:NE, :], ACT.Copy).then_inc(S("combine_t"), 1)
            act.wait_ge(*at_count("combine_t", 1))
            act.dma_start(combine_d, combine_t[0:NE, :]).then_inc(S("combine_stored"), 16)

            def silu(e, wait):
                for f in range(2):
                    act.wait_ge(*at_count("unit_done", e * 6 + (at["moe_units"] - 2 + f + 1 + (0 if wait else 2))))
                    if wait:
                        act.wait_ge(*at_count("moe_act", (e - 1) * 2 + f + 1))
                    act.activation(expert_silu[:, f, :], bank[f][:, :], ACT.Silu).then_inc(S("moe_silu"), 1)

            silu(0, False)
            silu(1, True)
            with act.Fori(0, (NE - 2) // 2) as i:
                for j in range(2):
                    silu(i * 2 + (2 + j), True)

        def dve_moe(dve, steps):
            def wide(x, n):
                return x.rearrange("p (t a) -> p t a", a=1).broadcast_to([P, TT, n])

            gm, gw, g_rank, m1, m2, w1, w2, rk = (tiny[:, i * TT:i * TT + TT] for i in (0, 1, 2, 3, 4, 5, 6, 7))
            dve.wait_ge(*at_count("router_done", 1))
            dve.tensor_tensor(logits[:, :, :], bank[at[("router",)]][:, 0:4 * 36].rearrange("p (t n) -> p t n", t=TT),
                              router_b.rearrange("p (a n) -> p a n", a=1).broadcast_to([P, TT, 36]), ALU.add).then_inc(S("logits"), 1)
            dve.wait_ge(*at_count("logits", 1))
            gl = logits[:, :, 0:NG]

            def step(ins):
                steps.mark(ins)
                steps.wait()

            def first_max(dst, src, top, ranks, n):
                step(dve.tensor_tensor(dst, src, wide(top, n), ALU.is_equal))
                step(dve.tensor_tensor(dst, dst, ranks.rearrange("p (a n) -> p a n", a=1).broadcast_to([P, TT, n]), ALU.mult))
                step(dve.tensor_reduce(rk, dst, AX.X, ALU.max))
                step(dve.tensor_tensor(dst, dst, wide(rk, n), ALU.is_equal))

            step(dve.tensor_reduce(gm, gl, AX.X, ALU.max))
            dve.tensor_tensor(exp_g[:, :, :], gl, wide(gm, NG), ALU.subtract).then_inc(S("group_arg"), 1)
            first_max(one_group[:, :, :], gl, gm, constant("rank4", 0, 4), NG)
            step(dve.tensor_tensor(masked_e.rearrange("p (t g e) -> p t g e", t=TT, g=NG), logits[:, :, NG:].rearrange("p t (g e) -> p t g e", g=NG),
                                   one_group.rearrange("p t (g a) -> p t g a", a=1).broadcast_to([P, TT, NG, EG]), ALU.mult))
            step(dve.tensor_reduce(chosen[:, :, :], masked_e.rearrange("p (t g e) -> p t e g", t=TT, g=NG), AX.X, ALU.add))
            step(dve.tensor_reduce(m1, chosen[:, :, :], AX.X, ALU.max))
            first_max(first[:, :, :], chosen[:, :, :], m1, constant("rank8", 0, 8), EG)
            step(dve.scalar_tensor_tensor(ranked[:, :, :], first[:, :, :], -3.0e38, chosen[:, :, :], ALU.mult, ALU.add))
            step(dve.tensor_reduce(m2, ranked[:, :, :], AX.X, ALU.max))
            first_max(second[:, :, :], ranked[:, :, :], m2, constant("rank8", 0, 8), EG)
            dve.tensor_tensor(m2, m2, m1, ALU.subtract).then_inc(S("second_arg"), 1)
            for o, within in zip(pick, (first, second)):
                steps.mark(dve.tensor_tensor(o.rearrange("p t (g e) -> p t g e", g=NG), one_group.rearrange("p t (g a) -> p t g a", a=1).broadcast_to([P, TT, NG, EG]),
                                             within.rearrange("p t (a e) -> p t a e", a=1).broadcast_to([P, TT, NG, EG]), ALU.mult))
            steps.wait()
            dve.tensor_tensor(assigned[:, :, :], pick[0], pick[1], ALU.add).then_inc(S("assigned"), 1)
            dve.wait_ge(*at_count("group_exp", 1))
            step(dve.tensor_reduce(gw, exp_g[:, :, :], AX.X, ALU.add))
            dve.wait_ge(*at_count("second_exp", 1))
            step(dve.tensor_scalar(w1, m2, 1.0, None, ALU.add))
            step(dve.tensor_tensor(w1, w1, gw, ALU.mult))
            step(dve.reciprocal(w1, w1))
            step(dve.tensor_tensor(w2, w1, m2, ALU.mult))
            dve.wait_ge(*at_count("ranks_done", 1))
            ranks = bank[at[("ranks",)]]
            experts = constant("expert_id", 0, NE).rearrange("p (a n) -> p a n", a=1).broadcast_to([P, TT, NE])
            steps.mark(dve.tensor_tensor(rank[:, :, :], ranks[:, 0:P].rearrange("p (t e) -> p t e", t=TT), assigned[:, :, :], ALU.subtract))
            dve.tensor_copy(totals[:, :], ranks[:, P:P + NE]).then_inc(S("totals"), 1)
            steps.wait()
            steps.mark(dve.scalar_tensor_tensor(table_row[:, :, :], rank[:, :, :], float(NE), experts, ALU.mult, ALU.add))
            steps.mark(dve.scalar_tensor_tensor(y_row[:, :, :], experts, float(P), rank[:, :, :], ALU.mult, ALU.add))
            dve.wait_ge(*at_count("totals", 1))
            steps.mark(dve.tensor_reduce(flag_f, totals[:, :], AX.X, ALU.max))
            steps.wait()
            for j in range(2):
                for i, rows in enumerate((table_row, y_row)):
                    step(dve.tensor_tensor(picked[:, :, :], pick[j], rows[:, :, :], ALU.mult))
                    o = (2 * i + j) * TT
                    step(dve.tensor_reduce(row_f[:, o:o + TT], picked[:, :, :], AX.X, ALU.add))
            steps.mark(dve.tensor_copy(rows_u[:, :], row_f[:, :]))
            pairs_t = pairs_u[:, :].rearrange("p (j t x) -> p j t x", j=2, x=2)
            pairs_f = pair_w.rearrange("p (j t x) -> p j t x", j=2, x=2)
            for j, w in enumerate((w1, w2)):
                steps.mark(dve.tensor_copy(pairs_t[:, j, :, 0], constant("token_id", 0, TT)))
                steps.mark(dve.tensor_copy(pairs_f[:, j, :, 1], w))
            steps.wait()
            dve.engine_nop().then_inc(S("slots"), 1)
            dve.tensor_scalar(flag[0:1, 0:1], flag_f[0:1, :], float(CAP_E), None, ALU.is_gt).then_inc(S("flag"), 1)
            dve.wait_ge(*at_count("flag", 1))
            overflow = dve.value_load(flag[0:1, 0:1], min_val=0, max_val=1)
            with dve.If(overflow):
                dve_dense(dve, pick, w1, w2)
            with dve.Else():
                dve_sparse(dve)

        def dve_dense(dve, pick, w1, w2):
            def wide(x, n):
                return x.rearrange("p (t a) -> p t a", a=1).broadcast_to([P, TT, n])

            dve.tensor_tensor(picked[:, :, :], pick[0], wide(w1, NE), ALU.mult).then_inc(S("weighed"), 1)
            dve.tensor_tensor(rank[:, :, :], pick[1], wide(w2, NE), ALU.mult).then_inc(S("weighed"), 1)
            dve.wait_ge(*at_count("weighed", 2))
            dve.tensor_tensor(combine[:, :, :], picked[:, :, :], rank[:, :, :], ALU.add).then_inc(S("combine"), 1)

            def weigh(e, par, wait):
                base = at["moe_units"] - 2 + (0 if wait else 2)
                for f in range(2):
                    dve.wait_ge(*at_count("unit_done", e * 6 + (base + 2 + f + 1)))
                    dve.wait_ge(*at_count("moe_silu", e * 2 + (f + 1)))
                    dve.tensor_tensor(expert_silu[:, f, :], expert_silu[:, f, :], bank[2 + f][:, :], ALU.mult).then_inc(S("moe_up"), 1)
                for f in range(2):
                    if f == 0:
                        dve.wait_ge(*at_count(f"expert_w{par}", weigh.landed))
                    dve.wait_ge(*at_count("moe_up", e * 2 + (f + 1)))
                    dve.tensor_tensor(expert_act[:, par, f, :], expert_silu[:, f, :], expert_w[:, par, :], ALU.mult).then_inc(S("moe_act"), 1)

            def add(e, first_one, last_one=False):
                for n in range(KD):
                    if n < KD - 1:
                        dve.wait_ge(*at_count("down_done", (e - 1) * 7 + (n + 1)))
                    else:
                        dve.wait_ge(*at_count("unit_done", e * 6 + (at["moe_units"] - 2 + 6) if not last_one else at["moe_units"] + 6 * NE))
                    b = bank[4 + n % 4][:, :]
                    if first_one:
                        dve.tensor_copy(moe_sum[:, n, :], b).then_inc(S("moe_add"), 1)
                    else:
                        if n == 0:
                            dve.wait_ge(*at_count("moe_add", (e - 1) * 8))
                        dve.tensor_tensor(moe_sum[:, n, :], moe_sum[:, n, :], b, ALU.add).then_inc(S("moe_add"), 1)

            weigh.landed = 16
            weigh(0, 0, False)
            weigh(1, 1, True)
            add(1, True)
            with dve.Fori(0, (NE - 2) // 2) as i:
                for j in range(2):
                    weigh.landed = i * 16 + 32
                    weigh(i * 2 + (2 + j), j, True)
                    add(i * 2 + (2 + j), False)
            add(NE, False, last_one=True)
            dve.wait_ge(*at_count("moe_add", KD * NE))
            for k in range(KD):
                dve.scalar_tensor_tensor(xT[:, k, :], moe_sum[:, k, :], mod[:, G_F + k:G_F + k + 1], xT[:, k, :],
                                         ALU.mult, ALU.add).then_inc(S("x_moe"), 1)

        def pool_moe(pool):
            pool.memset(slot_table[:, :], 0).then_inc(S("table_clear"), 1)
            pool.wait_ge(*at_count("table_clear", 1))
            table = table_d[0:CAP_E * NE, :].rearrange("(s e) x -> s (e x)", e=NE)
            pool.dma_start(table, slot_table[:, :]).then_inc(S("table_zeroed"), 16)
            pool.wait_ge(*at_count("table_zeroed", 16))
            pool.wait_ge(*at_count("slots", 1))
            for i in range(2 * TT):
                pool.indirect_dma_start(out=table_d, out_offset=bass.IndirectOffsetOnAxis(ap=rows_u[:, i:i + 1], axis=0),
                                        in_=pairs_u[:, 2 * i:2 * i + 2], in_offset=None).then_inc(S("table_filled"), 16)
            pool.wait_ge(*at_count("table_filled", 16 * 2 * TT))
            pool.dma_start(slot_table[:, :], table).then_inc(S("table_landed"), 16)
            pool.wait_ge(*at_count("flag", 1))
            overflow = pool.value_load(flag[0:1, 0:1], min_val=0, max_val=1)
            with pool.If(overflow):
                pool_dense(pool)
            with pool.Else():
                pool_sparse(pool)

        def pool_dense(pool):
            pool.wait_ge(*at_count("combine_stored", 16))
            for e in range(2):
                pool.dma_start(expert_w[:, e, :], combine_d[e:e + 1, :].broadcast_to([P, T])).then_inc(S(f"expert_w{e}"), 16)
            with pool.Fori(0, (NE - 2) // 2) as i:
                for j in range(2):
                    pool.wait_ge(*at_count("moe_act", i * 4 + 2 * (j + 1)))
                    pool.dma_start(expert_w[:, j, :], combine_d[bass.ds(i * 2 + (2 + j), 1), :].broadcast_to([P, T])).then_inc(S(f"expert_w{j}"), 16)

        def pe_sparse(pe, mm, weights):
            def turn_rows(e, par, first):
                pe.wait_ge(*at_count(f"gathered{par}", turn_rows.landed))
                for i in range(2):
                    if not first:
                        pe.wait_ge(*at_count("expert_in", (e - 1) * 2 + i + 1))
                    for n in range(4):
                        last = mm(bank[i][:, n * P:n * P + P], rows_in[:, par, (4 * i + n) * P:(4 * i + n + 1) * P], ident)
                    last.then_inc(S("rows_turned"), 1)

            def gate_up(e, par, first):
                pe.wait_ge(*at_count("expert_in", e * 2 + 2))
                for x in range(4):
                    w = weights(e, x)
                    if x % 2 == 0 and not first:
                        pe.wait_ge(*at_count("sparse_silu" if x < 2 else "sparse_act", e))
                    for k in range(KD):
                        last = mm(bank[2 + x // 2][:, x % 2 * P:x % 2 * P + P], w[:, k, :], rows_t[:, par, k * P:k * P + P], k == 0, k == KD - 1)
                    last.then_inc(S("unit_done"), 1)

            def down(e, par, first):
                w = [weights(e, 4), weights(e, 5)]
                pe.wait_ge(*at_count("sparse_act", e))
                for half in range(2):
                    if not first:
                        pe.wait_ge(*at_count("sparse_y", (e - 2) * 2 + half + 1))
                    for f in range(2):
                        last = mm(bank[4 + half][:, :], sparse_act[:, par, f * P:f * P + P],
                                  w[f].rearrange("p k n -> p (k n)")[:, half * 512:half * 512 + 512], f == 0, f == 1)
                        if half:
                            last.then_inc(S("unit_done"), 1)
                    if not half:
                        last.then_inc(S("sparse_down"), 1)

            def last_landed(e):
                turn_rows.landed = 16 * (e // 2 + 1)

            last_landed(0)
            turn_rows(0, 0, True)
            gate_up(0, 0, True)
            turn_rows(1, 1, False)
            gate_up(1, 1, False)
            down(1, 0, True)
            last_landed(2)
            turn_rows(2, 0, False)
            with pe.Fori(0, (NE - 4) // 2) as i:
                for j in range(2):
                    e = i * 2 + (2 + j)
                    gate_up(e, j, False)
                    down(e, 1 - j, False)
                    turn_rows.landed = i * 16 + 32 + 16 * j
                    turn_rows(e + 1, 1 - j, False)
            gate_up(NE - 2, 0, False)
            down(NE - 2, 1, False)
            last_landed(NE - 1)
            turn_rows(NE - 1, 1, False)
            gate_up(NE - 1, 1, False)
            down(NE - 1, 0, False)
            down(NE, 1, False)
            pe.wait_ge(*at_count("sparse_y", 2 * NE))
            for tt in range(TT):
                pe.wait_ge(*at_count("y_picked", tt + 1))
                for n in range(KD):
                    last = mm(bank[n][:, tt * P:tt * P + P], y_pick[:, 2 * tt % 4, n * P:n * P + P], ident)
                last.then_inc(S("y_turned"), 1)

        def act_sparse(act):
            def rows_out(e, par):
                for i in range(2):
                    act.wait_ge(*at_count("rows_turned", e * 2 + i + 1))
                    act.activation(rows_t[:, par, i * 512:i * 512 + 512], bank[i][:, :], ACT.Copy).then_inc(S("expert_in"), 1)

            def silu(e, first):
                if first:
                    act.wait_ge(*at_count("unit_done", at["moe_units"] + 2))
                else:
                    act.wait_ge(*at_count("unit_done", e * 6 + at["moe_units"]))
                    act.wait_ge(*at_count("sparse_act", e))
                act.activation(sparse_silu, bank[2][:, 0:2 * P], ACT.Silu).then_inc(S("sparse_silu"), 1)

            def store(e, par):
                act.wait_ge(*at_count("sparse_y", e * 2 + 2))
                act.dma_start(y_d[bass.ds(e * P, P), :] if not isinstance(e, int) else y_d[e * P:e * P + P, :],
                              y_rows[:, par, :]).then_inc(S(f"y_stored{par}"), 16)

            rows_out(0, 0)
            silu(0, True)
            rows_out(1, 1)
            silu(1, False)
            rows_out(2, 0)
            store(0, 0)
            with act.Fori(0, (NE - 4) // 2) as i:
                for j in range(2):
                    e = i * 2 + (2 + j)
                    silu(e, False)
                    rows_out(e + 1, 1 - j)
                    store(e - 1, 1 - j)
            silu(NE - 2, False)
            rows_out(NE - 1, 1)
            store(NE - 3, 1)
            silu(NE - 1, False)
            store(NE - 2, 0)
            store(NE - 1, 1)

        def dve_sparse(dve):
            def product(e, par, first):
                if first:
                    dve.wait_ge(*at_count("unit_done", at["moe_units"] + 4))
                else:
                    dve.wait_ge(*at_count("unit_done", e * 6 + (at["moe_units"] + 2)))
                dve.wait_ge(*at_count("sparse_silu", e + 1))
                dve.tensor_tensor(sparse_act[:, par, :], sparse_silu, bank[3][:, 0:2 * P], ALU.mult).then_inc(S("sparse_act"), 1)

            def weigh(e, par, weight):
                for half in range(2):
                    if half == 0:
                        dve.wait_ge(*at_count("sparse_down", e + 1))
                        if weigh.stored is not None:
                            dve.wait_ge(*at_count(f"y_stored{par}", weigh.stored))
                    else:
                        dve.wait_ge(*at_count("unit_done", (e + 1) * 6 + (at["moe_units"] + 4)) if not weigh.last
                                    else at_count("unit_done", at["moe_units"] + 6 * NE))
                    dve.tensor_scalar(y_rows[:, par, half * 512:half * 512 + 512], bank[4 + half][:, :], weight, None, ALU.mult).then_inc(S("sparse_y"), 1)

            def weight_of(e):
                return table_w[:, 2 * e + 1:2 * e + 2] if isinstance(e, int) else table_w[:, bass.ds(e * 2 + 1, 1)]

            weigh.last, weigh.stored = False, None
            dve.wait_ge(*at_count("table_landed", 16))
            product(0, 0, True)
            product(1, 1, False)
            weigh(0, 0, weight_of(0))
            product(2, 0, False)
            weigh(1, 1, weight_of(1))
            with dve.Fori(0, (NE - 4) // 2) as i:
                for j in range(2):
                    e = i * 2 + (3 + j)
                    weigh.stored = i * 16 + 16
                    product(e, 1 - j, False)
                    weigh(e - 1, j, weight_of(e - 1))
            product(NE - 1, 1, False)
            weigh.stored = 16 * (NE // 2 - 1)
            weigh(NE - 2, 0, weight_of(NE - 2))
            weigh.last = True
            weigh(NE - 1, 1, weight_of(NE - 1))
            for tt in range(TT):
                a, b = 2 * tt % 4, 2 * tt % 4 + 1
                dve.wait_ge(*at_count(f"picked{a}", 16 * (tt // 2 + 1)))
                dve.wait_ge(*at_count(f"picked{b}", 16 * (tt // 2 + 1)))
                dve.tensor_tensor(y_pick[:, a, :], y_pick[:, a, :], y_pick[:, b, :], ALU.add).then_inc(S("y_picked"), 1)
            for n in range(KD):
                dve.wait_ge(*at_count("y_turned", TT))
                dve.scalar_tensor_tensor(xT[:, n, :], bank[n][:, :], mod[:, G_F + n:G_F + n + 1], xT[:, n, :],
                                         ALU.mult, ALU.add).then_inc(S("x_moe"), 1)

        def pool_sparse(pool):
            pool.wait_ge(*at_count("table_landed", 16))
            for par in range(2):
                pool.wait_ge(*at_count(f"h_stored{par}", 16 * TT // 2))
            for e in range(NE):
                if e >= 2:
                    pool.wait_ge(*at_count("rows_turned", 2 * (e - 1)))
                pool.indirect_dma_start(out=rows_in[:, e % 2, :], out_offset=None, in_=h_d,
                                        in_offset=bass.IndirectOffsetOnAxis(ap=slot_table[:, 2 * e:2 * e + 1], axis=0)).then_inc(S(f"gathered{e % 2}"), 16)
            pool.wait_ge(*at_count("y_stored0", 16 * NE // 2))
            pool.wait_ge(*at_count("y_stored1", 16 * NE // 2))
            for tt in range(TT):
                for j in range(2):
                    i = 2 * tt + j
                    if tt >= 2:
                        pool.wait_ge(*at_count("y_turned", tt - 1))
                    r = 2 * TT + j * TT + tt
                    pool.indirect_dma_start(out=y_pick[:, i % 4, :], out_offset=None, in_=y_d,
                                            in_offset=bass.IndirectOffsetOnAxis(ap=rows_u[:, r:r + 1], axis=0)).then_inc(S(f"picked{i % 4}"), 16)
        SH = 8
        y_ssm = area(0, 16, T)
        conv_u = area(8192, 2, UP + T)
        conv_y = area(9276, KD, T)
        xbc_raw = area(13372, 6, TP)
        xbc = area(16468, 6, T)
        x_dt = area(19540, TT, 512)
        x_w = area(21588, 2, 512)
        b_tok2 = area(22612, TT, P)
        states = area(23124, TT - 1, 512)
        cb = area(24660, TT, P)
        seg = area(25172, 2, T)
        exp_acs = area(26196, T)
        row_acs, row_dtw = area(26708, T), area(27220, T)
        row_tmp, row_dt = rstd[:, 0, :], rstd[:, 1, :]
        ssm_cols = area(27732, 3 * TT * SH)
        last_exp = area(27828, SH * TT)
        a_pos = area(27860, NG)
        ln_square = area(13372, KD, T)
        merged = area(19540, KD, T)
        sig = area(25172, 2, T)
        G_UNITS = 14
        DT, DTW, ACS = range(3)

        def ssm_col(which, tt):
            c = (which * TT + tt) * SH
            return ssm_cols[:, c:c + SH]

        def channel(g, i):
            return 4 * g + i if i < 4 else (16 if i == 4 else 20) + g

        def pe_mix2(pe, mm, take, project, h_tiles):
            counts = [list(range(1, KD + 1))]

            def group_in(g):
                first = counts.pop() if counts else None
                for i in range(6):
                    project(("xbc", g, i), ("xbc_raw", 6 * g + i + 1), h_tiles, "norm_mix2_h", first if i == 0 else None)
                for i in range(4):
                    project(("z", g, i), ("z", 4 * g + i + 1), h_tiles, None, None)
                for i in range(2):
                    project(("conv_a", g, i), ("conv_u", 2 * g + i + 1), h_tiles, None, None)
                    project(("conv_b", g, i), ("conv_gate", 2 * g + i + 1), h_tiles, None, None)

            group_in(0)
            for g in range(NG):
                out = take(("dt", g), ("dt_raw", g + 1))
                for k in range(KD):
                    last = mm(out[0:SH, :], dt_w[:, k, SH * g:SH * g + SH], h_tiles[k], k == 0, k == KD - 1)
                last.then_inc(S("dt_done"), 1)
                if g < NG - 1:
                    group_in(g + 1)
                pe.wait_ge(*at_count("xbc", 6 * g + 6))
                out = take(("b_tok", g), ("b_tok", g + 1))
                for tt in range(TT):
                    last = mm(out[:, tt * P:tt * P + P], xbc[:, 4, tt * P:tt * P + P], ident)
                last.then_inc(S("b_turned"), 1)
                out = take(("ssm_cols", g), ("ssm_cols", 2 * g + 2))
                pe.wait_ge(*at_count("rows", g + 1))
                for which, row in ((DT, row_dt), (DTW, row_dtw), (ACS, row_acs)):
                    for tt in range(TT):
                        c = (which * TT + tt) * SH
                        mm(out[:, c:c + SH], row[0:SH, tt * P:tt * P + P], ident[0:SH, 0:SH])
                for h in range(SH):
                    last = mm(out[:, 96 + TT * h:96 + TT * h + TT], constant("sel8", h, rows=SH), row_acs[0:SH, P - 1:T:P])
                last.then_inc(S("ssm_cols_done"), 1)
                out = take(("cb", g), ("cb", g + 1))
                for tt in range(TT):
                    last = mm(out[:, tt * P:tt * P + P], xbc[:, 4, tt * P:tt * P + P], xbc[:, 5, tt * P:tt * P + P])
                last.then_inc(S("cb_done"), 1)
                for tt in range(TT):
                    out = take(("x_tok", g, tt), ("x_tok", 2 * (TT * g + tt) + 2))
                    for i in range(4):
                        last = mm(out[:, i * P:i * P + P], xbc[:, i, tt * P:tt * P + P], ident)
                    last.then_inc(S("x_turned"), 1)
                    if tt == 0:
                        pe.wait_ge(*at_count("b_tok", g + 1))
                    if tt < TT - 1:
                        pe.wait_ge(*at_count("x_tok", 2 * (TT * g + tt) + 2))
                        out = take(("states", g, tt), ("states", 3 * g + tt + 1))
                        mm(out[:, :], b_tok2[:, tt, :], x_w[:, tt % 2, :]).then_inc(S("states_done"), 1)
                for j in range(SH // 2):
                    n = 4 * g + j
                    diag = None
                    for o in range(2):
                        h, m = 2 * j + o, SH * g + 2 * j + o
                        out = take(("acs", m), ("seg_arg", TT * (m + 1)))
                        mm(out[:, :], constant("sel8", h, rows=SH), row_acs[0:SH, :]).then_inc(S("acs_done"), 1)
                    if j == 0:
                        pe.wait_ge(*at_count("states", 3 * g + 3))
                    out = take(("exp_acs", n), ("exp_acs", n + 1))
                    mm(out[:, :], constant("sel8_pair", j, rows=SH), row_acs[0:SH, :]).then_inc(S("pair_acs_done"), 1)
                    off = take(("y_off", n), ("y_off", n + 1))
                    for tt in range(1, TT):
                        last = mm(off[:, tt * P:tt * P + P], states[:, tt - 1, j * P:j * P + P], xbc[:, 5, tt * P:tt * P + P])
                    last.then_inc(S("y_off_done"), 1)
                    diag = take(("y_diag", n), ("y_skip", n + 1))
                    for o in range(2):
                        h, m = 2 * j + o, SH * g + 2 * j + o
                        pe.wait_ge(*at_count("seg", m + 1))
                        for tt in range(TT):
                            last = mm(diag[64 * o:64 * o + 64, tt * P:tt * P + P], x_dt[:, tt, h * 64:h * 64 + 64], seg[:, m % 2, tt * P:tt * P + P])
                        last.then_inc(S("y_diag_done"), 1)
                out = take(("group_sum", g), ("group_std", g + 1))
                for j in range(4):
                    pe.wait_ge(*at_count("group_square", 4 * g + j + 1))
                    last = mm(out[:, :], ones, xbc[:, j, :], j == 0, j == 3)
                last.then_inc(S("group_sum_done"), 1)
            out = take(("ln_mean",), ("ln_centred", KD))
            pe.wait_ge(*at_count("conv_y", KD * TAPS))
            for k in range(KD):
                last = mm(out[:, :], ones, conv_y[:, k, :], k == 0, k == KD - 1)
            last.then_inc(S("ln_mean_done"), 1)
            out = take(("ln_var",), ("ln_std", 1))
            for k in range(KD):
                pe.wait_ge(*at_count("ln_square", k + 1))
                last = mm(out[:, :], ones, ln_square[:, k, :], k == 0, k == KD - 1)
            last.then_inc(S("ln_var_done"), 1)
            conv_tiles = [conv_y[:, k, :] for k in range(KD)]
            ssm_tiles = [y_ssm[:, k, :] for k in range(16)]
            for n in range(KD):
                project(("g_conv", n), ("sig", 2 * n + 1), h_tiles, None, None)
                project(("conv_out", n), ("merge_conv", n + 1), conv_tiles, "conv_act", list(range(1, KD + 1)) if n == 0 else None)
                project(("g_ssm", n), ("sig", 2 * n + 2), h_tiles, None, None)
                if n == 0:
                    pe.wait_ge(*at_count("y_ssm", 16))
                project(("ssm_out", n), ("merge_ssm", n + 1), ssm_tiles, None, None)
            merged_tiles = [merged[:, k, :] for k in range(KD)]
            for n in range(KD):
                project(("w_out2", n), ("x_mix2", n + 1), merged_tiles, "merged", list(range(1, KD + 1)) if n == 0 else None)

        def act_mix2(act, steps):
            def group_out(g):
                for i in range(6):
                    act.wait_ge(*at_count("unit_done", at[("unit", "xbc", g, i)]))
                    if g:
                        act.wait_ge(*at_count("xbc_conv", 24 * g))
                    elif i == 0:
                        act.wait_ge(*at_count("pads2", 2))
                    act.activation(xbc_raw[:, i, PAD:TP], bank[at[("xbc", g, i)]][:, :], ACT.Copy).then_inc(S("xbc_raw"), 1)
                for i in range(4):
                    act.wait_ge(*at_count("unit_done", at[("unit", "z", g, i)]))
                    act.activation(y_ssm[:, 4 * g + i, :], bank[at[("z", g, i)]][:, :], ACT.Silu).then_inc(S("z"), 1)
                for i in range(2):
                    act.wait_ge(*at_count("unit_done", at[("unit", "conv_b", g, i)]))
                    if g:
                        act.wait_ge(*at_count("conv_y", 2 * g * TAPS))
                    act.activation(conv_u[:, i, UP:UP + T], bank[at[("conv_b", g, i)]][:, :], ACT.Sigmoid).then_inc(S("conv_gate"), 1)

            act.wait_ge(*at_count("x_moe", KD))
            act.activation(a_pos[0:SH, :], col[0:SH, COL["a_log_2"]:COL["a_log_2"] + NG], ACT.Exp).then_inc(S("a_pos"), 1)
            group_out(0)
            for g in range(NG):
                for i in range(6):
                    act.wait_ge(*at_count("xbc_conv", 24 * g + 18 + i + 1))
                    act.activation(xbc[:, i, :], xbc[:, i, :], ACT.Silu, bias=column("ssm_conv_b_2", channel(g, i))).then_inc(S("xbc"), 1)
                act.wait_ge(*at_count("dt_done", g + 1))
                if g == 0:
                    act.wait_ge(*at_count("norm_mix2_h", KD))
                act.activation(row_dt[0:SH, :], bank[at[("dt", g)]][0:SH, :], ACT.Identity, bias=column("dt_bias_2", g, SH)).then_inc(S("dt_raw"), 1)
                act.wait_ge(*at_count("dt_raw", g + 1))
                steps.mark(act.activation(row_tmp[0:SH, :], row_dt[0:SH, :], ACT.Abs))
                steps.wait()
                steps.mark(act.activation(row_tmp[0:SH, :], row_tmp[0:SH, :], ACT.Exp, scale=-1.0))
                steps.wait()
                act.activation(row_tmp[0:SH, :], row_tmp[0:SH, :], ACT.Ln, bias=column("one", rows=SH)).then_inc(S("dt_log"), 1)
                act.wait_ge(*at_count("end_arg", g + 1))
                act.activation(row_tmp[0:SH, :], row_tmp[0:SH, :], ACT.Exp).then_inc(S("end_exp"), 1)
                if g < NG - 1:
                    group_out(g + 1)
                act.wait_ge(*at_count("b_turned", g + 1))
                act.activation(b_tok2[:, :, :].rearrange("p a b -> p (a b)"), bank[at[("b_tok", g)]][:, :], ACT.Copy).then_inc(S("b_tok"), 1)
                act.wait_ge(*at_count("ssm_cols_done", g + 1))
                act.wait_ge(*at_count("ssm_cols", 2 * g + 1))
                act.activation(last_exp[:, :], bank[at[("ssm_cols", g)]][:, 96:96 + SH * TT], ACT.Exp, scale=-1.0).then_inc(S("ssm_cols"), 1)
                for j in range(4):
                    n = 4 * g + j
                    for o in range(2):
                        m = 2 * n + o
                        act.wait_ge(*at_count("seg_arg", TT * (m + 1)))
                        act.activation(seg[:, m % 2, :], seg[:, m % 2, :], ACT.Exp, scale=-1.0).then_inc(S("seg_exp"), 1)
                    act.wait_ge(*at_count("pair_acs_done", n + 1))
                    if n:
                        act.wait_ge(*at_count("y_sum", n))
                    act.activation(exp_acs, bank[at[("exp_acs", n)]][:, :], ACT.Exp, scale=-1.0).then_inc(S("exp_acs"), 1)
                for j in range(4):
                    act.wait_ge(*at_count("y_gated", 4 * g + j + 1))
                    act.activation(xbc[:, j, :], y_ssm[:, 4 * g + j, :], ACT.Square).then_inc(S("group_square"), 1)
                act.wait_ge(*at_count("group_sum_done", g + 1))
                act.activation(exp_acs, bank[at[("group_sum", g)]][:, :], ACT.Sqrt, bias=column("eps_norm"), scale=1 / 512).then_inc(S("group_std"), 1)
            for k in range(KD):
                act.wait_ge(*at_count("ln_centred", k + 1))
                act.activation(ln_square[:, k, :], conv_y[:, k, :], ACT.Square).then_inc(S("ln_square"), 1)
            act.wait_ge(*at_count("ln_var_done", 1))
            act.activation(rstd[:, 0, :], bank[at[("ln_var",)]][:, :], ACT.Sqrt, bias=column("eps_ln"), scale=1 / D).then_inc(S("ln_std"), 1)
            for k in range(KD):
                act.wait_ge(*at_count("ln_scaled", k + 1))
                act.activation(conv_y[:, k, :], conv_y[:, k, :], ACT.Silu, bias=column("conv_ln_b_2", k)).then_inc(S("conv_act"), 1)
            for n in range(KD):
                act.wait_ge(*at_count("unit_done", at[("unit", "g_conv", n)]))
                if n:
                    act.wait_ge(*at_count("merge_conv", n))
                act.activation(sig[:, 0, :], bank[at[("g_conv", n)]][:, :], ACT.Sigmoid).then_inc(S("sig"), 1)
                act.wait_ge(*at_count("unit_done", at[("unit", "g_ssm", n)]))
                if n:
                    act.wait_ge(*at_count("merged", n))
                act.activation(sig[:, 1, :], bank[at[("g_ssm", n)]][:, :], ACT.Sigmoid).then_inc(S("sig"), 1)

        def dve_mix2(dve, steps):
            def wide(x, n):
                return x.rearrange("p (h a) -> p h a", a=1).broadcast_to([P, x.shape[1], n])

            def by_head(x):
                return x.rearrange("p (h d) -> p h d", h=SH)

            dve.memset(xbc_raw[:, :, 0:PAD], 0.0).then_inc(S("pads2"), 1)
            dve.memset(conv_u[:, :, 0:UP], 0.0).then_inc(S("pads2"), 1)

            def gate_u(g):
                for i in range(2):
                    dve.wait_ge(*at_count("conv_gate", 2 * g + i + 1))
                    dve.wait_ge(*at_count("unit_done", at[("unit", "conv_a", g, i)]))
                    dve.tensor_tensor(conv_u[:, i, UP:UP + T], conv_u[:, i, UP:UP + T], bank[at[("conv_a", g, i)]][:, :], ALU.mult).then_inc(S("conv_u"), 1)

            dve.wait_ge(*at_count("pads2", 2))
            for g in range(NG):
                if g:
                    dve.wait_ge(*at_count("group_sum_done", g))
                for tap in range(4):
                    for i in range(6):
                        src = xbc_raw[:, i, PAD - 3 + tap:PAD - 3 + tap + T]
                        w = column("ssm_conv_w_2", 24 * tap + channel(g, i))
                        if tap == 0:
                            dve.wait_ge(*at_count("xbc_raw", 6 * g + i + 1))
                            dve.tensor_scalar(xbc[:, i, :], src, w, None, ALU.mult).then_inc(S("xbc_conv"), 1)
                        else:
                            dve.wait_ge(*at_count("xbc_conv", 24 * g + 6 * (tap - 1) + i + 1))
                            dve.scalar_tensor_tensor(xbc[:, i, :], src, w, xbc[:, i, :], ALU.mult, ALU.add).then_inc(S("xbc_conv"), 1)
                if g == 0:
                    dve.wait_ge(*at_count("a_pos", 1))
                    gate_u(0)
                dve.wait_ge(*at_count("dt_log", g + 1))
                steps.mark(dve.scalar_tensor_tensor(row_dt[0:SH, :], row_dt[0:SH, :], 0.0, row_tmp[0:SH, :], ALU.max, ALU.add))
                steps.wait()
                steps.mark(dve.tensor_scalar(row_tmp[0:SH, :], row_dt[0:SH, :], a_pos[0:SH, g:g + 1], None, ALU.mult))
                steps.wait()
                steps.mark(dve.tensor_tensor_scan(row_acs[0:SH, :], constant("reset128", 0, T, SH), row_tmp[0:SH, :], 0.0, ALU.mult, ALU.add))
                steps.wait()
                tiles = lambda x: x[0:SH, :].rearrange("h (c t) -> h c t", c=TT)
                dve.tensor_tensor(tiles(row_tmp), tiles(row_acs), row_acs[0:SH, P - 1:T:P].rearrange("h (c t) -> h c t", t=1).broadcast_to([SH, TT, P]),
                                  ALU.subtract).then_inc(S("end_arg"), 1)
                dve.wait_ge(*at_count("conv_u", 2 * g + 2))
                for tap in range(TAPS):
                    for i in range(2):
                        k = 2 * g + i
                        src = conv_u[:, i, tap:tap + T]
                        w = column("conv_dw_w_2", 8 * tap + k)
                        if tap == 0:
                            dve.tensor_scalar(conv_y[:, k, :], src, w, column("conv_dw_b_2", k), ALU.mult, ALU.add).then_inc(S("conv_y"), 1)
                        else:
                            dve.wait_ge(*at_count("conv_y", 2 * (g * TAPS + tap - 1) + i + 1))
                            dve.scalar_tensor_tensor(conv_y[:, k, :], src, w, conv_y[:, k, :], ALU.mult, ALU.add).then_inc(S("conv_y"), 1)
                dve.wait_ge(*at_count("end_exp", g + 1))
                dve.tensor_tensor(row_dtw[0:SH, :], row_tmp[0:SH, :], row_dt[0:SH, :], ALU.mult).then_inc(S("rows"), 1)
                if g < NG - 1:
                    dve.wait_ge(*at_count("conv_y", 2 * (g + 1) * TAPS))
                    gate_u(g + 1)
                dve.wait_ge(*at_count("ssm_cols_done", g + 1))
                dve.tensor_copy(ssm_cols[:, :], bank[at[("ssm_cols", g)]][:, 0:96]).then_inc(S("ssm_cols"), 1)
                dve.wait_ge(*at_count("cb_done", g + 1))
                dve.tensor_tensor(cb[:, :, :], bank[at[("cb", g)]][:, :].rearrange("p (c t) -> p c t", c=TT),
                                  constant("causal").rearrange("p (a t) -> p a t", a=1).broadcast_to([P, TT, P]), ALU.mult).then_inc(S("cb"), 1)
                dve.wait_ge(*at_count("ssm_cols", 2 * g + 2))
                for tt in range(TT):
                    dve.wait_ge(*at_count("x_turned", TT * g + tt + 1))
                    src = by_head(bank[at[("x_tok", g, tt)]][:, :])
                    dve.tensor_tensor(by_head(x_dt[:, tt, :]), src, wide(ssm_col(DT, tt), 64), ALU.mult).then_inc(S("x_tok"), 1)
                    if tt >= 2:
                        dve.wait_ge(*at_count("states_done", 3 * g + tt - 1))
                    dve.tensor_tensor(by_head(x_w[:, tt % 2, :]), src, wide(ssm_col(DTW, tt), 64), ALU.mult).then_inc(S("x_tok"), 1)
                    if tt == TT - 1:
                        continue
                    if tt:
                        dve.wait_ge(*at_count("states", 3 * g + tt))
                        steps.mark(dve.tensor_tensor(by_head(states[:, tt, :]), by_head(states[:, tt - 1, :]),
                                                     wide(last_exp[:, tt:SH * TT:TT], 64), ALU.mult))
                        steps.wait()
                    dve.wait_ge(*at_count("states_done", 3 * g + tt + 1))
                    new = bank[at[("states", g, tt)]][:, :]
                    if tt:
                        dve.tensor_tensor(states[:, tt, :], states[:, tt, :], new, ALU.add).then_inc(S("states"), 1)
                    else:
                        dve.tensor_copy(states[:, 0, :], new).then_inc(S("states"), 1)

                def decays(m):
                    dve.wait_ge(*at_count("acs_done", m + 1))
                    if m >= 2:
                        dve.wait_ge(*at_count("y_diag_done", m - 1))
                    for tt in range(TT):
                        dve.tensor_scalar(seg[:, m % 2, tt * P:tt * P + P], bank[at[("acs", m)]][:, tt * P:tt * P + P],
                                          ssm_col(ACS, tt)[:, m % SH:m % SH + 1], 0.0, ALU.subtract, ALU.max).then_inc(S("seg_arg"), 1)

                def weighted(m):
                    dve.wait_ge(*at_count("seg_exp", m + 1))
                    dve.wait_ge(*at_count("cb", g + 1))
                    dve.tensor_tensor(seg[:, m % 2, :], seg[:, m % 2, :], cb[:, :, :].rearrange("p a b -> p (a b)"), ALU.mult).then_inc(S("seg"), 1)

                for j in range(4):
                    n = 4 * g + j
                    decays(2 * n)
                    decays(2 * n + 1)
                    weighted(2 * n)
                    weighted(2 * n + 1)
                    dve.wait_ge(*at_count("exp_acs", n + 1))
                    dve.wait_ge(*at_count("y_off_done", n + 1))
                    dve.tensor_tensor(exp_acs[:, P:T], exp_acs[:, P:T], bank[at[("y_off", n)]][:, P:T], ALU.mult).then_inc(S("y_off"), 1)
                    dve.wait_ge(*at_count("y_diag_done", 2 * n + 2))
                    dve.scalar_tensor_tensor(xbc[:, j, :], xbc[:, j, :], column("d_skip_2", n), bank[at[("y_diag", n)]][:, :],
                                             ALU.mult, ALU.add).then_inc(S("y_skip"), 1)
                    dve.wait_ge(*at_count("y_skip", n + 1))
                    dve.wait_ge(*at_count("y_off", n + 1))
                    dve.tensor_tensor(xbc[:, j, P:T], xbc[:, j, P:T], exp_acs[:, P:T], ALU.add).then_inc(S("y_sum"), 1)
                    dve.wait_ge(*at_count("y_sum", n + 1))
                    dve.tensor_tensor(y_ssm[:, n, :], y_ssm[:, n, :], xbc[:, j, :], ALU.mult).then_inc(S("y_gated"), 1)
                dve.wait_ge(*at_count("group_std", g + 1))
                steps.mark(dve.reciprocal(exp_acs, exp_acs))
                steps.wait()
                for j in range(4):
                    n = 4 * g + j
                    dve.scalar_tensor_tensor(y_ssm[:, n, :], y_ssm[:, n, :], column("ssm_norm_w_2", n), exp_acs, ALU.mult, ALU.mult).then_inc(S("y_ssm"), 1)
            dve.wait_ge(*at_count("ln_mean_done", 1))
            for k in range(KD):
                dve.scalar_tensor_tensor(conv_y[:, k, :], bank[at[("ln_mean",)]][:, :], -1 / D, conv_y[:, k, :], ALU.mult, ALU.add).then_inc(S("ln_centred"), 1)
            dve.wait_ge(*at_count("ln_std", 1))
            steps.mark(dve.reciprocal(rstd[:, 1, :], rstd[:, 0, :]))
            steps.wait()
            for k in range(KD):
                dve.scalar_tensor_tensor(conv_y[:, k, :], conv_y[:, k, :], column("conv_ln_w_2", k), rstd[:, 1, :], ALU.mult, ALU.mult).then_inc(S("ln_scaled"), 1)
            for n in range(KD):
                dve.wait_ge(*at_count("sig", 2 * n + 1))
                dve.wait_ge(*at_count("unit_done", at[("unit", "conv_out", n)]))
                dve.tensor_tensor(merged[:, n, :], sig[:, 0, :], bank[at[("conv_out", n)]][:, :], ALU.mult).then_inc(S("merge_conv"), 1)
                dve.wait_ge(*at_count("sig", 2 * n + 2))
                dve.wait_ge(*at_count("unit_done", at[("unit", "ssm_out", n)]))
                dve.tensor_tensor(sig[:, 1, :], sig[:, 1, :], bank[at[("ssm_out", n)]][:, :], ALU.mult).then_inc(S("merge_ssm"), 1)
                dve.wait_ge(*at_count("merge_ssm", n + 1))
                dve.wait_ge(*at_count("merge_conv", n + 1))
                dve.tensor_tensor(merged[:, n, :], merged[:, n, :], sig[:, 1, :], ALU.add).then_inc(S("merged"), 1)
            for n in range(KD):
                dve.wait_ge(*at_count("unit_done", at[("unit", "w_out2", n)]))
                dve.scalar_tensor_tensor(xT[:, n, :], bank[at[("w_out2", n)]][:, :], mod[:, G_2 + n:G_2 + n + 1], xT[:, n, :],
                                         ALU.mult, ALU.add).then_inc(S("x_mix2"), 1)
        ffn_act = area(0, F_TILES, T)
        ffn_silu = area(11264, 2, T)
        ffn_act_r = halves("ffn_act_lo", "arena", 0, F_TILES, T)
        ffn_hi_r = halves("ffn_act_hi", "arena", 12288, F_TILES, T)
        ffn_h_hi_r = halves("ffn_h_hi", "arena", 23552, KD, T)

        def pe_ffn2(pe, mm, take, project):
            h_tiles = [(ffn_h_hi_r[:, k, :], hT_r[:, k, :]) for k in range(KD)]
            for n in range(F_TILES):
                first = list(range(1, KD + 1)) if n == 0 else None
                project(("ffn_gate", n), ("ffn_silu", n + 1), h_tiles, "norm_ffn2_h", first)
                project(("ffn_up", n), ("ffn_act", n + 1), h_tiles, None, None)
            act_tiles = [(ffn_hi_r[:, k, :], ffn_act_r[:, k, :]) for k in range(F_TILES)]
            for n in range(KD):
                project(("ffn_down", n), ("x_ffn2", n + 1), act_tiles, "ffn_lo", list(range(1, F_TILES + 1)) if n == 0 else None)

        def act_ffn2(act, steps):
            def upper(n):
                act.wait_ge(*at_count("ffn_act", n + 1))
                act.activation(ffn_hi_r[:, n, :], ffn_act[:, n, :], ACT.Copy).then_inc(S("ffn_hi"), 1)

            for n in range(F_TILES):
                act.wait_ge(*at_count("unit_done", at[("unit", "ffn_gate", n)]))
                if n >= 2:
                    act.wait_ge(*at_count("ffn_act", n - 1))
                act.activation(ffn_silu[:, n % 2, :], bank[at[("ffn_gate", n)]][:, :], ACT.Silu).then_inc(S("ffn_silu"), 1)
                if n:
                    upper(n - 1)
            upper(F_TILES - 1)

        def dve_ffn2(dve, steps):
            def lower(n):
                dve.wait_ge(*at_count("ffn_hi", n + 1))
                dve.tensor_tensor(ffn_act_r[:, n, :], ffn_act[:, n, :], ffn_hi_r[:, n, :].bitcast(F32), ALU.subtract).then_inc(S("ffn_lo"), 1)

            for n in range(F_TILES):
                dve.wait_ge(*at_count("ffn_silu", n + 1))
                dve.wait_ge(*at_count("unit_done", at[("unit", "ffn_up", n)]))
                dve.tensor_tensor(ffn_act[:, n, :], ffn_silu[:, n % 2, :], bank[at[("ffn_up", n)]][:, :], ALU.mult).then_inc(S("ffn_act"), 1)
                if n:
                    lower(n - 1)
            lower(F_TILES - 1)
            for n in range(KD):
                dve.wait_ge(*at_count("unit_done", at[("unit", "ffn_down", n)]))
                dve.scalar_tensor_tensor(xT[:, n, :], bank[at[("ffn_down", n)]][:, :], mod[:, G_3 + n:G_3 + n + 1], xT[:, n, :],
                                         ALU.mult, ALU.add).then_inc(S("x_ffn2"), 1)
        def act_square(act, name, k):
            act.activation(hT[:, k, :], xT[:, k, :], ACT.Square).then_inc(S(name + "_square"), 1)

        def act_std(act, name):
            act.wait_ge(*at_count(name + "_sum", 1))
            act.activation(rstd[:, 0, :], bank[at[(name, "sum")]][:, :], ACT.Sqrt, bias=column("eps_norm"), scale=1 / D).then_inc(S(name + "_std"), 1)

        def act_shift(act, name, shift):
            for k in range(KD):
                act.wait_ge(*at_count(name + "_scaled", k + 1))
                act.activation(hT[:, k, :], hT[:, k, :], ACT.Identity, bias=mod[:, shift + k:shift + k + 1]).then_inc(S(name + "_h"), 1)

        def dve_norm(dve, steps, name, weight, scale, in_place=False):
            if scale is not None:
                steps.mark(dve.scalar_tensor_tensor(gain[:, :], mod[:, scale:scale + KD], 1.0,
                                                    col[:, COL[weight]:COL[weight] + KD], ALU.add, ALU.mult))
            dve.wait_ge(*at_count(name + "_std", 1))
            steps.mark(dve.reciprocal(rstd[:, 1, :], rstd[:, 0, :]))
            steps.wait()
            for k in range(KD):
                g = gain[:, k:k + 1] if scale is not None else column(weight, k)
                dst = xT if in_place else hT
                dve.scalar_tensor_tensor(dst[:, k, :], xT[:, k, :], g, rstd[:, 1, :], ALU.mult, ALU.mult).then_inc(
                    S(name + ("_scaled" if scale is not None else "_h")), 1)

        def act_shift_split(act, name, shift, upper_r):
            for k in range(KD):
                act.wait_ge(*at_count(name + "_scaled", k + 1))
                act.activation(upper_r[:, k, :], hT[:, k, :], ACT.Identity, bias=mod[:, shift + k:shift + k + 1]).then_inc(S(name + "_hi"), 1)

        def dve_lower(dve, name, shift, upper_r):
            for k in range(KD):
                dve.wait_ge(*at_count(name + "_hi", k + 1))
                dve.scalar_tensor_tensor(hT_r[:, k, :], hT[:, k, :], mod[:, shift + k:shift + k + 1], upper_r[:, k, :].bitcast(F32),
                                         ALU.add, ALU.subtract).then_inc(S(name + "_h"), 1)

        def pool_split(pool, first, count):
            def split(u, slot, landed, used, done):
                pool.wait_ge(*at_count(f"landed{slot}", landed))
                pool.wait_ge(*at_count("unit_done", used))
                hi, w = hi_ring_r[:, u % 2, :], ring[:, slot, :]
                pool.tensor_tensor(hi, w, column("zero").broadcast_to([P, UNIT]), ALU.add).then_inc(S("split_hi"), 1)
                pool.wait_ge(*at_count("split_hi", done))
                pool.tensor_tensor(ring_r[:, slot, :], w, hi.bitcast(F32), ALU.subtract).then_inc(S("split"), 1)

            with pool.Fori(0, count // RING) as i:
                for j in range(RING):
                    u = first + j
                    split(u, u % RING, i * 16 + 16 * (u // RING + 1), i * RING + (u - 1), i * RING + (j + 1))
            for j in range(count // RING * RING, count):
                u = first + j
                split(u, u % RING, 16 * (u // RING + 1), u - 1, j + 1)

        block = ctx.enter_context(nc.Block())

        @block.tensor
        def _(pe):
            unit = [0]
            turn = [0]
            freed = [None] * 8

            def mm(out, lhsT, rhs, start=True, stop=True):
                return pe.matmul(out, lhsT, rhs, start=start, stop=stop, skip_group_check=True)

            def take(key, freed_by, b=None):
                if b is None:
                    b = turn[0]
                    turn[0] = (b + 1) % 8
                if freed[b] is not None:
                    pe.wait_ge(*at_count(*freed[b]))
                freed[b] = freed_by
                at[key] = b
                return bank[b]

            def unit_landed():
                u = unit[0]
                unit[0] += 1
                pe.wait_ge(*at_count(f"landed{u % RING}", 16 * (u // RING + 1)))
                return ring[:, u % RING, :].rearrange("p (k n) -> p k n", k=8)

            def project(key, freed_by, rhs, ready, counts):
                out = None
                n = len(rhs)
                for u in range(-(-n // 8)):
                    w = unit_landed()
                    if out is None:
                        out = take(key, freed_by)
                    for k in range(min(8, n - 8 * u)):
                        i = 8 * u + k
                        if counts:
                            pe.wait_ge(*at_count(ready, counts[i]))
                        last = mm(out[:, :], w[:, k, :], rhs[i], i == 0, i == n - 1)
                    last.then_inc(S("unit_done"), 1)
                at[("unit",) + key] = unit[0]

            def project_split(key, freed_by, rhs, ready, counts):
                out = None
                n = len(rhs)
                for u in range(-(-n // 8)):
                    w_hi, w_lo = (w.rearrange("p (k n) -> p k n", k=8) for w in (
                        hi_ring_r[:, unit[0] % 2, :], ring_r[:, unit[0] % RING, :]))
                    unit[0] += 1
                    pe.wait_ge(*at_count("split", unit[0] - at["first_split"]))
                    if out is None:
                        out = take(key, freed_by)
                    for k in range(min(8, n - 8 * u)):
                        i = 8 * u + k
                        if counts:
                            pe.wait_ge(*at_count(ready, counts[i]))
                        hi, lo = rhs[i]
                        mm(out[:, :], w_hi[:, k, :], hi, i == 0, False)
                        mm(out[:, :], w_lo[:, k, :], hi, False, False)
                        last = mm(out[:, :], w_hi[:, k, :], lo, False, i == n - 1)
                    last.then_inc(S("unit_done"), 1)
                at[("unit",) + key] = unit[0]

            def norm_sum(name, freed_by):
                out = take((name, "sum"), freed_by)
                for k in range(KD):
                    pe.wait_ge(*at_count(name + "_square", k + 1))
                    last = mm(out[:, :], ones, hT[:, k, :], k == 0, k == KD - 1)
                last.then_inc(S(name + "_sum"), 1)

            pe.wait_ge(*at_count("consts_landed", 16))
            norm_sum("norm_mix", ("norm_mix_std", 1))
            h_tiles = [hT[:, k, :] for k in range(KD)]

            def h_counts(first):
                return list(range(1, KD + 1)) if first else None

            for t in range(M_TILES):
                project(("m", t), ("m_proj", t + 1), h_tiles, "norm_mix_h", h_counts(t == 0))
            pe.wait_ge(*at_count("smalls_landed", 16))
            for i in range(2):
                out = take(("gate", i), ("gate_raw", i + 1))
                for k in range(KD):
                    last = mm(out[0:MH, :], gates_w[:, k, 4 * i:4 * i + 4], h_tiles[k], k == 0, k == 7)
                last.then_inc(S("gates_done"), 1)
            for t in range(R_TILES):
                project(("r", t), ("r_proj", t + 1), h_tiles, None, None)
            pe_mlstm(pe, mm, take)
            pe_rwkv(pe, mm, take)
            y_tiles = [y_rwkv[:, k, :] for k in range(4)] + [y_mlstm[:, k, :] for k in range(4)]
            pe.wait_ge(*at_count("y_mlstm", MH))
            pe.wait_ge(*at_count("y_rwkv", RW))
            for n in range(KD):
                project(("w_out", n), ("x_mix", n + 1), y_tiles, None, None)
            norm_sum("norm_ffn", ("norm_ffn_std", 1))
            pe_moe(pe, mm, take, unit, unit_landed, freed, turn)
            norm_sum("norm_out", ("norm_out_std", 1))
            norm_sum("norm_mix2", ("norm_mix2_std", 1))
            pe_mix2(pe, mm, take, project, h_tiles)
            norm_sum("norm_ffn2", ("norm_ffn2_std", 1))
            at["first_split"] = unit[0]
            pe_ffn2(pe, mm, take, project_split)
            at["splits"] = unit[0] - at["first_split"]
            norm_sum("norm_out2", ("norm_out2_std", 1))

        @block.sync
        def _(sp):
            def load_mod(i):
                slot = i % MOD_RING
                if i >= MOD_RING:
                    sp.wait_ge(*at_count("mod_used", i - MOD_RING + 1))
                sp.dma_start(mod_ring[:, slot, :], mod_w_d[i]).then_inc(S(f"mod_landed{slot}"), 16)

            sp.dma_start(silu_c[:, 0, :], c_d[0:1, :].broadcast_to([P, D])).then_inc(S("c_landed"), 16)
            for i in range(MOD_RING):
                load_mod(i)
            sp.dma_start(col[:, :], col_d).then_inc(S("columns_landed"), 16)
            sp.dma_start(xT[:, :, :].rearrange("p a b -> p (a b)"), x_d).then_inc(S("x_landed"), 16)
            for i in range(MOD_RING, MOD_EARLY):
                load_mod(i)
            sp.dma_start(con[:, :], con_d).then_inc(S("consts_landed"), 16)
            units = w_d.shape[0]
            for u in range(RING):
                sp.dma_start(ring[:, u, :], w_d[u]).then_inc(S(f"landed{u}"), 16)
                if u == 0:
                    sp.dma_start(silu_c[:, 1, :], c_d[1:2, :].broadcast_to([P, D])).then_inc(S("c_2_landed"), 16)
                    sp.dma_start(sma[:, :], sma_d).then_inc(S("smalls_landed"), 16)
            total = units
            rounds = total // RING
            mod_rounds = 3
            each = -(-(MODS - MOD_EARLY) // (mod_rounds * RING - 2))
            for u in range(RING, RING + mod_rounds * RING):
                first = MOD_EARLY + (u - RING) * each
                for i in range(first, min(first + each, MODS)):
                    load_mod(i)
                sp.wait_ge(*at_count("unit_done", u - RING + 1))
                sp.dma_start(ring[:, u % RING, :], w_d[u]).then_inc(S(f"landed{u % RING}"), 16)
            with sp.Fori(1 + mod_rounds, rounds) as i:
                for u in range(RING):
                    sp.wait_ge(*at_count("unit_done", (i - 1) * RING + u + 1))
                    sp.dma_start(ring[:, u, :], w_d[i * RING + u]).then_inc(S(f"landed{u}"), 16)
            for u in range(total % RING):
                sp.wait_ge(*at_count("unit_done", (rounds - 1) * RING + u + 1))
                sp.dma_start(ring[:, u, :], w_d[rounds * RING + u]).then_inc(S(f"landed{u}"), 16)
            for k in range(KD):
                sp.wait_ge(*at_count("norm_out2_h", k + 1))
                sp.dma_start(out_d[:, k * T:k * T + T], hT[:, k, :]).then_inc(S("stored"), 16)
            sp.wait_ge(*at_count("stored", 16 * KD))
        @block.scalar
        def _(act):
            steps = Steps(act, S("scalar_step"))
            act.wait_ge(*at_count("c_landed", 16))
            act.activation(silu_c[:, 0, :], silu_c[:, 0, :], ACT.Silu).then_inc(S("silu_c"), 1)
            act.wait_ge(*at_count("columns_landed", 16))
            act.wait_ge(*at_count("x_landed", 16))
            for k in range(KD):
                act_square(act, "norm_mix", k)
            act_std(act, "norm_mix")
            act_shift(act, "norm_mix", SH_M)
            act.wait_ge(*at_count("c_2_landed", 16))
            act.activation(silu_c[:, 1, :], silu_c[:, 1, :], ACT.Silu).then_inc(S("silu_c"), 1)
            act.wait_ge(*at_count("pads", 1))
            for t in range(M_TILES):
                act.wait_ge(*at_count("unit_done", at[("unit", "m", t)]))
                act.activation(m_proj[:, t, PAD:TP], bank[at[("m", t)]][:, :], ACT.Sigmoid if t >= 8 else ACT.Copy).then_inc(S("m_proj"), 1)
            act_mlstm_gates(act, steps)
            act.wait_ge(*at_count("pads", 2))
            for t in range(R_TILES):
                act.wait_ge(*at_count("unit_done", at[("unit", "r", t)]))
                act.activation(x_in(t), bank[at[("r", t)]][:, :], ACT.Copy).then_inc(S("r_proj"), 1)
            act_mlstm(act, steps)
            act_rwkv(act, steps)
            for k in range(KD):
                act.wait_ge(*at_count("x_mix", k + 1))
                act_square(act, "norm_ffn", k)
            act_std(act, "norm_ffn")
            act_shift(act, "norm_ffn", SH_F)
            act_moe(act, steps)
            for k in range(KD):
                act.wait_ge(*at_count("x_moe", k + 1))
                act_square(act, "norm_out", k)
            act_std(act, "norm_out")
            for k in range(KD):
                act.wait_ge(*at_count("norm_out_h", k + 1))
                act_square(act, "norm_mix2", k)
            act_std(act, "norm_mix2")
            act_shift(act, "norm_mix2", SH_2)
            act_mix2(act, steps)
            for k in range(KD):
                act.wait_ge(*at_count("x_mix2", k + 1))
                act_square(act, "norm_ffn2", k)
            act_std(act, "norm_ffn2")
            act_shift_split(act, "norm_ffn2", SH_3, ffn_h_hi_r)
            act_ffn2(act, steps)
            for k in range(KD):
                act.wait_ge(*at_count("x_ffn2", k + 1))
                act_square(act, "norm_out2", k)
            act_std(act, "norm_out2")

        @block.vector
        def _(dve):
            steps = Steps(dve, S("vector_step"))
            dve.wait_ge(*at_count("columns_landed", 16))
            for i, name in enumerate(("mlstm_i_b", "mlstm_f_b")):
                dve.tensor_scalar(m_small[0:MH, i:i + 1], column(name, rows=MH), 1 / CAP, None, ALU.mult).then_inc(S("gate_bias"), 1)

            def modulate(tiles):
                for i in tiles:
                    dve.wait_ge(*at_count(f"mod_landed{i % MOD_RING}", 16 * (i // MOD_RING + 1)))
                    if i in (0, 48):
                        dve.wait_ge(*at_count("silu_c", 1 + i // 48))
                    w = mod_ring[:, i % MOD_RING, :]
                    dve.tensor_tensor_reduce(w, w, silu_c[:, i // 48, :], 1.0, 0.0, ALU.mult, ALU.add,
                                             accum_out=mod[:, i:i + 1]).then_inc(S("mod_used"), 1)
                lo, hi = tiles[0], tiles[-1] + 1
                dve.wait_ge(*at_count("mod_used", hi))
                dve.tensor_tensor(mod[:, lo:hi], mod[:, lo:hi], col[:, COL["ada_b"] + lo:COL["ada_b"] + hi], ALU.add).then_inc(S("mod"), 1)

            modulate(range(MOD_EARLY))
            dve.wait_ge(*at_count("mod", 1))
            dve_norm(dve, steps, "norm_mix", "mix_norm_w", SC_M)
            modulate(range(MOD_EARLY, MODS))
            dve_mlstm(dve, steps)
            dve_rwkv(dve, steps)
            dve.wait_ge(*at_count("mod", 2))
            for n in range(KD):
                dve.wait_ge(*at_count("unit_done", at[("unit", "w_out", n)]))
                dve.scalar_tensor_tensor(xT[:, n, :], bank[at[("w_out", n)]][:, :], mod[:, G_M + n:G_M + n + 1], xT[:, n, :],
                                         ALU.mult, ALU.add).then_inc(S("x_mix"), 1)
            dve_norm(dve, steps, "norm_ffn", "ffn_norm_w", SC_F)
            dve_moe(dve, steps)
            dve.wait_ge(*at_count("x_moe", KD))
            dve_norm(dve, steps, "norm_out", "final_norm_w", None, in_place=True)
            dve.wait_ge(*at_count("norm_out_h", KD))
            dve_norm(dve, steps, "norm_mix2", "norm_mix_w_2", SC_2)
            dve_mix2(dve, steps)
            dve.wait_ge(*at_count("x_mix2", KD))
            dve_norm(dve, steps, "norm_ffn2", "norm_ffn_w_2", SC_3)
            dve_lower(dve, "norm_ffn2", SH_3, ffn_h_hi_r)
            dve_ffn2(dve, steps)
            dve.wait_ge(*at_count("x_ffn2", KD))
            dve_norm(dve, steps, "norm_out2", "final_norm_w_2", None)

        @block.gpsimd
        def _(pool):
            pool.memset(m_proj[:, :, 0:PAD], 0.0).then_inc(S("pads"), 1)
            pool.memset(r_proj[:, :, 0:PAD], 0.0).then_inc(S("pads"), 1)
            pool.memset(v_aug[:, :, :, P:2 * P], 1.0).then_inc(S("pads"), 1)
            pool_rwkv(pool)
            pool_moe(pool)
            pool_split(pool, at["first_split"], at["splits"])



def _units(w, columns=None):
    w = w if columns is None else w[:, columns]
    k, n = w.shape
    kt = k // P
    units = -(-kt // 8)
    t = w.reshape(kt, P, n // P, P).transpose(2, 1, 0, 3)
    if kt % 8:
        t = np.concatenate([t, np.zeros((n // P, P, units * 8 - kt, P), w.dtype)], axis=2)
    return t.reshape(n // P, P, units, UNIT).transpose(0, 2, 1, 3).reshape(-1, P, UNIT)


def weight_stream(a):
    w_in, w2 = a["w_in"][0], a["w_in_2"][0]
    parts = [_units(w_in, slice(1792, 1792 + 1536)), _units(w_in, slice(0, 1792))]
    parts += [_units(a["w_out"][0])]
    down = a["moe_w_down"][0].reshape(NE, 2, P, D)
    gate, up = ([_units(a[n][0, e]) for e in range(NE)] for n in ("moe_w_gate", "moe_w_up"))
    parts += [gate[0], up[0]]
    for e in range(1, NE):
        parts += [gate[e], up[e], down[e - 1]]
    parts += [down[NE - 1]]
    x0, z0 = 4096, 2048
    for g in range(NG):
        parts += [_units(w2, slice(x0 + 512 * g, x0 + 512 * g + 512)),
                  _units(w2, slice(x0 + 2048 + 128 * g, x0 + 2048 + 128 * g + 128)),
                  _units(w2, slice(x0 + 2560 + 128 * g, x0 + 2560 + 128 * g + 128)),
                  _units(w2, slice(z0 + 512 * g, z0 + 512 * g + 512))]
        ab = [_units(w2, slice(1024 * h + 128 * (2 * g + i), 1024 * h + 128 * (2 * g + i) + 128))
              for i in range(2) for h in range(2)]
        parts += ab
    g0 = x0 + 3072 + 32
    g_conv, g_ssm = _units(w2, slice(g0, g0 + 1024)), _units(w2, slice(g0 + 1024, g0 + 2048))
    conv_out, ssm_out = _units(a["w_conv_out_2"][0]), _units(a["w_ssm_out_2"][0])
    for n in range(KD):
        parts += [g_conv[n:n + 1], conv_out[n:n + 1], g_ssm[n:n + 1], ssm_out[2 * n:2 * n + 2]]
    parts += [_units(a["w_out_2"][0])]
    f_in = _units(a["w_ffn_in_2"][0])
    for n in range(F_TILES):
        parts += [f_in[n:n + 1], f_in[F_TILES + n:F_TILES + n + 1]]
    parts += [_units(a["w_ffn_down_2"][0])]
    return np.concatenate(parts)


def modulation_weights(a):
    w = np.concatenate([a["ada_w"][0], a["w_ada_mix_2"][0], a["w_ada_ffn_2"][0]], axis=1)
    return np.ascontiguousarray(w.T).reshape(MODS, P, D)


def column_array(a):
    out = np.zeros((P, NCOL), np.float32)

    def put(name, v):
        v = v.reshape(-1, P).T
        out[:, COL[name]:COL[name] + v.shape[1]] = v

    for name, _ in COLUMNS:
        if name == "d_skip_2":
            put(name, np.repeat(a[name][0], 64))
        elif name in ("mlstm_i_b", "mlstm_f_b"):
            out[:4, COL[name]] = a[name][0]
        elif name in ("dt_bias_2", "a_log_2"):
            out[:8, COL[name]:COL[name] + 4] = a[name][0].reshape(4, 8).T
        elif name.startswith("eps") or name in ("one", "zero"):
            out[:, COL[name]] = {"eps_norm": 1e-6, "eps_gn": 64e-5, "eps_ln": 1e-5, "one": 1.0, "zero": 0.0}[name]
        else:
            put(name, a[name])
    return out


def const_array():
    i = np.arange(P)
    s, t = i[:, None], i[None, :]
    out = np.zeros((P, NCON), np.float32)

    def put(name, v):
        out[:v.shape[0], CON[name]:CON[name] + v.shape[1]] = v

    put("ident", s == t)
    put("ones", np.ones((P, P)))
    same = s // 64 == t // 64
    put("head_ones", same)
    put("same_head", same)
    put("strict64", same & (s < t))
    put("causal64", same & (s <= t))
    put("causal", s <= t)
    put("levels", np.concatenate([(s // (2 << l) == t // (2 << l)) & ((s >> l) % 2 == 0) & ((t >> l) % 2 == 1)
                                  for l in range(6)], axis=1))
    tok = np.arange(T)
    put("reset64", np.broadcast_to(tok % 64 != 0, (P, T)))
    put("reset128", np.broadcast_to(tok % 128 != 0, (P, T)))
    put("sel4", np.concatenate([np.arange(4)[:, None] == h + 0 * t for h in range(4)], axis=1))
    put("token_id", s + P * np.arange(TT))
    put("expert_id", np.broadcast_to(np.arange(NE), (P, NE)))
    put("sel8", np.concatenate([np.arange(8)[:, None] == h + 0 * t for h in range(8)], axis=1))
    put("sel8_pair", np.concatenate([np.arange(8)[:, None] == 2 * j + t // 64 for j in range(4)], axis=1))
    put("rank4", np.broadcast_to(4.0 - np.arange(4), (P, 4)))
    put("rank8", np.broadcast_to(8.0 - np.arange(8), (P, 8)))
    put("half_col", np.stack([i < 64, i >= 64], axis=1))
    return out


def small_array(a):
    out = np.zeros((P, NSMA), np.float32)

    def put(name, v):
        out[:, SMA[name]:SMA[name] + v.shape[1]] = v

    rows = lambda w: w.reshape(KD, P, -1).transpose(1, 0, 2).reshape(P, -1)
    put("gates", rows(a["w_in"][0][:, 3328:]))
    put("router", rows(np.concatenate([a["moe_w_group"][0], a["moe_w_router"][0]], axis=1)))
    put("dt", rows(a["w_in_2"][0][:, 7168:7200]))
    put("lora_up", np.concatenate([a["rwkv_w_up"][0], a["rwkv_a_up"][0]], axis=0))
    put("g_up", a["rwkv_g_up"][0])
    put("router_b", np.broadcast_to(np.concatenate([a["moe_b_group"][0], a["moe_b_router"][0]]), (P, 36)))
    return out


def kernel(**inputs):
    import concourse.bacc as _bacc
    from concourse.bass_utils import run_bass_kernel_spmd as _run

    a = {k: np.asarray(v) for k, v in inputs.items()}
    arrays = {
        "x_dram": np.ascontiguousarray(a["x"][0].reshape(T, KD, P).transpose(2, 1, 0).reshape(P, KD * T)),
        "weights_dram": weight_stream(a),
        "mod_weights_dram": modulation_weights(a),
        "c_dram": np.concatenate([a["c"].reshape(1, D), a["c_2"].reshape(1, D)]),
        "columns_dram": column_array(a),
        "consts_dram": const_array(),
        "smalls_dram": small_array(a),
    }
    nc = _bacc.Bacc("TRN2", target_bir_lowering=False, num_devices=1)
    args = [nc.dram_tensor(n, v.shape, F32, kind="ExternalInput").ap() for n, v in arrays.items()]
    out = nc.dram_tensor("out_dram", (P, KD * T), F32, kind="ExternalOutput").ap()
    combine = nc.dram_tensor("combine_dram", (NE, T), F32, kind="Internal").ap()
    h_rows = nc.dram_tensor("h_dram", (T, D), F32, kind="Internal").ap()
    y_rows = nc.dram_tensor("y_dram", (NE * P, D), F32, kind="Internal").ap()
    table = nc.dram_tensor("table_dram", (T * NE, 2), mybir.dt.uint32, kind="Internal").ap()
    two_block_program(nc, *args, combine, h_rows, y_rows, table, out)
    r = _run(nc, [arrays], core_ids=[0])
    y = r.results[0]["out_dram"]
    return np.ascontiguousarray(np.asarray(y).reshape(P, KD, T).transpose(2, 1, 0)).reshape(1, T, D)
```

```python
from contextlib import ExitStack

import numpy as np
import concourse.bass as bass
from concourse import mybir

ALU = mybir.AluOpType
ACT = mybir.ActivationFunctionType
F32 = mybir.dt.float32
F32R = mybir.dt.float32r
AX = mybir.AxisListType

P = 128
T = 512
D = 1024
KD = D // P
TT = T // P
RING = 6
UNIT = 8 * P
PAD = 4
TP = T + PAD

RW = 4
R_TILES = 14
M_TILES = 12
C64 = 64
DECAY = float(np.exp(-0.5))
MH = 4
CAP = 15.0
NE = 32
NG = 4
EG = 8
F_TILES = 22
TAPS = 31
UP = 30

COLUMNS = [
    ("ada_b", 48), ("b_ada_mix_2", 24), ("b_ada_ffn_2", 24),
    ("mix_norm_w", 8), ("ffn_norm_w", 8), ("final_norm_w", 8), ("norm_mix_w_2", 8),
    ("norm_ffn_w_2", 8), ("final_norm_w_2", 8), ("rwkv_mu", 14), ("rwkv_w0", 4), ("rwkv_a0", 4),
    ("rwkv_k_k", 4), ("rwkv_k_a", 4), ("rwkv_r_k", 4), ("rwkv_gn_w", 4), ("rwkv_gn_b", 4),
    ("mlstm_conv_w", 16), ("mlstm_conv_b", 4), ("mlstm_hn_w", 4), ("mlstm_i_b", 1),
    ("mlstm_f_b", 1), ("conv_dw_w_2", TAPS * 8), ("conv_dw_b_2", 8), ("conv_ln_w_2", 8),
    ("conv_ln_b_2", 8), ("ssm_conv_w_2", 4 * 24), ("ssm_conv_b_2", 24), ("ssm_norm_w_2", 16),
    ("d_skip_2", 16), ("dt_bias_2", 4), ("a_log_2", 4),
    ("eps_norm", 1), ("eps_gn", 1), ("eps_ln", 1), ("one", 1), ("zero", 1),
]
COL, NCOL = {}, 0
for _name, _n in COLUMNS:
    COL[_name] = NCOL
    NCOL += _n

CONSTS = [
    ("ident", 128), ("ones", 128), ("head_ones", 128), ("strict64", 128), ("causal64", 128),
    ("causal", 128), ("levels", 6 * 128), ("same_head", 128), ("reset64", T), ("reset128", T),
    ("sel4", 4 * 128), ("sel8", 8 * 128), ("sel8_pair", 4 * 128),
    ("rank4", 4), ("rank8", 8), ("half_col", 2), ("token_id", 4), ("expert_id", 32),
]
CON, NCON = {}, 0
for _name, _n in CONSTS:
    CON[_name] = NCON
    NCON += _n

SMALLS = [("gates", 8 * 8), ("router", 8 * 36), ("dt", 8 * 32), ("lora_up", 512), ("g_up", 512),
          ("router_b", 36)]
SMA, NSMA = {}, 0
for _name, _n in SMALLS:
    SMA[_name] = NSMA
    NSMA += _n

MODS = 96
MOD_EARLY = 16
MOD_RING = 4
SH_M, SC_M, G_M, SH_F, SC_F, G_F = (8 * i for i in range(6))
SH_2, SC_2, G_2, SH_3, SC_3, G_3 = (48 + 8 * i for i in range(6))


GOES_ON = {
    "dt_done": ("v_turned", 4),
    "b_turned": ("gate_cols_done", 1),
    "ssm_cols_done": ("max_done", 4),
    "cb_done": ("inter_done", 4),
    "x_turned": ("k_turned", 2),
    "states_done": ("qk_done", 4),
    "acs_done": ("exp_m_done", 4),
    "pair_acs_done": ("num_done", 4),
    "y_off_done": ("den_done", 4),
    "y_diag_done": ("m_state_done", 3),
    "group_sum_done": ("m_sum_done", 4),
    "ln_mean_done": ("lora_done", 12),
    "ln_var_done": ("kk_sum_done", 4),
    "xbc_raw": ("gate_raw", 2),
    "z": ("forget", 1),
    "conv_gate": ("q_k", 4),
    "a_pos": ("v_tok", 4),
    "xbc": ("m_weights", 3),
    "dt_raw": ("exp_m", 1),
    "dt_log": ("decay", 4),
    "end_exp": ("den_abs", 4),
    "b_tok": ("m_square", 4),
    "seg_exp": ("m_std", 4),
    "exp_acs": ("r_lora", 2),
    "group_square": ("rate", 4),
    "group_std": ("r_a", 4),
    "ln_square": ("gate_r", 4),
    "ln_std": ("kk_square", 4),
    "conv_act": ("kk_std", 4),
    "sig": ("cum", 12),
    "ffn_silu": ("r_tok", 16),
    "pads2": ("m_conv", 16),
    "conv_u": ("m_logs", 4),
    "xbc_conv": ("q_head", 4),
    "end_arg": ("gate_cols", 5),
    "conv_y": ("decay_arg", 16),
    "rows": ("q_inter", 4),
    "cb": ("k_tok", 4),
    "x_tok": ("decay_masked", 4),
    "states": ("probs", 4),
    "seg_arg": ("m_state", 3),
    "seg": ("den", 4),
    "y_off": ("m_out", 4),
    "y_skip": ("shift_diff", 14),
    "y_sum": ("shifted", 14),
    "y_gated": ("kk_raw", 4),
    "y_ssm": ("bonus_in", 4),
    "ln_centred": ("kk_unit", 4),
    "ln_scaled": ("rate_sums", 4),
    "merge_conv": ("rate_before", 4),
    "merge_ssm": ("bonus", 4),
    "merged": ("r_ready", 16),
    "x_mix2": ("r_state", 8),
    "ffn_act": ("pairs", 32),
    "x_ffn2": ("inv", 88),
    "norm_ffn_square": ("norm_mix_square", 8),
    "norm_ffn_sum": ("norm_mix_sum", 1),
    "norm_ffn_std": ("norm_mix_std", 1),
    "norm_ffn_scaled": ("norm_mix_scaled", 8),
    "norm_ffn_h": ("norm_mix_h", 8),
    "norm_mix2_square": ("norm_ffn_square", 8),
    "norm_mix2_sum": ("norm_ffn_sum", 1),
    "norm_mix2_std": ("norm_ffn_std", 1),
    "norm_mix2_scaled": ("norm_ffn_scaled", 8),
    "norm_mix2_h": ("norm_ffn_h", 8),
    "norm_ffn2_square": ("norm_mix2_square", 8),
    "norm_ffn2_sum": ("norm_mix2_sum", 1),
    "norm_ffn2_std": ("norm_mix2_std", 1),
    "norm_ffn2_scaled": ("norm_mix2_scaled", 8),
    "norm_ffn2_h": ("norm_mix2_h", 8),
    "norm_out2_square": ("norm_out_square", 8),
    "norm_out2_sum": ("norm_out_sum", 1),
    "norm_out2_std": ("norm_out_std", 1),
    "norm_out2_h": ("norm_out_h", 8),
    "router_done": ("bonus_done", 4),
    "h_turned": ("r_turned", 16),
    "ranks_done": ("pairs_done", 32),
    "down_done": ("ox_done", 48),
    "combine_turned": ("xox_done", 72),
    "rows_turned": ("w_done", 8),
    "sparse_down": ("bv_done", 8),
    "y_turned": ("u_done", 8),
    "group_exp": ("prod", 40),
    "second_exp": ("gn_square", 4),
    "h_tok": ("gn_std", 4),
    "logits": ("w_t", 8),
    "group_arg": ("bv", 8),
    "second_arg": ("u", 8),
    "assigned": ("sa", 8),
    "totals": ("r_state_sum", 7),
    "combine": ("y_state", 4),
    "moe_up": ("y_raw", 4),
    "sparse_act": ("gn_centred", 4),
    "norm_ffn2_hi": ("norm_mix2_hi", 8),
    "ffn_hi": ("ssm_hi", 16),
    "ffn_lo": ("ssm_lo", 16),
    "x_kept": ("mod_landed0", 384),
    "x_back": ("mod_landed1", 384),
    "h_stored0": ("mod_landed2", 384),
    "h_stored1": ("mod_landed3", 384),
    "y_stored0": ("c_landed", 16),
    "y_stored1": ("c_2_landed", 16),
    "norm_mix2_hi": ("norm_mix_hi", 8),
    "conv_lo": ("y_state_done", 8),
    "conv_hi": ("new_state_done", 7),
    "merged_lo": ("ws_done", 8),
    "dt_hi": ("y_in_done", 4),
    "dt_lo": ("gn_mean_done", 4),
    "merged_hi": ("gn_var_done", 4),
    "sparse_y": ("y_lo", 8),
    "expert_in": ("y_hi", 8),
    "sparse_silu": ("gates_hi", 1),
    "y_picked": ("gates_lo", 1),
}


class Steps:

    def __init__(self, engine, semaphore):
        self.engine, self.semaphore, self.count = engine, semaphore, 0

    def mark(self, instruction):
        instruction.then_inc(self.semaphore, 1)
        self.count += 1

    def wait(self):
        self.engine.wait_ge(self.semaphore, self.count)


def two_block_program(nc, x_d, w_d, mod_w_d, c_d, col_d, con_d, sma_d, combine_d, h_d, y_d, table_d, x_kept_d, out_d):
    with ExitStack() as ctx:
        signals = {}

        def S(name):
            while name in GOES_ON:
                name = GOES_ON[name][0]
            if name not in signals:
                signals[name] = ctx.enter_context(nc.semaphore(name))
            return signals[name]

        def at_count(name, n):
            semaphore = S(name)
            while name in GOES_ON:
                name, before = GOES_ON[name]
                n = n + before
            return semaphore, n

        base = {}

        def sb(name, shape):
            base[name] = -(-nc.sbuf_base // 32) * 32
            return ctx.enter_context(nc.sbuf_tensor(name, shape, F32))

        def halves(name, over, offset, *shape):
            return nc.alloc_sbuf_tensor_at(name, [P, *shape], F32R, offset=base[over] + 4 * offset)

        ring = sb("ring", [P, RING, UNIT])
        xT = sb("xT", [P, KD, T])
        hT = sb("hT", [P, KD, T])
        col = sb("col", [P, NCOL])
        con = sb("con", [P, NCON])
        sma = sb("sma", [P, NSMA])
        mod = sb("mod", [P, 96])
        rstd = sb("rstd", [P, 2, T])
        gain = sb("gain", [P, 8])
        U32 = mybir.dt.uint32
        slot_table = ctx.enter_context(nc.sbuf_tensor("slot_table", [P, 2 * NE], U32))
        pairs_u = ctx.enter_context(nc.sbuf_tensor("pairs_u", [P, 4 * TT], U32))
        rows_u = ctx.enter_context(nc.sbuf_tensor("rows_u", [P, 4 * TT], U32))
        flag = ctx.enter_context(nc.sbuf_tensor("flag", [1, 1], U32))
        AW = 29920
        arena = sb("arena", [P, AW])
        bank = [ctx.enter_context(nc.psum_tensor(f"bank{b}", [P, T], F32)) for b in range(8)]

        def area(offset, *shape):
            n = int(np.prod(shape))
            assert offset + n <= AW, (offset, n)
            v = arena[:, offset:offset + n]
            if len(shape) == 2:
                v = v.rearrange("p (a b) -> p a b", a=shape[0])
            if len(shape) == 3:
                v = v.rearrange("p (a b c) -> p a b c", a=shape[0], b=shape[1])
            return v

        def column(name, i=0, rows=P):
            return col[0:rows, COL[name] + i:COL[name] + i + 1]

        def constant(name, i=0, n=P, rows=P):
            return con[0:rows, CON[name] + i * n:CON[name] + i * n + n]

        ident, ones, head_ones = constant("ident"), constant("ones"), constant("head_ones")
        gates_w = sma[:, SMA["gates"]:SMA["gates"] + 64].rearrange("p (k n) -> p k n", k=8)
        router_w = sma[:, SMA["router"]:SMA["router"] + 288].rearrange("p (k n) -> p k n", k=8)
        dt_w = sma[:, SMA["dt"]:SMA["dt"] + 256].rearrange("p (k n) -> p k n", k=8)
        lora_up = sma[:, SMA["lora_up"]:SMA["lora_up"] + 512]
        g_up = sma[:, SMA["g_up"]:SMA["g_up"] + 512]
        router_b = sma[:, SMA["router_b"]:SMA["router_b"] + 36]

        hi_ring_1 = [halves("hi_ring_1a", "arena", 23656, UNIT), halves("hi_ring_1b", "arena", 27752, UNIT)]
        hi_ring_2 = halves("hi_ring_2", "arena", AW - 2 * UNIT, 2, UNIT)
        SPLIT_1 = M_TILES + R_TILES + KD

        def hi_unit(u):
            return hi_ring_1[u % 2][:, :] if u < SPLIT_1 else hi_ring_2[:, u % 2, :]

        in_h_hi_r = halves("in_h_hi", "arena", 15464, KD, T)
        gates_lo_r = halves("gates_lo", "sma", SMA["gates"], 8, 8)
        gates_hi_r = ctx.enter_context(nc.sbuf_tensor("gates_hi", [P, 8, 8], F32R))
        ring_r = halves("lo_ring", "ring", 0, RING, UNIT)
        hT_r = halves("h_lo", "hT", 0, KD, T)
        mix_h_hi_r = halves("mix_h_hi", "xT", 0, KD, T)
        dt_lo_r = halves("dt_lo", "sma", SMA["dt"], 8, 32)
        dt_hi_r = ctx.enter_context(nc.sbuf_tensor("dt_hi", [P, 8, 32], F32R))
        m_proj = area(0, M_TILES, TP)
        r_proj = area(6192, R_TILES, TP)
        q_k = area(13416, 4, T)
        v_aug = area(15464, TT, MH, 256)
        k_tok = area(19560, TT, 256)
        q_head = area(20584, MH, T)
        q_inter = area(22632, MH, T)
        gate_row = [area(24680 + T * i, T) for i in range(6)]
        probs = area(27752, 2, MH * P)
        m_state = area(28776, 2, 256)
        m_cols = area(29288, 2 * TT * MH)
        m_carry = area(29320, MH * TT)
        m_small = area(29336, 64)
        mod_ring = area(19560, MOD_RING, D)
        silu_c = area(13416, 2, D)
        y_mlstm = area(2064, 4, T)

        def x_in(t, lo=0, n=T):
            return r_proj[:, t, PAD + lo:PAD + lo + n]

        at = {}


        def column_half(i):
            return con[:, CON["half_col"] + i:CON["half_col"] + i + 1]

        y_hi_r = halves("y_hi", "arena", 15464, KD, T)
        y_mlstm_r = halves("y_mlstm_lo", "arena", 2064, 4, T)
        y_rwkv_r = halves("y_rwkv_lo", "arena", 6192 + 4 * TP, RW, TP)[:, :, PAD:TP]

        decay = area(0, TT, MH * P)
        g_row, f_row, b_row, max_row, w_row, k_row = gate_row

        def m_rows(row, lo=0, n=T):
            return row[0:MH, lo:lo + n]

        def pe_mlstm(pe, mm, take):
            for tt in range(TT):
                out = take(("v_tok", tt), ("v_tok", tt + 1))
                if tt == 0:
                    pe.wait_ge(*at_count("m_proj", 8))
                for h in range(MH):
                    last = mm(out[:, h * P:h * P + P], m_proj[:, 4 + h, PAD + tt * P:PAD + tt * P + P], ident)
                last.then_inc(S("v_turned"), 1)
            out = take(("gate_cols",), ("gate_cols", 5))
            pe.wait_ge(*at_count("m_weights", 3))
            for i, row in enumerate((g_row, k_row)):
                for tt in range(TT):
                    c = (i * TT + tt) * MH
                    mm(out[:, c:c + MH], m_rows(row, tt * P, P), ident[0:MH, 0:MH])
            for h in range(MH):
                last = mm(out[:, 32 + TT * h:32 + TT * h + TT], constant("sel4", h, rows=MH), m_small[0:MH, 16:16 + TT])
            last.then_inc(S("gate_cols_done"), 1)
            for h in range(MH):
                out = take(("max", h), ("decay_arg", TT * (h + 1)))
                mm(out[:, :], constant("sel4", h, rows=MH), m_rows(max_row)).then_inc(S("max_done"), 1)
            for h in range(MH):
                out = take(("inter", h), ("q_inter", h + 1))
                mm(out[:, :], constant("sel4", h, rows=MH), m_rows(w_row)).then_inc(S("inter_done"), 1)
            pe.wait_ge(*at_count("q_k", 4))
            for i in range(2):
                out = take(("k_tok", i), ("k_tok", 2 * i + 2))
                for tt in range(2):
                    for j in range(2):
                        last = mm(out[:, tt * 256 + j * P:tt * 256 + j * P + P],
                                  q_k[:, 2 + j, (2 * i + tt) * P:(2 * i + tt + 1) * P], ident)
                last.then_inc(S("k_turned"), 1)
            pe.wait_ge(*at_count("q_head", MH))
            pe.wait_ge(*at_count("pads", 3))
            pe.wait_ge(*at_count("exp_m", 1))
            for tt in range(TT):
                tok = slice(tt * P, tt * P + P)
                out = take(("qk", tt), ("probs", tt + 1))
                for h in range(MH):
                    last = mm(out[:, h * P:h * P + P], q_k[:, 2 + h // 2, tok], q_head[:, h, tok])
                last.then_inc(S("qk_done"), 1)
                out = take(("exp_m", tt), ("den", tt + 1))
                for h in range(MH):
                    last = mm(out[:, h * P:h * P + P], constant("sel4", h, rows=MH), m_rows(f_row, tt * P, P))
                last.then_inc(S("exp_m_done"), 1)
                pe.wait_ge(*at_count("probs", tt + 1))
                if tt:
                    pe.wait_ge(*at_count("m_state", tt))
                    pe.wait_ge(*at_count("q_inter", MH))
                else:
                    pe.wait_ge(*at_count("v_tok", TT))
                num = take(("num", tt), ("m_out", tt + 1))
                for h in range(MH):
                    last = mm(num[:, h * P:h * P + P], v_aug[:, tt, h, 0:P], probs[:, tt % 2, h * P:h * P + P], True, tt == 0)
                    if tt:
                        last = mm(num[:, h * P:h * P + P], m_state[:, h // 2, 0:P], q_inter[:, h, tok], False, True)
                last.then_inc(S("num_done"), 1)
                den = take(("den", tt), ("den_abs", tt + 1))
                last = mm(den[:, :], ones, probs[:, tt % 2, :], True, tt == 0)
                if tt:
                    for h in range(MH):
                        last = mm(den[:, h * P:h * P + P], m_state[:, h // 2, P:2 * P], q_inter[:, h, tok], False, True)
                last.then_inc(S("den_done"), 1)
                if tt < TT - 1:
                    out = take(("m_state", tt), ("m_state", tt + 1))
                    pe.wait_ge(*at_count("k_tok", tt + 1))
                    for h in range(MH):
                        r = 64 * (h % 2)
                        last = mm(out[r:r + 64, h // 2 * 256:h // 2 * 256 + 256], k_tok[:, tt, h * 64:h * 64 + 64], v_aug[:, tt, h, :])
                    last.then_inc(S("m_state_done"), 1)
            for h in range(MH):
                out = take(("m_sum", h), ("m_std", h + 1))
                pe.wait_ge(*at_count("m_square", h + 1))
                mm(out[:, :], ones, q_head[:, h, :]).then_inc(S("m_sum_done"), 1)

        def act_mlstm_gates(act, steps):
            act.wait_ge(*at_count("gate_bias", 2))
            for i, row in enumerate((g_row, f_row)):
                act.wait_ge(*at_count("gates_done", i + 1))
                act.activation(m_rows(row), bank[at[("gate", i)]][0:MH, :], ACT.Tanh, bias=m_small[0:MH, i:i + 1],
                               scale=1 / CAP).then_inc(S("gate_raw"), 1)
            act.wait_ge(*at_count("gate_raw", 2))
            steps.mark(act.activation(m_rows(f_row), m_rows(f_row), ACT.Exp, scale=-CAP))
            steps.wait()
            act.activation(m_rows(f_row), m_rows(f_row), ACT.Ln, bias=column("one", rows=MH)).then_inc(S("forget"), 1)

        def act_q_k(act):
            for t in range(4):
                act.wait_ge(*at_count("m_conv", 16 + t - 3))
                act.activation(q_k[:, t, :], q_k[:, t, :], ACT.Silu, bias=column("mlstm_conv_b", t)).then_inc(S("q_k"), 1)

        def act_mlstm(act, steps):
            for tt in range(TT):
                act.wait_ge(*at_count("v_turned", tt + 1))
                act.activation(v_aug[:, tt, :, 0:P], bank[at[("v_tok", tt)]][:, :].rearrange("p (h v) -> p h v", h=MH),
                               ACT.Copy).then_inc(S("v_tok"), 1)
            act.wait_ge(*at_count("m_logs", 4))
            act.activation(m_rows(w_row), m_rows(w_row), ACT.Exp, scale=-1.0).then_inc(S("m_weights"), 1)
            act.activation(m_rows(k_row), m_rows(k_row), ACT.Exp).then_inc(S("m_weights"), 1)
            act.activation(m_small[0:MH, 16:16 + TT], m_small[0:MH, 8:8 + TT], ACT.Exp, scale=-1.0).then_inc(S("m_weights"), 1)
            act.activation(m_rows(f_row), m_rows(f_row), ACT.Exp).then_inc(S("exp_m"), 1)
            for tt in range(TT):
                act.wait_ge(*at_count("decay_arg", MH * TT))
                act.activation(decay[:, tt, :], decay[:, tt, :], ACT.Exp, scale=-1.0).then_inc(S("decay"), 1)
            for tt in range(TT):
                act.wait_ge(*at_count("den_done", tt + 1))
                if tt:
                    act.wait_ge(*at_count("den", tt))
                act.activation(den_abs[:, :], bank[at[("den", tt)]][:, :], ACT.Abs).then_inc(S("den_abs"), 1)
            for h in range(MH):
                act.wait_ge(*at_count("m_out", TT))
                act.activation(q_head[:, h, :], y_mlstm[:, h, :], ACT.Square).then_inc(S("m_square"), 1)
            for h in range(MH):
                act.wait_ge(*at_count("m_sum_done", h + 1))
                act.activation(q_inter[:, h, :], bank[at[("m_sum", h)]][:, :], ACT.Sqrt, bias=column("eps_norm"),
                               scale=1 / P).then_inc(S("m_std"), 1)

        den_abs = rstd[:, 0, :]
        den_max = rstd[:, 1, :]

        def dve_mlstm(dve, steps):
            dve.wait_ge(*at_count("pads", 2))
            for tap in range(4):
                for t in range(4):
                    src = m_proj[:, t, PAD - 3 + tap:PAD - 3 + tap + T]
                    w = column("mlstm_conv_w", 4 * tap + t)
                    if tap == 0:
                        dve.wait_ge(*at_count("m_proj", t + 1))
                        dve.tensor_scalar(q_k[:, t, :], src, w, None, ALU.mult).then_inc(S("m_conv"), 1)
                    else:
                        dve.wait_ge(*at_count("m_conv", 4 * (tap - 1) + t + 1))
                        dve.scalar_tensor_tensor(q_k[:, t, :], src, w, q_k[:, t, :], ALU.mult, ALU.add).then_inc(S("m_conv"), 1)
            dve.wait_ge(*at_count("forget", 1))
            steps.mark(dve.tensor_tensor_scan(m_rows(b_row), constant("reset128", 0, T, MH), m_rows(f_row), 0.0, ALU.mult, ALU.add))
            steps.mark(dve.memset(m_rows(w_row), 0.0))
            steps.wait()
            steps.mark(dve.scalar_tensor_tensor(m_rows(g_row), m_rows(g_row), CAP, m_rows(b_row), ALU.mult, ALU.add))
            steps.mark(dve.tensor_scalar(w_row[0:MH, P:T:P], b_row[0:MH, P - 1:T - P:P], -1.0, None, ALU.mult))
            steps.wait()
            steps.mark(dve.tensor_tensor_scan(m_rows(max_row), m_rows(w_row), m_rows(g_row), 0.0, ALU.add, ALU.max))
            steps.mark(dve.memset(m_small[0:MH, 4:4 + TT], 0.0))
            steps.wait()
            steps.mark(dve.tensor_tensor(m_small[0:MH, 5:4 + TT], max_row[0:MH, P - 1:T - P:P], b_row[0:MH, P - 1:T - P:P], ALU.subtract))
            steps.wait()

            def by_tile(x):
                return x.rearrange("h (c t) -> h c t", c=TT)

            carried = m_small[0:MH, 4:4 + TT].rearrange("h (c t) -> h c t", t=1).broadcast_to([MH, TT, P])
            m_last = max_row[0:MH, P - 1:T:P]
            last_b = m_last.rearrange("h (c t) -> h c t", t=1).broadcast_to([MH, TT, P])
            dve.tensor_tensor(by_tile(m_rows(w_row)), by_tile(m_rows(max_row)), carried, ALU.subtract).then_inc(S("m_logs"), 1)
            dve.tensor_tensor(by_tile(m_rows(k_row)), by_tile(m_rows(g_row)), last_b, ALU.subtract).then_inc(S("m_logs"), 1)
            dve.tensor_tensor(m_small[0:MH, 8:8 + TT], m_last, m_small[0:MH, 4:4 + TT], ALU.subtract).then_inc(S("m_logs"), 1)
            dve.tensor_tensor(m_rows(f_row), m_rows(b_row), m_rows(max_row), ALU.subtract).then_inc(S("m_logs"), 1)
            dve_shift(dve)
            for h in range(MH):
                dve.wait_ge(*at_count("q_k", h // 2 + 1))
                dve.tensor_scalar(q_head[:, h, :], q_k[:, h // 2, :], column_half(h % 2), 0.125, ALU.mult, ALU.mult).then_inc(S("q_head"), 1)
            dve.wait_ge(*at_count("gate_cols_done", 1))
            cols = bank[at[("gate_cols",)]]
            dve.tensor_copy(m_cols[:, :], cols[:, 0:32]).then_inc(S("gate_cols"), 1)
            for h in range(MH):
                r = slice(64 * (h % 2), 64 * (h % 2) + 64)
                dve.tensor_copy(m_carry[r, h // 2 * TT:h // 2 * TT + TT], cols[r, 32 + TT * h:32 + TT * h + TT]).then_inc(S("gate_cols"), 1)
            dve.wait_ge(*at_count("gate_cols", 5))
            dve.wait_ge(*at_count("m_conv", 16))
            for h in range(MH):
                dve.wait_ge(*at_count("max_done", h + 1))
                for tt in range(TT):
                    dve.tensor_scalar(decay[:, tt, h * P:h * P + P], bank[at[("max", h)]][:, tt * P:tt * P + P],
                                      m_cols[:, tt * MH + h:tt * MH + h + 1], 0.0, ALU.subtract, ALU.max).then_inc(S("decay_arg"), 1)
            dve.wait_ge(*at_count("q_head", MH))
            for h in range(MH):
                dve.wait_ge(*at_count("inter_done", h + 1))
                dve.tensor_tensor(q_inter[:, h, :], q_head[:, h, :], bank[at[("inter", h)]][:, :], ALU.mult).then_inc(S("q_inter"), 1)
            for tt in range(TT):
                dve.wait_ge(*at_count("k_turned", tt // 2 + 1))
                dve.tensor_tensor(k_tok[:, tt, :].rearrange("p (h d) -> p h d", h=MH),
                                  bank[at[("k_tok", tt // 2)]][:, tt % 2 * 256:tt % 2 * 256 + 256].rearrange("p (h d) -> p h d", h=MH),
                                  m_cols[:, (TT + tt) * MH:(TT + tt + 1) * MH].rearrange("p (h d) -> p h d", d=1).broadcast_to([P, MH, 64]),
                                  ALU.mult).then_inc(S("k_tok"), 1)
            for tt in range(TT):
                dve.wait_ge(*at_count("decay", tt + 1))
                dve.tensor_tensor(decay[:, tt, :].rearrange("p (h t) -> p h t", h=MH), decay[:, tt, :].rearrange("p (h t) -> p h t", h=MH),
                                  constant("causal").rearrange("p (a t) -> p a t", a=1).broadcast_to([P, MH, P]), ALU.mult).then_inc(S("decay_masked"), 1)
            for tt in range(TT):
                dve.wait_ge(*at_count("decay_masked", tt + 1))
                dve.wait_ge(*at_count("qk_done", tt + 1))
                if tt >= 2:
                    dve.wait_ge(*at_count("den_done", tt - 1))
                dve.tensor_tensor(probs[:, tt % 2, :], bank[at[("qk", tt)]][:, :], decay[:, tt, :], ALU.mult).then_inc(S("probs"), 1)
                if tt < TT - 1:
                    dve.wait_ge(*at_count("m_state_done", tt + 1))
                    new = bank[at[("m_state", tt)]][:, :]
                    if tt == 0:
                        dve.tensor_copy(m_state[:, :, :].rearrange("p a b -> p (a b)"), new).then_inc(S("m_state"), 1)
                    else:
                        dve.wait_ge(*at_count("den_done", tt + 1))
                        for j in range(2):
                            ins = dve.scalar_tensor_tensor(m_state[:, j, :], m_state[:, j, :], m_carry[:, j * TT + tt:j * TT + tt + 1],
                                                           new[:, j * 256:j * 256 + 256], ALU.mult, ALU.add)
                        ins.then_inc(S("m_state"), 1)
                dve.wait_ge(*at_count("den_abs", tt + 1))
                dve.wait_ge(*at_count("exp_m_done", tt + 1))
                dve.tensor_tensor(den_max, den_abs, bank[at[("exp_m", tt)]][:, :], ALU.max).then_inc(S("den"), 1)
                dve.wait_ge(*at_count("den", tt + 1))
                steps.mark(dve.reciprocal(den_max, den_max))
                steps.wait()
                dve.wait_ge(*at_count("num_done", tt + 1))
                dve.tensor_tensor(y_mlstm[:, :, tt * P:tt * P + P], bank[at[("num", tt)]][:, :].rearrange("p (h t) -> p h t", h=MH),
                                  den_max.rearrange("p (h t) -> p h t", h=MH), ALU.mult).then_inc(S("m_out"), 1)
            for h in range(MH):
                dve.wait_ge(*at_count("m_std", h + 1))
                steps.mark(dve.reciprocal(q_inter[:, h, :], q_inter[:, h, :]))
                steps.wait()
                steps.mark(dve.scalar_tensor_tensor(y_mlstm[:, h, :], y_mlstm[:, h, :], column("mlstm_hn_w", h), q_inter[:, h, :], ALU.mult, ALU.mult))
                steps.wait()
                dve.tensor_tensor(y_mlstm[:, h, :], y_mlstm[:, h, :], m_proj[:, 8 + h, PAD:TP], ALU.mult).then_inc(S("y_mlstm"), 1)
        WA_TILE, G_TILE = 12, 13
        rate = area(13416, RW, T)
        b_in = area(15464, RW, T)
        kk = area(17512, RW, T)
        gate_r = area(19560, RW, T)
        bonus = area(21608, RW, T)
        sums = area(23656, RW, T)
        cum_p = area(25704, RW, T)
        cum_inv = area(27752, RW, T)
        v_tok_r, b_tok = area(13416, TT, 512), area(23656, TT, 512)
        k_tok_r, kk_tok = hT[:, 0:4, :], hT[:, 4:8, :]
        r_b = area(25704, 8 * P)
        r_k = area(27752, 8 * P)
        k_scale = area(4128, 4, T)
        shift_diff = area(29408, T)
        V0 = 6192 + 8 * TP
        inv_x, inv_xt = [area(0, 4 * P), area(26728, 4 * P)], [area(512, 4 * P), area(27240, 4 * P)]
        level_t, prod_t = [area(1024, 4 * P), area(28776, 4 * P)], [area(4128, 4 * P), area(29288, 4 * P)]
        a_t, bk_t = [area(4640, 4 * P), area(V0 + 1024, 4 * P)], [area(5152, 4 * P), area(V0 + 1536, 4 * P)]
        bv = [area(5664, 4, 64), area(5920, 4, 64)]
        w_t, u_tok = area(V0, 4, P), area(V0 + 512, 512)
        S0 = 6192 + 12 * TP
        sa = area(S0, 512)
        r_state = area(1536, 4, P)
        chunk_p = rstd[:, 0, :].rearrange("p (r c x) -> p r c x", r=4, c=8)[:, :, :, 0:1]
        y_rwkv = area(6192 + 4 * TP, RW, TP)[:, :, PAD:TP]
        masked_p = gain

        def heads(parity):
            return [parity, parity + 2, parity + 4, parity + 6]

        def n_level(tt, l, par):
            return 12 * tt + 2 * l + par + 1

        def n_pairs(tt, i, par):
            return 8 * tt + i // 2 * 4 + 2 * par + i % 2 + 1

        def n_prod(tt, l, par):
            return 10 * tt + 2 * (l - 1) + par + 1

        def n_xox(tt, l, par):
            return 18 * tt + (4 * (l - 1) + 2 * par + 2 if l < 5 else 16 + par + 1)

        def n_inv_xt(tt, l, par):
            return 22 * tt + (4 * l + 2 * par + 1 if l < 5 else 20 + par + 1)

        def n_inv_x(tt, l, par):
            return n_inv_xt(tt, l, par) + 1

        def pe_rwkv(pe, mm, take):
            pe.wait_ge(*at_count("r_lora", 2))
            for n in range(RW):
                out = take(("decay_up", n), ("rate", n + 1))
                mm(out[:, :], lora_up[0:64, n * P:n * P + P], r_proj[0:64, WA_TILE, PAD:TP]).then_inc(S("lora_done"), 1)
            for n in range(RW):
                out = take(("a_up", n), ("r_a", n + 1))
                mm(out[:, :], lora_up[64:128, n * P:n * P + P], r_proj[64:128, WA_TILE, PAD:TP]).then_inc(S("lora_done"), 1)
            for n in range(RW):
                out = take(("g_up", n), ("gate_r", n + 1))
                mm(out[:, :], g_up[:, n * P:n * P + P], r_proj[:, G_TILE, PAD:TP]).then_inc(S("lora_done"), 1)
            for n in range(RW):
                out = take(("kk_sum", n), ("kk_std", n + 1))
                pe.wait_ge(*at_count("kk_square", n + 1))
                mm(out[:, :], head_ones, sums[:, n, :]).then_inc(S("kk_sum_done"), 1)
            for n in range(RW):
                out = take(("bonus_sum", n), ("bonus", n + 1))
                pe.wait_ge(*at_count("bonus_in", n + 1))
                mm(out[:, :], head_ones, bonus[:, n, :]).then_inc(S("bonus_done"), 1)
            pe.wait_ge(*at_count("r_ready", 4 * RW))
            for i, src in enumerate((r_proj[:, 8:12, PAD:TP], b_in, r_proj[:, 4:8, PAD:TP], kk)):
                for tt in range(TT):
                    out = take(("r_tok", i, tt), ("r_tok", 4 * i + tt + 1))
                    for n in range(RW):
                        last = mm(out[:, n * P:n * P + P], src[:, n, tt * P:tt * P + P], ident)
                    last.then_inc(S("r_turned"), 1)
            for tt in range(TT):
                tok = slice(tt * P, tt * P + P)

                def pairs(key, i, par, lhs, rhs):
                    rows = slice(64 * par, 64 * par + 64)
                    out = take((key, tt, par), ("pairs", n_pairs(tt, i, par)))
                    for j, h in enumerate(heads(par)):
                        last = mm(out[:, j * P:j * P + P], lhs[rows, h // 2, tok], rhs[rows, h // 2, tok])
                    last.then_inc(S("pairs_done"), 1)

                r_f, k_f = r_proj[:, 0:4, PAD:TP], r_proj[:, 4:8, PAD:TP]
                for par in range(2):
                    pairs("a_t", 0, par, b_in, kk)
                    pairs("bk_t", 1, par, k_f, kk)
                for l in range(6):
                    for par in range(2):
                        pe.wait_ge(*at_count("level", n_level(tt, l, par)))
                        if l:
                            pe.wait_ge(*at_count("inv", n_inv_x(tt, l - 1, par)))
                        out = take(("ox", tt, par, l), ("prod", n_prod(tt, l, par)) if l else ("inv", n_inv_x(tt, 0, par)))
                        for i in range(4):
                            c = slice(i * P, i * P + P)
                            last = mm(out[:, c], level_t[par][:, c], ident if l == 0 else inv_x[par][:, c])
                        last.then_inc(S("ox_done"), 1)
                    for par in range(2):
                        if l == 0:
                            g = 2 * tt + par
                            pe.wait_ge(*at_count("pairs", n_pairs(tt, 1, par)))
                            out = take(("bv", g), ("bv", g + 1))
                            for i, h in enumerate(heads(par)):
                                last = mm(out[:, i * 64:i * 64 + 64], bk_t[par][:, i * P:i * P + P], v_tok_r[:, tt, h * 64:h * 64 + 64])
                            last.then_inc(S("bv_done"), 1)
                            continue
                        pe.wait_ge(*at_count("prod", n_prod(tt, l, par)))
                        out_t = take(("xox_t", tt, par, l), ("inv", n_inv_xt(tt, l, par)))
                        for i in range(4):
                            c = slice(i * P, i * P + P)
                            last = mm(out_t[:, c], prod_t[par][:, c], inv_xt[par][:, c])
                        last.then_inc(S("xox_done"), 1)
                        if l == 5:
                            continue
                        out = take(("xox", tt, par, l), ("inv", n_inv_x(tt, l, par)))
                        for i in range(4):
                            c = slice(i * P, i * P + P)
                            last = mm(out[:, c], inv_xt[par][:, c], prod_t[par][:, c])
                        last.then_inc(S("xox_done"), 1)
                    if l == 1:
                        for par in range(2):
                            pairs("r_b", 2, par, b_in, r_f)
                            pairs("r_k", 3, par, k_f, r_f)
                for par in range(2):
                    g, rows = 2 * tt + par, slice(64 * par, 64 * par + 64)
                    pe.wait_ge(*at_count("inv", n_inv_xt(tt, 5, par)))
                    out = take(("w_t", g), ("w_t", g + 1))
                    for i, h in enumerate(heads(par)):
                        last = mm(out[rows, i * P:i * P + P], kk_tok[:, tt, h * 64:h * 64 + 64], inv_xt[par][:, i * P:i * P + P])
                    last.then_inc(S("w_done"), 1)
                    pe.wait_ge(*at_count("bv", g + 1))
                    out = take(("u", g), ("u", g + 1))
                    for i, h in enumerate(heads(par)):
                        last = mm(out[:, i * 64:i * 64 + 64], inv_xt[par][:, i * P:i * P + P], bv[par][:, i, :])
                    last.then_inc(S("u_done"), 1)
                y_state = None
                for half in range(2):
                    c = 2 * tt + half
                    rows = slice(64 * half, 64 * half + 64)
                    pe.wait_ge(*at_count("r_state", c + 1))
                    if half == 0:
                        pe.wait_ge(*at_count("w_t", 2 * tt + 2))
                    out = take(("ws", c), ("sa", c + 1))
                    for n in range(RW):
                        last = mm(out[:, n * P:n * P + P], w_t[:, n, :], r_state[:, n, :])
                    last.then_inc(S("ws_done"), 1)
                    if half == 0:
                        y_state = take(("y_state", tt), ("y_state", tt + 1))
                    for n in range(RW):
                        last = mm(y_state[:, n * P + 64 * half:n * P + 64 * half + 64], r_state[:, n, :],
                                  r_proj[:, n, PAD + c * C64:PAD + c * C64 + C64])
                    last.then_inc(S("y_state_done"), 1)
                    pe.wait_ge(*at_count("sa", c + 1))
                    if c < 7:
                        out = take(("new_state", c), ("r_state_sum", c + 1))
                        for n in range(RW):
                            cc = slice(n * P, n * P + P)
                            mm(out[:, cc], b_tok[rows, tt, cc], sa[rows, cc], True, False)
                            last = mm(out[:, cc], k_tok_r[rows, tt, cc], v_tok_r[rows, tt, cc], False, True)
                        last.then_inc(S("new_state_done"), 1)
                out = take(("y_in", tt), ("y_raw", tt + 1))
                for h in range(8):
                    cc, o = slice(h // 2 * P, h // 2 * P + P), slice(64 * (h % 2), 64 * (h % 2) + 64)
                    m = (h % 2 * 4 + h // 2) * P
                    mm(out[o, cc], sa[:, h * 64:h * 64 + 64], r_b[:, m:m + P], True, False)
                    last = mm(out[o, cc], v_tok_r[:, tt, h * 64:h * 64 + 64], r_k[:, m:m + P], False, True)
                last.then_inc(S("y_in_done"), 1)
            for n in range(RW):
                out = take(("gn_mean", n), ("gn_centred", n + 1))
                if n == 0:
                    pe.wait_ge(*at_count("y_raw", TT))
                mm(out[:, :], head_ones, y_rwkv[:, n, :]).then_inc(S("gn_mean_done"), 1)
            for n in range(RW):
                out = take(("gn_var", n), ("gn_std", n + 1))
                pe.wait_ge(*at_count("gn_square", n + 1))
                mm(out[:, :], head_ones, rate[:, n, :]).then_inc(S("gn_var_done"), 1)

        def act_rwkv(act, steps):
            act.wait_ge(*at_count("shifted", R_TILES))
            act.activation(r_proj[0:64, WA_TILE, PAD:TP], r_proj[0:64, WA_TILE, PAD:TP], ACT.Tanh).then_inc(S("r_lora"), 1)
            act.activation(x_in(G_TILE), x_in(G_TILE), ACT.Sigmoid).then_inc(S("r_lora"), 1)
            act.wait_ge(*at_count("y_mlstm", MH))
            for n in range(RW):
                act.wait_ge(*at_count("lora_done", n + 1))
                act.activation(rate[:, n, :], bank[at[("decay_up", n)]][:, :], ACT.Sigmoid, bias=column("rwkv_w0", n)).then_inc(S("rate"), 1)
            for n in range(RW):
                act.wait_ge(*at_count("lora_done", RW + n + 1))
                act.activation(b_in[:, n, :], bank[at[("a_up", n)]][:, :], ACT.Sigmoid, bias=column("rwkv_a0", n)).then_inc(S("r_a"), 1)
            for n in range(RW):
                act.wait_ge(*at_count("lora_done", 2 * RW + n + 1))
                act.activation(gate_r[:, n, :], bank[at[("g_up", n)]][:, :], ACT.Copy).then_inc(S("gate_r"), 1)
            for n in range(RW):
                act.wait_ge(*at_count("kk_raw", n + 1))
                act.activation(sums[:, n, :], kk[:, n, :], ACT.Square).then_inc(S("kk_square"), 1)
            for n in range(RW):
                act.wait_ge(*at_count("kk_sum_done", n + 1))
                act.activation(cum_p[:, n, :], bank[at[("kk_sum", n)]][:, :], ACT.Sqrt).then_inc(S("kk_std"), 1)
            for n in range(RW):
                act.wait_ge(*at_count("kk_unit", n + 1))
                act.wait_ge(*at_count("rate_before", n + 1))
                act.activation(cum_p[:, n, :], sums[:, n, :], ACT.Exp, scale=-DECAY).then_inc(S("cum"), 1)
                act.activation(cum_inv[:, n, :], sums[:, n, :], ACT.Exp, scale=DECAY).then_inc(S("cum"), 1)
                act.activation(rate[:, n, :], rate[:, n, :], ACT.Exp, scale=-DECAY).then_inc(S("cum"), 1)
            act.wait_ge(*at_count("bonus", RW))
            act.wait_ge(*at_count("r_ready", 4 * RW))
            for i, dst in enumerate((v_tok_r, b_tok, k_tok_r, kk_tok)):
                for tt in range(TT):
                    act.wait_ge(*at_count("r_turned", 4 * i + tt + 1))
                    act.activation(dst[:, tt, :], bank[at[("r_tok", i, tt)]][:, :], ACT.Copy).then_inc(S("r_tok"), 1)
            for tt in range(TT):
                for l in range(1, 6):
                    for par in range(2):
                        act.wait_ge(*at_count("ox_done", n_level(tt, l, par)))
                        if tt or l > 1:
                            act.wait_ge(*at_count("xox_done", n_xox(tt, l - 1, par) if l > 1 else n_xox(tt - 1, 5, par)))
                        act.activation(prod_t[par][:, :], bank[at[("ox", tt, par, l)]][:, :], ACT.Copy).then_inc(S("prod"), 1)
            act.wait_ge(*at_count("y_in_done", TT))
            for n in range(MH):
                act.activation(y_hi_r[:, RW + n, :], y_mlstm[:, n, :], ACT.Copy).then_inc(S("y_hi"), 1)
            for n in range(RW):
                act.wait_ge(*at_count("gn_centred", n + 1))
                act.activation(rate[:, n, :], y_rwkv[:, n, :], ACT.Square).then_inc(S("gn_square"), 1)
            for n in range(RW):
                act.wait_ge(*at_count("gn_var_done", n + 1))
                act.activation(cum_p[:, n, :], bank[at[("gn_var", n)]][:, :], ACT.Sqrt, bias=column("eps_gn"), scale=1 / 64).then_inc(S("gn_std"), 1)
            for n in range(RW):
                act.wait_ge(*at_count("y_rwkv", n + 1))
                act.activation(y_hi_r[:, n, :], y_rwkv[:, n, :], ACT.Copy).then_inc(S("y_hi"), 1)

        def dve_shift(dve):
            for t in range(R_TILES):
                dve.wait_ge(*at_count("r_proj", t + 1))
                if t:
                    dve.wait_ge(*at_count("shifted", t))
                dve.tensor_tensor(shift_diff, x_in(t, -1), x_in(t), ALU.subtract).then_inc(S("shift_diff"), 1)
                dve.wait_ge(*at_count("shift_diff", t + 1))
                dve.scalar_tensor_tensor(x_in(t), shift_diff, column("rwkv_mu", t), x_in(t), ALU.mult, ALU.add).then_inc(S("shifted"), 1)

        def dve_rwkv(dve, steps):
            dve.wait_ge(*at_count("shifted", R_TILES))
            for n in range(RW):
                dve.tensor_scalar(kk[:, n, :], x_in(4 + n), column("rwkv_k_k", n), None, ALU.mult).then_inc(S("kk_raw"), 1)
            steps.mark(dve.tensor_scalar(gain[:, 0:4], col[:, COL["rwkv_k_a"]:COL["rwkv_k_a"] + 4], -1.0, 1.0, ALU.mult, ALU.add))
            steps.wait()
            for n in range(RW):
                dve.wait_ge(*at_count("r_a", n + 1))
                steps.mark(dve.tensor_scalar(k_scale[:, n, :], b_in[:, n, :], column("rwkv_k_a", n), gain[:, n:n + 1], ALU.mult, ALU.add))
            steps.wait()
            dve.wait_ge(*at_count("kk_raw", RW))
            for n in range(RW):
                steps.mark(dve.tensor_tensor(x_in(4 + n), x_in(4 + n), k_scale[:, n, :], ALU.mult))
            steps.wait()
            for n in range(RW):
                dve.scalar_tensor_tensor(bonus[:, n, :], x_in(n), column("rwkv_r_k", n), x_in(4 + n), ALU.mult, ALU.mult).then_inc(S("bonus_in"), 1)
            for n in range(RW):
                dve.wait_ge(*at_count("kk_std", n + 1))
                steps.mark(dve.tensor_scalar(cum_p[:, n, :], cum_p[:, n, :], 1e-12, None, ALU.max))
            steps.wait()
            for n in range(RW):
                steps.mark(dve.reciprocal(cum_p[:, n, :], cum_p[:, n, :]))
            steps.wait()
            for n in range(RW):
                dve.wait_ge(*at_count("kk_square", n + 1))
                dve.tensor_tensor(kk[:, n, :], kk[:, n, :], cum_p[:, n, :], ALU.mult).then_inc(S("kk_unit"), 1)
            for n in range(RW):
                dve.wait_ge(*at_count("rate", n + 1))
                dve.wait_ge(*at_count("kk_sum_done", n + 1))
                dve.tensor_tensor_scan(sums[:, n, :], constant("reset64", 0, T), rate[:, n, :], 0.0, ALU.mult, ALU.add).then_inc(S("rate_sums"), 1)
            dve.wait_ge(*at_count("rate_sums", RW))
            for n in range(RW):
                dve.tensor_tensor(rate[:, n, :], sums[:, n, :], rate[:, n, :], ALU.subtract).then_inc(S("rate_before"), 1)
            dve.wait_ge(*at_count("kk_unit", RW))
            for n in range(RW):
                steps.mark(dve.tensor_tensor(b_in[:, n, :], b_in[:, n, :], kk[:, n, :], ALU.mult))
            steps.wait()
            for n in range(RW):
                dve.wait_ge(*at_count("bonus_done", n + 1))
                dve.tensor_tensor(bonus[:, n, :], bank[at[("bonus_sum", n)]][:, :], x_in(8 + n), ALU.mult).then_inc(S("bonus"), 1)
            for n in range(RW):
                dve.wait_ge(*at_count("cum", 3 * n + 3))
                for x, f in ((kk, rate), (b_in, cum_inv), (r_proj[:, 4:8, PAD:TP], cum_inv), (r_proj[:, 0:4, PAD:TP], cum_p)):
                    dve.tensor_tensor(x[:, n, :], x[:, n, :], f[:, n, :], ALU.mult).then_inc(S("r_ready"), 1)
            steps.mark(dve.tensor_copy(chunk_p, cum_p[:, :, C64 - 1:T:C64]))
            dve.memset(r_state[:, :, :], 0.0).then_inc(S("r_state"), 1)
            steps.wait()
            dve.wait_ge(*at_count("r_turned", 4 * TT))
            dve.wait_ge(*at_count("r_ready", 4 * RW))

            def masked(dst, key, tt, i, par, mask):
                dve.wait_ge(*at_count("pairs_done", n_pairs(tt, i, par)))
                dve.tensor_tensor(dst.rearrange("p (h t) -> p h t", h=4), bank[at[(key, tt, par)]][:, :].rearrange("p (h t) -> p h t", h=4),
                                  constant(mask).rearrange("p (a t) -> p a t", a=1).broadcast_to([P, 4, P]), ALU.mult).then_inc(S("pairs"), 1)

            def wide(x):
                return x.rearrange("p (h t) -> p h t", h=4)

            eye = ident.rearrange("p (a t) -> p a t", a=1).broadcast_to([P, 4, P])
            for tt in range(TT):
                if tt:
                    dve.wait_ge(*at_count("level", n_level(tt - 1, 5, 1)))
                    dve.wait_ge(*at_count("bv_done", 2 * tt))
                    dve.wait_ge(*at_count("y_in_done", tt))
                for par in range(2):
                    masked(a_t[par], "a_t", tt, 0, par, "strict64")
                    masked(bk_t[par], "bk_t", tt, 1, par, "strict64")
                for l in range(6):
                    for par in range(2):
                        g = 2 * tt + par
                        if l == 0:
                            dve.wait_ge(*at_count("level", n_level(tt, 0, par)))
                            if tt:
                                dve.wait_ge(*at_count("u_done", 2 * tt))
                            dve.tensor_tensor(wide(inv_xt[par]), eye, wide(level_t[par]), ALU.subtract).then_inc(S("inv"), 1)
                            dve.wait_ge(*at_count("ox_done", n_level(tt, 0, par)))
                            dve.tensor_tensor(wide(inv_x[par]), eye, wide(bank[at[("ox", tt, par, 0)]][:, :]), ALU.subtract).then_inc(S("inv"), 1)
                            continue
                        dve.wait_ge(*at_count("inv", n_inv_x(tt, l - 1, par)))
                        dve.wait_ge(*at_count("xox_done", n_xox(tt, l, par)))
                        dve.tensor_tensor(inv_xt[par], inv_xt[par], bank[at[("xox_t", tt, par, l)]][:, :], ALU.subtract).then_inc(S("inv"), 1)
                        if l < 5:
                            dve.tensor_tensor(inv_x[par], inv_x[par], bank[at[("xox", tt, par, l)]][:, :], ALU.subtract).then_inc(S("inv"), 1)
                    for par in range(2):
                        g = 2 * tt + par
                        if l == 0:
                            dve.wait_ge(*at_count("bv_done", g + 1))
                            dve.tensor_copy(bv[par].rearrange("p a b -> p (a b)"), bank[at[("bv", g)]][:, 0:256]).then_inc(S("bv"), 1)
                        if l == 1:
                            masked(r_b[:, par * 512:par * 512 + 512], "r_b", tt, 2, par, "causal64")
                            masked(r_k[:, par * 512:par * 512 + 512], "r_k", tt, 3, par, "causal64")
                for par in range(2):
                    g, rows = 2 * tt + par, slice(64 * par, 64 * par + 64)
                    dve.wait_ge(*at_count("w_done", g + 1))
                    dve.tensor_copy(w_t[rows, :, :], wide(bank[at[("w_t", g)]][rows, :])).then_inc(S("w_t"), 1)
                    dve.wait_ge(*at_count("u_done", g + 1))
                    dve.tensor_copy(u_tok.rearrange("p (n two d) -> p n two d", n=4, two=2)[:, :, par, :],
                                    bank[at[("u", g)]][:, 0:256].rearrange("p (n d) -> p n d", n=4)).then_inc(S("u"), 1)
                dve.wait_ge(*at_count("u", 2 * tt + 2))
                for half in range(2):
                    c = 2 * tt + half
                    rows = slice(64 * half, 64 * half + 64)
                    dve.wait_ge(*at_count("ws_done", c + 1))
                    if tt:
                        dve.wait_ge(*at_count("y_in_done", tt))
                    dve.scalar_tensor_tensor(sa[rows, :], bank[at[("ws", c)]][rows, :], -1.0, u_tok[rows, :], ALU.mult, ALU.subtract).then_inc(S("sa"), 1)
                    if c == 7:
                        continue
                    dve.wait_ge(*at_count("new_state_done", c + 1))
                    dve.wait_ge(*at_count("r_state", c + 1))
                    dve.tensor_tensor(r_state[:, :, :].rearrange("p n i -> p (n i)"), r_state[:, :, :].rearrange("p n i -> p (n i)"),
                                      bank[at[("new_state", c)]][:, :], ALU.add).then_inc(S("r_state_sum"), 1)
                    dve.wait_ge(*at_count("r_state_sum", c + 1))
                    for n in range(RW):
                        ins = dve.scalar_tensor_tensor(r_state[:, n, :], r_state[:, n, :], chunk_p[:, n, c, :], constant("same_head"), ALU.mult, ALU.mult)
                    ins.then_inc(S("r_state"), 1)
                dve.wait_ge(*at_count("y_state_done", 2 * tt + 2))
                dve.tensor_copy(y_rwkv[:, :, tt * P:tt * P + P], wide(bank[at[("y_state", tt)]][:, :])).then_inc(S("y_state"), 1)
                dve.wait_ge(*at_count("y_state", tt + 1))
                dve.wait_ge(*at_count("y_in_done", tt + 1))
                dve.tensor_tensor(y_rwkv[:, :, tt * P:tt * P + P], y_rwkv[:, :, tt * P:tt * P + P], wide(bank[at[("y_in", tt)]][:, :]), ALU.add).then_inc(S("y_raw"), 1)
            dve.wait_ge(*at_count("y_raw", TT))
            for n in range(RW):
                dve.wait_ge(*at_count("gn_mean_done", n + 1))
                dve.scalar_tensor_tensor(y_rwkv[:, n, :], bank[at[("gn_mean", n)]][:, :], -1 / 64, y_rwkv[:, n, :], ALU.mult, ALU.add).then_inc(S("gn_centred"), 1)
            for n in range(MH):
                dve.wait_ge(*at_count("y_hi", n + 1))
                dve.tensor_tensor(y_mlstm_r[:, n, :], y_mlstm[:, n, :], y_hi_r[:, RW + n, :].bitcast(F32), ALU.subtract).then_inc(S("y_lo"), 1)
            for n in range(RW):
                dve.wait_ge(*at_count("gn_std", n + 1))
                steps.mark(dve.reciprocal(cum_p[:, n, :], cum_p[:, n, :]))
            steps.wait()
            for n in range(RW):
                steps.mark(dve.scalar_tensor_tensor(y_rwkv[:, n, :], y_rwkv[:, n, :], column("rwkv_gn_w", n), cum_p[:, n, :], ALU.mult, ALU.mult))
            steps.wait()
            for n in range(RW):
                steps.mark(dve.scalar_tensor_tensor(y_rwkv[:, n, :], y_rwkv[:, n, :], column("rwkv_gn_b", n), bonus[:, n, :], ALU.add, ALU.add))
            steps.wait()
            for n in range(RW):
                dve.wait_ge(*at_count("gate_r", n + 1))
                dve.tensor_tensor(y_rwkv[:, n, :], y_rwkv[:, n, :], gate_r[:, n, :], ALU.mult).then_inc(S("y_rwkv"), 1)
            for n in range(RW):
                dve.wait_ge(*at_count("y_hi", MH + n + 1))
                dve.tensor_tensor(y_rwkv_r[:, n, :], y_rwkv[:, n, :], y_hi_r[:, n, :].bitcast(F32), ALU.subtract).then_inc(S("y_lo"), 1)

        def pool_rwkv(pool):
            for tt in range(TT):
                for l in range(6):
                    for par in range(2):
                        if l == 0:
                            pool.wait_ge(*at_count("pairs", n_pairs(tt, 0, par)))
                        if tt or l:
                            pool.wait_ge(*at_count("ox_done", n_level(tt, l - 1, par) if l else n_level(tt - 1, 5, par)))
                        if l == 1:
                            pool.wait_ge(*at_count("inv", n_inv_xt(tt, 0, par)))
                        pool.tensor_tensor(level_t[par].rearrange("p (h t) -> p h t", h=4), a_t[par].rearrange("p (h t) -> p h t", h=4),
                                           constant("levels", l).rearrange("p (a t) -> p a t", a=1).broadcast_to([P, 4, P]), ALU.mult).then_inc(S("level"), 1)
        moe_sum = area(0, KD, T)
        expert_act = area(4096, 2, 2, T)
        expert_silu = area(6144, 2, T)
        expert_w = area(7168, 2, T)
        logits = area(8192, TT, 36)
        one_group, masked_e = area(8400, TT, NG), area(8464, TT * NG * EG)
        chosen = area(8600, TT, EG)
        ranked = area(8640, TT, EG)
        first, second = area(8680, TT, EG), area(8720, TT, EG)
        tiny = area(8760, 12 * TT)
        combine = area(8820, TT, NE)
        combine_t = area(8960, T)
        exp_g = area(9480, TT, NG)
        CAP_E = P
        h_tok = area(10000, 2, D)
        rows_in = area(12048, 2, D)
        rows_t = area(14096, 2, KD * P)
        sparse_silu, sparse_act = area(16144, 2 * P), area(16400, 2, 2 * P)
        y_rows = area(16912, 2, D)
        y_pick = area(18960, 4, D)
        pick = [area(23056, TT, NE), area(23184, TT, NE)]
        assigned, rank = area(23312, TT, NE), area(23440, TT, NE)
        table_row, y_row = area(23568, TT, NE), area(23696, TT, NE)
        picked = area(23824, TT, NE)
        totals = area(23952, NE)
        row_f = area(23984, 4 * TT)
        flag_f = area(24000, 1)
        table_w = slot_table[:, :].bitcast(F32)
        pair_w = pairs_u[:, :].bitcast(F32)

        def expert_unit(e, x):
            return at["moe_units"] + 6 * e - 2 + x

        def pe_moe(pe, mm, take, unit, unit_landed, freed, turn):
            out = take(("router",), ("logits", 1))
            pe.wait_ge(*at_count("norm_ffn_h", KD))
            for tt in range(TT):
                for k in range(KD):
                    last = mm(out[:, tt * 36:tt * 36 + 36], hT[:, k, tt * P:tt * P + P], router_w[:, k, :], k == 0, k == KD - 1)
            last.then_inc(S("router_done"), 1)
            for i in range(2 * TT):
                out = take(("h_tok", i), ("h_tok", i + 1))
                for n in range(4):
                    last = mm(out[:, n * P:n * P + P], hT[:, i % 2 * 4 + n, i // 2 * P:i // 2 * P + P], ident)
                last.then_inc(S("h_turned"), 1)
            out = take(("ranks",), ("totals", 1))
            pe.wait_ge(*at_count("assigned", 1))
            for tt in range(TT):
                for before in range(tt):
                    mm(out[:, tt * NE:tt * NE + NE], ones, assigned[:, before, :], before == 0, False)
                mm(out[:, tt * NE:tt * NE + NE], constant("causal"), assigned[:, tt, :], tt == 0, True)
            for tt in range(TT):
                last = mm(out[:, P:P + NE], ones, assigned[:, tt, :], tt == 0, tt == TT - 1)
            last.then_inc(S("ranks_done"), 1)
            u0 = at["moe_units"] = unit[0]

            def weights(e, x):
                if isinstance(e, int):
                    x = x + 2 if e == 0 else x - 4 if e == NE else x
                q, slot = divmod(u0 - 2 + x, RING)
                pe.wait_ge(*at_count(f"landed{slot}", (e + (q + 1)) * 16))
                return ring[:, slot, :].rearrange("p (k n) -> p k n", k=8)

            def gate_up(e, wait):
                for x in range(4):
                    w = weights(e, x)
                    if wait:
                        pe.wait_ge(*at_count("moe_silu" if x < 2 else "moe_up", (e - 1) * 2 + x % 2 + 1))
                    for k in range(KD):
                        last = mm(bank[x][:, :], w[:, k, :], hT[:, k, :], k == 0, k == KD - 1)
                    last.then_inc(S("unit_done"), 1)

            def down(e, first):
                w = [weights(e, 4), weights(e, 5)]
                pe.wait_ge(*at_count("moe_act", e * 2))
                for n in range(KD):
                    if n >= 4:
                        pe.wait_ge(*at_count("moe_add", (e - 1) * 8 + (n - 3)))
                    elif not first:
                        pe.wait_ge(*at_count("moe_add", (e - 2) * 8 + (n + 5)))
                    par = down.parity
                    for f in range(2):
                        last = mm(bank[4 + n % 4][:, :], w[f][:, n, :], expert_act[:, par, f, :], f == 0, f == 1)
                        if n == KD - 1:
                            last.then_inc(S("unit_done"), 1)
                    if n < KD - 1:
                        last.then_inc(S("down_done"), 1)

            for b in range(8):
                pe.wait_ge(*at_count(*freed[b]))
            pe.wait_ge(*at_count("flag", 1))
            overflow = pe.value_load(flag[0:1, 0:1], min_val=0, max_val=1)
            with pe.If(overflow):
                pe_dense(pe, mm, weights, gate_up, down, u0)
            with pe.Else():
                pe_sparse(pe, mm, weights)
            unit[0] = u0 + 6 * NE
            freed[:] = [("x_moe", KD)] * 8

        def pe_dense(pe, mm, weights, gate_up, down, u0):
            pe.wait_ge(*at_count("combine", 1))
            for tt in range(TT):
                last = mm(bank[4][0:NE, tt * P:tt * P + P], combine[:, tt, :], ident)
            last.then_inc(S("combine_turned"), 1)
            for x in range(4):
                w = weights(0, x)
                for k in range(KD):
                    last = mm(bank[x][:, :], w[:, k, :], hT[:, k, :], k == 0, k == KD - 1)
                last.then_inc(S("unit_done"), 1)
            gate_up(1, True)
            down.parity = 0
            pe.wait_ge(*at_count("combine_t", 1))
            down(1, True)
            with pe.Fori(0, (NE - 2) // 2) as i:
                for j in range(2):
                    e = i * 2 + (2 + j)
                    gate_up(e, True)
                    down.parity = (j + 1) % 2
                    down(e, False)
            pe_last_down(pe, mm, u0)

        def pe_last_down(pe, mm, u0):
            u = u0 + 4 + 6 * (NE - 1)
            w = []
            for f in range(2):
                pe.wait_ge(*at_count(f"landed{(u + f) % RING}", 16 * ((u + f) // RING + 1)))
                w.append(ring[:, (u + f) % RING, :].rearrange("p (k n) -> p k n", k=8))
            pe.wait_ge(*at_count("moe_act", 2 * NE))
            for n in range(KD):
                pe.wait_ge(*at_count("moe_add", KD * (NE - 1) + n - 3))
                for f in range(2):
                    last = mm(bank[4 + n % 4][:, :], w[f][:, n, :], expert_act[:, (NE - 1) % 2, f, :], f == 0, f == 1)
                    if n == KD - 1:
                        last.then_inc(S("unit_done"), 1)
                if n < KD - 1:
                    last.then_inc(S("down_done"), 1)

        def act_moe(act, steps):
            act.wait_ge(*at_count("group_arg", 1))
            act.activation(exp_g[:, :, :], exp_g[:, :, :], ACT.Exp).then_inc(S("group_exp"), 1)
            act.wait_ge(*at_count("second_arg", 1))
            act.activation(tiny[:, 4 * TT:5 * TT], tiny[:, 4 * TT:5 * TT], ACT.Exp).then_inc(S("second_exp"), 1)
            for i in range(2 * TT):
                tt, half = divmod(i, 2)
                act.wait_ge(*at_count("h_turned", i + 1))
                if tt >= 2 and half == 0:
                    act.wait_ge(*at_count(f"h_stored{tt % 2}", 16 * (tt // 2)))
                act.activation(h_tok[:, tt % 2, half * 512:half * 512 + 512], bank[at[("h_tok", i)]][:, :], ACT.Copy).then_inc(S("h_tok"), 1)
                if half:
                    act.wait_ge(*at_count("h_tok", i + 1))
                    act.dma_start(h_d[tt * P:tt * P + P, :], h_tok[:, tt % 2, :]).then_inc(S(f"h_stored{tt % 2}"), 16)
            act.wait_ge(*at_count("flag", 1))
            overflow = act.value_load(flag[0:1, 0:1], min_val=0, max_val=1)
            with act.If(overflow):
                act_dense(act)
            with act.Else():
                act_sparse(act)

        def act_dense(act):
            act.wait_ge(*at_count("combine_turned", 1))
            act.activation(combine_t[0:NE, :], bank[4][0:NE, :], ACT.Copy).then_inc(S("combine_t"), 1)
            act.wait_ge(*at_count("combine_t", 1))
            act.dma_start(combine_d, combine_t[0:NE, :]).then_inc(S("combine_stored"), 16)

            def silu(e, wait):
                for f in range(2):
                    act.wait_ge(*at_count("unit_done", e * 6 + (at["moe_units"] - 2 + f + 1 + (0 if wait else 2))))
                    if wait:
                        act.wait_ge(*at_count("moe_act", (e - 1) * 2 + f + 1))
                    act.activation(expert_silu[:, f, :], bank[f][:, :], ACT.Silu).then_inc(S("moe_silu"), 1)

            silu(0, False)
            silu(1, True)
            with act.Fori(0, (NE - 2) // 2) as i:
                for j in range(2):
                    silu(i * 2 + (2 + j), True)

        def dve_moe(dve, steps):
            def wide(x, n):
                return x.rearrange("p (t a) -> p t a", a=1).broadcast_to([P, TT, n])

            gm, gw, g_rank, m1, m2, w1, w2, rk = (tiny[:, i * TT:i * TT + TT] for i in (0, 1, 2, 3, 4, 5, 6, 7))
            dve.wait_ge(*at_count("router_done", 1))
            dve.tensor_tensor(logits[:, :, :], bank[at[("router",)]][:, 0:4 * 36].rearrange("p (t n) -> p t n", t=TT),
                              router_b.rearrange("p (a n) -> p a n", a=1).broadcast_to([P, TT, 36]), ALU.add).then_inc(S("logits"), 1)
            dve.wait_ge(*at_count("logits", 1))
            gl = logits[:, :, 0:NG]

            def step(ins):
                steps.mark(ins)
                steps.wait()

            def first_max(dst, src, top, ranks, n):
                step(dve.tensor_tensor(dst, src, wide(top, n), ALU.is_equal))
                step(dve.tensor_tensor(dst, dst, ranks.rearrange("p (a n) -> p a n", a=1).broadcast_to([P, TT, n]), ALU.mult))
                step(dve.tensor_reduce(rk, dst, AX.X, ALU.max))
                step(dve.tensor_tensor(dst, dst, wide(rk, n), ALU.is_equal))

            step(dve.tensor_reduce(gm, gl, AX.X, ALU.max))
            dve.tensor_tensor(exp_g[:, :, :], gl, wide(gm, NG), ALU.subtract).then_inc(S("group_arg"), 1)
            first_max(one_group[:, :, :], gl, gm, constant("rank4", 0, 4), NG)
            step(dve.tensor_tensor(masked_e.rearrange("p (t g e) -> p t g e", t=TT, g=NG), logits[:, :, NG:].rearrange("p t (g e) -> p t g e", g=NG),
                                   one_group.rearrange("p t (g a) -> p t g a", a=1).broadcast_to([P, TT, NG, EG]), ALU.mult))
            step(dve.tensor_reduce(chosen[:, :, :], masked_e.rearrange("p (t g e) -> p t e g", t=TT, g=NG), AX.X, ALU.add))
            step(dve.tensor_reduce(m1, chosen[:, :, :], AX.X, ALU.max))
            first_max(first[:, :, :], chosen[:, :, :], m1, constant("rank8", 0, 8), EG)
            step(dve.scalar_tensor_tensor(ranked[:, :, :], first[:, :, :], -3.0e38, chosen[:, :, :], ALU.mult, ALU.add))
            step(dve.tensor_reduce(m2, ranked[:, :, :], AX.X, ALU.max))
            first_max(second[:, :, :], ranked[:, :, :], m2, constant("rank8", 0, 8), EG)
            dve.tensor_tensor(m2, m2, m1, ALU.subtract).then_inc(S("second_arg"), 1)
            for o, within in zip(pick, (first, second)):
                steps.mark(dve.tensor_tensor(o.rearrange("p t (g e) -> p t g e", g=NG), one_group.rearrange("p t (g a) -> p t g a", a=1).broadcast_to([P, TT, NG, EG]),
                                             within.rearrange("p t (a e) -> p t a e", a=1).broadcast_to([P, TT, NG, EG]), ALU.mult))
            steps.wait()
            dve.tensor_tensor(assigned[:, :, :], pick[0], pick[1], ALU.add).then_inc(S("assigned"), 1)
            dve.wait_ge(*at_count("group_exp", 1))
            step(dve.tensor_reduce(gw, exp_g[:, :, :], AX.X, ALU.add))
            dve.wait_ge(*at_count("second_exp", 1))
            step(dve.tensor_scalar(w1, m2, 1.0, None, ALU.add))
            step(dve.tensor_tensor(w1, w1, gw, ALU.mult))
            step(dve.reciprocal(w1, w1))
            step(dve.tensor_tensor(w2, w1, m2, ALU.mult))
            dve.wait_ge(*at_count("ranks_done", 1))
            ranks = bank[at[("ranks",)]]
            experts = constant("expert_id", 0, NE).rearrange("p (a n) -> p a n", a=1).broadcast_to([P, TT, NE])
            steps.mark(dve.tensor_tensor(rank[:, :, :], ranks[:, 0:P].rearrange("p (t e) -> p t e", t=TT), assigned[:, :, :], ALU.subtract))
            dve.tensor_copy(totals[:, :], ranks[:, P:P + NE]).then_inc(S("totals"), 1)
            steps.wait()
            steps.mark(dve.scalar_tensor_tensor(table_row[:, :, :], rank[:, :, :], float(NE), experts, ALU.mult, ALU.add))
            steps.mark(dve.scalar_tensor_tensor(y_row[:, :, :], experts, float(P), rank[:, :, :], ALU.mult, ALU.add))
            dve.wait_ge(*at_count("totals", 1))
            steps.mark(dve.tensor_reduce(flag_f, totals[:, :], AX.X, ALU.max))
            steps.wait()
            for j in range(2):
                for i, rows in enumerate((table_row, y_row)):
                    step(dve.tensor_tensor(picked[:, :, :], pick[j], rows[:, :, :], ALU.mult))
                    o = (2 * i + j) * TT
                    step(dve.tensor_reduce(row_f[:, o:o + TT], picked[:, :, :], AX.X, ALU.add))
            steps.mark(dve.tensor_copy(rows_u[:, :], row_f[:, :]))
            pairs_t = pairs_u[:, :].rearrange("p (j t x) -> p j t x", j=2, x=2)
            pairs_f = pair_w.rearrange("p (j t x) -> p j t x", j=2, x=2)
            for j, w in enumerate((w1, w2)):
                steps.mark(dve.tensor_copy(pairs_t[:, j, :, 0], constant("token_id", 0, TT)))
                steps.mark(dve.tensor_copy(pairs_f[:, j, :, 1], w))
            steps.wait()
            dve.engine_nop().then_inc(S("slots"), 1)
            dve.tensor_scalar(flag[0:1, 0:1], flag_f[0:1, :], float(CAP_E), None, ALU.is_gt).then_inc(S("flag"), 1)
            dve.wait_ge(*at_count("flag", 1))
            overflow = dve.value_load(flag[0:1, 0:1], min_val=0, max_val=1)
            with dve.If(overflow):
                dve_dense(dve, pick, w1, w2)
            with dve.Else():
                dve_sparse(dve)

        def dve_dense(dve, pick, w1, w2):
            def wide(x, n):
                return x.rearrange("p (t a) -> p t a", a=1).broadcast_to([P, TT, n])

            dve.tensor_tensor(picked[:, :, :], pick[0], wide(w1, NE), ALU.mult).then_inc(S("weighed"), 1)
            dve.tensor_tensor(rank[:, :, :], pick[1], wide(w2, NE), ALU.mult).then_inc(S("weighed"), 1)
            dve.wait_ge(*at_count("weighed", 2))
            dve.tensor_tensor(combine[:, :, :], picked[:, :, :], rank[:, :, :], ALU.add).then_inc(S("combine"), 1)

            def weigh(e, par, wait):
                base = at["moe_units"] - 2 + (0 if wait else 2)
                for f in range(2):
                    dve.wait_ge(*at_count("unit_done", e * 6 + (base + 2 + f + 1)))
                    dve.wait_ge(*at_count("moe_silu", e * 2 + (f + 1)))
                    dve.tensor_tensor(expert_silu[:, f, :], expert_silu[:, f, :], bank[2 + f][:, :], ALU.mult).then_inc(S("moe_up"), 1)
                for f in range(2):
                    if f == 0:
                        dve.wait_ge(*at_count(f"expert_w{par}", weigh.landed))
                    dve.wait_ge(*at_count("moe_up", e * 2 + (f + 1)))
                    dve.tensor_tensor(expert_act[:, par, f, :], expert_silu[:, f, :], expert_w[:, par, :], ALU.mult).then_inc(S("moe_act"), 1)

            def add(e, first_one, last_one=False):
                for n in range(KD):
                    if n < KD - 1:
                        dve.wait_ge(*at_count("down_done", (e - 1) * 7 + (n + 1)))
                    else:
                        dve.wait_ge(*at_count("unit_done", e * 6 + (at["moe_units"] - 2 + 6) if not last_one else at["moe_units"] + 6 * NE))
                    b = bank[4 + n % 4][:, :]
                    if first_one:
                        dve.tensor_copy(moe_sum[:, n, :], b).then_inc(S("moe_add"), 1)
                    else:
                        if n == 0:
                            dve.wait_ge(*at_count("moe_add", (e - 1) * 8))
                        dve.tensor_tensor(moe_sum[:, n, :], moe_sum[:, n, :], b, ALU.add).then_inc(S("moe_add"), 1)

            weigh.landed = 16
            weigh(0, 0, False)
            weigh(1, 1, True)
            add(1, True)
            with dve.Fori(0, (NE - 2) // 2) as i:
                for j in range(2):
                    weigh.landed = i * 16 + 32
                    weigh(i * 2 + (2 + j), j, True)
                    add(i * 2 + (2 + j), False)
            add(NE, False, last_one=True)
            dve.wait_ge(*at_count("moe_add", KD * NE))
            for k in range(KD):
                dve.scalar_tensor_tensor(xT[:, k, :], moe_sum[:, k, :], mod[:, G_F + k:G_F + k + 1], xT[:, k, :],
                                         ALU.mult, ALU.add).then_inc(S("x_moe"), 1)

        def pool_moe(pool):
            pool.memset(slot_table[:, :], 0).then_inc(S("table_clear"), 1)
            pool.wait_ge(*at_count("table_clear", 1))
            table = table_d[0:CAP_E * NE, :].rearrange("(s e) x -> s (e x)", e=NE)
            pool.dma_start(table, slot_table[:, :]).then_inc(S("table_zeroed"), 16)
            pool.wait_ge(*at_count("table_zeroed", 16))
            pool.wait_ge(*at_count("slots", 1))
            for i in range(2 * TT):
                pool.indirect_dma_start(out=table_d, out_offset=bass.IndirectOffsetOnAxis(ap=rows_u[:, i:i + 1], axis=0),
                                        in_=pairs_u[:, 2 * i:2 * i + 2], in_offset=None).then_inc(S("table_filled"), 16)
            pool.wait_ge(*at_count("table_filled", 16 * 2 * TT))
            pool.dma_start(slot_table[:, :], table).then_inc(S("table_landed"), 16)
            pool.wait_ge(*at_count("flag", 1))
            overflow = pool.value_load(flag[0:1, 0:1], min_val=0, max_val=1)
            with pool.If(overflow):
                pool_dense(pool)
            with pool.Else():
                pool_sparse(pool)

        def pool_dense(pool):
            pool.wait_ge(*at_count("combine_stored", 16))
            for e in range(2):
                pool.dma_start(expert_w[:, e, :], combine_d[e:e + 1, :].broadcast_to([P, T])).then_inc(S(f"expert_w{e}"), 16)
            with pool.Fori(0, (NE - 2) // 2) as i:
                for j in range(2):
                    pool.wait_ge(*at_count("moe_act", i * 4 + 2 * (j + 1)))
                    pool.dma_start(expert_w[:, j, :], combine_d[bass.ds(i * 2 + (2 + j), 1), :].broadcast_to([P, T])).then_inc(S(f"expert_w{j}"), 16)

        def pe_sparse(pe, mm, weights):
            def turn_rows(e, par, first):
                pe.wait_ge(*at_count(f"gathered{par}", turn_rows.landed))
                for i in range(2):
                    if not first:
                        pe.wait_ge(*at_count("expert_in", (e - 1) * 2 + i + 1))
                    for n in range(4):
                        last = mm(bank[i][:, n * P:n * P + P], rows_in[:, par, (4 * i + n) * P:(4 * i + n + 1) * P], ident)
                    last.then_inc(S("rows_turned"), 1)

            def gate_up(e, par, first):
                pe.wait_ge(*at_count("expert_in", e * 2 + 2))
                for x in range(4):
                    w = weights(e, x)
                    if x % 2 == 0 and not first:
                        pe.wait_ge(*at_count("sparse_silu" if x < 2 else "sparse_act", e))
                    for k in range(KD):
                        last = mm(bank[2 + x // 2][:, x % 2 * P:x % 2 * P + P], w[:, k, :], rows_t[:, par, k * P:k * P + P], k == 0, k == KD - 1)
                    last.then_inc(S("unit_done"), 1)

            def down(e, par, first):
                w = [weights(e, 4), weights(e, 5)]
                pe.wait_ge(*at_count("sparse_act", e))
                for half in range(2):
                    if not first:
                        pe.wait_ge(*at_count("sparse_y", (e - 2) * 2 + half + 1))
                    for f in range(2):
                        last = mm(bank[4 + half][:, :], sparse_act[:, par, f * P:f * P + P],
                                  w[f].rearrange("p k n -> p (k n)")[:, half * 512:half * 512 + 512], f == 0, f == 1)
                        if half:
                            last.then_inc(S("unit_done"), 1)
                    if not half:
                        last.then_inc(S("sparse_down"), 1)

            def last_landed(e):
                turn_rows.landed = 16 * (e // 2 + 1)

            last_landed(0)
            turn_rows(0, 0, True)
            gate_up(0, 0, True)
            turn_rows(1, 1, False)
            gate_up(1, 1, False)
            last_landed(2)
            turn_rows(2, 0, False)
            down(1, 0, True)
            with pe.Fori(0, (NE - 4) // 2) as i:
                for j in range(2):
                    e = i * 2 + (2 + j)
                    gate_up(e, j, False)
                    turn_rows.landed = i * 16 + 32 + 16 * j
                    turn_rows(e + 1, 1 - j, False)
                    down(e, 1 - j, False)
            gate_up(NE - 2, 0, False)
            last_landed(NE - 1)
            turn_rows(NE - 1, 1, False)
            down(NE - 2, 1, False)
            gate_up(NE - 1, 1, False)
            down(NE - 1, 0, False)
            down(NE, 1, False)
            pe.wait_ge(*at_count("sparse_y", 2 * NE))
            for tt in range(TT):
                pe.wait_ge(*at_count("y_picked", tt + 1))
                for n in range(KD):
                    last = mm(bank[n][:, tt * P:tt * P + P], y_pick[:, 2 * tt % 4, n * P:n * P + P], ident)
                last.then_inc(S("y_turned"), 1)

        def act_sparse(act):
            def rows_out(e, par):
                for i in range(2):
                    act.wait_ge(*at_count("rows_turned", e * 2 + i + 1))
                    act.activation(rows_t[:, par, i * 512:i * 512 + 512], bank[i][:, :], ACT.Copy).then_inc(S("expert_in"), 1)

            def silu(e, first):
                if first:
                    act.wait_ge(*at_count("unit_done", at["moe_units"] + 2))
                else:
                    act.wait_ge(*at_count("unit_done", e * 6 + at["moe_units"]))
                    act.wait_ge(*at_count("sparse_act", e))
                act.activation(sparse_silu, bank[2][:, 0:2 * P], ACT.Silu).then_inc(S("sparse_silu"), 1)

            def store(e, par):
                act.wait_ge(*at_count("sparse_y", e * 2 + 2))
                act.dma_start(y_d[bass.ds(e * P, P), :] if not isinstance(e, int) else y_d[e * P:e * P + P, :],
                              y_rows[:, par, :]).then_inc(S(f"y_stored{par}"), 16)

            rows_out(0, 0)
            silu(0, True)
            rows_out(1, 1)
            silu(1, False)
            rows_out(2, 0)
            store(0, 0)
            with act.Fori(0, (NE - 4) // 2) as i:
                for j in range(2):
                    e = i * 2 + (2 + j)
                    silu(e, False)
                    rows_out(e + 1, 1 - j)
                    store(e - 1, 1 - j)
            silu(NE - 2, False)
            rows_out(NE - 1, 1)
            store(NE - 3, 1)
            silu(NE - 1, False)
            store(NE - 2, 0)
            store(NE - 1, 1)

        def dve_sparse(dve):
            def product(e, par, first):
                if first:
                    dve.wait_ge(*at_count("unit_done", at["moe_units"] + 4))
                else:
                    dve.wait_ge(*at_count("unit_done", e * 6 + (at["moe_units"] + 2)))
                dve.wait_ge(*at_count("sparse_silu", e + 1))
                dve.tensor_tensor(sparse_act[:, par, :], sparse_silu, bank[3][:, 0:2 * P], ALU.mult).then_inc(S("sparse_act"), 1)

            def weigh(e, par, weight):
                for half in range(2):
                    if half == 0:
                        dve.wait_ge(*at_count("sparse_down", e + 1))
                        if weigh.stored is not None:
                            dve.wait_ge(*at_count(f"y_stored{par}", weigh.stored))
                    else:
                        dve.wait_ge(*at_count("unit_done", (e + 1) * 6 + (at["moe_units"] + 4)) if not weigh.last
                                    else at_count("unit_done", at["moe_units"] + 6 * NE))
                    dve.tensor_scalar(y_rows[:, par, half * 512:half * 512 + 512], bank[4 + half][:, :], weight, None, ALU.mult).then_inc(S("sparse_y"), 1)

            def weight_of(e):
                return table_w[:, 2 * e + 1:2 * e + 2] if isinstance(e, int) else table_w[:, bass.ds(e * 2 + 1, 1)]

            weigh.last, weigh.stored = False, None
            dve.wait_ge(*at_count("table_landed", 16))
            product(0, 0, True)
            product(1, 1, False)
            weigh(0, 0, weight_of(0))
            product(2, 0, False)
            weigh(1, 1, weight_of(1))
            with dve.Fori(0, (NE - 4) // 2) as i:
                for j in range(2):
                    e = i * 2 + (3 + j)
                    weigh.stored = i * 16 + 16
                    product(e, 1 - j, False)
                    weigh(e - 1, j, weight_of(e - 1))
            product(NE - 1, 1, False)
            weigh.stored = 16 * (NE // 2 - 1)
            weigh(NE - 2, 0, weight_of(NE - 2))
            weigh.last = True
            weigh(NE - 1, 1, weight_of(NE - 1))
            for tt in range(TT):
                a, b = 2 * tt % 4, 2 * tt % 4 + 1
                dve.wait_ge(*at_count(f"picked{a}", 16 * (tt // 2 + 1)))
                dve.wait_ge(*at_count(f"picked{b}", 16 * (tt // 2 + 1)))
                dve.tensor_tensor(y_pick[:, a, :], y_pick[:, a, :], y_pick[:, b, :], ALU.add).then_inc(S("y_picked"), 1)
            for n in range(KD):
                dve.wait_ge(*at_count("y_turned", TT))
                dve.scalar_tensor_tensor(xT[:, n, :], bank[n][:, :], mod[:, G_F + n:G_F + n + 1], xT[:, n, :],
                                         ALU.mult, ALU.add).then_inc(S("x_moe"), 1)

        def pool_sparse(pool):
            pool.wait_ge(*at_count("table_landed", 16))
            for par in range(2):
                pool.wait_ge(*at_count(f"h_stored{par}", 16 * TT // 2))
            for e in range(NE):
                if e >= 2:
                    pool.wait_ge(*at_count("rows_turned", 2 * (e - 1)))
                pool.indirect_dma_start(out=rows_in[:, e % 2, :], out_offset=None, in_=h_d,
                                        in_offset=bass.IndirectOffsetOnAxis(ap=slot_table[:, 2 * e:2 * e + 1], axis=0)).then_inc(S(f"gathered{e % 2}"), 16)
            pool.wait_ge(*at_count("y_stored0", 16 * NE // 2))
            pool.wait_ge(*at_count("y_stored1", 16 * NE // 2))
            for tt in range(TT):
                for j in range(2):
                    i = 2 * tt + j
                    if tt >= 2:
                        pool.wait_ge(*at_count("y_turned", tt - 1))
                    r = 2 * TT + j * TT + tt
                    pool.indirect_dma_start(out=y_pick[:, i % 4, :], out_offset=None, in_=y_d,
                                            in_offset=bass.IndirectOffsetOnAxis(ap=rows_u[:, r:r + 1], axis=0)).then_inc(S(f"picked{i % 4}"), 16)
        SH = 8
        y_ssm = area(0, 16, T)
        conv_u = area(8192, 2, UP + T)
        conv_y = area(9280, KD, T)
        xbc_raw = area(13376, 6, TP)
        xbc = area(16472, 6, T)
        x_dt = area(19544, TT, 512)
        x_w = area(21592, 2, 512)
        b_tok2 = area(22616, TT, P)
        states = area(23128, TT - 1, 512)
        cb = area(24664, TT, P)
        seg = area(25176, 2, T)
        exp_acs = area(26200, T)
        row_acs, row_dtw = area(26712, T), area(27224, T)
        row_tmp, row_dt = rstd[:, 0, :], rstd[:, 1, :]
        ssm_cols = area(27736, 3 * TT * SH)
        last_exp = area(27832, SH * TT)
        a_pos = area(27864, NG)
        ln_square = area(13376, KD, T)
        merged = area(19544, KD, T)
        sig = area(17472, 2, T)
        conv_y_r, conv_hi_r = halves("conv_lo", "arena", 9280, KD, T), halves("conv_hi", "arena", 13376, KD, T)
        y_ssm_r, ssm_hi_r = halves("y_ssm_lo", "arena", 0, 16, T), halves("y_ssm_hi", "arena", 9280, 16, T)
        merged_r, merged_hi_r = halves("merged_lo", "arena", 19544, KD, T), halves("merged_hi", "arena", 23640, KD, T)
        DT, DTW, ACS = range(3)

        def ssm_col(which, tt):
            c = (which * TT + tt) * SH
            return ssm_cols[:, c:c + SH]

        def channel(g, i):
            return 4 * g + i if i < 4 else (16 if i == 4 else 20) + g

        def pe_mix2(pe, mm, take, project):
            h_tiles = [(mix_h_hi_r[:, k, :], hT_r[:, k, :]) for k in range(KD)]
            counts = [list(range(1, KD + 1))]

            def group_in(g):
                first = counts.pop() if counts else None
                for i in range(6):
                    project(("xbc", g, i), ("xbc_raw", 6 * g + i + 1), h_tiles, "norm_mix2_h", first if i == 0 else None)
                for i in range(4):
                    project(("z", g, i), ("z", 4 * g + i + 1), h_tiles, None, None)
                for i in range(2):
                    project(("conv_a", g, i), ("conv_u", 2 * g + i + 1), h_tiles, None, None)
                    project(("conv_b", g, i), ("conv_gate", 2 * g + i + 1), h_tiles, None, None)

            group_in(0)
            for g in range(NG):
                out = take(("dt", g), ("dt_raw", g + 1))
                if g == 0:
                    pe.wait_ge(*at_count("dt_lo", 1))
                for k in range(KD):
                    w_hi, w_lo = (w[:, k, SH * g:SH * g + SH] for w in (dt_hi_r, dt_lo_r))
                    hi, lo = h_tiles[k]
                    mm(out[0:SH, :], w_hi, hi, k == 0, False)
                    mm(out[0:SH, :], w_lo, hi, False, False)
                    last = mm(out[0:SH, :], w_hi, lo, False, k == KD - 1)
                last.then_inc(S("dt_done"), 1)
                if g < NG - 1:
                    group_in(g + 1)
                pe.wait_ge(*at_count("xbc", 6 * g + 6))
                out = take(("b_tok", g), ("b_tok", g + 1))
                for tt in range(TT):
                    last = mm(out[:, tt * P:tt * P + P], xbc[:, 4, tt * P:tt * P + P], ident)
                last.then_inc(S("b_turned"), 1)
                out = take(("ssm_cols", g), ("ssm_cols", 2 * g + 2))
                pe.wait_ge(*at_count("rows", g + 1))
                for which, row in ((DT, row_dt), (DTW, row_dtw), (ACS, row_acs)):
                    for tt in range(TT):
                        c = (which * TT + tt) * SH
                        mm(out[:, c:c + SH], row[0:SH, tt * P:tt * P + P], ident[0:SH, 0:SH])
                for h in range(SH):
                    last = mm(out[:, 96 + TT * h:96 + TT * h + TT], constant("sel8", h, rows=SH), row_acs[0:SH, P - 1:T:P])
                last.then_inc(S("ssm_cols_done"), 1)
                out = take(("cb", g), ("cb", g + 1))
                for tt in range(TT):
                    last = mm(out[:, tt * P:tt * P + P], xbc[:, 4, tt * P:tt * P + P], xbc[:, 5, tt * P:tt * P + P])
                last.then_inc(S("cb_done"), 1)
                for tt in range(TT):
                    out = take(("x_tok", g, tt), ("x_tok", 2 * (TT * g + tt) + 2))
                    for i in range(4):
                        last = mm(out[:, i * P:i * P + P], xbc[:, i, tt * P:tt * P + P], ident)
                    last.then_inc(S("x_turned"), 1)
                    if tt == 0:
                        pe.wait_ge(*at_count("b_tok", g + 1))
                    if tt < TT - 1:
                        pe.wait_ge(*at_count("x_tok", 2 * (TT * g + tt) + 2))
                        out = take(("states", g, tt), ("states", 3 * g + tt + 1))
                        mm(out[:, :], b_tok2[:, tt, :], x_w[:, tt % 2, :]).then_inc(S("states_done"), 1)
                for j in range(SH // 2):
                    n = 4 * g + j
                    diag = None
                    for o in range(2):
                        h, m = 2 * j + o, SH * g + 2 * j + o
                        out = take(("acs", m), ("seg_arg", TT * (m + 1)))
                        mm(out[:, :], constant("sel8", h, rows=SH), row_acs[0:SH, :]).then_inc(S("acs_done"), 1)
                    if j == 0:
                        pe.wait_ge(*at_count("states", 3 * g + 3))
                    out = take(("exp_acs", n), ("exp_acs", n + 1))
                    mm(out[:, :], constant("sel8_pair", j, rows=SH), row_acs[0:SH, :]).then_inc(S("pair_acs_done"), 1)
                    off = take(("y_off", n), ("y_off", n + 1))
                    for tt in range(1, TT):
                        last = mm(off[:, tt * P:tt * P + P], states[:, tt - 1, j * P:j * P + P], xbc[:, 5, tt * P:tt * P + P])
                    last.then_inc(S("y_off_done"), 1)
                    diag = take(("y_diag", n), ("y_skip", n + 1))
                    for o in range(2):
                        h, m = 2 * j + o, SH * g + 2 * j + o
                        pe.wait_ge(*at_count("seg", m + 1))
                        for tt in range(TT):
                            last = mm(diag[64 * o:64 * o + 64, tt * P:tt * P + P], x_dt[:, tt, h * 64:h * 64 + 64], seg[:, m % 2, tt * P:tt * P + P])
                        last.then_inc(S("y_diag_done"), 1)
                out = take(("group_sum", g), ("group_std", g + 1))
                for j in range(4):
                    pe.wait_ge(*at_count("group_square", 4 * g + j + 1))
                    last = mm(out[:, :], ones, xbc[:, j, :], j == 0, j == 3)
                last.then_inc(S("group_sum_done"), 1)
            out = take(("ln_mean",), ("ln_centred", KD))
            pe.wait_ge(*at_count("conv_y", KD * TAPS))
            for k in range(KD):
                last = mm(out[:, :], ones, conv_y[:, k, :], k == 0, k == KD - 1)
            last.then_inc(S("ln_mean_done"), 1)
            out = take(("ln_var",), ("ln_std", 1))
            for k in range(KD):
                pe.wait_ge(*at_count("ln_square", k + 1))
                last = mm(out[:, :], ones, ln_square[:, k, :], k == 0, k == KD - 1)
            last.then_inc(S("ln_var_done"), 1)
            conv_tiles = [(conv_hi_r[:, k, :], conv_y_r[:, k, :]) for k in range(KD)]
            ssm_tiles = [(ssm_hi_r[:, k, :], y_ssm_r[:, k, :]) for k in range(16)]
            for n in range(KD):
                project(("g_conv", n), ("sig", n + 1), h_tiles, None, None)
                project(("conv_out", n), ("merge_conv", n + 1), conv_tiles, "conv_lo", list(range(1, KD + 1)) if n == 0 else None)
            for n in range(KD):
                project(("g_ssm", n), ("sig", KD + n + 1), h_tiles, None, None)
                project(("ssm_out", n), ("merge_ssm", n + 1), ssm_tiles, "ssm_lo", list(range(1, 17)) if n == 0 else None)
            merged_tiles = [(merged_hi_r[:, k, :], merged_r[:, k, :]) for k in range(KD)]
            for n in range(KD):
                project(("w_out2", n), ("x_mix2", n + 1), merged_tiles, "merged_lo", list(range(1, KD + 1)) if n == 0 else None)

        def act_mix2(act, steps):
            def group_out(g):
                for i in range(6):
                    act.wait_ge(*at_count("unit_done", at[("unit", "xbc", g, i)]))
                    if g:
                        act.wait_ge(*at_count("xbc_conv", 24 * g))
                    elif i == 0:
                        act.wait_ge(*at_count("pads2", 2))
                    act.activation(xbc_raw[:, i, PAD:TP], bank[at[("xbc", g, i)]][:, :], ACT.Copy).then_inc(S("xbc_raw"), 1)
                for i in range(4):
                    act.wait_ge(*at_count("unit_done", at[("unit", "z", g, i)]))
                    act.activation(y_ssm[:, 4 * g + i, :], bank[at[("z", g, i)]][:, :], ACT.Silu).then_inc(S("z"), 1)
                for i in range(2):
                    act.wait_ge(*at_count("unit_done", at[("unit", "conv_b", g, i)]))
                    if g:
                        act.wait_ge(*at_count("conv_y", 2 * g * TAPS))
                    act.activation(conv_u[:, i, UP:UP + T], bank[at[("conv_b", g, i)]][:, :], ACT.Sigmoid).then_inc(S("conv_gate"), 1)

            act.wait_ge(*at_count("x_moe", KD))
            act.activation(a_pos[0:SH, :], col[0:SH, COL["a_log_2"]:COL["a_log_2"] + NG], ACT.Exp).then_inc(S("a_pos"), 1)
            group_out(0)
            for g in range(NG):
                for i in range(6):
                    act.wait_ge(*at_count("xbc_conv", 24 * g + 18 + i + 1))
                    act.activation(xbc[:, i, :], xbc[:, i, :], ACT.Silu, bias=column("ssm_conv_b_2", channel(g, i))).then_inc(S("xbc"), 1)
                act.wait_ge(*at_count("dt_done", g + 1))
                if g == 0:
                    act.wait_ge(*at_count("norm_mix2_h", KD))
                act.activation(row_dt[0:SH, :], bank[at[("dt", g)]][0:SH, :], ACT.Identity, bias=column("dt_bias_2", g, SH)).then_inc(S("dt_raw"), 1)
                act.wait_ge(*at_count("dt_raw", g + 1))
                steps.mark(act.activation(row_tmp[0:SH, :], row_dt[0:SH, :], ACT.Abs))
                steps.wait()
                steps.mark(act.activation(row_tmp[0:SH, :], row_tmp[0:SH, :], ACT.Exp, scale=-1.0))
                steps.wait()
                act.activation(row_tmp[0:SH, :], row_tmp[0:SH, :], ACT.Ln, bias=column("one", rows=SH)).then_inc(S("dt_log"), 1)
                act.wait_ge(*at_count("end_arg", g + 1))
                act.activation(row_tmp[0:SH, :], row_tmp[0:SH, :], ACT.Exp).then_inc(S("end_exp"), 1)
                if g < NG - 1:
                    group_out(g + 1)
                act.wait_ge(*at_count("b_turned", g + 1))
                act.activation(b_tok2[:, :, :].rearrange("p a b -> p (a b)"), bank[at[("b_tok", g)]][:, :], ACT.Copy).then_inc(S("b_tok"), 1)
                act.wait_ge(*at_count("ssm_cols_done", g + 1))
                act.wait_ge(*at_count("ssm_cols", 2 * g + 1))
                act.activation(last_exp[:, :], bank[at[("ssm_cols", g)]][:, 96:96 + SH * TT], ACT.Exp, scale=-1.0).then_inc(S("ssm_cols"), 1)
                for j in range(4):
                    n = 4 * g + j
                    for o in range(2):
                        m = 2 * n + o
                        act.wait_ge(*at_count("seg_arg", TT * (m + 1)))
                        act.activation(seg[:, m % 2, :], seg[:, m % 2, :], ACT.Exp, scale=-1.0).then_inc(S("seg_exp"), 1)
                    act.wait_ge(*at_count("pair_acs_done", n + 1))
                    if n:
                        act.wait_ge(*at_count("y_sum", n))
                    act.activation(exp_acs, bank[at[("exp_acs", n)]][:, :], ACT.Exp, scale=-1.0).then_inc(S("exp_acs"), 1)
                for j in range(4):
                    act.wait_ge(*at_count("y_gated", 4 * g + j + 1))
                    act.activation(xbc[:, j, :], y_ssm[:, 4 * g + j, :], ACT.Square).then_inc(S("group_square"), 1)
                act.wait_ge(*at_count("group_sum_done", g + 1))
                act.activation(exp_acs, bank[at[("group_sum", g)]][:, :], ACT.Sqrt, bias=column("eps_norm"), scale=1 / 512).then_inc(S("group_std"), 1)
            for k in range(KD):
                act.wait_ge(*at_count("ln_centred", k + 1))
                act.activation(ln_square[:, k, :], conv_y[:, k, :], ACT.Square).then_inc(S("ln_square"), 1)
            act.wait_ge(*at_count("ln_var_done", 1))
            act.activation(rstd[:, 0, :], bank[at[("ln_var",)]][:, :], ACT.Sqrt, bias=column("eps_ln"), scale=1 / D).then_inc(S("ln_std"), 1)
            for k in range(KD):
                act.wait_ge(*at_count("ln_scaled", k + 1))
                act.activation(conv_hi_r[:, k, :], conv_y[:, k, :], ACT.Silu, bias=column("conv_ln_b_2", k)).then_inc(S("conv_hi"), 1)
                act.activation(conv_y[:, k, :], conv_y[:, k, :], ACT.Silu, bias=column("conv_ln_b_2", k)).then_inc(S("conv_act"), 1)
            for n in range(KD):
                act.wait_ge(*at_count("unit_done", at[("unit", "g_conv", n)]))
                if n >= 2:
                    act.wait_ge(*at_count("merge_conv", n - 1))
                act.activation(sig[:, n % 2, :], bank[at[("g_conv", n)]][:, :], ACT.Sigmoid).then_inc(S("sig"), 1)
            act.wait_ge(*at_count("unit_done", at[("unit", "conv_out", KD - 1)]))
            act.wait_ge(*at_count("y_ssm", 16))
            for k in range(16):
                act.activation(ssm_hi_r[:, k, :], y_ssm[:, k, :], ACT.Copy).then_inc(S("ssm_hi"), 1)

            def merged_upper(n):
                act.wait_ge(*at_count("merged", n + 1))
                act.activation(merged_hi_r[:, n, :], merged[:, n, :], ACT.Copy).then_inc(S("merged_hi"), 1)

            for n in range(KD):
                act.wait_ge(*at_count("unit_done", at[("unit", "g_ssm", n)]))
                act.wait_ge(*(at_count("merged", n - 1) if n >= 2 else at_count("merge_conv", KD)))
                act.activation(sig[:, n % 2, :], bank[at[("g_ssm", n)]][:, :], ACT.Sigmoid).then_inc(S("sig"), 1)
                if n == KD - 1:
                    act.dma_start(xT[:, :, :].rearrange("p a b -> p (a b)"), x_kept_d).then_inc(S("x_back"), 16)
                if n:
                    merged_upper(n - 1)
            merged_upper(KD - 1)

        def dve_mix2(dve, steps):
            def wide(x, n):
                return x.rearrange("p (h a) -> p h a", a=1).broadcast_to([P, x.shape[1], n])

            def by_head(x):
                return x.rearrange("p (h d) -> p h d", h=SH)

            dve.memset(xbc_raw[:, :, 0:PAD], 0.0).then_inc(S("pads2"), 1)
            dve.memset(conv_u[:, :, 0:UP], 0.0).then_inc(S("pads2"), 1)

            def gate_u(g):
                for i in range(2):
                    dve.wait_ge(*at_count("conv_gate", 2 * g + i + 1))
                    dve.wait_ge(*at_count("unit_done", at[("unit", "conv_a", g, i)]))
                    dve.tensor_tensor(conv_u[:, i, UP:UP + T], conv_u[:, i, UP:UP + T], bank[at[("conv_a", g, i)]][:, :], ALU.mult).then_inc(S("conv_u"), 1)

            dve.wait_ge(*at_count("pads2", 2))
            for g in range(NG):
                if g:
                    dve.wait_ge(*at_count("group_sum_done", g))
                for tap in range(4):
                    for i in range(6):
                        src = xbc_raw[:, i, PAD - 3 + tap:PAD - 3 + tap + T]
                        w = column("ssm_conv_w_2", 24 * tap + channel(g, i))
                        if tap == 0:
                            dve.wait_ge(*at_count("xbc_raw", 6 * g + i + 1))
                            dve.tensor_scalar(xbc[:, i, :], src, w, None, ALU.mult).then_inc(S("xbc_conv"), 1)
                        else:
                            dve.wait_ge(*at_count("xbc_conv", 24 * g + 6 * (tap - 1) + i + 1))
                            dve.scalar_tensor_tensor(xbc[:, i, :], src, w, xbc[:, i, :], ALU.mult, ALU.add).then_inc(S("xbc_conv"), 1)
                if g == 0:
                    dve.wait_ge(*at_count("a_pos", 1))
                    gate_u(0)
                dve.wait_ge(*at_count("dt_log", g + 1))
                steps.mark(dve.scalar_tensor_tensor(row_dt[0:SH, :], row_dt[0:SH, :], 0.0, row_tmp[0:SH, :], ALU.max, ALU.add))
                steps.wait()
                steps.mark(dve.tensor_scalar(row_tmp[0:SH, :], row_dt[0:SH, :], a_pos[0:SH, g:g + 1], None, ALU.mult))
                steps.wait()
                steps.mark(dve.tensor_tensor_scan(row_acs[0:SH, :], constant("reset128", 0, T, SH), row_tmp[0:SH, :], 0.0, ALU.mult, ALU.add))
                steps.wait()
                tiles = lambda x: x[0:SH, :].rearrange("h (c t) -> h c t", c=TT)
                dve.tensor_tensor(tiles(row_tmp), tiles(row_acs), row_acs[0:SH, P - 1:T:P].rearrange("h (c t) -> h c t", t=1).broadcast_to([SH, TT, P]),
                                  ALU.subtract).then_inc(S("end_arg"), 1)
                dve.wait_ge(*at_count("conv_u", 2 * g + 2))
                for tap in range(TAPS):
                    for i in range(2):
                        k = 2 * g + i
                        src = conv_u[:, i, tap:tap + T]
                        w = column("conv_dw_w_2", 8 * tap + k)
                        if tap == 0:
                            dve.tensor_scalar(conv_y[:, k, :], src, w, column("conv_dw_b_2", k), ALU.mult, ALU.add).then_inc(S("conv_y"), 1)
                        else:
                            dve.wait_ge(*at_count("conv_y", 2 * (g * TAPS + tap - 1) + i + 1))
                            dve.scalar_tensor_tensor(conv_y[:, k, :], src, w, conv_y[:, k, :], ALU.mult, ALU.add).then_inc(S("conv_y"), 1)
                dve.wait_ge(*at_count("end_exp", g + 1))
                dve.tensor_tensor(row_dtw[0:SH, :], row_tmp[0:SH, :], row_dt[0:SH, :], ALU.mult).then_inc(S("rows"), 1)
                if g < NG - 1:
                    dve.wait_ge(*at_count("conv_y", 2 * (g + 1) * TAPS))
                    gate_u(g + 1)
                dve.wait_ge(*at_count("ssm_cols_done", g + 1))
                dve.tensor_copy(ssm_cols[:, :], bank[at[("ssm_cols", g)]][:, 0:96]).then_inc(S("ssm_cols"), 1)
                dve.wait_ge(*at_count("cb_done", g + 1))
                dve.tensor_tensor(cb[:, :, :], bank[at[("cb", g)]][:, :].rearrange("p (c t) -> p c t", c=TT),
                                  constant("causal").rearrange("p (a t) -> p a t", a=1).broadcast_to([P, TT, P]), ALU.mult).then_inc(S("cb"), 1)
                dve.wait_ge(*at_count("ssm_cols", 2 * g + 2))
                for tt in range(TT):
                    dve.wait_ge(*at_count("x_turned", TT * g + tt + 1))
                    src = by_head(bank[at[("x_tok", g, tt)]][:, :])
                    dve.tensor_tensor(by_head(x_dt[:, tt, :]), src, wide(ssm_col(DT, tt), 64), ALU.mult).then_inc(S("x_tok"), 1)
                    if tt >= 2:
                        dve.wait_ge(*at_count("states_done", 3 * g + tt - 1))
                    dve.tensor_tensor(by_head(x_w[:, tt % 2, :]), src, wide(ssm_col(DTW, tt), 64), ALU.mult).then_inc(S("x_tok"), 1)
                    if tt == TT - 1:
                        continue
                    if tt:
                        dve.wait_ge(*at_count("states", 3 * g + tt))
                        steps.mark(dve.tensor_tensor(by_head(states[:, tt, :]), by_head(states[:, tt - 1, :]),
                                                     wide(last_exp[:, tt:SH * TT:TT], 64), ALU.mult))
                        steps.wait()
                    dve.wait_ge(*at_count("states_done", 3 * g + tt + 1))
                    new = bank[at[("states", g, tt)]][:, :]
                    if tt:
                        dve.tensor_tensor(states[:, tt, :], states[:, tt, :], new, ALU.add).then_inc(S("states"), 1)
                    else:
                        dve.tensor_copy(states[:, 0, :], new).then_inc(S("states"), 1)

                def decays(m):
                    dve.wait_ge(*at_count("acs_done", m + 1))
                    if m >= 2:
                        dve.wait_ge(*at_count("y_diag_done", m - 1))
                    for tt in range(TT):
                        dve.tensor_scalar(seg[:, m % 2, tt * P:tt * P + P], bank[at[("acs", m)]][:, tt * P:tt * P + P],
                                          ssm_col(ACS, tt)[:, m % SH:m % SH + 1], 0.0, ALU.subtract, ALU.max).then_inc(S("seg_arg"), 1)

                def weighted(m):
                    dve.wait_ge(*at_count("seg_exp", m + 1))
                    dve.wait_ge(*at_count("cb", g + 1))
                    dve.tensor_tensor(seg[:, m % 2, :], seg[:, m % 2, :], cb[:, :, :].rearrange("p a b -> p (a b)"), ALU.mult).then_inc(S("seg"), 1)

                for j in range(4):
                    n = 4 * g + j
                    decays(2 * n)
                    decays(2 * n + 1)
                    weighted(2 * n)
                    weighted(2 * n + 1)
                    dve.wait_ge(*at_count("exp_acs", n + 1))
                    dve.wait_ge(*at_count("y_off_done", n + 1))
                    dve.tensor_tensor(exp_acs[:, P:T], exp_acs[:, P:T], bank[at[("y_off", n)]][:, P:T], ALU.mult).then_inc(S("y_off"), 1)
                    dve.wait_ge(*at_count("y_diag_done", 2 * n + 2))
                    dve.scalar_tensor_tensor(xbc[:, j, :], xbc[:, j, :], column("d_skip_2", n), bank[at[("y_diag", n)]][:, :],
                                             ALU.mult, ALU.add).then_inc(S("y_skip"), 1)
                    dve.wait_ge(*at_count("y_skip", n + 1))
                    dve.wait_ge(*at_count("y_off", n + 1))
                    dve.tensor_tensor(xbc[:, j, P:T], xbc[:, j, P:T], exp_acs[:, P:T], ALU.add).then_inc(S("y_sum"), 1)
                    dve.wait_ge(*at_count("y_sum", n + 1))
                    dve.tensor_tensor(y_ssm[:, n, :], y_ssm[:, n, :], xbc[:, j, :], ALU.mult).then_inc(S("y_gated"), 1)
                dve.wait_ge(*at_count("group_std", g + 1))
                steps.mark(dve.reciprocal(exp_acs, exp_acs))
                steps.wait()
                for j in range(4):
                    n = 4 * g + j
                    dve.scalar_tensor_tensor(y_ssm[:, n, :], y_ssm[:, n, :], column("ssm_norm_w_2", n), exp_acs, ALU.mult, ALU.mult).then_inc(S("y_ssm"), 1)
            dve.wait_ge(*at_count("ln_mean_done", 1))
            for k in range(KD):
                dve.scalar_tensor_tensor(conv_y[:, k, :], bank[at[("ln_mean",)]][:, :], -1 / D, conv_y[:, k, :], ALU.mult, ALU.add).then_inc(S("ln_centred"), 1)
            dve.wait_ge(*at_count("ln_std", 1))
            steps.mark(dve.reciprocal(rstd[:, 1, :], rstd[:, 0, :]))
            steps.wait()
            for k in range(KD):
                dve.scalar_tensor_tensor(conv_y[:, k, :], conv_y[:, k, :], column("conv_ln_w_2", k), rstd[:, 1, :], ALU.mult, ALU.mult).then_inc(S("ln_scaled"), 1)
            for k in range(KD):
                dve.wait_ge(*at_count("conv_hi", k + 1))
                dve.wait_ge(*at_count("conv_act", k + 1))
                dve.tensor_tensor(conv_y_r[:, k, :], conv_y[:, k, :], conv_hi_r[:, k, :].bitcast(F32), ALU.subtract).then_inc(S("conv_lo"), 1)
            for n in range(KD):
                dve.wait_ge(*at_count("sig", n + 1))
                dve.wait_ge(*at_count("unit_done", at[("unit", "conv_out", n)]))
                dve.tensor_tensor(merged[:, n, :], sig[:, n % 2, :], bank[at[("conv_out", n)]][:, :], ALU.mult).then_inc(S("merge_conv"), 1)
            for k in range(16):
                dve.wait_ge(*at_count("ssm_hi", k + 1))
                dve.tensor_tensor(y_ssm_r[:, k, :], y_ssm[:, k, :], ssm_hi_r[:, k, :].bitcast(F32), ALU.subtract).then_inc(S("ssm_lo"), 1)

            def merged_lower(n):
                dve.wait_ge(*at_count("merged_hi", n + 1))
                dve.tensor_tensor(merged_r[:, n, :], merged[:, n, :], merged_hi_r[:, n, :].bitcast(F32), ALU.subtract).then_inc(S("merged_lo"), 1)

            for n in range(KD):
                dve.wait_ge(*at_count("sig", KD + n + 1))
                dve.wait_ge(*at_count("unit_done", at[("unit", "ssm_out", n)]))
                dve.tensor_tensor(sig[:, n % 2, :], sig[:, n % 2, :], bank[at[("ssm_out", n)]][:, :], ALU.mult).then_inc(S("merge_ssm"), 1)
                dve.wait_ge(*at_count("merge_ssm", n + 1))
                dve.wait_ge(*at_count("merge_conv", n + 1))
                dve.tensor_tensor(merged[:, n, :], merged[:, n, :], sig[:, n % 2, :], ALU.add).then_inc(S("merged"), 1)
                if n:
                    merged_lower(n - 1)
            merged_lower(KD - 1)
            dve.wait_ge(*at_count("x_back", 16))
            for n in range(KD):
                dve.wait_ge(*at_count("unit_done", at[("unit", "w_out2", n)]))
                dve.scalar_tensor_tensor(xT[:, n, :], bank[at[("w_out2", n)]][:, :], mod[:, G_2 + n:G_2 + n + 1], xT[:, n, :],
                                         ALU.mult, ALU.add).then_inc(S("x_mix2"), 1)

        ffn_act = area(0, F_TILES, T)
        ffn_silu = area(11264, 2, T)
        ffn_act_r = halves("ffn_act_lo", "arena", 0, F_TILES, T)
        ffn_hi_r = halves("ffn_act_hi", "arena", 12288, F_TILES, T)
        ffn_h_hi_r = halves("ffn_h_hi", "arena", 23552, KD, T)

        def pe_ffn2(pe, mm, take, project):
            h_tiles = [(ffn_h_hi_r[:, k, :], hT_r[:, k, :]) for k in range(KD)]
            for n in range(F_TILES):
                first = list(range(1, KD + 1)) if n == 0 else None
                project(("ffn_gate", n), ("ffn_silu", n + 1), h_tiles, "norm_ffn2_h", first)
                project(("ffn_up", n), ("ffn_act", n + 1), h_tiles, None, None)
            act_tiles = [(ffn_hi_r[:, k, :], ffn_act_r[:, k, :]) for k in range(F_TILES)]
            for n in range(KD):
                project(("ffn_down", n), ("x_ffn2", n + 1), act_tiles, "ffn_lo", list(range(1, F_TILES + 1)) if n == 0 else None)

        def act_ffn2(act, steps):
            def upper(n):
                act.wait_ge(*at_count("ffn_act", n + 1))
                act.activation(ffn_hi_r[:, n, :], ffn_act[:, n, :], ACT.Copy).then_inc(S("ffn_hi"), 1)

            for n in range(F_TILES):
                act.wait_ge(*at_count("unit_done", at[("unit", "ffn_gate", n)]))
                if n >= 2:
                    act.wait_ge(*at_count("ffn_act", n - 1))
                act.activation(ffn_silu[:, n % 2, :], bank[at[("ffn_gate", n)]][:, :], ACT.Silu).then_inc(S("ffn_silu"), 1)
                if n:
                    upper(n - 1)
            upper(F_TILES - 1)

        def dve_ffn2(dve, steps):
            def lower(n):
                dve.wait_ge(*at_count("ffn_hi", n + 1))
                dve.tensor_tensor(ffn_act_r[:, n, :], ffn_act[:, n, :], ffn_hi_r[:, n, :].bitcast(F32), ALU.subtract).then_inc(S("ffn_lo"), 1)

            for n in range(F_TILES):
                dve.wait_ge(*at_count("ffn_silu", n + 1))
                dve.wait_ge(*at_count("unit_done", at[("unit", "ffn_up", n)]))
                dve.tensor_tensor(ffn_act[:, n, :], ffn_silu[:, n % 2, :], bank[at[("ffn_up", n)]][:, :], ALU.mult).then_inc(S("ffn_act"), 1)
                if n:
                    lower(n - 1)
            lower(F_TILES - 1)
            for n in range(KD):
                dve.wait_ge(*at_count("unit_done", at[("unit", "ffn_down", n)]))
                dve.scalar_tensor_tensor(xT[:, n, :], bank[at[("ffn_down", n)]][:, :], mod[:, G_3 + n:G_3 + n + 1], xT[:, n, :],
                                         ALU.mult, ALU.add).then_inc(S("x_ffn2"), 1)
        def act_square(act, name, k):
            act.activation(hT[:, k, :], xT[:, k, :], ACT.Square).then_inc(S(name + "_square"), 1)

        def act_std(act, name):
            act.wait_ge(*at_count(name + "_sum", 1))
            act.activation(rstd[:, 0, :], bank[at[(name, "sum")]][:, :], ACT.Sqrt, bias=column("eps_norm"), scale=1 / D).then_inc(S(name + "_std"), 1)

        def act_shift(act, name, shift):
            for k in range(KD):
                act.wait_ge(*at_count(name + "_scaled", k + 1))
                act.activation(hT[:, k, :], hT[:, k, :], ACT.Identity, bias=mod[:, shift + k:shift + k + 1]).then_inc(S(name + "_h"), 1)

        def dve_norm(dve, steps, name, weight, scale, in_place=False):
            if scale is not None:
                steps.mark(dve.scalar_tensor_tensor(gain[:, :], mod[:, scale:scale + KD], 1.0,
                                                    col[:, COL[weight]:COL[weight] + KD], ALU.add, ALU.mult))
            dve.wait_ge(*at_count(name + "_std", 1))
            steps.mark(dve.reciprocal(rstd[:, 1, :], rstd[:, 0, :]))
            steps.wait()
            for k in range(KD):
                g = gain[:, k:k + 1] if scale is not None else column(weight, k)
                dst = xT if in_place else hT
                dve.scalar_tensor_tensor(dst[:, k, :], xT[:, k, :], g, rstd[:, 1, :], ALU.mult, ALU.mult).then_inc(
                    S(name + ("_scaled" if scale is not None else "_h")), 1)

        def act_shift_split(act, name, shift, upper_r):
            for k in range(KD):
                act.wait_ge(*at_count(name + "_scaled", k + 1))
                act.activation(upper_r[:, k, :], hT[:, k, :], ACT.Identity, bias=mod[:, shift + k:shift + k + 1]).then_inc(S(name + "_hi"), 1)

        def dve_lower(dve, name, shift, upper_r):
            for k in range(KD):
                dve.wait_ge(*at_count(name + "_hi", k + 1))
                dve.scalar_tensor_tensor(hT_r[:, k, :], hT[:, k, :], mod[:, shift + k:shift + k + 1], upper_r[:, k, :].bitcast(F32),
                                         ALU.add, ALU.subtract).then_inc(S(name + "_h"), 1)

        def pool_split(pool, first, count, before):
            def split(u, landed, used, done):
                pool.wait_ge(*at_count(f"landed{u % RING}", landed))
                if used is not None:
                    pool.wait_ge(*at_count("unit_done", used))
                hi, w = hi_unit(u), ring[:, u % RING, :]
                pool.tensor_tensor(hi, w, column("zero").broadcast_to([P, UNIT]), ALU.add).then_inc(S("split_hi"), 1)
                pool.wait_ge(*at_count("split_hi", done))
                pool.tensor_tensor(ring_r[:, u % RING, :], w, hi.bitcast(F32), ALU.subtract).then_inc(S("split"), 1)

            start = 0
            if first == 0:
                for u in range(RING):
                    split(u, 16, u - 1 if u >= 2 else None, u + 1)
                split_gates(pool)
                start = 1
            with pool.Fori(start, count // RING) as i:
                for j in range(RING):
                    u = first + j
                    split(u, i * 16 + 16 * (u // RING + 1), i * RING + (u - 1), i * RING + (before + j + 1))
            for j in range(count // RING * RING, count):
                u = first + j
                split(u, 16 * (u // RING + 1), u - 1, before + j + 1)

        def split_gates(pool):
            pool.wait_ge(*at_count("smalls_landed", 16))
            pool.tensor_tensor(gates_hi_r[:, :, :], gates_w, column("zero").rearrange("p (a b) -> p a b", a=1).broadcast_to([P, KD, 8]), ALU.add).then_inc(S("gates_hi"), 1)
            pool.wait_ge(*at_count("gates_hi", 1))
            pool.tensor_tensor(gates_lo_r[:, :, :], gates_w, gates_hi_r[:, :, :].bitcast(F32), ALU.subtract).then_inc(S("gates_lo"), 1)

        block = ctx.enter_context(nc.Block())

        @block.tensor
        def _(pe):
            unsplit = [0]
            unit = [0]
            turn = [0]
            freed = [None] * 8

            def mm(out, lhsT, rhs, start=True, stop=True):
                return pe.matmul(out, lhsT, rhs, start=start, stop=stop, skip_group_check=True)

            def take(key, freed_by, b=None):
                if b is None:
                    b = turn[0]
                    turn[0] = (b + 1) % 8
                if freed[b] is not None:
                    pe.wait_ge(*at_count(*freed[b]))
                freed[b] = freed_by
                at[key] = b
                return bank[b]

            def unit_landed():
                u = unit[0]
                unit[0] += 1
                pe.wait_ge(*at_count(f"landed{u % RING}", 16 * (u // RING + 1)))
                return ring[:, u % RING, :].rearrange("p (k n) -> p k n", k=8)

            def project_split(key, freed_by, rhs, ready, counts):
                out = None
                n = len(rhs)
                for u in range(-(-n // 8)):
                    w_hi, w_lo = (w.rearrange("p (k n) -> p k n", k=8) for w in (
                        hi_unit(unit[0]), ring_r[:, unit[0] % RING, :]))
                    unit[0] += 1
                    pe.wait_ge(*at_count("split", unit[0] - unsplit[0]))
                    if out is None:
                        out = take(key, freed_by)
                    for k in range(min(8, n - 8 * u)):
                        i = 8 * u + k
                        if counts:
                            pe.wait_ge(*at_count(ready, counts[i]))
                        hi, lo = rhs[i]
                        mm(out[:, :], w_hi[:, k, :], hi, i == 0, False)
                        mm(out[:, :], w_lo[:, k, :], hi, False, False)
                        last = mm(out[:, :], w_hi[:, k, :], lo, False, i == n - 1)
                    last.then_inc(S("unit_done"), 1)
                at[("unit",) + key] = unit[0]

            def norm_sum(name, freed_by):
                out = take((name, "sum"), freed_by)
                for k in range(KD):
                    pe.wait_ge(*at_count(name + "_square", k + 1))
                    last = mm(out[:, :], ones, hT[:, k, :], k == 0, k == KD - 1)
                last.then_inc(S(name + "_sum"), 1)

            pe.wait_ge(*at_count("consts_landed", 16))
            norm_sum("norm_mix", ("norm_mix_std", 1))
            h_tiles = [(in_h_hi_r[:, k, :], hT_r[:, k, :]) for k in range(KD)]

            def h_counts(first):
                return list(range(1, KD + 1)) if first else None

            for t in range(M_TILES):
                project_split(("m", t), ("m_proj", t + 1), h_tiles, "norm_mix_h", h_counts(t == 0))
            pe.wait_ge(*at_count("gates_lo", 1))
            for i in range(2):
                out = take(("gate", i), ("gate_raw", i + 1))
                for k in range(KD):
                    w_hi, w_lo = (w[:, k, 4 * i:4 * i + 4] for w in (gates_hi_r, gates_lo_r))
                    hi, lo = h_tiles[k]
                    mm(out[0:MH, :], w_hi, hi, k == 0, False)
                    mm(out[0:MH, :], w_lo, hi, False, False)
                    last = mm(out[0:MH, :], w_hi, lo, False, k == 7)
                last.then_inc(S("gates_done"), 1)
            for t in range(R_TILES):
                project_split(("r", t), ("r_proj", t + 1), h_tiles, None, None)
            pe_mlstm(pe, mm, take)
            pe_rwkv(pe, mm, take)
            y_tiles = [(y_hi_r[:, k, :], y_rwkv_r[:, k, :] if k < RW else y_mlstm_r[:, k - RW, :]) for k in range(KD)]
            for n in range(KD):
                project_split(("w_out", n), ("x_mix", n + 1), y_tiles, "y_lo", [5, 6, 7, 8, 1, 2, 3, 4] if n == 0 else None)
            norm_sum("norm_ffn", ("norm_ffn_std", 1))
            pe_moe(pe, mm, take, unit, unit_landed, freed, turn)
            norm_sum("norm_out", ("norm_out_std", 1))
            norm_sum("norm_mix2", ("norm_mix2_std", 1))
            at["first_split"] = unit[0]
            unsplit[0] = unit[0] - SPLIT_1
            pe_mix2(pe, mm, take, project_split)
            at["splits"] = unit[0] - at["first_split"]
            norm_sum("norm_ffn2", ("norm_ffn2_std", 1))
            pe_ffn2(pe, mm, take, project_split)
            at["splits"] = unit[0] - at["first_split"]
            norm_sum("norm_out2", ("norm_out2_std", 1))

        @block.sync
        def _(sp):
            def load_mod(i):
                slot = i % MOD_RING
                if i >= MOD_RING:
                    sp.wait_ge(*at_count("mod_used", i - MOD_RING + 1))
                sp.dma_start(mod_ring[:, slot, :], mod_w_d[i]).then_inc(S(f"mod_landed{slot}"), 16)

            sp.dma_start(silu_c[:, 0, :], c_d[0:1, :].broadcast_to([P, D])).then_inc(S("c_landed"), 16)
            for i in range(MOD_RING):
                load_mod(i)
            sp.dma_start(col[:, :], col_d).then_inc(S("columns_landed"), 16)
            sp.dma_start(xT[:, :, :].rearrange("p a b -> p (a b)"), x_d).then_inc(S("x_landed"), 16)
            for i in range(MOD_RING, MOD_EARLY):
                load_mod(i)
            sp.dma_start(con[:, :], con_d).then_inc(S("consts_landed"), 16)
            units = w_d.shape[0]
            for u in range(RING):
                sp.dma_start(ring[:, u, :], w_d[u]).then_inc(S(f"landed{u}"), 16)
                if u == 0:
                    sp.dma_start(silu_c[:, 1, :], c_d[1:2, :].broadcast_to([P, D])).then_inc(S("c_2_landed"), 16)
                    sp.dma_start(sma[:, :], sma_d).then_inc(S("smalls_landed"), 16)
            total = units
            rounds = total // RING
            mod_rounds = 3
            each = -(-(MODS - MOD_EARLY) // (mod_rounds * RING - 2))
            for u in range(RING, RING + mod_rounds * RING):
                first = MOD_EARLY + (u - RING) * each
                for i in range(first, min(first + each, MODS)):
                    load_mod(i)
                sp.wait_ge(*at_count("unit_done", u - RING + 1))
                sp.dma_start(ring[:, u % RING, :], w_d[u]).then_inc(S(f"landed{u % RING}"), 16)
            with sp.Fori(1 + mod_rounds, rounds) as i:
                for u in range(RING):
                    sp.wait_ge(*at_count("unit_done", (i - 1) * RING + u + 1))
                    sp.dma_start(ring[:, u, :], w_d[i * RING + u]).then_inc(S(f"landed{u}"), 16)
            for u in range(total % RING):
                sp.wait_ge(*at_count("unit_done", (rounds - 1) * RING + u + 1))
                sp.dma_start(ring[:, u, :], w_d[rounds * RING + u]).then_inc(S(f"landed{u}"), 16)
            for k in range(KD):
                sp.wait_ge(*at_count("norm_out2_h", k + 1))
                sp.dma_start(out_d[:, k * T:k * T + T], hT[:, k, :]).then_inc(S("stored"), 16)
            sp.wait_ge(*at_count("stored", 16 * KD))
        @block.scalar
        def _(act):
            steps = Steps(act, S("scalar_step"))
            act.wait_ge(*at_count("c_landed", 16))
            act.activation(silu_c[:, 0, :], silu_c[:, 0, :], ACT.Silu).then_inc(S("silu_c"), 1)
            act.wait_ge(*at_count("columns_landed", 16))
            act.wait_ge(*at_count("x_landed", 16))
            for k in range(KD):
                act_square(act, "norm_mix", k)
            act_std(act, "norm_mix")
            act_shift_split(act, "norm_mix", SH_M, in_h_hi_r)
            act.wait_ge(*at_count("c_2_landed", 16))
            act.activation(silu_c[:, 1, :], silu_c[:, 1, :], ACT.Silu).then_inc(S("silu_c"), 1)
            act.wait_ge(*at_count("pads", 1))
            for t in range(M_TILES):
                act.wait_ge(*at_count("unit_done", at[("unit", "m", t)]))
                act.activation(m_proj[:, t, PAD:TP], bank[at[("m", t)]][:, :], ACT.Sigmoid if t >= 8 else ACT.Copy).then_inc(S("m_proj"), 1)
            act_mlstm_gates(act, steps)
            act.wait_ge(*at_count("pads", 2))
            for t in range(R_TILES):
                act.wait_ge(*at_count("unit_done", at[("unit", "r", t)]))
                act.activation(x_in(t), bank[at[("r", t)]][:, :], ACT.Copy).then_inc(S("r_proj"), 1)
                if t == 11:
                    act_q_k(act)
            act_mlstm(act, steps)
            act_rwkv(act, steps)
            for k in range(KD):
                act.wait_ge(*at_count("x_mix", k + 1))
                act_square(act, "norm_ffn", k)
            act_std(act, "norm_ffn")
            act_shift(act, "norm_ffn", SH_F)
            act_moe(act, steps)
            for k in range(KD):
                act.wait_ge(*at_count("x_moe", k + 1))
                act_square(act, "norm_out", k)
            act_std(act, "norm_out")
            for k in range(KD):
                act.wait_ge(*at_count("norm_out_h", k + 1))
                act.dma_start(x_kept_d[:, k * T:k * T + T], xT[:, k, :]).then_inc(S("x_kept"), 16)
                act_square(act, "norm_mix2", k)
            act_std(act, "norm_mix2")
            act.wait_ge(*at_count("x_kept", 16 * KD))
            act_shift_split(act, "norm_mix2", SH_2, mix_h_hi_r)
            act_mix2(act, steps)
            for k in range(KD):
                act.wait_ge(*at_count("x_mix2", k + 1))
                act_square(act, "norm_ffn2", k)
            act_std(act, "norm_ffn2")
            act_shift_split(act, "norm_ffn2", SH_3, ffn_h_hi_r)
            act_ffn2(act, steps)
            for k in range(KD):
                act.wait_ge(*at_count("x_ffn2", k + 1))
                act_square(act, "norm_out2", k)
            act_std(act, "norm_out2")

        @block.vector
        def _(dve):
            steps = Steps(dve, S("vector_step"))
            dve.wait_ge(*at_count("columns_landed", 16))
            for i, name in enumerate(("mlstm_i_b", "mlstm_f_b")):
                dve.tensor_scalar(m_small[0:MH, i:i + 1], column(name, rows=MH), 1 / CAP, None, ALU.mult).then_inc(S("gate_bias"), 1)

            def modulate(tiles):
                for i in tiles:
                    dve.wait_ge(*at_count(f"mod_landed{i % MOD_RING}", 16 * (i // MOD_RING + 1)))
                    if i in (0, 48):
                        dve.wait_ge(*at_count("silu_c", 1 + i // 48))
                    w = mod_ring[:, i % MOD_RING, :]
                    dve.tensor_tensor_reduce(w, w, silu_c[:, i // 48, :], 1.0, 0.0, ALU.mult, ALU.add,
                                             accum_out=mod[:, i:i + 1]).then_inc(S("mod_used"), 1)
                lo, hi = tiles[0], tiles[-1] + 1
                dve.wait_ge(*at_count("mod_used", hi))
                dve.tensor_tensor(mod[:, lo:hi], mod[:, lo:hi], col[:, COL["ada_b"] + lo:COL["ada_b"] + hi], ALU.add).then_inc(S("mod"), 1)

            modulate(range(MOD_EARLY))
            dve.wait_ge(*at_count("mod", 1))
            dve_norm(dve, steps, "norm_mix", "mix_norm_w", SC_M)
            dve_lower(dve, "norm_mix", SH_M, in_h_hi_r)
            modulate(range(MOD_EARLY, MODS))
            dve_mlstm(dve, steps)
            dve_rwkv(dve, steps)
            dve.wait_ge(*at_count("mod", 2))
            for n in range(KD):
                dve.wait_ge(*at_count("unit_done", at[("unit", "w_out", n)]))
                dve.scalar_tensor_tensor(xT[:, n, :], bank[at[("w_out", n)]][:, :], mod[:, G_M + n:G_M + n + 1], xT[:, n, :],
                                         ALU.mult, ALU.add).then_inc(S("x_mix"), 1)
            dve_norm(dve, steps, "norm_ffn", "ffn_norm_w", SC_F)
            dve_moe(dve, steps)
            dve.wait_ge(*at_count("x_moe", KD))
            dve_norm(dve, steps, "norm_out", "final_norm_w", None, in_place=True)
            dve.wait_ge(*at_count("norm_out_h", KD))
            dve_norm(dve, steps, "norm_mix2", "norm_mix_w_2", SC_2)
            dve_lower(dve, "norm_mix2", SH_2, mix_h_hi_r)
            dve_mix2(dve, steps)
            dve.wait_ge(*at_count("x_mix2", KD))
            dve_norm(dve, steps, "norm_ffn2", "norm_ffn_w_2", SC_3)
            dve_lower(dve, "norm_ffn2", SH_3, ffn_h_hi_r)
            dve_ffn2(dve, steps)
            dve.wait_ge(*at_count("x_ffn2", KD))
            dve_norm(dve, steps, "norm_out2", "final_norm_w_2", None)

        @block.gpsimd
        def _(pool):
            pool.memset(m_proj[:, :, 0:PAD], 0.0).then_inc(S("pads"), 1)
            pool.memset(r_proj[:, :, 0:PAD], 0.0).then_inc(S("pads"), 1)
            pool.wait_ge(*at_count("columns_landed", 16))
            pool_split(pool, 0, M_TILES + R_TILES, 0)
            pool.wait_ge(*at_count("unit_done", M_TILES + R_TILES))
            pool.memset(v_aug[:, :, :, P:2 * P], 1.0).then_inc(S("pads"), 1)
            pool_rwkv(pool)
            pool.wait_ge(*at_count("y_in_done", TT))
            pool_split(pool, M_TILES + R_TILES, KD, M_TILES + R_TILES)
            pool_moe(pool)
            pool.wait_ge(*at_count("smalls_landed", 16))
            pool.tensor_tensor(dt_hi_r[:, :, :], dt_w, column("zero").rearrange("p (a b) -> p a b", a=1).broadcast_to([P, KD, 32]), ALU.add).then_inc(S("dt_hi"), 1)
            pool.wait_ge(*at_count("dt_hi", 1))
            pool.tensor_tensor(dt_lo_r[:, :, :], dt_w, dt_hi_r[:, :, :].bitcast(F32), ALU.subtract).then_inc(S("dt_lo"), 1)
            pool_split(pool, at["first_split"], at["splits"], SPLIT_1)



def _units(w, columns=None):
    w = w if columns is None else w[:, columns]
    k, n = w.shape
    kt = k // P
    units = -(-kt // 8)
    t = w.reshape(kt, P, n // P, P).transpose(2, 1, 0, 3)
    if kt % 8:
        t = np.concatenate([t, np.zeros((n // P, P, units * 8 - kt, P), w.dtype)], axis=2)
    return t.reshape(n // P, P, units, UNIT).transpose(0, 2, 1, 3).reshape(-1, P, UNIT)


def weight_stream(a):
    w_in, w2 = a["w_in"][0], a["w_in_2"][0]
    parts = [_units(w_in, slice(1792, 1792 + 1536)), _units(w_in, slice(0, 1792))]
    parts += [_units(a["w_out"][0])]
    down = a["moe_w_down"][0].reshape(NE, 2, P, D)
    gate, up = ([_units(a[n][0, e]) for e in range(NE)] for n in ("moe_w_gate", "moe_w_up"))
    parts += [gate[0], up[0]]
    for e in range(1, NE):
        parts += [gate[e], up[e], down[e - 1]]
    parts += [down[NE - 1]]
    x0, z0 = 4096, 2048
    for g in range(NG):
        parts += [_units(w2, slice(x0 + 512 * g, x0 + 512 * g + 512)),
                  _units(w2, slice(x0 + 2048 + 128 * g, x0 + 2048 + 128 * g + 128)),
                  _units(w2, slice(x0 + 2560 + 128 * g, x0 + 2560 + 128 * g + 128)),
                  _units(w2, slice(z0 + 512 * g, z0 + 512 * g + 512))]
        ab = [_units(w2, slice(1024 * h + 128 * (2 * g + i), 1024 * h + 128 * (2 * g + i) + 128))
              for i in range(2) for h in range(2)]
        parts += ab
    g0 = x0 + 3072 + 32
    g_conv, g_ssm = _units(w2, slice(g0, g0 + 1024)), _units(w2, slice(g0 + 1024, g0 + 2048))
    conv_out, ssm_out = _units(a["w_conv_out_2"][0]), _units(a["w_ssm_out_2"][0])
    for n in range(KD):
        parts += [g_conv[n:n + 1], conv_out[n:n + 1]]
    for n in range(KD):
        parts += [g_ssm[n:n + 1], ssm_out[2 * n:2 * n + 2]]
    parts += [_units(a["w_out_2"][0])]
    f_in = _units(a["w_ffn_in_2"][0])
    for n in range(F_TILES):
        parts += [f_in[n:n + 1], f_in[F_TILES + n:F_TILES + n + 1]]
    parts += [_units(a["w_ffn_down_2"][0])]
    return np.concatenate(parts)


def modulation_weights(a):
    w = np.concatenate([a["ada_w"][0], a["w_ada_mix_2"][0], a["w_ada_ffn_2"][0]], axis=1)
    return np.ascontiguousarray(w.T).reshape(MODS, P, D)


def column_array(a):
    out = np.zeros((P, NCOL), np.float32)

    def put(name, v):
        v = v.reshape(-1, P).T
        out[:, COL[name]:COL[name] + v.shape[1]] = v

    for name, _ in COLUMNS:
        if name == "d_skip_2":
            put(name, np.repeat(a[name][0], 64))
        elif name in ("mlstm_i_b", "mlstm_f_b"):
            out[:4, COL[name]] = a[name][0]
        elif name in ("dt_bias_2", "a_log_2"):
            out[:8, COL[name]:COL[name] + 4] = a[name][0].reshape(4, 8).T
        elif name.startswith("eps") or name in ("one", "zero"):
            out[:, COL[name]] = {"eps_norm": 1e-6, "eps_gn": 64e-5, "eps_ln": 1e-5, "one": 1.0, "zero": 0.0}[name]
        else:
            put(name, a[name])
    return out


def const_array():
    i = np.arange(P)
    s, t = i[:, None], i[None, :]
    out = np.zeros((P, NCON), np.float32)

    def put(name, v):
        out[:v.shape[0], CON[name]:CON[name] + v.shape[1]] = v

    put("ident", s == t)
    put("ones", np.ones((P, P)))
    same = s // 64 == t // 64
    put("head_ones", same)
    put("same_head", same)
    put("strict64", same & (s < t))
    put("causal64", same & (s <= t))
    put("causal", s <= t)
    put("levels", np.concatenate([(s // (2 << l) == t // (2 << l)) & ((s >> l) % 2 == 0) & ((t >> l) % 2 == 1)
                                  for l in range(6)], axis=1))
    tok = np.arange(T)
    put("reset64", np.broadcast_to(tok % 64 != 0, (P, T)))
    put("reset128", np.broadcast_to(tok % 128 != 0, (P, T)))
    put("sel4", np.concatenate([np.arange(4)[:, None] == h + 0 * t for h in range(4)], axis=1))
    put("token_id", s + P * np.arange(TT))
    put("expert_id", np.broadcast_to(np.arange(NE), (P, NE)))
    put("sel8", np.concatenate([np.arange(8)[:, None] == h + 0 * t for h in range(8)], axis=1))
    put("sel8_pair", np.concatenate([np.arange(8)[:, None] == 2 * j + t // 64 for j in range(4)], axis=1))
    put("rank4", np.broadcast_to(4.0 - np.arange(4), (P, 4)))
    put("rank8", np.broadcast_to(8.0 - np.arange(8), (P, 8)))
    put("half_col", np.stack([i < 64, i >= 64], axis=1))
    return out


def small_array(a):
    out = np.zeros((P, NSMA), np.float32)

    def put(name, v):
        out[:, SMA[name]:SMA[name] + v.shape[1]] = v

    rows = lambda w: w.reshape(KD, P, -1).transpose(1, 0, 2).reshape(P, -1)
    put("gates", rows(a["w_in"][0][:, 3328:]))
    put("router", rows(np.concatenate([a["moe_w_group"][0], a["moe_w_router"][0]], axis=1)))
    put("dt", rows(a["w_in_2"][0][:, 7168:7200]))
    put("lora_up", np.concatenate([a["rwkv_w_up"][0], a["rwkv_a_up"][0]], axis=0))
    put("g_up", a["rwkv_g_up"][0])
    put("router_b", np.broadcast_to(np.concatenate([a["moe_b_group"][0], a["moe_b_router"][0]]), (P, 36)))
    return out


def kernel(**inputs):
    import concourse.bacc as _bacc
    from concourse.bass_utils import run_bass_kernel_spmd as _run

    a = {k: np.asarray(v) for k, v in inputs.items()}
    arrays = {
        "x_dram": np.ascontiguousarray(a["x"][0].reshape(T, KD, P).transpose(2, 1, 0).reshape(P, KD * T)),
        "weights_dram": weight_stream(a),
        "mod_weights_dram": modulation_weights(a),
        "c_dram": np.concatenate([a["c"].reshape(1, D), a["c_2"].reshape(1, D)]),
        "columns_dram": column_array(a),
        "consts_dram": const_array(),
        "smalls_dram": small_array(a),
    }
    nc = _bacc.Bacc("TRN2", target_bir_lowering=False, num_devices=1)
    args = [nc.dram_tensor(n, v.shape, F32, kind="ExternalInput").ap() for n, v in arrays.items()]
    out = nc.dram_tensor("out_dram", (P, KD * T), F32, kind="ExternalOutput").ap()
    combine = nc.dram_tensor("combine_dram", (NE, T), F32, kind="Internal").ap()
    h_rows = nc.dram_tensor("h_dram", (T, D), F32, kind="Internal").ap()
    y_rows = nc.dram_tensor("y_dram", (NE * P, D), F32, kind="Internal").ap()
    x_kept = nc.dram_tensor("x_kept_dram", (P, KD * T), F32, kind="Internal").ap()
    table = nc.dram_tensor("table_dram", (T * NE, 2), mybir.dt.uint32, kind="Internal").ap()
    two_block_program(nc, *args, combine, h_rows, y_rows, table, x_kept, out)
    r = _run(nc, [arrays], core_ids=[0])
    y = r.results[0]["out_dram"]
    return np.ascontiguousarray(np.asarray(y).reshape(P, KD, T).transpose(2, 1, 0)).reshape(1, T, D)
```
